# Optimizing a Trainium2 kernel written in Bass

```python
import math
import jax, jax.numpy as jnp
from jax import lax
import numpy as np

D_MODEL = 1024
BATCH = 1
SEQ = 1024
DEPTH = 1
DEC_BATCH = 8
DEC_SEQ = 4
PAST_LEN = 2048
PAGE_SIZE = 128

D_MIX = D_MODEL
D_A = D_MIX // 2
N_BLK_A = 8
BLK_W_A = D_A // N_BLK_A
CONV_W = 4
RG_C = 8.0
D_B = D_MIX - D_A
HEAD_DIM = 64
N_HEADS_B = D_B // HEAD_DIM
DILATED_CFG = ((128, 1), (512, 4), (2048, 16))
WIN_MAX = max(w for w, _ in DILATED_CFG)
Q_BLK = 128
ROPE_THETA = 10000.0
N_GROUPS = 4
N_EXP_PER_GROUP = 4
N_EXPERTS = N_GROUPS * N_EXP_PER_GROUP
TOP_K_INNER = 2
D_EXPERT = 512
DN_ALPHA = (2.0 * DEPTH) ** 0.25
DN_BETA = (8.0 * DEPTH) ** -0.25
LN_EPS = 1e-5
NEG_INF = -1e30

kernel_name = "hymba_rglru_dilated_hmoe_step"

F32 = jnp.float32

def layer_norm(x, g, b):
    x32 = x.astype(F32)
    mu = x32.mean(-1, keepdims=True)
    var = jnp.square(x32 - mu).mean(-1, keepdims=True)
    return ((x32 - mu) * lax.rsqrt(var + LN_EPS) * g + b).astype(x.dtype)

def rms_norm(y, g):
    y32 = y.astype(F32)
    return (y32 * lax.rsqrt(jnp.square(y32).mean(-1, keepdims=True) + LN_EPS) * g).astype(y.dtype)

def rope(t, pos):
    half = HEAD_DIM // 2
    inv = ROPE_THETA ** (-jnp.arange(half, dtype=F32) * 2.0 / HEAD_DIM)
    ang = pos.astype(F32)[:, None] * inv[None, :]
    cos = jnp.cos(ang)[None, :, None, :]
    sin = jnp.sin(ang)[None, :, None, :]
    t32 = t.astype(F32)
    t1, t2 = t32[..., :half], t32[..., half:]
    return jnp.concatenate([t1 * cos - t2 * sin, t2 * cos + t1 * sin], -1).astype(t.dtype)

def rglru_branch(xa, ga, conv_state, h0, conv_w, conv_b, w_rg_a, b_rg_a, w_rg_x, b_rg_x, rg_lambda):
    b, t, _ = xa.shape
    xp = jnp.concatenate([conv_state.astype(xa.dtype), xa], axis=1)
    xc = conv_b + sum(xp[:, j:j + t] * conv_w[j] for j in range(CONV_W))
    new_conv = xp[:, -(CONV_W - 1):]
    xb = xc.reshape(b, t, N_BLK_A, BLK_W_A)
    r = jax.nn.sigmoid(jnp.einsum('bthi,hij->bthj', xb, w_rg_a, preferred_element_type=F32) + b_rg_a).reshape(b, t, D_A)
    i = jax.nn.sigmoid(jnp.einsum('bthi,hij->bthj', xb, w_rg_x, preferred_element_type=F32) + b_rg_x).reshape(b, t, D_A)
    log_a = -RG_C * r * jax.nn.softplus(-rg_lambda.astype(F32))
    a = jnp.exp(log_a)
    u = jnp.sqrt(-jnp.expm1(2.0 * log_a)) * (i * xc.astype(F32))
    u = u.at[:, 0].add(a[:, 0] * h0.astype(F32))

    def combine(left, right):
        a1, b1 = left
        a2, b2 = right
        return a1 * a2, a2 * b1 + b2

    _, h = lax.associative_scan(combine, (a, u), axis=1)
    y = (h * jax.nn.gelu(ga.astype(F32))).astype(xa.dtype)
    return y, new_conv, h[:, -1]

def dilated_branch_prompt(q, k, v, window, dil):
    b, s, h, hd = q.shape
    n_keys = window // dil
    sd = s // dil
    nb = -(-sd // Q_BLK)
    sp = nb * Q_BLK

    def strided(t):
        return t.reshape(b, sd, dil, h, hd).transpose(0, 2, 1, 3, 4)

    qs = jnp.pad(strided(q), ((0, 0), (0, 0), (0, sp - sd), (0, 0), (0, 0))).reshape(b, dil, nb, Q_BLK, h, hd)

    def kv_blocks(t):
        tp = jnp.pad(strided(t), ((0, 0), (0, 0), (Q_BLK, sp - sd), (0, 0), (0, 0))).reshape(b, dil, nb + 1, Q_BLK, h, hd)
        return jnp.concatenate([tp[:, :, :-1], tp[:, :, 1:]], axis=3)

    kb, vb = kv_blocks(k), kv_blocks(v)
    sc = jnp.einsum('bgnqhd,bgnkhd->bgnhqk', qs, kb, preferred_element_type=F32) * (hd ** -0.5)
    qi = jnp.arange(Q_BLK)
    ki = jnp.arange(2 * Q_BLK)
    dist = Q_BLK + qi[:, None] - ki[None, :]
    band = (dist >= 0) & (dist <= n_keys)
    key_row = jnp.arange(nb)[:, None] * Q_BLK + ki[None, :] - Q_BLK
    mask = band[None] & (key_row >= 0)[:, None, :]
    sc = jnp.where(mask[:, None], sc, NEG_INF)
    m = sc.max(-1)
    p = jnp.exp(sc - m[..., None])
    l = p.sum(-1)
    acc = jnp.einsum('bgnhqk,bgnkhd->bgnqhd', p, vb.astype(F32))

    def unstride_stat(t):
        t = t.transpose(0, 1, 2, 4, 3).reshape(b, dil, sp, h)[:, :, :sd]
        return t.transpose(0, 2, 1, 3).reshape(b, s, h)

    acc = acc.reshape(b, dil, sp, h, hd)[:, :, :sd].transpose(0, 2, 1, 3, 4).reshape(b, s, h, hd)
    return unstride_stat(m), unstride_stat(l), acc

def dilated_branch_sample(q, k_full, v_full, window, dil):
    b, t, h, hd = q.shape
    n_buf = k_full.shape[1] - t
    n_keys = window // dil
    idx = n_buf + jnp.arange(t)[:, None] - dil * jnp.arange(n_keys + 1)[None, :]
    valid = idx >= 0
    idx = jnp.maximum(idx, 0)
    kg = k_full[:, idx]
    vg = v_full[:, idx]
    sc = jnp.einsum('bthd,btkhd->bthk', q, kg, preferred_element_type=F32) * (hd ** -0.5)
    sc = jnp.where(valid[None, :, None, :], sc, NEG_INF)
    m = sc.max(-1)
    p = jnp.exp(sc - m[..., None])
    l = p.sum(-1)
    acc = jnp.einsum('bthk,btkhd->bthd', p, vg.astype(F32))
    return m, l, acc

def merge_branches(stats):
    m = jnp.stack([s[0] for s in stats])
    l = jnp.stack([s[1] for s in stats])
    acc = jnp.stack([s[2] for s in stats])
    w = jnp.exp(m - m.max(0))
    return (w[..., None] * acc).sum(0) / (w * l).sum(0)[..., None]

def hier_moe(u, w_router_group, b_router_group, w_router_expert, b_router_expert, w_exp_gate, w_exp_up, w_exp_down):
    b, t, _ = u.shape
    g_logits = jnp.einsum('btd,dg->btg', u, w_router_group, preferred_element_type=F32) + b_router_group
    g_prob = jax.nn.softmax(g_logits, -1)
    _, g_idx = lax.top_k(g_logits, 1)
    p_group = jnp.take_along_axis(g_prob, g_idx, -1)
    e_logits = jnp.einsum('btd,gde->btge', u, w_router_expert, preferred_element_type=F32) + b_router_expert
    e_logits = jnp.take_along_axis(e_logits, g_idx[..., None], axis=2)[:, :, 0]
    top_v, top_i = lax.top_k(e_logits, TOP_K_INNER)
    w_top = jax.nn.softmax(top_v, -1) * p_group
    expert_id = g_idx * N_EXP_PER_GROUP + top_i
    comb = jnp.sum(jax.nn.one_hot(expert_id, N_EXPERTS, dtype=F32) * w_top[..., None], axis=-2)
    comb = comb.reshape(b, t, N_GROUPS, N_EXP_PER_GROUP).astype(u.dtype)
    wg = w_exp_gate.reshape(N_GROUPS, N_EXP_PER_GROUP, D_MODEL, D_EXPERT)
    wu = w_exp_up.reshape(N_GROUPS, N_EXP_PER_GROUP, D_MODEL, D_EXPERT)
    wd = w_exp_down.reshape(N_GROUPS, N_EXP_PER_GROUP, D_EXPERT, D_MODEL)
    out = jnp.zeros(u.shape, F32)
    for g in range(N_GROUPS):
        hg = jnp.einsum('btd,edf->btef', u, wg[g])
        hu = jnp.einsum('btd,edf->btef', u, wu[g])
        act = jax.nn.silu(hg) * hu * comb[:, :, g, :, None]
        out = out + jnp.einsum('btef,efd->btd', act, wd[g], preferred_element_type=F32)
    return out.astype(u.dtype)

def decoder_layer(x, c, pos, conv_state, h0, k_buf, v_buf, w_ada, b_ada, w_in, conv_w, conv_b,
                  w_rg_a, b_rg_a, w_rg_x, b_rg_x, rg_lambda, g_norm_a, g_norm_b, w_out, ln1_g, ln1_b,
                  w_router_group, b_router_group, w_router_expert, b_router_expert,
                  w_exp_gate, w_exp_up, w_exp_down, ln2_g, ln2_b):
    b, t, _ = x.shape
    mod = jax.nn.silu(c) @ w_ada + b_ada
    sh1, sc1, gt1, sh2, sc2, gt2 = jnp.split(mod[:, None, :], 6, axis=-1)
    u = x * (1 + sc1) + sh1
    proj = u @ w_in
    xa, ga, q, k, v = jnp.split(proj, [D_A, 2 * D_A, 2 * D_A + D_B, 2 * D_A + 2 * D_B], axis=-1)
    y_a, new_conv, h_last = rglru_branch(xa, ga, conv_state, h0, conv_w, conv_b,
                                         w_rg_a, b_rg_a, w_rg_x, b_rg_x, rg_lambda)
    q = rope(q.reshape(b, t, N_HEADS_B, HEAD_DIM), pos)
    k = rope(k.reshape(b, t, N_HEADS_B, HEAD_DIM), pos)
    v = v.reshape(b, t, N_HEADS_B, HEAD_DIM)
    if k_buf is None:
        k_all, v_all = k, v
        stats = [dilated_branch_prompt(q, k, v, w, d) for w, d in DILATED_CFG]
    else:
        k_all = jnp.concatenate([k_buf.astype(k.dtype), k], axis=1)
        v_all = jnp.concatenate([v_buf.astype(v.dtype), v], axis=1)
        stats = [dilated_branch_sample(q, k_all, v_all, w, d) for w, d in DILATED_CFG]
    keep = min(WIN_MAX, k_all.shape[1])
    new_k, new_v = k_all[:, -keep:], v_all[:, -keep:]
    y_b = merge_branches(stats).astype(x.dtype).reshape(b, t, D_B)
    mixed = jnp.concatenate([rms_norm(y_a, g_norm_a), rms_norm(y_b, g_norm_b)], axis=-1) @ w_out
    x = layer_norm(DN_ALPHA * x + gt1 * mixed, ln1_g, ln1_b)
    u2 = x * (1 + sc2) + sh2
    ffn = hier_moe(u2, w_router_group, b_router_group, w_router_expert, b_router_expert,
                   w_exp_gate, w_exp_up, w_exp_down)
    x = layer_norm(DN_ALPHA * x + gt2 * ffn, ln2_g, ln2_b)
    return x, new_conv, h_last, new_k, new_v

def setup_inputs(seed: int = 0) -> dict:
    key = jax.random.key(seed)
    ks = iter(jax.random.split(key, 40))

    def nrm(shape, scale):
        return jax.random.normal(next(ks), shape, F32) * scale

    wb = min(WIN_MAX, PAST_LEN)
    u_a = jax.random.uniform(next(ks), (D_A,), F32, 0.9, 0.999) ** (1.0 / RG_C)
    rg_lambda = jnp.log(u_a) - jnp.log1p(-u_a)
    return {
        "x_prompt": nrm((BATCH, SEQ, D_MODEL), 1.0),
        "x_sample": nrm((DEC_BATCH, DEC_SEQ, D_MODEL), 1.0),
        "state_conv": nrm((DEC_BATCH, CONV_W - 1, D_A), 1.0),
        "state_rglru": nrm((DEC_BATCH, D_A), 0.5),
        "cache_win_k": nrm((DEC_BATCH, wb, N_HEADS_B, HEAD_DIM), 1.0),
        "cache_win_v": nrm((DEC_BATCH, wb, N_HEADS_B, HEAD_DIM), 1.0),
        "c_prompt": nrm((BATCH, D_MODEL), 1.0),
        "c_sample": nrm((DEC_BATCH, D_MODEL), 1.0),
        "w_ada": nrm((D_MODEL, 6 * D_MODEL), D_MODEL ** -0.5),
        "b_ada": nrm((6 * D_MODEL,), 0.02),
        "w_in": nrm((D_MODEL, 2 * D_A + 3 * D_B), D_MODEL ** -0.5),
        "conv_w": nrm((CONV_W, D_A), CONV_W ** -0.5),
        "conv_b": nrm((D_A,), 0.02),
        "w_rg_a": nrm((N_BLK_A, BLK_W_A, BLK_W_A), BLK_W_A ** -0.5),
        "b_rg_a": nrm((N_BLK_A, BLK_W_A), 0.02),
        "w_rg_x": nrm((N_BLK_A, BLK_W_A, BLK_W_A), BLK_W_A ** -0.5),
        "b_rg_x": nrm((N_BLK_A, BLK_W_A), 0.02),
        "rg_lambda": rg_lambda,
        "g_norm_a": 1.0 + nrm((D_A,), 0.02),
        "g_norm_b": 1.0 + nrm((D_B,), 0.02),
        "w_out": nrm((D_MIX, D_MODEL), DN_BETA * D_MIX ** -0.5),
        "ln1_g": 1.0 + nrm((D_MODEL,), 0.02),
        "ln1_b": nrm((D_MODEL,), 0.02),
        "w_router_group": nrm((D_MODEL, N_GROUPS), D_MODEL ** -0.5),
        "b_router_group": nrm((N_GROUPS,), 0.01),
        "w_router_expert": nrm((N_GROUPS, D_MODEL, N_EXP_PER_GROUP), D_MODEL ** -0.5),
        "b_router_expert": nrm((N_GROUPS, N_EXP_PER_GROUP), 0.01),
        "w_exp_gate": nrm((N_EXPERTS, D_MODEL, D_EXPERT), D_MODEL ** -0.5),
        "w_exp_up": nrm((N_EXPERTS, D_MODEL, D_EXPERT), D_MODEL ** -0.5),
        "w_exp_down": nrm((N_EXPERTS, D_EXPERT, D_MODEL), DN_BETA * D_EXPERT ** -0.5),
        "ln2_g": 1.0 + nrm((D_MODEL,), 0.02),
        "ln2_b": nrm((D_MODEL,), 0.02),
    }

def reference(x_prompt, x_sample, state_conv, state_rglru, cache_win_k, cache_win_v, c_prompt, c_sample,
              w_ada, b_ada, w_in, conv_w, conv_b, w_rg_a, b_rg_a, w_rg_x, b_rg_x, rg_lambda,
              g_norm_a, g_norm_b, w_out, ln1_g, ln1_b, w_router_group, b_router_group,
              w_router_expert, b_router_expert, w_exp_gate, w_exp_up, w_exp_down, ln2_g, ln2_b):
    weights = (w_ada, b_ada, w_in, conv_w, conv_b, w_rg_a, b_rg_a, w_rg_x, b_rg_x, rg_lambda,
               g_norm_a, g_norm_b, w_out, ln1_g, ln1_b, w_router_group, b_router_group,
               w_router_expert, b_router_expert, w_exp_gate, w_exp_up, w_exp_down, ln2_g, ln2_b)
    b_p, s_p, _ = x_prompt.shape
    t_s = x_sample.shape[1]
    pos_p = jnp.arange(s_p)
    pos_s = PAST_LEN + jnp.arange(t_s)
    conv0 = jnp.zeros((b_p, CONV_W - 1, D_A), x_prompt.dtype)
    h0 = jnp.zeros((b_p, D_A), F32)
    y_prompt, y_sample = x_prompt, x_sample
    for layer in range(DEPTH):
        y_prompt, conv_p, h_p, k_p, v_p = decoder_layer(
            y_prompt, c_prompt, pos_p, conv0, h0, None, None, *weights)
        y_sample, conv_s, h_s, k_s, v_s = decoder_layer(
            y_sample, c_sample, pos_s, state_conv, state_rglru, cache_win_k, cache_win_v, *weights)
    return (y_prompt, y_sample, conv_p, h_p, k_p, v_p, conv_s, h_s, k_s, v_s)


_drawn_inputs = setup_inputs


def setup_inputs(seed=0):
    import zlib

    import numpy as np

    out = dict(_drawn_inputs(seed))
    spreads = {}
    factors = {'b_rg_a': 8.0,
     'b_rg_x': 8.0,
     'g_norm_a': 8.0,
     'g_norm_b': 8.0,
     'b_router_group': 8.0,
     'b_router_expert': 64.0,
     'ln2_g': 7.646,
     'ln2_b': 8.016}
    for name, (base, spread) in spreads.items():
        noise = np.random.default_rng([zlib.crc32(name.encode()), seed]).standard_normal(out[name].shape)
        drawn = base * np.exp(spread * noise) if base else spread * noise
        out[name] = __import__('jax').numpy.asarray(drawn.astype(out[name].dtype))
    for name, factor in factors.items():
        out[name] = (out[name] * factor).astype(out[name].dtype)
    return out
```

```python
import math
from contextlib import ExitStack

import numpy as np
import concourse.bass as bass
from concourse import mybir

F32 = mybir.dt.float32
I32 = mybir.dt.int32
ALU = mybir.AluOpType
ACT = mybir.ActivationFunctionType
X = mybir.AxisListType.X

P = 128
D = 1024
KD = D // P
SEQ = 1024
NT = SEQ // P
B = 8
TS = 4
NS = B * TS
TOK = SEQ + NS
DA = 512
CT = DA // P
DB = 512
H = 8
HD = 64
PAIRS = H // 2
PAST = 2048
NMOD = 6
NE = 16
NG = 4
FE = 512
KF = FE // P
SLOT_TILES = 2 * TOK // P + NE
ALPHA = 2.0 ** 0.25
EPS = 1e-5
NEG = -1e30
CONVW = 4
NEAR = 512
FARM = (PAST - NEAR) // 16
SKEYS = NEAR + TS * FARM + NS
DEBUG = False


def ds(a, n):
    return bass.ds(a, n)


class Sem:

    def __init__(self, sem, unit=1, credit=0):
        self.sem, self.unit, self.credit = sem, unit, credit

    def at(self, events):
        value = (events + self.credit) * self.unit
        assert not isinstance(value, int) or value > 0, "no wait is needed here"
        return value


class Steps:

    def __init__(self, eng, handle):
        self.eng, self.handle, self.base, self.n = eng, handle, 0, 0

    def after(self, ins):
        self.n += 1
        ins.then_inc(self.handle, 1)
        return ins

    def last(self):
        self.eng.wait_ge(self.handle, self.base + self.n)

    def link(self, ins):
        self.after(ins)
        self.last()

    def enter(self, per):
        self.outer, self.per = self.base + self.n, per

    def round(self, i):
        self.base, self.n = self.outer + i * self.per, 0

    def leave(self, rounds):
        assert self.n == self.per, (self.n, self.per)
        self.base, self.n = self.outer + rounds * self.per, 0


def block_semaphores(nc, ctx):
    taken = []

    def new(name):
        taken.append(nc.alloc_semaphore(name))
        return taken[-1]

    def clear():
        nc.clear_and_free_semaphores(taken)
        nc.all_engine_barrier()

    ctx.callback(clear)
    return new


def program(nc, a, out, dram):
    ctx = ExitStack()
    with ctx:
        def alloc(c):
            return lambda name, shape, dt=F32: c.enter_context(nc.sbuf_tensor(name, shape, dt))

        sb = alloc(ctx)
        ident = sb("ident", [P, P])
        cols = sb("cols", [P, 40])
        modulation(nc, a, dram, ident, cols)
        with ExitStack() as late:
            sbl = alloc(late)
            gelu_in = sbl("gelu_in", [P, CT, TOK])
            ssq = sbl("ssq", [P, NT + 1, CT])
            logits = sbl("logits", [P, NT + 1, NG + NE])
            with ExitStack() as c2:
                sb2 = alloc(c2)
                qT = sb2("qT", [P, PAIRS, TOK])
                kT = sb2("kT", [P, PAIRS, TOK])
                v = sb2("v", [P, NT + 1, DB])
                with ExitStack() as c3:
                    uT = alloc(c3)("uT", [P, KD, TOK])
                    projection(nc, a, out, dram, ident, qT, kT, v, uT)
                    xa = alloc(c3)("xa", [P, CT, CONVW - 1 + SEQ])
                    xs = alloc(c3)("xs", [P, CT, B, CONVW - 1 + TS])
                    branch_in(nc, a, uT, xa, xs, gelu_in)
                    recurrence(nc, a, out, ident, cols, xa, xs, gelu_in, ssq)
                yb = sb2("yb", [P, NT + 1, DB])
                attention(nc, a, out, dram, ident, qT, kT, v, yb)
                sampling(nc, a, ident, qT, kT, v, yb)
                mixing(nc, a, out, dram, ident, cols, gelu_in, yb, ssq, logits)
            with ExitStack() as c4:
                sb4 = alloc(c4)
                route = {
                    "w": sb4("w12", [P, 2, NT + 1]),
                    "slot": sb4("slot_i", [P, 2, NT + 1], I32),
                    "expert": sb4("expert_i", [1, SLOT_TILES], I32),
                    "end": sb4("end_i", [1, NE], I32),
                    "ids": sb4("ids", [P, SLOT_TILES], I32),
                }
                routing(nc, a, out, dram, ident, logits, route)
                experts(nc, a, out, dram, ident, route)
                finish(nc, a, out, dram, route)


def modulation(nc, a, dram, ident, cols):
    NSEQ = 1 + B
    W = 512
    NCH = NMOD * D // W
    RING = 3
    with ExitStack() as ctx:
        new_sem = block_semaphores(nc, ctx)
        sb = lambda n, s, dt=F32: ctx.enter_context(nc.sbuf_tensor(n, s, dt))
        ps = lambda n, s: ctx.enter_context(nc.psum_tensor(n, s, F32))
        crow = sb("crow", [NSEQ, D])
        th = sb("th", [NSEQ, D])
        cs = sb("cs", [NSEQ, D])
        cT = sb("cT", [P, KD, P])
        wring = sb("wring", [P, RING, KD, W])
        brow = sb("brow", [1, NMOD * D])
        ones = sb("ones9", [1, P])
        mod = sb("mod", [NSEQ, NMOD * D])
        rows = sb("rows", [40, P])
        psT = ps("m_psT", [P, KD * NSEQ])
        psR = ps("m_psR", [P, 40])
        psM = ps("m_psM", [P, 2, W])
        s_c = new_sem("m_c")
        s_rows = new_sem("m_rows")
        s_w = [Sem(new_sem(f"m_w{r}"), 16) for r in range(RING)]
        s_th = new_sem("m_th")
        s_v = new_sem("m_v")
        s_pe = new_sem("m_pe")
        s_cT = new_sem("m_cT")
        s_mm = Sem(new_sem("m_mm"), 1, RING)
        s_ev = Sem(new_sem("m_ev"), 1, 2)
        s_out = new_sem("m_out")
        s_ones = new_sem("m_ones")
        block = ctx.enter_context(nc.Block())
        w = a["w_ada"].rearrange("(k p) n -> p k n", p=P)

        @block.sync
        def _(sp):
            sp.dma_start(crow[0:1, :], a["c_prompt"]).then_inc(s_c, 16)
            sp.dma_start(crow[1:NSEQ, :], a["c_sample"]).then_inc(s_c, 16)
            sp.dma_start(ident[:, :], a["k_ident"]).then_inc(s_c, 16)
            sp.dma_start(brow[:, :], a["b_ada"].rearrange("(o n) -> o n", o=1)).then_inc(s_c, 16)
            r = 0
            for name, v in (("conv_w", a["conv_w"].rearrange("j (c p) -> (j c) p", p=P)),
                            ("conv_b", a["conv_b"].rearrange("(c p) -> c p", p=P)),
                            ("b_rg_a", a["b_rg_a"].rearrange("(c h) w -> c (h w)", h=2)),
                            ("b_rg_x", a["b_rg_x"].rearrange("(c h) w -> c (h w)", h=2)),
                            ("rg_lambda", a["rg_lambda"].rearrange("(c p) -> c p", p=P)),
                            ("g_norm_a", a["g_norm_a"].rearrange("(c p) -> c p", p=P)),
                            ("g_norm_b", a["g_norm_b"].rearrange("(c p) -> c p", p=P))):
                n = v.shape[0]
                sp.dma_start(rows[r:r + n, :], v).then_inc(s_rows, 16)
                r += n
            with sp.Fori(0, NCH // RING) as i:
                for r in range(RING):
                    sp.wait_ge(s_mm.sem, s_mm.at(RING * i + r + 1 - RING))
                    sp.dma_start(wring[:, r, :, :], w[:, :, ds((RING * i + r) * W, W)]).then_inc(s_w[r].sem, s_w[r].unit)
            sp.wait_ge(s_ev.sem, s_ev.at(NCH))
            sp.dma_start(dram["mod"], mod[:, :]).then_inc(s_out, 16)
            sp.wait_ge(s_out, 16)

        @block.gpsimd
        def _(pool):
            pool.sem_inc(s_mm.sem, RING)
            pool.sem_inc(s_ev.sem, 2)
            nc.gpsimd.memset(ones[:, :], 1.0).then_inc(s_ones, 1)
            nc.gpsimd.memset(cT[:, :, :], 0.0).then_inc(s_ones, 1)

        @block.scalar
        def _(act):
            act.wait_ge(s_c, 64)
            nc.scalar.activation(th[:, :], crow[:, :], ACT.Tanh, scale=0.5).then_inc(s_th, 1)
            with act.Fori(0, NCH) as i:
                act.wait_ge(s_mm.sem, s_mm.at(i + 1))
                nc.scalar.copy(mod[:, ds(i * W, W)], psM[0:NSEQ, ds(i % 2, 1), :]).then_inc(s_ev.sem, s_ev.unit)

        @block.vector
        def _(v):
            v.wait_ge(s_th, 1)
            nc.vector.scalar_tensor_tensor(out=cs[:, :], in0=th[:, :], scalar=1.0, in1=crow[:, :],
                                           op0=ALU.add, op1=ALU.mult).then_inc(s_v, 1)
            v.wait_ge(s_pe, 1)
            v.wait_ge(s_ones, 2)
            nc.vector.tensor_scalar(cT[:, :, 0:NSEQ], psT[:, :].rearrange("p (k s) -> p k s", k=KD), 0.5, None,
                                    ALU.mult).then_inc(s_cT, 1)
            v.wait_ge(s_pe, 2)
            nc.vector.tensor_copy(cols[:, :], psR[:, :]).then_inc(s_v, 1)

        @block.tensor
        def _(pe):
            pe.wait_ge(s_v, 1)
            for k in range(KD):
                last = nc.tensor.transpose(psT[:, k * NSEQ:(k + 1) * NSEQ], cs[:, k * P:(k + 1) * P],
                                           ident[0:NSEQ, 0:NSEQ])
            last.then_inc(s_pe, 1)
            pe.wait_ge(s_rows, 16 * 7)
            nc.tensor.transpose(psR[:, :], rows[:, :], ident[0:40, 0:40]).then_inc(s_pe, 1)
            pe.wait_ge(s_cT, 1)
            pe.wait_ge(s_ones, 2)
            with pe.Fori(0, NCH // RING) as j:
                for r in range(RING):
                    i = RING * j + r
                    pe.wait_ge(s_w[r].sem, s_w[r].at(j + 1))
                    pe.wait_ge(s_ev.sem, s_ev.at(i - 1))
                    for k in range(KD):
                        nc.tensor.matmul(psM[:, ds(i % 2, 1), :], cT[:, k, :], wring[:, r, k, :], start=(k == 0), stop=False)
                    nc.tensor.matmul(psM[:, ds(i % 2, 1), :], ones[:, :],
                                               brow[:, ds(i * W, W)], start=False, stop=True).then_inc(s_mm.sem, s_mm.unit)


def projection(nc, a, out, dram, ident, qT, kT, v_all, uT):
    with ExitStack() as ctx:
        new_sem = block_semaphores(nc, ctx)
        sb = lambda n, s, dt=F32: ctx.enter_context(nc.sbuf_tensor(n, s, dt))
        ps = lambda n, s: ctx.enter_context(nc.psum_tensor(n, s, F32))
        S = lambda n, unit=1, credit=0: Sem(new_sem(n), unit, credit)
        wq = sb("wqkv", [P, KD, 3 * DB])
        mods = {k: sb(f"mod_{k}", [P, D]) for k in ("sh", "sc")}
        modq = {k: sb(f"mods_{k}", [NS, D]) for k in ("sh", "sc")}
        xt = sb("xt", [P, 2, D])
        ut = xt
        uTs = sb("uTs", [P, 2, KD, P])
        qk = sb("qk", [P, 2, 2, DB])
        rot = sb("rot", [P, 2, 2, DB])
        tmp = sb("tmpr", [P, 2, DB])
        cos = sb("cos", [P, NT + 1, HD // 2])
        sin = sb("sin", [P, NT + 1, HD])
        psT = ps("p_psT", [P, KD, P])
        psQKV = ps("p_qkv", [P, 3, DB])
        psQ = ps("p_qT", [P, 2, PAIRS, P])
        s_in = S("p_in", 16)
        s_wq = S("p_wq", 16)
        s_x = [S(f"p_x{p}", 16) for p in range(2)]
        s_ch = new_sem("p_ch")
        s_u = S("p_u", 1, 2)
        s_uT = S("p_uT", 1, 2)
        s_uTs = S("p_uTs", 1, 1)
        s_big = S("p_big", 1, 2)
        s_qkv = S("p_sqkv", 1)
        s_ev = S("p_ev", 1, 3)
        s_rot = S("p_rot", 1, 4)
        s_qT = S("p_sqT", 1, 4)
        s_qe = S("p_qe", 1, 2)
        s_ko = [S(f"p_ko{p}", 16, 1) for p in range(2)]
        s_out = new_sem("p_out")
        block = ctx.enter_context(nc.Block())
        modrow = dram["mod"]

        @block.gpsimd
        def _(pool):
            for s in (s_u, s_uT, s_uTs, s_big, s_ev, s_rot, s_qT, s_qe):
                pool.sem_inc(s.sem, s.credit)
            for s in s_ko:
                pool.sem_inc(s.sem, 16)

            def tile(t, par, rows):
                pool.wait_ge(s_uTs.sem, s_uTs.at(t + 1))
                nc.gpsimd.tensor_copy(uT[:, :, ds(t * P, rows)], uTs[:, par, :, 0:rows]).then_inc(s_big.sem, s_big.unit)

            with pool.Fori(0, NT // 2) as i:
                for par in range(2):
                    tile(2 * i + par, par, P)
            tile(NT, 0, NS)

        @block.sync
        def _(sp):
            def bcast(j, n, row):
                return modrow[row:row + 1, j * D:(j + 1) * D].to_broadcast([n, D])

            def load(t, par, rows, src):
                sp.wait_ge(s_uT.sem, s_uT.at(t - 1))
                sp.dma_start(xt[0:rows, par, :], src).then_inc(s_x[par].sem, s_x[par].unit)

            for j, k in ((0, "sh"), (1, "sc")):
                sp.dma_start(mods[k][:, :], bcast(j, P, 0)).then_inc(s_in.sem, s_in.unit)
                for b in range(B):
                    sp.dma_start(modq[k][TS * b:TS * (b + 1), :], bcast(j, TS, 1 + b)).then_inc(s_in.sem, s_in.unit)
            sp.dma_start(cos[:, :, :], a["k_cos"]).then_inc(s_in.sem, s_in.unit)
            sp.dma_start(sin[:, :, :], a["k_sin"]).then_inc(s_in.sem, s_in.unit)
            xp = a["x_prompt"].rearrange("o s d -> (o s) d")
            load(0, 0, P, xp[0:P, :])
            load(1, 1, P, xp[P:2 * P, :])
            w = a["w_in"].rearrange("(k p) n -> p k n", p=P)
            for j in range(3):
                sp.dma_start(wq[:, :, j * DB:(j + 1) * DB], w[:, :, 2 * DA + j * DB:2 * DA + (j + 1) * DB]).then_inc(s_wq.sem, s_wq.unit)
            with sp.Fori(1, NT // 2) as i:
                for par in range(2):
                    load(2 * i + par, par, P, xp[ds((2 * i + par) * P, P), :])
            load(NT, 0, NS, a["x_sample"].rearrange("b t d -> (b t) d"))

        @block.scalar
        def _(act):
            def tile(t, par, rows, k_dst, v_dst):
                act.wait_ge(s_uT.sem, s_uT.at(t + 1))
                act.wait_ge(s_big.sem, s_big.at(t - 1))
                nc.scalar.copy(uTs[:, par, :, 0:rows], psT[:, :, 0:rows]).then_inc(s_uTs.sem, s_uTs.unit)
                for j in range(2):
                    act.wait_ge(s_qkv.sem, s_qkv.at(3 * t + j + 1))
                    act.wait_ge(s_rot.sem, s_rot.at(2 * (t - 2) + j + 1))
                    nc.scalar.copy(qk[0:rows, par, j, :], psQKV[0:rows, j, :]).then_inc(s_ev.sem, s_ev.unit)
                act.wait_ge(s_qkv.sem, s_qkv.at(3 * t + 3))
                nc.scalar.copy(v_all[0:rows, ds(t, 1), :], psQKV[0:rows, 2:3, :]).then_inc(s_ev.sem, s_ev.unit)
                for j, dst in enumerate((qT, kT)):
                    act.wait_ge(s_qT.sem, s_qT.at(2 * t + j + 1))
                    nc.scalar.copy(dst[:, :, ds(t * P, rows)], psQ[:, j, :, 0:rows]).then_inc(s_qe.sem, s_qe.unit)
                act.wait_ge(s_rot.sem, s_rot.at(2 * t + 2))
                act.dma_start(k_dst, rot[0:rows, par, 1, :]).then_inc(s_ko[par].sem, s_ko[par].unit)
                act.wait_ge(s_ev.sem, s_ev.at(3 * t + 3))
                act.dma_start(v_dst, v_all[0:rows, ds(t, 1), :]).then_inc(s_out, 16)

            kp, vp = (out[n].rearrange("o s h d -> (o s) (h d)") for n in ("k_p", "v_p"))
            with act.Fori(0, NT // 2) as i:
                for par in range(2):
                    t = 2 * i + par
                    tile(t, par, P, kp[ds(t * P, P), :], vp[ds(t * P, P), :].unsqueeze(1))
            tile(NT, 0, NS, dram["k_new"], dram["v_new"].unsqueeze(1))
            act.wait_ge(s_out, 16 * (NT + 1))
            act.wait_ge(s_ko[0].sem, s_ko[0].at(NT // 2 + 1))
            act.wait_ge(s_ko[1].sem, s_ko[1].at(NT // 2))

        @block.vector
        def _(v):
            st = Steps(v, s_ch)
            v.wait_ge(s_in.sem, s_in.at(20))
            st.after(nc.vector.tensor_scalar(mods["sc"][:, :], mods["sc"][:, :], 1.0, None, ALU.add))
            st.after(nc.vector.tensor_scalar(modq["sc"][:, :], modq["sc"][:, :], 1.0, None, ALU.add))
            st.last()

            def modulate(t, par, rows, m):
                v.wait_ge(s_x[par].sem, s_x[par].at(t // 2 + 1))
                v.wait_ge(s_uT.sem, s_uT.at(t - 1))
                st.link(nc.vector.tensor_tensor(ut[0:rows, par, :], xt[0:rows, par, :], m["sc"][0:rows, :], ALU.mult))
                nc.vector.tensor_tensor(ut[0:rows, par, :], ut[0:rows, par, :], m["sh"][0:rows, :], ALU.add).then_inc(s_u.sem, s_u.unit)

            def rotate(t, par, rows):
                for j in range(2):
                    v.wait_ge(s_ev.sem, s_ev.at(3 * t + j + 1))
                    src = qk[0:rows, par, j, :].rearrange("p (h s e) -> p h s e", s=2, e=HD // 2)
                    o = rot[0:rows, par, j, :].rearrange("p (h s e) -> p h s e", s=2, e=HD // 2)
                    straight = tmp[0:rows, 0, :].rearrange("p (h e) -> p h e", e=HD // 2)
                    crossed = tmp[0:rows, 1, :].rearrange("p (h s e) -> p h s e", s=2, e=HD // 2)
                    c = cos[0:rows, ds(t, 1), :].to_broadcast([rows, 2 * H, HD // 2])
                    st.after(nc.vector.tensor_tensor(straight, qk[0:rows, par, j, :].rearrange("p (h e) -> p h e", e=HD // 2), c, ALU.mult))
                    for s in range(2):
                        sn = sin[0:rows, ds(t, 1), s * HD // 2:(s + 1) * HD // 2].to_broadcast([rows, H, HD // 2])
                        st.after(nc.vector.tensor_tensor(crossed[:, :, s, :], src[:, :, 1 - s, :], sn, ALU.mult))
                    st.last()
                    v.wait_ge(s_qT.sem, s_qT.at(2 * (t - 2) + j + 1))
                    if j == 1:
                        v.wait_ge(s_ko[par].sem, s_ko[par].at(t // 2))
                    nc.vector.tensor_tensor(rot[0:rows, par, j, :], tmp[0:rows, 0, :], tmp[0:rows, 1, :], ALU.add).then_inc(s_rot.sem, s_rot.unit)
                    v.wait_ge(s_rot.sem, s_rot.at(2 * t + j + 1))

            modulate(0, 0, P, mods)
            modulate(1, 1, P, mods)
            rotate(0, 0, P)
            modulate(2, 0, P, mods)
            rotate(1, 1, P)
            modulate(3, 1, P, mods)
            st.enter(14)
            with v.Fori(1, NT // 2 - 1) as i:
                st.round(i - 1)
                for par in range(2):
                    t = 2 * i + par
                    rotate(t, par, P)
                    modulate(t + 2, par, P, mods)
            st.leave(NT // 2 - 2)
            rotate(NT - 2, 0, P)
            modulate(NT, 0, NS, modq)
            rotate(NT - 1, 1, P)
            rotate(NT, 0, NS)

        @block.tensor
        def _(pe):
            def turn(t, par, rows):
                pe.wait_ge(s_u.sem, s_u.at(t + 1))
                pe.wait_ge(s_uTs.sem, s_uTs.at(t))
                for k in range(KD):
                    last = nc.tensor.transpose(psT[:, k, 0:rows], ut[0:rows, par, k * P:(k + 1) * P],
                                               ident[0:rows, 0:rows])
                last.then_inc(s_uT.sem, s_uT.unit)

            def multiply(t, par, rows):
                pe.wait_ge(s_uTs.sem, s_uTs.at(t + 1))
                for j in range(3):
                    pe.wait_ge(s_ev.sem, s_ev.at(3 * (t - 1) + j + 1))
                    for k in range(KD):
                        last = nc.tensor.matmul(psQKV[0:rows, j, :], uTs[:, par, k, 0:rows],
                                                wq[:, k, j * DB:(j + 1) * DB], start=(k == 0), stop=(k == KD - 1))
                    last.then_inc(s_qkv.sem, s_qkv.unit)

            def turn_qk(t, par, rows):
                for j in range(2):
                    pe.wait_ge(s_rot.sem, s_rot.at(2 * t + j + 1))
                    pe.wait_ge(s_qe.sem, s_qe.at(2 * (t - 1) + j + 1))
                    for p in range(PAIRS):
                        last = nc.tensor.transpose(psQ[:, j, p, 0:rows], rot[0:rows, par, j, p * P:(p + 1) * P],
                                                   ident[0:rows, 0:rows])
                    last.then_inc(s_qT.sem, s_qT.unit)

            turn(0, 0, P)
            pe.wait_ge(s_wq.sem, s_wq.at(3))
            with pe.Fori(0, NT // 2) as i:
                for par in range(2):
                    t = 2 * i + par
                    multiply(t, par, P)
                    if par == 0:
                        turn(t + 1, 1, P)
                    turn_qk(t, par, P)
                    if par == 1:
                        pe.wait_ge(s_u.sem, s_u.at(t + 2))
                        pe.wait_ge(s_uTs.sem, s_uTs.at(t + 1))
                        for k in range(KD):
                            last = nc.tensor.transpose(psT[:, k, :], ut[:, 0, k * P:(k + 1) * P], ident[:, :])
                        last.then_inc(s_uT.sem, s_uT.unit)
            multiply(NT, 0, NS)
            turn_qk(NT, 0, NS)


def branch_in(nc, a, uT, xa, xs, ga):
    with ExitStack() as ctx:
        new_sem = block_semaphores(nc, ctx)
        sb = lambda n, s, dt=F32: ctx.enter_context(nc.sbuf_tensor(n, s, dt))
        ps = lambda n, s: ctx.enter_context(nc.psum_tensor(n, s, F32))
        S = lambda n, unit=1, credit=0: Sem(new_sem(n), unit, credit)
        w = sb("w_xg", [P, KD, 2 * DA])
        psP = ps("b_psP", [P, 2, 2, 512])
        psS = ps("b_psS", [P, 2, 512])
        s_w = [S(f"b_w{j}", 16) for j in range(4)]
        s_mm = S("b_mm")
        s_ev = S("b_ev")
        s_es = S("b_es")
        s_z = S("b_z")
        block = ctx.enter_context(nc.Block())
        wi = a["w_in"].rearrange("(k p) n -> p k n", p=P)

        @block.sync
        def _(sp):
            for j in range(4):
                sp.dma_start(w[:, :, j * 256:(j + 1) * 256], wi[:, :, j * 256:(j + 1) * 256]).then_inc(s_w[j].sem, s_w[j].unit)

        @block.gpsimd
        def _(pool):
            nc.gpsimd.memset(xa[:, :, 0:CONVW - 1], 0.0).then_inc(s_z.sem, s_z.unit)

        @block.tensor
        def _(pe):
            for c in range(2 * CT):
                pe.wait_ge(s_w[c // 2].sem, s_w[c // 2].at(1))
                if c >= 2:
                    pe.wait_ge(s_ev.sem, s_ev.at(c - 1))
                if c >= 2:
                    pe.wait_ge(s_es.sem, s_es.at(c - 1))
                for dst, lo, n in ((psP[:, c % 2, 0, :], 0, 512), (psP[:, c % 2, 1, :], 512, 512),
                                   (psS[:, c % 2, 0:NS], SEQ, NS)):
                    for k in range(KD):
                        last = nc.tensor.matmul(dst, w[:, k, c * P:(c + 1) * P], uT[:, k, lo:lo + n],
                                                start=(k == 0), stop=(k == KD - 1))
                last.then_inc(s_mm.sem, s_mm.unit)

        @block.scalar
        def _(act):
            for c in range(2 * CT):
                act.wait_ge(s_mm.sem, s_mm.at(c + 1))
                dst = xa[:, c, CONVW - 1:].rearrange("p (h n) -> p h n", h=2) if c < CT else \
                    ga[:, c - CT, 0:SEQ].rearrange("p (h n) -> p h n", h=2)
                nc.scalar.copy(dst, psP[:, c % 2, :, :]).then_inc(s_ev.sem, s_ev.unit)

        @block.vector
        def _(v):
            for c in range(2 * CT):
                v.wait_ge(s_mm.sem, s_mm.at(c + 1))
                dst = xs[:, c, :, CONVW - 1:] if c < CT else ga[:, c - CT, SEQ:].rearrange("p (b t) -> p b t", t=TS)
                nc.vector.tensor_copy(dst, psS[:, c % 2, 0:NS].rearrange("p (b t) -> p b t", t=TS)).then_inc(s_es.sem, s_es.unit)


def recurrence(nc, a, out, ident, cols, xa, xs, ga, ssq):
    CV, CB, BA, BX, LM = 0, 16, 20, 24, 28
    with ExitStack() as ctx:
        new_sem = block_semaphores(nc, ctx)
        sb = lambda n, s, dt=F32: ctx.enter_context(nc.sbuf_tensor(n, s, dt))
        ps = lambda n, s: ctx.enter_context(nc.psum_tensor(n, s, F32))
        S = lambda n, unit=1, credit=0: Sem(new_sem(n), unit, credit)
        wa = sb("wa", [P, CT, P])
        wx = sb("wx", [P, CT, P])
        st_rows = sb("st_rows", [B * (CONVW - 1) + B, DA])
        h0 = sb("h0", [P, CT, B])
        sm = sb("sm", [P, 10, CT])
        xc = sb("xc", [P, 2, TOK])
        tr = sb("tr", [P, TOK])
        ti = sb("ti", [P, TOK])
        av = sb("av", [P, TOK])
        tl = sb("tl", [P, TOK])
        gg = sb("gg", [P, TOK])
        t2 = sb("t2", [P, TOK])
        hh = sb("hh", [P, TOK])
        sq = sb("sq", [P, TOK])
        NTAIL = B * TS + (CONVW - 1) + 1 + B
        tail = sb("tail", [P, CT, NTAIL])
        tail_rows = sb("tail_rows", [NTAIL, DA])
        one = sb("one_col", [P, 1])
        NSR = B * (CONVW - 1) + B
        psG = ps("r_psG", [P, 2, 3, 512])
        psX = ps("r_psX", [P, 512])
        psQ = ps("r_psQ", [P, 512])
        s_z = S("r_z")
        s_w = S("r_w", 16)
        s_st = S("r_st", 16)
        s_t = S("r_t")
        s_ch = new_sem("r_ch")
        s_xc = S("r_xc")
        s_g = S("r_g")
        s_a = S("r_a")
        s_ga = S("r_ga")
        s_v = S("r_v")
        s_v2 = S("r_v2")
        s_v3 = S("r_v3")
        s_cc = S("r_cc")
        s_sq = S("r_sq")
        s_ss = S("r_ss")
        s_tl = S("r_tl")
        s_tt = S("r_tt")
        s_tr = S("r_tr")
        s_out = new_sem("r_out")
        s_ac = new_sem("r_ac")
        block = ctx.enter_context(nc.Block())
        TAIL_S, TAIL_P, TAIL_HP, TAIL_HS = 0, NS, NS + 3, NS + 4

        @block.gpsimd
        def _(pool):
            nc.gpsimd.memset(wa[:, :, :], 0.0).then_inc(s_z.sem, s_z.unit)
            nc.gpsimd.memset(wx[:, :, :], 0.0).then_inc(s_z.sem, s_z.unit)
            nc.gpsimd.memset(one[:, :], 1.0).then_inc(s_z.sem, s_z.unit)

        @block.sync
        def _(sp):
            sp.dma_start(st_rows[0:B * (CONVW - 1), :], a["state_conv"].rearrange("b j n -> (b j) n")).then_inc(s_st.sem, s_st.unit)
            sp.dma_start(st_rows[B * (CONVW - 1):NSR, :], a["state_rglru"]).then_inc(s_st.sem, s_st.unit)
            sp.wait_ge(s_z.sem, s_z.at(3))
            for w, src in ((wa, a["w_rg_a"]), (wx, a["w_rg_x"])):
                for h in range(2):
                    sp.dma_start(w[h * 64:(h + 1) * 64, :, h * 64:(h + 1) * 64],
                                          src.rearrange("(c h) i j -> h i c j", h=2)[h]).then_inc(s_w.sem, s_w.unit)
            sp.wait_ge(s_tr.sem, s_tr.at(1))
            rows = tail_rows
            for b in range(B):
                sp.dma_start(out["conv_s"][b, :, :], rows[TS * b + 1:TS * b + TS, :]).then_inc(s_out, 16)
            sp.dma_start(out["conv_p"][0, :, :], rows[TAIL_P:TAIL_P + 3, :]).then_inc(s_out, 16)
            sp.dma_start(out["h_p"], rows[TAIL_HP:TAIL_HP + 1, :]).then_inc(s_out, 16)
            sp.dma_start(out["h_s"], rows[TAIL_HS:TAIL_HS + B, :]).then_inc(s_out, 16)
            sp.wait_ge(s_out, 16 * (B + 3))

        @block.tensor
        def _(pe):
            pe.wait_ge(s_st.sem, s_st.at(2))
            for c in range(CT):
                last = nc.tensor.transpose(psX[:, c * NSR:(c + 1) * NSR], st_rows[:, c * P:(c + 1) * P], ident[0:NSR, 0:NSR])
            last.then_inc(s_t.sem, s_t.unit)
            pe.wait_ge(s_w.sem, s_w.at(4))
            for c in range(CT + 1):
                if c < CT:
                    pe.wait_ge(s_xc.sem, s_xc.at(c + 1))
                    if c >= 1:
                        pe.wait_ge(s_a.sem, s_a.at(2 * c))
                    for j, w in enumerate((wa, wx)):
                        for n, lo, m in ((0, 0, 512), (1, 512, 512), (2, 1024, NS)):
                            last = nc.tensor.matmul(psG[:, j, n, 0:m], w[:, c, :], xc[:, c % 2, lo:lo + m], start=True, stop=True)
                        last.then_inc(s_g.sem, s_g.unit)
                if c > 0:
                    pe.wait_ge(s_sq.sem, s_sq.at(c))
                    pe.wait_ge(s_z.sem, s_z.at(3))
                    for t in range(NT + 1):
                        rows = P if t < NT else NS
                        last = nc.tensor.matmul(psQ[0:rows, t * CT + c - 1:t * CT + c], sq[:, t * P:t * P + rows], one[:, :],
                                                start=True, stop=True)
                    last.then_inc(s_ss.sem, s_ss.unit)
            pe.wait_ge(s_tl.sem, s_tl.at(CT))
            for c in range(CT):
                last = nc.tensor.transpose(psX[0:NTAIL, c * P:(c + 1) * P], tail[:, c, :], ident[:, :])
            last.then_inc(s_tt.sem, s_tt.unit)

        @block.scalar
        def _(act):
            nc.scalar.activation(sm[:, 0, :], cols[:, LM:LM + CT], ACT.Abs).then_inc(s_ac, 1)
            act.wait_ge(s_ac, 1)
            nc.scalar.activation(sm[:, 1, :], sm[:, 0, :], ACT.Exp, scale=-1.0).then_inc(s_ac, 1)
            act.wait_ge(s_ac, 2)
            nc.scalar.activation(sm[:, 2, :], sm[:, 1, :], ACT.Ln, bias=1.0).then_inc(s_ac, 1)
            act.wait_ge(s_cc.sem, s_cc.at(1))
            for c in range(CT):
                for j, (dst, b) in enumerate(((tr, 6), (ti, 7))):
                    act.wait_ge(s_g.sem, s_g.at(2 * c + j + 1))
                    if c >= 1:
                        act.wait_ge(s_v.sem, s_v.at(c))
                    nc.scalar.activation(dst[:, 0:SEQ].rearrange("p (h n) -> p h n", h=2), psG[:, j, 0:2, :], ACT.Tanh,
                                         scale=0.5, bias=sm[:, b, c:c + 1]).then_inc(s_ac, 1)
                    nc.scalar.activation(dst[:, SEQ:TOK], psG[:, j, 2, 0:NS], ACT.Tanh,
                                                  scale=0.5, bias=sm[:, b, c:c + 1]).then_inc(s_a.sem, s_a.unit)
                n = 3 + 3 * c
                act.wait_ge(s_ac, n + 2)
                act.wait_ge(s_a.sem, s_a.at(2 * c + 2))
                nc.scalar.activation(av[:, :], tr[:, :], ACT.Exp, scale=sm[:, 4, c:c + 1], bias=sm[:, 4, c:c + 1]).then_inc(s_ga.sem, s_ga.unit)
                nc.scalar.activation(tl[:, :], tr[:, :], ACT.Tanh, scale=sm[:, 5, c:c + 1], bias=sm[:, 5, c:c + 1]).then_inc(s_ga.sem, s_ga.unit)
                act.wait_ge(s_v3.sem, s_v3.at(c + 1))
                nc.scalar.activation(gg[:, :], t2[:, :], ACT.Tanh, scale=math.sqrt(2.0 / math.pi)).then_inc(s_ga.sem, s_ga.unit)
                act.wait_ge(s_v2.sem, s_v2.at(c + 1))
                nc.scalar.activation(tl[:, :], tl[:, :], ACT.Sqrt, scale=0.25).then_inc(s_ga.sem, s_ga.unit)
                act.wait_ge(s_v.sem, s_v.at(c + 1))
                if c >= 1:
                    act.wait_ge(s_ss.sem, s_ss.at(c))
                nc.scalar.activation(sq[:, :], ga[:, c, :], ACT.Square).then_inc(s_sq.sem, s_sq.unit)
                nc.scalar.copy(tail[:, c, TAIL_HP:TAIL_HP + 1], hh[:, SEQ - 1:SEQ]).then_inc(s_ac, 1)
                act.wait_ge(s_ac, n + 3)
                nc.scalar.copy(tail[:, c, TAIL_HS:], hh[:, SEQ:TOK].rearrange("p (b t) -> p b t", t=TS)[:, :, TS - 1]).then_inc(s_tl.sem, s_tl.unit)

        @block.vector
        def _(v):
            st = Steps(v, s_ch)
            v.wait_ge(s_t.sem, s_t.at(1))
            states = psX[:, 0:CT * NSR].rearrange("p (c r) -> p c r", c=CT)
            for c in range(CT):
                st.after(nc.vector.tensor_copy(xs[:, c, :, 0:CONVW - 1], states[:, c, 0:24].rearrange("p (b j) -> p b j", b=B)))
            st.after(nc.vector.tensor_copy(h0[:, :, :], states[:, :, 24:NSR]))
            for c in range(CT):
                st.after(nc.vector.tensor_copy(tail[:, c, 0:NS].rearrange("p (b t) -> p b t", t=TS), xs[:, c, :, CONVW - 1:]))
            st.link(nc.vector.tensor_copy(tail[:, :, TAIL_P:TAIL_P + 3], xa[:, :, SEQ:SEQ + 3]))
            v.wait_ge(s_ac, 3)
            st.link(nc.vector.tensor_scalar(sm[:, 3, :], cols[:, LM:LM + CT], -1.0, 0.0, ALU.mult, ALU.max))
            st.link(nc.vector.tensor_tensor(sm[:, 3, :], sm[:, 3, :], sm[:, 2, :], ALU.add))
            st.after(nc.vector.tensor_scalar(sm[:, 4, :], sm[:, 3, :], -4.0, None, ALU.mult))
            st.after(nc.vector.tensor_scalar(sm[:, 5, :], sm[:, 3, :], 4.0, None, ALU.mult))
            st.after(nc.vector.tensor_scalar(sm[:, 6, :], cols[:, BA:BA + CT], 0.5, None, ALU.mult))
            st.after(nc.vector.tensor_scalar(sm[:, 7, :], cols[:, BX:BX + CT], 0.5, None, ALU.mult))
            st.last()
            nc.vector.tensor_copy(sm[:, 8, :], sm[:, 7, :]).then_inc(s_cc.sem, s_cc.unit)
            for c in range(CT):
                x = xc[:, c % 2, :]
                xq = x[:, SEQ:TOK].rearrange("p (b t) -> p b t", t=TS)
                for j in range(CONVW):
                    wj = cols[:, CV + 4 * j + c:CV + 4 * j + c + 1]
                    src, srq = xa[:, c, j:j + SEQ], xs[:, c, :, j:j + TS]
                    if j == 0:
                        cb = cols[:, CB + c:CB + c + 1]
                        st.after(nc.vector.tensor_scalar(x[:, 0:SEQ], src, wj, cb, ALU.mult, ALU.add))
                        st.link(nc.vector.tensor_scalar(xq, srq, wj, cb, ALU.mult, ALU.add))
                    elif j < CONVW - 1:
                        st.after(nc.vector.scalar_tensor_tensor(out=x[:, 0:SEQ], in0=src, scalar=wj, in1=x[:, 0:SEQ], op0=ALU.mult, op1=ALU.add))
                        st.link(nc.vector.scalar_tensor_tensor(out=xq, in0=srq, scalar=wj, in1=xq, op0=ALU.mult, op1=ALU.add))
                    else:
                        st.link(nc.vector.scalar_tensor_tensor(out=x[:, 0:SEQ], in0=src, scalar=wj, in1=x[:, 0:SEQ], op0=ALU.mult, op1=ALU.add))
                        nc.vector.scalar_tensor_tensor(out=xq, in0=srq, scalar=wj, in1=xq, op0=ALU.mult, op1=ALU.add).then_inc(s_xc.sem, s_xc.unit)
                g = ga[:, c, :]
                if c >= 1:
                    v.wait_ge(s_sq.sem, s_sq.at(c))
                st.link(nc.vector.tensor_tensor(t2[:, :], g, g, ALU.mult))
                st.link(nc.vector.tensor_scalar(t2[:, :], t2[:, :], 0.044715, 1.0, ALU.mult, ALU.add))
                nc.vector.tensor_tensor(t2[:, :], t2[:, :], g, ALU.mult).then_inc(s_v3.sem, s_v3.unit)
                v.wait_ge(s_ga.sem, s_ga.at(4 * c + 2))
                v.wait_ge(s_v3.sem, s_v3.at(c + 1))
                if c >= 1:
                    v.wait_ge(s_tl.sem, s_tl.at(c))
                st.link(nc.vector.tensor_tensor(hh[:, :], av[:, :], av[:, :], ALU.mult))
                nc.vector.scalar_tensor_tensor(out=tl[:, :], in0=hh[:, :], scalar=1.0, in1=tl[:, :], op0=ALU.add, op1=ALU.mult).then_inc(s_v2.sem, s_v2.unit)
                v.wait_ge(s_xc.sem, s_xc.at(c + 1))
                v.wait_ge(s_v2.sem, s_v2.at(c + 1))
                v.wait_ge(s_ga.sem, s_ga.at(4 * c + 3))
                st.after(nc.vector.scalar_tensor_tensor(out=ti[:, :], in0=ti[:, :], scalar=1.0, in1=x, op0=ALU.add, op1=ALU.mult))
                st.after(nc.vector.scalar_tensor_tensor(out=gg[:, :], in0=gg[:, :], scalar=1.0, in1=g, op0=ALU.add, op1=ALU.mult))
                v.wait_ge(s_ga.sem, s_ga.at(4 * c + 4))
                st.last()
                st.link(nc.vector.tensor_tensor(ti[:, :], ti[:, :], tl[:, :], ALU.mult))
                st.after(nc.vector.tensor_tensor_scan(hh[:, 0:SEQ], av[:, 0:SEQ], ti[:, 0:SEQ], 0.0, ALU.mult, ALU.add))
                hq, aq, uq = (z[:, SEQ:TOK].rearrange("p (b t) -> p b t", t=TS) for z in (hh, av, ti))
                for t in range(TS):
                    prev = h0[:, c, :] if t == 0 else hq[:, :, t - 1]
                    st.link(nc.vector.tensor_tensor(hq[:, :, t], aq[:, :, t], prev, ALU.mult))
                    st.link(nc.vector.tensor_tensor(hq[:, :, t], hq[:, :, t], uq[:, :, t], ALU.add))
                nc.vector.scalar_tensor_tensor(out=g, in0=gg[:, :], scalar=0.5, in1=hh[:, :], op0=ALU.mult, op1=ALU.mult).then_inc(s_v.sem, s_v.unit)
                v.wait_ge(s_v.sem, s_v.at(c + 1))
            v.wait_ge(s_ss.sem, s_ss.at(CT))
            st.after(nc.vector.tensor_copy(ssq[:, 0:NT, :], psQ[:, 0:NT * CT].rearrange("p (t c) -> p t c", c=CT)))
            st.after(nc.vector.tensor_copy(ssq[0:NS, NT, :], psQ[0:NS, NT * CT:(NT + 1) * CT]))
            v.wait_ge(s_tt.sem, s_tt.at(1))
            nc.vector.tensor_copy(tail_rows[:, :], psX[0:NTAIL, :]).then_inc(s_tr.sem, s_tr.unit)


def attention(nc, a, out, dram, ident, qT, kT, v_all, yb):
    with ExitStack() as ctx:
        new_sem = block_semaphores(nc, ctx)
        sb = lambda n, s, dt=F32: ctx.enter_context(nc.sbuf_tensor(n, s, dt))
        ps = lambda n, s: ctx.enter_context(nc.psum_tensor(n, s, F32))
        S = lambda n, unit=1, credit=0: Sem(new_sem(n), unit, credit)
        s_pass = new_sem("a_pass")
        bias = sb("bias", [P, SEQ])
        qp = sb("qp", [P, SEQ])
        kp = sb("kp", [P, SEQ])
        lg = sb("lg", [P, 2, SEQ])
        pr = sb("pr", [P, 2, SEQ])
        pT = sb("pT", [P, 2, NT, P])
        mn = sb("mn", [P, 2])
        den = sb("den", [P, 2])
        rden = sb("rden", [P, 2])
        psS = ps("a_psS", [P, 2, SEQ])
        psT = ps("a_psT", [P, 2, 4, P])
        psO = ps("a_psO", [P, 2, 512])
        s_in = S("a_in", 16)
        s_cp = S("a_cp", 16)
        N = 2 * NT
        s_pair = S("a_pair", 1, 0)
        s_s = S("a_s", 1, 2)
        s_lg = S("a_lg", 1, 2)
        s_p = S("a_p", 1, 2)
        s_t = S("a_t", 1, 3)
        s_tc = S("a_tc", 1, 2)
        s_o = S("a_o", 1, 2)
        s_y = S("a_y", 1, 2)
        s_r = S("a_r", 1, 2)
        block = ctx.enter_context(nc.Block())
        halves = [(t + 4) // 4 for _ in range(2) for t in range(NT)]
        before = [sum(halves[:n]) for n in range(N + 1)]
        TB = before[N]
        ck, cv = (a[n].rearrange("b s h d -> b s (h d)") for n in ("cache_win_k", "cache_win_v"))
        ok, ov = (out[n].rearrange("b s h d -> b s (h d)") for n in ("k_s", "v_s"))

        @block.sync
        def _(sp):
            sp.dma_start(bias[:, :], a["k_bias"]).then_inc(s_in.sem, s_in.unit)
            with sp.Fori(0, B) as b:
                for src, dst, new in ((ck, ok, "k_new"), (cv, ov, "v_new")):
                    sp.dma_start(dst[ds(b, 1), 0:PAST - TS, :], src[ds(b, 1), TS:PAST, :]).then_inc(s_cp.sem, s_cp.unit)
                    sp.dma_start(dst[ds(b, 1), PAST - TS:PAST, :],
                                 dram[new].rearrange("(b t) n -> b t n", t=TS)[ds(b, 1), :, :]).then_inc(s_cp.sem, s_cp.unit)
            sp.wait_ge(s_cp.sem, s_cp.at(4 * B))

        @block.gpsimd
        def _(pool):
            for s in (s_s, s_lg, s_p, s_t, s_tc, s_o, s_y, s_r):
                pool.sem_inc(s.sem, s.credit)
            with pool.Fori(0, PAIRS) as p:
                pool.wait_ge(s_s.sem, s_s.at(N * p))
                nc.gpsimd.tensor_copy(qp[:, :], qT[:, ds(p, 1), 0:SEQ])
                nc.gpsimd.tensor_copy(kp[:, :], kT[:, ds(p, 1), 0:SEQ]).then_inc(s_pair.sem, s_pair.unit)

        @block.tensor
        def _(pe):
            with pe.Fori(0, PAIRS) as p:
                def scores(n):
                    hh, t = divmod(n, NT)
                    pe.wait_ge(s_lg.sem, s_lg.at(N * p + n - 1))
                    keys = (t + 1) * P
                    for lo in range(0, keys, 512):
                        m = min(512, keys - lo)
                        last = nc.tensor.matmul(psS[:, n % 2, lo:lo + m], qp[64 * hh:64 * hh + 64, t * P:(t + 1) * P],
                                                kp[64 * hh:64 * hh + 64, lo:lo + m], start=True, stop=True)
                    last.then_inc(s_s.sem, s_s.unit)

                def turn(n):
                    t = n % NT
                    pe.wait_ge(s_p.sem, s_p.at(N * p + n + 1))
                    for half in range(halves[n]):
                        pe.wait_ge(s_tc.sem, s_tc.at(TB * p + before[n] + half - 1))
                        for b in range(4 * half, min(4 * half + 4, t + 1)):
                            last = nc.tensor.transpose(psT[:, (before[n] + half) % 2, b % 4, :], pr[:, n % 2, b * P:(b + 1) * P], ident[:, :])
                        last.then_inc(s_t.sem, s_t.unit)

                def values(n):
                    hh, t = divmod(n, NT)
                    pe.wait_ge(s_tc.sem, s_tc.at(TB * p + before[n + 1]))
                    pe.wait_ge(s_y.sem, s_y.at(N * p + n - 1))
                    for b in range(t + 1):
                        last = nc.tensor.matmul(psO[:, n % 2, 0:HD], pT[:, n % 2, b, :],
                                                v_all[:, b, ds(p * P + hh * HD, HD)], start=(b == 0), stop=(b == t))
                    last.then_inc(s_o.sem, s_o.unit)

                pe.wait_ge(s_pair.sem, s_pair.at(p + 1))
                scores(0)
                for n in range(N):
                    if n + 1 < N:
                        scores(n + 1)
                    turn(n)
                    if n > 0:
                        values(n - 1)
                values(N - 1)

        @block.vector
        def _(v):
            v.wait_ge(s_in.sem, s_in.at(1))
            with v.Fori(0, PAIRS) as p:
                def mask(n):
                    t = n % NT
                    keys = (t + 1) * P
                    v.wait_ge(s_s.sem, s_s.at(N * p + n + 1))
                    v.wait_ge(s_p.sem, s_p.at(N * p + n - 1))
                    v.sem_inc(s_pass, 1)
                    nc.vector.tensor_tensor_reduce(
                        out=lg[:, n % 2, 0:keys], in0=psS[:, n % 2, 0:keys], in1=bias[:, SEQ - keys:SEQ],
                        scale=-0.125, scalar=3e38, op0=ALU.add, op1=ALU.min, accum_out=mn[:, n % 2:n % 2 + 1]).then_inc(s_lg.sem, s_lg.unit)

                def copy_odd(n):
                    for half in range(halves[n]):
                        k = before[n] + half
                        if k % 2 == 1:
                            t = n % NT
                            m = min(4, t + 1 - 4 * half)
                            v.wait_ge(s_t.sem, s_t.at(TB * p + k + 1))
                            v.wait_ge(s_tc.sem, s_tc.at(TB * p + k))
                            v.wait_ge(s_o.sem, s_o.at(N * p + n - 1))
                            nc.vector.tensor_copy(pT[:, n % 2, 4 * half:4 * half + m, :], psT[:, 1, 0:m, :]).then_inc(s_tc.sem, s_tc.unit)

                def write(n):
                    hh, t = divmod(n, NT)
                    v.wait_ge(s_p.sem, s_p.at(N * p + n + 1))
                    nc.vector.reciprocal(rden[:, n % 2:n % 2 + 1], den[:, n % 2:n % 2 + 1]).then_inc(s_r.sem, s_r.unit)
                    v.wait_ge(s_o.sem, s_o.at(N * p + n + 1))
                    v.wait_ge(s_r.sem, s_r.at(N * p + n + 1))
                    nc.vector.tensor_scalar(yb[:, t, ds(p * P + hh * HD, HD)], psO[:, n % 2, 0:HD],
                                                     rden[:, n % 2:n % 2 + 1], None, ALU.mult).then_inc(s_y.sem, s_y.unit)

                mask(0)
                for n in range(N):
                    if n + 1 < N:
                        mask(n + 1)
                    copy_odd(n)
                    if n > 0:
                        write(n - 1)
                write(N - 1)

        @block.scalar
        def _(act):
            with act.Fori(0, PAIRS) as p:
                for n in range(N):
                    t = n % NT
                    keys = (t + 1) * P
                    act.wait_ge(s_lg.sem, s_lg.at(N * p + n + 1))
                    act.wait_ge(s_t.sem, s_t.at(TB * p + (before[n - 1] if n else before[0] - halves[N - 1])))
                    act.wait_ge(s_r.sem, s_r.at(N * p + n - 1))
                    nc.scalar.activation(pr[:, n % 2, 0:keys], lg[:, n % 2, 0:keys], ACT.Exp, scale=-1.0,
                                                  bias=mn[:, n % 2:n % 2 + 1], accum_out=den[:, n % 2:n % 2 + 1]).then_inc(s_p.sem, s_p.unit)
                    for half in range(halves[n]):
                        k = before[n] + half
                        if k % 2 == 0:
                            m = min(4, t + 1 - 4 * half)
                            act.wait_ge(s_t.sem, s_t.at(TB * p + k + 1))
                            act.wait_ge(s_tc.sem, s_tc.at(TB * p + k))
                            act.wait_ge(s_o.sem, s_o.at(N * p + n - 1))
                            nc.scalar.copy(pT[:, n % 2, 4 * half:4 * half + m, :], psT[:, 0, 0:m, :]).then_inc(s_tc.sem, s_tc.unit)


def sampling(nc, a, ident, qT, kT, v_all, yb):
    G = B // 4
    with ExitStack() as ctx:
        new_sem = block_semaphores(nc, ctx)
        sb = lambda n, s, dt=F32: ctx.enter_context(nc.sbuf_tensor(n, s, dt))
        ps = lambda n, s: ctx.enter_context(nc.psum_tensor(n, s, F32))
        S = lambda n, unit=1, credit=0: Sem(new_sem(n), unit, credit)
        s_pass = new_sem("s_pass")
        KT_ = 8
        kt = sb("s_kt", [P, KT_, DB])
        vt = sb("s_vt", [P, 4, KT_, DB])
        kTs = sb("s_kTs", [P, PAIRS, SKEYS - NS])
        qz = sb("s_qz", [P, B, PAIRS, NS])
        qst = sb("s_qst", [P, PAIRS, NS])
        bias = sb("s_bias", [P, SKEYS])
        lg = sb("s_lg", [P, SKEYS])
        pr = lg
        pT = sb("s_pT", [P, KT_ + 1, P])
        own = sb("s_own", [P, DB])
        om = sb("s_om", [P, DB])
        sel = sb("s_sel", [P, G, NS])
        selst = sb("s_selst", [P, NS])
        mn = sb("s_mn", [P, 1])
        den = sb("s_den", [P, 1])
        rden = sb("s_rden", [P, 1])
        psK = ps("s_psK", [P, 2, PAIRS, P])
        psS = ps("s_psS", [P, 2, 512])
        psP = ps("s_psP", [P, 2, 4, P])
        psO = ps("s_psO", [P, DB])
        psY = ps("s_psY", [P, DB])
        s_in = S("s_in", 16)
        s_b = S("s_b", 16)
        s_k = [S(f"s_k{j}", 16) for j in range(2)]

        s_v = S("s_v", 16)
        s_z = S("s_z")
        s_q = S("s_q")
        s_qs = S("s_qs", 1, 1)
        s_tp = S("s_tp", 1, KT_ + 1)
        s_tc = S("s_tc", 1, 2)
        s_sc = S("s_sc", 1, 1)
        s_lg = S("s_slg", 1, 1)
        s_pr = S("s_spr", 1, 1)
        s_pt = S("s_pt", 1, 2)
        s_pc = S("s_pc", 1, 2)
        s_o = S("s_o", 1, 1)
        s_sel = S("s_ssel", 1, 1)
        s_r = S("s_r", 1)
        s_om = S("s_om", 1, 1)
        s_y = S("s_sy", 1, 1)
        s_yy = S("s_syy", 1, 1)
        block = ctx.enter_context(nc.Block())
        near = [P] * 4 + [FARM] * 4
        at = [0, P, 2 * P, 3 * P] + [NEAR + FARM * i for i in range(4)]

        @block.gpsimd
        def _(pool):
            for s in (s_qs, s_tp, s_tc, s_sc, s_lg, s_pr, s_pt, s_pc, s_o, s_sel, s_om, s_y, s_yy):
                pool.sem_inc(s.sem, s.credit)
            nc.gpsimd.memset(qz[:, :, :, :], 0.0).then_inc(s_z.sem, s_z.unit)
            nc.gpsimd.memset(yb[:, NT, :], 0.0).then_inc(s_z.sem, s_z.unit)
            pool.wait_ge(s_q.sem, s_q.at(1))
            with pool.Fori(0, G) as g:
                for c in range(4):
                    pool.wait_ge(s_sc.sem, s_sc.at(4 * g + c))
                    nc.gpsimd.tensor_copy(qst[:, :, :], qz[:, ds(4 * g + c, 1), :, :]).then_inc(s_qs.sem, s_qs.unit)
                pool.wait_ge(s_y.sem, s_y.at(g))
                pool.wait_ge(s_in.sem, s_in.at(2))
                nc.gpsimd.tensor_copy(selst[:, :], sel[:, ds(g, 1), :]).then_inc(s_sel.sem, s_sel.unit)

        @block.sync
        def _(sp):
            sp.dma_start(own[:, :], a["k_own"]).then_inc(s_in.sem, s_in.unit)
            sp.dma_start(sel[:, :, :], a["k_sel"]).then_inc(s_in.sem, s_in.unit)

            def load(cache, b, dst, s, far_free=None):
                rows = cache[ds(b, 1), :, :, :].rearrange("o s h d -> (o s) (h d)")
                sp.dma_start(dst[:, 0:4, :], rows[PAST - NEAR:PAST, :].rearrange("(p i) n -> p i n", i=4)).then_inc(s[0].sem, s[0].unit)
                if far_free is not None:
                    sp.wait_ge(s_tp.sem, s_tp.at(far_free))
                    sp.sem_inc(s_pass, 1)
                sp.dma_start(dst[0:FARM, 4:8, :], rows[0:PAST - NEAR, :].rearrange("(m i) n -> m i n", i=16)[:, 0:4, :]).then_inc(s[1].sem, s[1].unit)

            with sp.Fori(0, G) as g:
                sp.wait_ge(s_lg.sem, s_lg.at(g))
                sp.dma_start(bias[:, :], a["k_sbias"][:, ds(g, 1), :].rearrange("p o n -> p (o n)")).then_inc(s_b.sem, s_b.unit)
                for c in range(4):
                    sp.wait_ge(s_tp.sem, s_tp.at(KT_ * (4 * g + c - 1) + 4))
                    sp.sem_inc(s_pass, 1)
                    load(a["cache_win_k"], 4 * g + c, kt, s_k, KT_ * (4 * g + c))
                    if c == 0:
                        sp.wait_ge(s_o.sem, s_o.at(g))
                        sp.sem_inc(s_pass, 1)
                    load(a["cache_win_v"], 4 * g + c, vt[:, c, :, :], (s_v, s_v))

        @block.tensor
        def _(pe):
            with pe.Fori(0, G) as g:
                for c in range(4):
                    for i in range(KT_):
                        if i % 4 == 0:
                            pe.wait_ge(s_k[i // 4].sem, s_k[i // 4].at(4 * g + c + 1))
                        n = KT_ * (4 * g + c) + i
                        pe.wait_ge(s_tc.sem, s_tc.at(n - 1))
                        for p in range(PAIRS):
                            last = nc.tensor.transpose(psK[:, i % 2, p, 0:near[i]], kt[0:near[i], i, p * P:(p + 1) * P],
                                                       ident[0:near[i], 0:near[i]])
                        last.then_inc(s_tp.sem, s_tp.unit)
                    pe.wait_ge(s_tc.sem, s_tc.at(KT_ * (4 * g + c) + KT_))
                    pe.wait_ge(s_qs.sem, s_qs.at(4 * g + c + 1))
                    if c == 0:
                        pe.wait_ge(s_lg.sem, s_lg.at(g))
                    for lo, n, src in ((0, 512, kTs[:, :, 0:512]), (512, 384, kTs[:, :, 512:896]), (896, NS, kT[:, :, SEQ:TOK])):
                        for p in range(PAIRS):
                            last = nc.tensor.matmul(psS[NS * c:NS * (c + 1), lo // 512, lo % 512:lo % 512 + n], qst[:, p, :], src[:, p, :],
                                                    start=(p == 0), stop=(p == PAIRS - 1))
                    last.then_inc(s_sc.sem, s_sc.unit)
                pe.wait_ge(s_pr.sem, s_pr.at(g + 1))
                keys = near + [NS]
                start = at + [SKEYS - NS]
                for r, tiles in enumerate(((0, 1, 2, 3), (4, 5, 6, 7), (8,))):
                    pe.wait_ge(s_pc.sem, s_pc.at(3 * g + max(0, r - 1)))
                    for j, i in enumerate(tiles):
                        last = nc.tensor.transpose(psP[0:keys[i], r % 2, j, :],
                                                   pr[:, start[i]:start[i] + keys[i]], ident[:, :])
                    last.then_inc(s_pt.sem, s_pt.unit)
                pe.wait_ge(s_pc.sem, s_pc.at(3 * g + 3))
                pe.wait_ge(s_v.sem, s_v.at(8 * g + 8))
                pe.wait_ge(s_om.sem, s_om.at(g))
                for c in range(4):
                    for i in range(KT_ + 1):
                        rhs = vt[0:keys[i], c, i, :] if i < KT_ else v_all[0:NS, NT, :]
                        last = nc.tensor.matmul(psO[NS * c:NS * (c + 1), :], pT[0:keys[i], i, NS * c:NS * (c + 1)], rhs,
                                                start=(i == 0), stop=(i == KT_))
                last.then_inc(s_o.sem, s_o.unit)
                pe.wait_ge(s_om.sem, s_om.at(g + 1))
                pe.wait_ge(s_sel.sem, s_sel.at(g + 1))
                pe.wait_ge(s_yy.sem, s_yy.at(g))
                nc.tensor.matmul(psY[0:NS, :], selst[:, :], om[:, :], start=True, stop=True).then_inc(s_y.sem, s_y.unit)

        @block.scalar
        def _(act):
            with act.Fori(0, G) as g:
                for c in range(4):
                    for i in range(1, KT_, 2):
                        n = KT_ * (4 * g + c) + i
                        act.wait_ge(s_tp.sem, s_tp.at(n + 1))
                        act.wait_ge(s_tc.sem, s_tc.at(n))
                        act.wait_ge(s_sc.sem, s_sc.at(4 * g + c))
                        nc.scalar.copy(kTs[:, :, at[i]:at[i] + near[i]], psK[:, i % 2, :, 0:near[i]]).then_inc(s_tc.sem, s_tc.unit)
                act.wait_ge(s_lg.sem, s_lg.at(g + 1))
                act.wait_ge(s_pt.sem, s_pt.at(3 * g))
                nc.scalar.activation(pr[:, :], lg[:, :], ACT.Exp, scale=-1.0, bias=mn[:, :], accum_out=den[:, :]).then_inc(s_pr.sem, s_pr.unit)
                act.wait_ge(s_pt.sem, s_pt.at(3 * g + 2))
                act.wait_ge(s_pc.sem, s_pc.at(3 * g + 1))
                act.wait_ge(s_o.sem, s_o.at(g))
                nc.scalar.copy(pT[0:FARM, 4:8, :], psP[0:FARM, 1, :, :]).then_inc(s_pc.sem, s_pc.unit)

        @block.vector
        def _(v):
            v.wait_ge(s_z.sem, s_z.at(2))
            for p in range(PAIRS):
                for hh in range(2):
                    part = slice(64 * hh, 64 * hh + 64)
                    h = 2 * p + hh
                    last = nc.vector.tensor_copy(qz[part, :, p, TS * h:TS * (h + 1)],
                                                 qT[part, p, SEQ:TOK].rearrange("p (b t) -> p b t", t=TS))
            last.then_inc(s_q.sem, s_q.unit)
            v.wait_ge(s_in.sem, s_in.at(2))
            with v.Fori(0, G) as g:
                for c in range(4):
                    for i in range(0, KT_, 2):
                        n = KT_ * (4 * g + c) + i
                        v.wait_ge(s_tp.sem, s_tp.at(n + 1))
                        v.wait_ge(s_tc.sem, s_tc.at(n))
                        v.wait_ge(s_sc.sem, s_sc.at(4 * g + c))
                        nc.vector.tensor_copy(kTs[:, :, at[i]:at[i] + near[i]], psK[:, i % 2, :, 0:near[i]]).then_inc(s_tc.sem, s_tc.unit)
                v.wait_ge(s_sc.sem, s_sc.at(4 * g + 4))
                v.wait_ge(s_pt.sem, s_pt.at(3 * g))
                v.wait_ge(s_b.sem, s_b.at(g + 1))
                v.sem_inc(s_pass, 1)
                nc.vector.tensor_tensor_reduce(
                    out=lg[:, :], in0=psS[:, :, :].rearrange("p a n -> p (a n)")[:, 0:SKEYS], in1=bias[:, :],
                    scale=-0.125, scalar=3e38, op0=ALU.add, op1=ALU.min, accum_out=mn[:, :]).then_inc(s_lg.sem, s_lg.unit)
                v.wait_ge(s_pt.sem, s_pt.at(3 * g + 1))
                v.wait_ge(s_pc.sem, s_pc.at(3 * g))
                v.wait_ge(s_o.sem, s_o.at(g))
                nc.vector.tensor_copy(pT[:, 0:4, :], psP[:, 0, :, :]).then_inc(s_pc.sem, s_pc.unit)
                v.wait_ge(s_pt.sem, s_pt.at(3 * g + 3))
                v.wait_ge(s_pc.sem, s_pc.at(3 * g + 2))
                nc.vector.tensor_copy(pT[0:NS, 8, :], psP[0:NS, 0, 0, :]).then_inc(s_pc.sem, s_pc.unit)
                nc.vector.reciprocal(rden[:, :], den[:, :]).then_inc(s_r.sem, s_r.unit)
                v.wait_ge(s_r.sem, s_r.at(g + 1))
                v.wait_ge(s_o.sem, s_o.at(g + 1))
                v.wait_ge(s_y.sem, s_y.at(g))
                nc.vector.scalar_tensor_tensor(out=om[:, :], in0=psO[:, :], scalar=rden[:, :], in1=own[:, :],
                                                         op0=ALU.mult, op1=ALU.mult).then_inc(s_om.sem, s_om.unit)
                v.wait_ge(s_y.sem, s_y.at(g + 1))
                v.wait_ge(s_yy.sem, s_yy.at(g))
                nc.vector.tensor_tensor(yb[0:NS, NT, :], yb[0:NS, NT, :], psY[0:NS, :], ALU.add).then_inc(s_yy.sem, s_yy.unit)


def mixing(nc, a, out, dram, ident, cols, ya, yb, ssq, logits):
    GA, GB = 32, 36
    with ExitStack() as ctx:
        new_sem = block_semaphores(nc, ctx)
        sb = lambda n, s, dt=F32: ctx.enter_context(nc.sbuf_tensor(n, s, dt))
        ps = lambda n, s: ctx.enter_context(nc.psum_tensor(n, s, F32))
        S = lambda n, unit=1, credit=0: Sem(new_sem(n), unit, credit)
        s_pass = new_sem("x_pass")
        wo = sb("wo", [P, 2 * CT, D])
        names = {"gt1": 2, "sh2": 3, "sc2": 4}
        mods = {k: sb(f"x_{k}", [P, D]) for k in names}
        modq = {k: sb(f"xs_{k}", [NS, D]) for k in names}
        lng = sb("x_lng", [P, D])
        lnb = sb("x_lnb", [P, D])
        wr = sb("x_wr", [P, KD, NG + NE])
        br = sb("x_br", [P, NG + NE])
        yas = sb("x_yas", [P, 2, CT, P])
        ybs = sb("x_ybs", [P, 2, DB])
        ybT = sb("x_ybT", [P, CT, P])
        xt = sb("x_xt", [P, 2, D])
        tb = sb("x_tb", [P, D])
        z = sb("x_z", [P, 2, D])
        x1 = sb("x_x1", [P, 2, D])
        u2 = sb("x_u2", [P, 2, D])
        u2T = sb("x_u2T", [P, KD, P])
        sqd = sb("x_sqd", [P, DB])
        rab = sb("x_rab", [P, 2, NT + 1])
        half = sb("x_half", [P, 2 * (NT + 1)])
        stt = sb("x_st", [P, 2, 6])
        mv = sb("x_mv", [P, 2])
        rs = sb("x_rs", [P, 1])
        mv9 = sb("x_ssb", [P, NT + 1])
        psA = ps("x_psA", [P, 2, 512])
        psB = ps("x_psB", [P, 2, 512])
        psY = ps("x_psY", [P, CT, P])
        psU = ps("x_psU", [P, KD, P])
        psL = ps("x_psL", [P, 512])
        s_w = [S(f"x_w{j}", 16) for j in range(2)]
        s_c = S("x_c", 16)
        s_x = [S(f"x_xt{p}", 16) for p in range(2)]
        s_z0 = S("x_z0")
        s_ss = S("x_ss")
        s_rab = S("x_rab")
        s_sqd = new_sem("x_sqd")
        s_ws = S("x_ws")
        s_ya = S("x_ya", 1)
        s_yt = S("x_yt", 1, 1)
        s_ye = S("x_ye", 1, 1)
        s_mb = S("x_mb")
        s_mm = S("x_mm", 1, 2)
        s_tb = S("x_tb", 1, 1)
        s_z = S("x_z", 1, 2)
        s_ch = new_sem("x_ch")
        s_gain = S("x_gain")
        s_var = S("x_var", 1)
        s_rs = S("x_rs", 1)
        s_xn = S("x_xn", 1, 2)
        s_x1 = S("x_x1", 1, 2)
        s_u2 = S("x_u2", 1, 2)
        s_ut = S("x_ut", 1, 2)
        s_ue = S("x_ue", 1, 1)
        s_l = S("x_l", 1, 1)
        s_lo = S("x_lo", 1, 1)
        s_o1 = [S(f"x_o1{p}", 16, 1) for p in range(2)]
        s_o2 = [S(f"x_o2{p}", 16, 1) for p in range(2)]
        block = ctx.enter_context(nc.Block())
        modrow = dram["mod"]
        xp = a["x_prompt"].rearrange("o s d -> (o s) d")
        xsm = a["x_sample"].rearrange("b t d -> (b t) d")

        @block.sync
        def _(sp):
            w = a["w_out"].rearrange("(k p) n -> p k n", p=P)
            for j in (1, 0):
                sp.dma_start(wo[:, j * CT:(j + 1) * CT, :], w[:, j * CT:(j + 1) * CT, :]).then_inc(s_w[j].sem, s_w[j].unit)
            sp.dma_start(wr[:, :, 0:NG], a["w_router_group"].rearrange("(k p) g -> p k g", p=P)).then_inc(s_c.sem, s_c.unit)
            for g in range(NG):
                sp.dma_start(wr[:, :, NG + 4 * g:NG + 4 * g + 4], a["w_router_expert"][g].rearrange("(k p) e -> p k e", p=P)).then_inc(s_c.sem, s_c.unit)
            sp.dma_start(br[:, 0:NG], a["b_router_group"].rearrange("(o n) -> o n", o=1).to_broadcast([P, NG])).then_inc(s_c.sem, s_c.unit)
            sp.dma_start(br[:, NG:], a["b_router_expert"].rearrange("(o g) e -> o (g e)", o=1).to_broadcast([P, NE])).then_inc(s_c.sem, s_c.unit)
            sp.dma_start(lng[:, :], a["ln1_g"].rearrange("(o n) -> o n", o=1).to_broadcast([P, D])).then_inc(s_c.sem, s_c.unit)
            sp.dma_start(lnb[:, :], a["ln1_b"].rearrange("(o n) -> o n", o=1).to_broadcast([P, D])).then_inc(s_c.sem, s_c.unit)
            for k, j in names.items():
                sp.dma_start(mods[k][:, :], modrow[0:1, j * D:(j + 1) * D].to_broadcast([P, D])).then_inc(s_c.sem, s_c.unit)
                for b in range(B):
                    sp.dma_start(modq[k][TS * b:TS * (b + 1), :], modrow[1 + b:2 + b, j * D:(j + 1) * D].to_broadcast([TS, D])).then_inc(s_c.sem, s_c.unit)

            def load(t, par, rows):
                sp.wait_ge(s_z.sem, s_z.at(t - 1))
                sp.dma_start(xt[0:rows, par, :], xp[ds(t * P, P), :] if rows == P else xsm).then_inc(s_x[par].sem, s_x[par].unit)

            def store(t, par, rows):
                sp.wait_ge(s_x1.sem, s_x1.at(t + 1))
                sp.dma_start(dram["x1"][ds(t * P, rows), :], x1[0:rows, par, :]).then_inc(s_o1[par].sem, s_o1[par].unit)
                sp.wait_ge(s_u2.sem, s_u2.at(t + 1))
                sp.dma_start(dram["u2"][ds(t * P, rows), :], u2[0:rows, par, :]).then_inc(s_o2[par].sem, s_o2[par].unit)

            load(0, 0, P)
            load(1, 1, P)
            with sp.Fori(0, NT // 2 - 1) as i:
                for par in range(2):
                    load(2 * i + par + 2, par, P)
                    store(2 * i + par, par, P)
            load(NT, 0, NS)
            store(NT - 2, 0, P)
            store(NT - 1, 1, P)
            store(NT, 0, NS)
            for s in (s_o1, s_o2):
                sp.wait_ge(s[0].sem, s[0].at(NT // 2 + 1))
                sp.wait_ge(s[1].sem, s[1].at(NT // 2))

        NC = 9 + 3 * (1 + B)

        @block.gpsimd
        def _(pool):
            for s in (s_yt, s_ye, s_mm, s_tb, s_z, s_xn, s_x1, s_u2, s_ut, s_ue, s_l, s_lo):
                pool.sem_inc(s.sem, s.credit)
            for s in (*s_o1, *s_o2):
                pool.sem_inc(s.sem, 16)
            nc.gpsimd.memset(half[:, :], -0.5).then_inc(s_z0.sem, s_z0.unit)
            nc.gpsimd.memset(logits[:, NT, :], 0.0).then_inc(s_z0.sem, s_z0.unit)
            pool.wait_ge(s_ss.sem, s_ss.at(2))
            pool.wait_ge(s_z0.sem, s_z0.at(1))
            nc.gpsimd.tensor_tensor(rab[:, :, :].rearrange("p a t -> p (a t)"), rab[:, :, :].rearrange("p a t -> p (a t)"),
                                               half[:, :], ALU.pow).then_inc(s_rab.sem, s_rab.unit)
            pool.wait_ge(s_c.sem, s_c.at(NC))

            def tile(t, par, rows):
                pool.wait_ge(s_var.sem, s_var.at(t + 1))
                nc.gpsimd.tensor_tensor(rs[0:rows, :], mv[0:rows, 1:2], half[0:rows, 0:1], ALU.pow).then_inc(s_rs.sem, s_rs.unit)
                pool.wait_ge(s_xn.sem, s_xn.at(t + 1))
                pool.wait_ge(s_o1[par].sem, s_o1[par].at(t // 2))
                pool.wait_ge(s_u2.sem, s_u2.at(t - 1))
                nc.gpsimd.tensor_tensor(x1[0:rows, par, :], z[0:rows, par, :], lng[0:rows, :], ALU.mult).then_inc(s_gain.sem, s_gain.unit)
                pool.wait_ge(s_gain.sem, s_gain.at(t + 1))
                nc.gpsimd.tensor_tensor(x1[0:rows, par, :], x1[0:rows, par, :], lnb[0:rows, :], ALU.add).then_inc(s_x1.sem, s_x1.unit)

            with pool.Fori(0, NT // 2) as i:
                for par in range(2):
                    tile(2 * i + par, par, P)
            tile(NT, 0, NS)

        @block.vector
        def _(v):
            st = Steps(v, s_ch)
            v.wait_ge(s_c.sem, s_c.at(NC))
            st.after(nc.vector.memset(rab[:, :, NT], 1.0))
            v.wait_ge(s_ss.sem, s_ss.at(1))
            st.last()
            st.link(nc.vector.tensor_reduce(rab[:, 0, 0:NT], ssq[:, 0:NT, :], X, ALU.add))
            st.link(nc.vector.tensor_reduce(rab[0:NS, 0, NT:NT + 1], ssq[0:NS, NT, :], X, ALU.add))
            st.after(nc.vector.tensor_copy(rab[:, 1, 0:NT], mv9[:, 0:NT]))
            st.link(nc.vector.tensor_copy(rab[0:NS, 1, NT:NT + 1], mv9[0:NS, NT:NT + 1]))
            nc.vector.tensor_scalar(rab[:, :, :], rab[:, :, :], 1.0 / DA, EPS, ALU.mult, ALU.add).then_inc(s_ss.sem, s_ss.unit)
            for j in (1, 0):
                v.wait_ge(s_w[j].sem, s_w[j].at(1))
                for k in range(j * CT, (j + 1) * CT):
                    last = nc.vector.tensor_scalar(wo[:, k, :], wo[:, k, :], cols[:, GA + k:GA + k + 1], None, ALU.mult)
                last.then_inc(s_ws.sem, s_ws.unit)
            st.after(nc.vector.tensor_scalar(mods["sc2"][:, :], mods["sc2"][:, :], 1.0, None, ALU.add))
            st.link(nc.vector.tensor_scalar(modq["sc2"][:, :], modq["sc2"][:, :], 1.0, None, ALU.add))
            v.wait_ge(s_rab.sem, s_rab.at(1))

            def residual(t, par, rows):
                m = mods if rows == P else modq
                v.wait_ge(s_mm.sem, s_mm.at(t + 1))
                v.wait_ge(s_tb.sem, s_tb.at(t + 1))
                v.wait_ge(s_x1.sem, s_x1.at(t - 1))
                zt = z[0:rows, par, :]
                st.link(nc.vector.scalar_tensor_tensor(out=zt, in0=psA[0:rows, :, :].rearrange("p a n -> p (a n)"),
                                                       scalar=rab[0:rows, 0, ds(t, 1)], in1=tb[0:rows, :], op0=ALU.mult, op1=ALU.add))
                st.link(nc.vector.tensor_tensor(zt, zt, m["gt1"][0:rows, :], ALU.mult))
                v.wait_ge(s_x[par].sem, s_x[par].at(t // 2 + 1))
                nc.vector.scalar_tensor_tensor(out=zt, in0=xt[0:rows, par, :], scalar=ALPHA, in1=zt, op0=ALU.mult, op1=ALU.add).then_inc(s_z.sem, s_z.unit)
                v.wait_ge(s_z.sem, s_z.at(t + 1))
                for j in range(2):
                    st.after(nc.vector.bn_stats(stt[0:rows, j, :], z[0:rows, par, j * 512:(j + 1) * 512]))
                st.last()
                v.sem_inc(s_pass, 1)
                st.link(nc.vector.bn_aggr(mv[0:rows, :], stt[0:rows, :, :]))
                nc.vector.tensor_scalar(mv[0:rows, 1:2], mv[0:rows, 1:2], EPS, None, ALU.add).then_inc(s_var.sem, s_var.unit)

            def normalize(t, par, rows):
                v.wait_ge(s_rs.sem, s_rs.at(t + 1))
                nc.vector.tensor_scalar(z[0:rows, par, :], z[0:rows, par, :], mv[0:rows, 0:1], rs[0:rows, :], ALU.subtract, ALU.mult).then_inc(s_xn.sem, s_xn.unit)

            def modulate(t, par, rows):
                m = mods if rows == P else modq
                v.wait_ge(s_x1.sem, s_x1.at(t + 1))
                v.wait_ge(s_o2[par].sem, s_o2[par].at(t // 2))
                v.wait_ge(s_ut.sem, s_ut.at(t - 1))
                st.link(nc.vector.tensor_tensor(u2[0:rows, par, :], x1[0:rows, par, :], m["sc2"][0:rows, :], ALU.mult))
                nc.vector.tensor_tensor(u2[0:rows, par, :], u2[0:rows, par, :], m["sh2"][0:rows, :], ALU.add).then_inc(s_u2.sem, s_u2.unit)

            def route(t, rows):
                v.wait_ge(s_l.sem, s_l.at(t + 1))
                nc.vector.tensor_tensor(logits[0:rows, ds(t, 1), :], psL[0:rows, 0:NG + NE].unsqueeze(1), br[0:rows, :].unsqueeze(1), ALU.add).then_inc(s_lo.sem, s_lo.unit)

            def step(t, par, rows):
                residual(t, par, rows)
                modulate(t - 1, 1 - par, P)
                normalize(t, par, rows)
                route(t - 2, P)

            residual(0, 0, P)
            normalize(0, 0, P)
            residual(1, 1, P)
            modulate(0, 0, P)
            normalize(1, 1, P)
            st.enter(12)
            with v.Fori(1, NT // 2) as i:
                st.round(i - 1)
                for par in range(2):
                    step(2 * i + par, par, P)
            st.leave(NT // 2 - 1)
            step(NT, 0, NS)
            modulate(NT, 0, NS)
            route(NT - 1, P)
            route(NT, NS)

        @block.scalar
        def _(act):
            for t in range(NT + 1):
                rows = P if t < NT else NS
                nc.scalar.activation(sqd[0:rows, :], yb[0:rows, t, :], ACT.Square,
                                     accum_out=mv9[0:rows, t:t + 1]).then_inc(s_sqd, 1)
                act.wait_ge(s_sqd, t + 1)
            nc.scalar.copy(sqd[0:1, 0:1], mv9[0:1, 0:1]).then_inc(s_ss.sem, s_ss.unit)

            def stage(t, par, rows):
                act.wait_ge(s_mm.sem, s_mm.at(t - 1))
                nc.scalar.copy(ybs[0:rows, par, :], yb[0:rows, ds(t, 1), :])
                nc.scalar.copy(yas[:, par, :, 0:rows], ya[:, :, ds(t * P, rows)]).then_inc(s_ya.sem, s_ya.unit)

            def turned_y(t, rows):
                act.wait_ge(s_yt.sem, s_yt.at(t + 1))
                nc.scalar.copy(ybT[:, :, 0:rows], psY[:, :, 0:rows]).then_inc(s_ye.sem, s_ye.unit)

            def scaled(t, rows):
                act.wait_ge(s_mb.sem, s_mb.at(t + 1))
                act.wait_ge(s_z.sem, s_z.at(t))
                nc.scalar.activation(tb[0:rows, :], psB[0:rows, :, :].rearrange("p a n -> p (a n)"), ACT.Copy,
                                               scale=rab[0:rows, 1, ds(t, 1)]).then_inc(s_tb.sem, s_tb.unit)

            def turned_u(t, rows):
                act.wait_ge(s_ut.sem, s_ut.at(t + 1))
                act.wait_ge(s_l.sem, s_l.at(t))
                nc.scalar.copy(u2T[:, :, 0:rows], psU[:, :, 0:rows]).then_inc(s_ue.sem, s_ue.unit)

            stage(0, 0, P)
            stage(1, 1, P)
            turned_y(0, P)
            act.wait_ge(s_rab.sem, s_rab.at(1))
            for t in range(2):
                scaled(t, P)
                turned_y(t + 1, P)
                stage(t + 2, t, P)
            with act.Fori(1, NT // 2 - 1) as i:
                for par in range(2):
                    t = 2 * i + par
                    scaled(t, P)
                    turned_y(t + 1, P)
                    turned_u(t - 2, P)
                    stage(t + 2, par, P)
            scaled(NT - 2, P)
            turned_y(NT - 1, P)
            turned_u(NT - 4, P)
            stage(NT, 0, NS)
            scaled(NT - 1, P)
            turned_y(NT, NS)
            turned_u(NT - 3, P)
            scaled(NT, NS)
            turned_u(NT - 2, P)
            turned_u(NT - 1, P)
            turned_u(NT, NS)

        @block.tensor
        def _(pe):
            def turn_y(t, par, rows):
                pe.wait_ge(s_ya.sem, s_ya.at(t + 1))
                pe.wait_ge(s_ye.sem, s_ye.at(t))
                for k in range(CT):
                    last = nc.tensor.transpose(psY[:, k, 0:rows], ybs[0:rows, par, k * P:(k + 1) * P], ident[0:rows, 0:rows])
                last.then_inc(s_yt.sem, s_yt.unit)

            def product_b(t, rows):
                pe.wait_ge(s_ye.sem, s_ye.at(t + 1))
                pe.wait_ge(s_tb.sem, s_tb.at(t))
                for n in range(2):
                    for k in range(CT):
                        last = nc.tensor.matmul(psB[0:rows, n, :], ybT[:, k, 0:rows], wo[:, CT + k, n * 512:(n + 1) * 512],
                                                start=(k == 0), stop=(k == CT - 1))
                last.then_inc(s_mb.sem, s_mb.unit)

            def product_a(t, par, rows):
                pe.wait_ge(s_z.sem, s_z.at(t))
                for n in range(2):
                    for k in range(CT):
                        last = nc.tensor.matmul(psA[0:rows, n, :], yas[:, par, k, 0:rows], wo[:, k, n * 512:(n + 1) * 512],
                                                start=(k == 0), stop=(k == CT - 1))
                last.then_inc(s_mm.sem, s_mm.unit)

            def turn_u(t, par, rows):
                pe.wait_ge(s_u2.sem, s_u2.at(t + 1))
                pe.wait_ge(s_ue.sem, s_ue.at(t))
                for k in range(KD):
                    last = nc.tensor.transpose(psU[:, k, 0:rows], u2[0:rows, par, k * P:(k + 1) * P], ident[0:rows, 0:rows])
                last.then_inc(s_ut.sem, s_ut.unit)

            def router(t, rows):
                pe.wait_ge(s_ue.sem, s_ue.at(t + 1))
                pe.wait_ge(s_lo.sem, s_lo.at(t))
                for k in range(KD):
                    last = nc.tensor.matmul(psL[0:rows, 0:NG + NE], u2T[:, k, 0:rows], wr[:, k, :], start=(k == 0), stop=(k == KD - 1))
                last.then_inc(s_l.sem, s_l.unit)

            turn_y(0, 0, P)
            pe.wait_ge(s_ws.sem, s_ws.at(1))
            product_b(0, P)
            turn_y(1, 1, P)
            pe.wait_ge(s_ws.sem, s_ws.at(2))
            product_a(0, 0, P)
            product_b(1, P)
            turn_y(2, 0, P)
            product_a(1, 1, P)
            pe.wait_ge(s_c.sem, s_c.at(NC))
            with pe.Fori(1, NT // 2 - 1) as i:
                for par in range(2):
                    t = 2 * i + par
                    product_b(t, P)
                    turn_y(t + 1, 1 - par, P)
                    turn_u(t - 2, par, P)
                    product_a(t, par, P)
                    router(t - 2, P)
            product_b(NT - 2, P)
            turn_y(NT - 1, 1, P)
            turn_u(NT - 4, 0, P)
            product_a(NT - 2, 0, P)
            router(NT - 4, P)
            product_b(NT - 1, P)
            turn_y(NT, 0, NS)
            turn_u(NT - 3, 1, P)
            product_a(NT - 1, 1, P)
            router(NT - 3, P)
            product_b(NT, NS)
            turn_u(NT - 2, 0, P)
            product_a(NT, 0, NS)
            router(NT - 2, P)
            turn_u(NT - 1, 1, P)
            router(NT - 1, P)
            turn_u(NT, 0, NS)
            router(NT, NS)


def routing(nc, a, out, dram, ident, logits, route):
    NTT = NT + 1
    with ExitStack() as ctx:
        new_sem = block_semaphores(nc, ctx)
        sb = lambda n, s, dt=F32: ctx.enter_context(nc.sbuf_tensor(n, s, dt))
        ps = lambda n, s: ctx.enter_context(nc.psum_tensor(n, s, F32))
        S = lambda n, unit=1, credit=0: Sem(new_sem(n), unit, credit)
        ranks = sb("ranks", [P, 4])
        valid = sb("valid", [P, NTT])
        before = sb("before", [P, P])
        ones = sb("ones_r", [P, P])
        restart = sb("restart", [P, NE, NTT])
        steps_ = sb("steps", [P, NTT])
        tiles_k = sb("tiles_k", [P, SLOT_TILES])
        tokid = sb("tokid", [P, NTT])
        zero = sb("zero_r", [SLOT_TILES, P])
        m1 = sb("m1", [P, NTT])
        m2 = sb("m2", [P, NTT])
        pg = sb("pg", [P, NTT])
        e1 = sb("e1", [P, NTT])
        r1 = sb("r1", [P, NTT])
        d4 = sb("d4", [P, NTT, 4])
        x4 = sb("x4", [P, NTT, 4])
        oh = sb("oh", [P, 3, NTT, 4])
        sel = sb("rsel", [P, NTT, 4])
        t16 = sb("t16", [P, NTT, 4, 4])
        hot = sb("hot", [P, 2, NTT, NE])
        both = sb("both", [P, NTT, NE])
        tot = sb("tot", [P, NE, NTT])
        base = sb("base", [P, NE, NTT])
        shifted = sb("shifted", [P, NE, NTT])
        count = sb("count", [P, NE])
        cmp = sb("cmp", [P, NE, NTT - 1])
        ntl = sb("ntl", [P, NE])
        one16 = sb("one16", [P, NE])
        end = sb("end_f", [P, NE])
        first = sb("first_f", [P, NE])
        slotE = sb("slotE", [P, NE, NTT])
        pick = sb("pick", [P, NTT, NE])
        slot = sb("slot_f", [P, 2, NTT])
        ek = sb("ek", [P, SLOT_TILES, NE])
        ekr = sb("ekr", [P, SLOT_TILES])
        idrow = sb("idrow", [SLOT_TILES, P])
        psW = ps("o_psW", [P, NTT, NE])
        psC = ps("o_psC", [P, NTT, NE])
        psI = ps("o_psI", [P, SLOT_TILES])
        s_in = S("o_in", 16)
        s_zr = S("o_zr")
        s_z = S("o_z", 16)
        s_ch = new_sem("o_ch")
        s_d = S("o_d")
        s_e = S("o_e")
        s_m = S("o_m")
        s_pe = S("o_pe")
        s_slot = S("o_slot")
        s_sc = S("o_sc", 16)
        s_id = S("o_id", 16)
        s_it = S("o_it")
        block = ctx.enter_context(nc.Block())

        @block.sync
        def _(sp):
            for t, n in ((ranks, "k_ranks"), (valid, "k_valid"), (before, "k_before"), (restart, "k_restart"),
                         (steps_, "k_steps"), (tiles_k, "k_tiles"), (tokid, "k_tokid")):
                sp.dma_start(t[tuple(slice(None) for _ in t.shape)], a[n]).then_inc(s_in.sem, s_in.unit)
            sp.wait_ge(s_zr.sem, s_zr.at(1))
            sp.dma_start(dram["tok"].rearrange("(k p) o -> k (p o)", p=P), zero[:, :]).then_inc(s_z.sem, s_z.unit)
            sp.wait_ge(s_sc.sem, s_sc.at(2 * NTT))
            sp.dma_start(idrow[:, :], dram["tok"].rearrange("(k p) o -> k (p o)", p=P)).then_inc(s_id.sem, s_id.unit)

        @block.gpsimd
        def _(pool):
            nc.gpsimd.memset(zero[:, :], 0.0).then_inc(s_zr.sem, s_zr.unit)
            pool.wait_ge(s_slot.sem, s_slot.at(1))
            pool.wait_ge(s_z.sem, s_z.at(1))
            pool.wait_ge(s_in.sem, s_in.at(7))
            for t in range(NTT):
                rows = P if t < NT else NS
                for k in range(2):
                    nc.gpsimd.indirect_dma_start(
                        out=dram["tok"], out_offset=bass.IndirectOffsetOnAxis(ap=route["slot"][0:rows, k, t:t + 1], axis=0),
                        in_=tokid[0:rows, t:t + 1], in_offset=None).then_inc(s_sc.sem, s_sc.unit)

        @block.scalar
        def _(act):
            act.wait_ge(s_d.sem, s_d.at(1))
            nc.scalar.activation(x4[:, :, :], d4[:, :, :], ACT.Exp).then_inc(s_e.sem, s_e.unit)
            act.wait_ge(s_d.sem, s_d.at(2))
            nc.scalar.activation(e1[:, :], m2[:, :], ACT.Exp).then_inc(s_e.sem, s_e.unit)

        @block.tensor
        def _(pe):
            pe.wait_ge(s_m.sem, s_m.at(1))
            pe.wait_ge(s_in.sem, s_in.at(7))
            nc.tensor.matmul(psW[:, :, :], before[:, :], both[:, :, :], start=True, stop=True)
            nc.tensor.matmul(psC[:, :, :], ones[:, :], both[:, :, :], start=True, stop=True).then_inc(s_pe.sem, s_pe.unit)
            pe.wait_ge(s_id.sem, s_id.at(1))
            nc.tensor.transpose(psI[:, :], idrow[:, :], ident[0:SLOT_TILES, 0:SLOT_TILES]).then_inc(s_it.sem, s_it.unit)

        @block.vector
        def _(v):
            st = Steps(v, s_ch)
            v.wait_ge(s_in.sem, s_in.at(7))
            g = logits[:, :, 0:NG]
            wide = lambda t: t.unsqueeze(2).to_broadcast([P, NTT, 4])
            r4 = ranks[:, :].unsqueeze(1).to_broadcast([P, NTT, 4])

            def first_of_max(src, mx, dst):
                st.link(nc.vector.tensor_reduce(mx, src, X, ALU.max))
                st.link(nc.vector.tensor_tensor(d4[:, :, :], src, wide(mx), ALU.is_equal))
                st.link(nc.vector.tensor_tensor(d4[:, :, :], d4[:, :, :], r4, ALU.mult))
                st.link(nc.vector.tensor_reduce(r1[:, :], d4[:, :, :], X, ALU.max))
                st.link(nc.vector.tensor_tensor(dst, d4[:, :, :], wide(r1[:, :]), ALU.is_equal))

            st.after(nc.vector.memset(ones[:, :], 1.0))
            st.after(nc.vector.memset(one16[:, :], 1.0))
            st.after(nc.vector.memset(shifted[:, :, :], 0.0))
            first_of_max(g, m1[:, :], oh[:, 0, :, :])
            nc.vector.tensor_tensor(d4[:, :, :], g, wide(m1[:, :]), ALU.subtract).then_inc(s_d.sem, s_d.unit)
            v.wait_ge(s_e.sem, s_e.at(1))
            st.link(nc.vector.tensor_reduce(r1[:, :], x4[:, :, :], X, ALU.add))
            st.link(nc.vector.reciprocal(pg[:, :], r1[:, :]))
            le = logits[:, :, NG:].rearrange("p t (g e) -> p t e g", g=NG)
            for e in range(4):
                st.after(nc.vector.tensor_tensor(t16[:, :, e, :], le[:, :, e, :], oh[:, 0, :, :], ALU.mult))
            st.last()
            st.link(nc.vector.tensor_reduce(sel[:, :, :], t16[:, :, :, :], X, ALU.add))
            first_of_max(sel[:, :, :], m1[:, :], oh[:, 1, :, :])
            st.link(nc.vector.scalar_tensor_tensor(out=sel[:, :, :], in0=oh[:, 1, :, :], scalar=NEG, in1=sel[:, :, :], op0=ALU.mult, op1=ALU.add))
            first_of_max(sel[:, :, :], m2[:, :], oh[:, 2, :, :])
            nc.vector.tensor_tensor(m2[:, :], m2[:, :], m1[:, :], ALU.subtract).then_inc(s_d.sem, s_d.unit)
            v.wait_ge(s_e.sem, s_e.at(2))
            st.link(nc.vector.tensor_scalar(r1[:, :], e1[:, :], 1.0, None, ALU.add))
            st.link(nc.vector.reciprocal(r1[:, :], r1[:, :]))
            st.link(nc.vector.tensor_tensor(route["w"][:, 0, :], r1[:, :], pg[:, :], ALU.mult))
            st.after(nc.vector.tensor_tensor(route["w"][:, 1, :], route["w"][:, 0, :], e1[:, :], ALU.mult))
            for k in range(2):
                h4 = hot[:, k, :, :].rearrange("p t (g e) -> p t g e", g=NG)
                for q in range(NG):
                    st.after(nc.vector.tensor_tensor(h4[:, :, q, :], oh[:, 1 + k, :, :],
                                                     oh[:, 0, :, q:q + 1].to_broadcast([P, NTT, 4]), ALU.mult))
            st.last()
            st.link(nc.vector.tensor_tensor(both[:, :, :], hot[:, 0, :, :], hot[:, 1, :, :], ALU.add))
            nc.vector.tensor_tensor(both[:, :, :], both[:, :, :], valid[:, :].unsqueeze(2).to_broadcast([P, NTT, NE]), ALU.mult).then_inc(s_m.sem, s_m.unit)
            v.wait_ge(s_pe.sem, s_pe.at(1))
            st.link(nc.vector.tensor_copy(tot[:, :, :], psC[:, :, :].rearrange("p t e -> p e t")))
            st.link(nc.vector.tensor_copy(shifted[:, :, 1:NTT], tot[:, :, 0:NT]))
            flat = lambda t: t[:, :, :].rearrange("p e t -> p (e t)")
            st.link(nc.vector.tensor_tensor_scan(flat(base), flat(restart), flat(shifted), 0.0, ALU.mult, ALU.add))
            st.link(nc.vector.tensor_tensor(count[:, :], base[:, :, NT], tot[:, :, NT], ALU.add))
            st.link(nc.vector.tensor_tensor(cmp[:, :, :], count[:, :].unsqueeze(2).to_broadcast([P, NE, NT]),
                                            steps_[:, 0:NT].unsqueeze(1).to_broadcast([P, NE, NT]), ALU.is_gt))
            st.link(nc.vector.tensor_reduce(ntl[:, :], cmp[:, :, :], X, ALU.add))
            st.link(nc.vector.tensor_scalar(ntl[:, :], ntl[:, :], 1.0, None, ALU.add))
            st.link(nc.vector.tensor_tensor_scan(end[:, :], one16[:, :], ntl[:, :], 0.0, ALU.mult, ALU.add))
            st.link(nc.vector.tensor_tensor(first[:, :], end[:, :], ntl[:, :], ALU.subtract))
            st.link(nc.vector.tensor_scalar(first[:, :], first[:, :], float(P), None, ALU.mult))
            st.link(nc.vector.tensor_tensor(slotE[:, :, :], psW[:, :, :].rearrange("p t e -> p e t"), base[:, :, :], ALU.add))
            st.link(nc.vector.tensor_tensor(slotE[:, :, :], slotE[:, :, :], first[:, :].unsqueeze(2).to_broadcast([P, NE, NTT]), ALU.add))
            for k in range(2):
                st.link(nc.vector.tensor_tensor(pick[:, :, :], hot[:, k, :, :], slotE[:, :, :].rearrange("p e t -> p t e"), ALU.mult))
                st.link(nc.vector.tensor_reduce(slot[:, k, :], pick[:, :, :], X, ALU.add))
            nc.vector.tensor_copy(route["slot"][:, :, :], slot[:, :, :]).then_inc(s_slot.sem, s_slot.unit)
            st.link(nc.vector.tensor_tensor(ek[:, :, :], end[:, :].unsqueeze(1).to_broadcast([P, SLOT_TILES, NE]),
                                            tiles_k[:, :].unsqueeze(2).to_broadcast([P, SLOT_TILES, NE]), ALU.is_le))
            st.link(nc.vector.tensor_reduce(ekr[:, :], ek[:, :, :], X, ALU.add))
            st.link(nc.vector.tensor_scalar(ekr[:, :], ekr[:, :], float(NE - 1), None, ALU.min))
            st.link(nc.vector.tensor_copy(route["expert"][:, :], ekr[0:1, :]))
            st.link(nc.vector.tensor_copy(route["end"][:, :], end[0:1, :]))
            v.wait_ge(s_it.sem, s_it.at(1))
            st.link(nc.vector.tensor_copy(route["ids"][:, :], psI[:, :]))


def experts(nc, a, out, dram, ident, route):
    with ExitStack() as ctx:
        new_sem = block_semaphores(nc, ctx)
        sb = lambda n, s, dt=F32: ctx.enter_context(nc.sbuf_tensor(n, s, dt))
        ps = lambda n, s: ctx.enter_context(nc.psum_tensor(n, s, F32))
        S = lambda n, unit=1, credit=0: Sem(new_sem(n), unit, credit)
        s_pass = new_sem("e_pass")
        wg = sb("e_wg", [P, 2 * KD, FE])
        wu = sb("e_wu", [P, 2 * KD, FE])
        wd = sb("e_wd", [P, 2 * KF, D])
        ids = sb("e_ids", [P, 2], I32)
        xg = sb("e_x", [P, 2, D])
        xT = sb("e_xT", [P, 2, KD, P])
        th = sb("e_th", [P, FE])
        th2 = sb("e_th2", [P, FE])
        hs = sb("e_h", [P, FE])
        hT = sb("e_hT", [P, 2, KF, P])
        y = sb("e_y", [P, 2, D])
        psT = ps("e_psT", [P, 4, P])
        psG = ps("e_psG", [P, 2, 2, FE])
        psH = ps("e_psH", [P, KF, P])
        psY = ps("e_psY", [P, 2, 512])
        s_gu_w = [S(f"e_wgu{p}", 16, p) for p in range(2)]
        s_d_w = [S(f"e_wd{p}", 16, p) for p in range(2)]
        s_id = S("e_id")
        s_x = [S(f"e_x{p}", 16) for p in range(2)]
        s_t = S("e_t", 1, 4)
        s_tc = S("e_tc", 1, 2)
        s_gu = S("e_gu", 1, 2)
        s_th = S("e_th", 1)
        s_h1 = S("e_h1", 1)
        s_h2 = S("e_h2", 1, 1)
        s_h = S("e_h", 1, 2)
        s_ht = S("e_ht", 1, 1)
        s_hc = S("e_hc", 1, 1)
        s_dn = S("e_dn", 1, 2)
        s_y = S("e_y", 1, 2)
        s_o = [S(f"e_o{p}", 16, 1) for p in range(2)]
        block = ctx.enter_context(nc.Block())

        @block.sync
        def _(sp):
            def load(e, slot):
                sp.dma_start(wg[:, slot * KD:(slot + 1) * KD, :],
                                      a["w_exp_gate"][ds(e, 1), :, :].rearrange("o (k p) f -> p (o k) f", p=P)).then_inc(s_gu_w[slot].sem, s_gu_w[slot].unit)
                sp.dma_start(wu[:, slot * KD:(slot + 1) * KD, :],
                                      a["w_exp_up"][ds(e, 1), :, :].rearrange("o (k p) f -> p (o k) f", p=P)).then_inc(s_gu_w[slot].sem, s_gu_w[slot].unit)
                sp.dma_start(wd[:, slot * KF:(slot + 1) * KF, :],
                                      a["w_exp_down"][ds(e, 1), :, :].rearrange("o (k p) f -> p (o k) f", p=P)).then_inc(s_d_w[slot].sem, s_d_w[slot].unit)

            load(0, 0)
            load(1, 1)
            with sp.Fori(1, NE // 2) as i:
                for slot in range(2):
                    last = sp.value_load(route["end"][0:1, ds(2 * i + slot - 2, 1)], min_val=1, max_val=SLOT_TILES)
                    sp.wait_ge(s_dn.sem, s_dn.at(last))
                    load(2 * i + slot, slot)

        @block.scalar
        def _(act):
            def x_half(t, par, half):
                act.wait_ge(s_t.sem, s_t.at(2 * t + half + 1))
                act.wait_ge(s_gu.sem, s_gu.at(t - 1))
                nc.scalar.copy(xT[:, par, 4 * half:4 * half + 4, :], psT[:, :, :]).then_inc(s_tc.sem, s_tc.unit)

            def tile(t, par):
                act.wait_ge(s_gu.sem, s_gu.at(t + 1))
                act.wait_ge(s_h1.sem, s_h1.at(t))
                nc.scalar.activation(th[:, :], psG[:, par, 0, :], ACT.Tanh, scale=0.5).then_inc(s_th.sem, s_th.unit)
                act.wait_ge(s_ht.sem, s_ht.at(t + 1))
                act.wait_ge(s_dn.sem, s_dn.at(t - 1))
                nc.scalar.copy(hT[:, par, :, :], psH[:, :, :]).then_inc(s_hc.sem, s_hc.unit)
                act.wait_ge(s_dn.sem, s_dn.at(t + 1))
                act.wait_ge(s_o[par].sem, s_o[par].at(t // 2))
                for half in range(2):
                    nc.scalar.copy(y[:, par, half * 512:(half + 1) * 512], psY[:, half, :]).then_inc(s_y.sem, s_y.unit)
                act.wait_ge(s_y.sem, s_y.at(2 * t + 2))
                act.dma_start(dram["y"][ds(t * P, P), :], y[:, par, :]).then_inc(s_o[par].sem, s_o[par].unit)

            x_half(0, 0, 0)
            x_half(0, 0, 1)
            with act.Fori(0, SLOT_TILES // 2 - 1) as i:
                for par in range(2):
                    t = 2 * i + par
                    x_half(t + 1, 1 - par, 0)
                    x_half(t + 1, 1 - par, 1)
                    tile(t, par)
            t = SLOT_TILES - 2
            x_half(t + 1, 1, 0)
            x_half(t + 1, 1, 1)
            tile(t, 0)
            tile(t + 1, 1)
            for p in range(2):
                act.wait_ge(s_o[p].sem, s_o[p].at(SLOT_TILES // 2))

        @block.gpsimd
        def _(pool):
            for s in (s_t, s_tc, s_gu, s_h2, s_h, s_ht, s_hc, s_dn, s_y):
                pool.sem_inc(s.sem, s.credit)
            for s in (*s_o, s_gu_w[1], s_d_w[1]):
                pool.sem_inc(s.sem, 16)
            with pool.Fori(0, SLOT_TILES // 2) as i:
                for par in range(2):
                    t = 2 * i + par
                    pool.wait_ge(s_t.sem, s_t.at(2 * (t - 1)))
                    nc.gpsimd.tensor_copy(ids[:, par:par + 1], route["ids"][:, ds(t, 1)]).then_inc(s_id.sem, s_id.unit)
                    pool.wait_ge(s_id.sem, s_id.at(t + 1))
                    pool.sem_inc(s_pass, 1)
                    nc.gpsimd.indirect_dma_start(
                        out=xg[:, par, :], out_offset=None, in_=dram["u2"],
                        in_offset=bass.IndirectOffsetOnAxis(ap=ids[:, par:par + 1], axis=0)).then_inc(s_x[par].sem, s_x[par].unit)

        @block.vector
        def _(v):
            with v.Fori(0, SLOT_TILES // 2) as i:
                for par in range(2):
                    t = 2 * i + par
                    v.wait_ge(s_th.sem, s_th.at(t + 1))
                    nc.vector.scalar_tensor_tensor(out=th2[:, :], in0=th[:, :], scalar=1.0, in1=psG[:, par, 0, :],
                                                             op0=ALU.add, op1=ALU.mult).then_inc(s_h1.sem, s_h1.unit)
                    v.wait_ge(s_h1.sem, s_h1.at(t + 1))
                    v.wait_ge(s_ht.sem, s_ht.at(t))
                    nc.vector.scalar_tensor_tensor(out=hs[:, :], in0=th2[:, :], scalar=0.5, in1=psG[:, par, 1, :],
                                                            op0=ALU.mult, op1=ALU.mult).then_inc(s_h.sem, s_h.unit)

        @block.tensor
        def _(pe):
            def turn(t, par):
                pe.wait_ge(s_x[par].sem, s_x[par].at(t // 2 + 1))
                for half in range(2):
                    pe.wait_ge(s_tc.sem, s_tc.at(2 * t + half))
                    for b in range(4):
                        k = 4 * half + b
                        last = nc.tensor.transpose(psT[:, b, :], xg[:, par, k * P:(k + 1) * P], ident[:, :])
                    last.then_inc(s_t.sem, s_t.unit)

            def up(t, par):
                e = pe.value_load(route["expert"][0:1, ds(t, 1)], min_val=0, max_val=NE - 1)
                pe.wait_ge(s_gu_w[0].sem, s_gu_w[0].at(2 * ((e + 2) // 2)))
                pe.wait_ge(s_gu_w[1].sem, s_gu_w[1].at(2 * ((e + 1) // 2)))
                pe.wait_ge(s_tc.sem, s_tc.at(2 * t + 2))
                pe.wait_ge(s_h.sem, s_h.at(t - 1))
                for j, w in enumerate((wg, wu)):
                    for k in range(KD):
                        last = nc.tensor.matmul(psG[:, par, j, :], xT[:, par, k, :], w[:, ds((e % 2) * KD + k, 1), :],
                                                start=(k == 0), stop=(k == KD - 1))
                last.then_inc(s_gu.sem, s_gu.unit)

            def down(t, par):
                pe.wait_ge(s_h.sem, s_h.at(t + 1))
                pe.wait_ge(s_hc.sem, s_hc.at(t))
                for k in range(KF):
                    last = nc.tensor.transpose(psH[:, k, :], hs[:, k * P:(k + 1) * P], ident[:, :])
                last.then_inc(s_ht.sem, s_ht.unit)
                e = pe.value_load(route["expert"][0:1, ds(t, 1)], min_val=0, max_val=NE - 1)
                pe.wait_ge(s_d_w[0].sem, s_d_w[0].at((e + 2) // 2))
                pe.wait_ge(s_d_w[1].sem, s_d_w[1].at((e + 1) // 2))
                pe.wait_ge(s_hc.sem, s_hc.at(t + 1))
                pe.wait_ge(s_y.sem, s_y.at(2 * t))
                for n in range(2):
                    for k in range(KF):
                        last = nc.tensor.matmul(psY[:, n, :], hT[:, par, k, :], wd[:, ds((e % 2) * KF + k, 1), n * 512:(n + 1) * 512],
                                                start=(k == 0), stop=(k == KF - 1))
                last.then_inc(s_dn.sem, s_dn.unit)

            turn(0, 0)
            up(0, 0)
            turn(1, 1)
            with pe.Fori(0, SLOT_TILES // 2 - 1) as i:
                for par in range(2):
                    t = 2 * i + par
                    up(t + 1, 1 - par)
                    down(t, par)
                    turn(t + 2, par)
            t = SLOT_TILES - 2
            up(t + 1, 1)
            down(t, 0)
            down(t + 1, 1)


def finish(nc, a, out, dram, route):
    with ExitStack() as ctx:
        new_sem = block_semaphores(nc, ctx)
        sb = lambda n, s, dt=F32: ctx.enter_context(nc.sbuf_tensor(n, s, dt))
        S = lambda n, unit=1, credit=0: Sem(new_sem(n), unit, credit)
        s_pass = new_sem("f_pass")
        gt = sb("f_gt", [P, D])
        gq = sb("f_gq", [NS, D])
        lng = sb("f_lng", [P, D])
        lnb = sb("f_lnb", [P, D])
        idx = sb("f_idx", [P, 2, 2], I32)
        y1 = sb("f_y1", [P, 2, D])
        y2 = sb("f_y2", [P, 2, D])
        x1 = sb("f_x1", [P, 2, D])
        z = sb("f_z", [P, 2, D])
        o = sb("f_o", [P, 2, D])
        stt = sb("f_st", [P, 2, 6])
        mv = sb("f_mv", [P, 2])
        rs = sb("f_rs", [P, 1])
        half = sb("f_half", [P, 1])
        s_c = S("f_c", 16)
        s_h = S("f_h")
        s_ix = S("f_ix")
        s_y = [S(f"f_y{p}", 16) for p in range(2)]
        s_x = [S(f"f_x{p}", 16) for p in range(2)]
        s_ch = new_sem("f_ch")
        s_z = S("f_sz", 1, 2)
        s_var = S("f_var")
        s_rs = S("f_rs")
        s_xn = S("f_xn", 1, 2)
        s_o = S("f_so", 1, 2)
        s_p1 = S("f_p1")
        s_out = [S(f"f_out{p}", 16, 1) for p in range(2)]
        block = ctx.enter_context(nc.Block())
        modrow = dram["mod"]
        J = 5
        yp = out["y_p"].rearrange("o s d -> (o s) d")
        ys = out["y_s"].rearrange("b t d -> (b t) d")

        def each(eng, fn):
            with eng.Fori(0, NT // 2) as i:
                for par in range(2):
                    fn(2 * i + par, par, P)
            fn(NT, 0, NS)

        @block.sync
        def _(sp):
            sp.dma_start(gt[:, :], modrow[0:1, J * D:(J + 1) * D].to_broadcast([P, D])).then_inc(s_c.sem, s_c.unit)
            for b in range(B):
                sp.dma_start(gq[TS * b:TS * (b + 1), :], modrow[1 + b:2 + b, J * D:(J + 1) * D].to_broadcast([TS, D])).then_inc(s_c.sem, s_c.unit)
            sp.dma_start(lng[:, :], a["ln2_g"].rearrange("(o n) -> o n", o=1).to_broadcast([P, D])).then_inc(s_c.sem, s_c.unit)
            sp.dma_start(lnb[:, :], a["ln2_b"].rearrange("(o n) -> o n", o=1).to_broadcast([P, D])).then_inc(s_c.sem, s_c.unit)

            def tile(t, par, rows):
                sp.wait_ge(s_z.sem, s_z.at(t - 1))
                sp.dma_start(x1[0:rows, par, :], dram["x1"][ds(t * P, rows), :]).then_inc(s_x[par].sem, s_x[par].unit)

            each(sp, tile)

        @block.scalar
        def _(act):
            def tile(t, par, rows):
                act.wait_ge(s_o.sem, s_o.at(t + 1))
                act.dma_start(yp[ds(t * P, P), :] if rows == P else ys, o[0:rows, par, :]).then_inc(s_out[par].sem, s_out[par].unit)

            each(act, tile)
            act.wait_ge(s_out[0].sem, s_out[0].at(NT // 2 + 1))
            act.wait_ge(s_out[1].sem, s_out[1].at(NT // 2))

        @block.gpsimd
        def _(pool):
            for s in (s_z, s_xn, s_o):
                pool.sem_inc(s.sem, s.credit)
            for s in s_out:
                pool.sem_inc(s.sem, 16)
            nc.gpsimd.memset(half[:, :], -0.5).then_inc(s_h.sem, s_h.unit)
            pool.wait_ge(s_h.sem, s_h.at(1))

            def fetch(t, par, rows):
                pool.wait_ge(s_z.sem, s_z.at(t - 1))
                nc.gpsimd.tensor_copy(idx[0:rows, par, :], route["slot"][0:rows, :, ds(t, 1)].rearrange("p k o -> p (k o)")).then_inc(s_ix.sem, s_ix.unit)
                pool.wait_ge(s_ix.sem, s_ix.at(t + 1))
                pool.sem_inc(s_pass, 1)
                for k, y in enumerate((y1, y2)):
                    nc.gpsimd.indirect_dma_start(
                        out=y[0:rows, par, :], out_offset=None, in_=dram["y"],
                        in_offset=bass.IndirectOffsetOnAxis(ap=idx[0:rows, par, k:k + 1], axis=0)).then_inc(s_y[par].sem, s_y[par].unit)

            def norm(t, par, rows):
                pool.wait_ge(s_var.sem, s_var.at(t + 1))
                nc.gpsimd.tensor_tensor(rs[0:rows, :], mv[0:rows, 1:2], half[0:rows, :], ALU.pow).then_inc(s_rs.sem, s_rs.unit)
                pool.wait_ge(s_xn.sem, s_xn.at(t + 1))
                pool.wait_ge(s_out[par].sem, s_out[par].at(t // 2))
                nc.gpsimd.tensor_tensor(o[0:rows, par, :], z[0:rows, par, :], lng[0:rows, :], ALU.mult).then_inc(s_p1.sem, s_p1.unit)
                pool.wait_ge(s_p1.sem, s_p1.at(t + 1))
                nc.gpsimd.tensor_tensor(o[0:rows, par, :], o[0:rows, par, :], lnb[0:rows, :], ALU.add).then_inc(s_o.sem, s_o.unit)

            pool.wait_ge(s_c.sem, s_c.at(3 + B))
            fetch(0, 0, P)
            with pool.Fori(0, NT // 2 - 1) as i:
                for par in range(2):
                    fetch(2 * i + par + 1, 1 - par, P)
                    norm(2 * i + par, par, P)
            fetch(NT - 1, 1, P)
            norm(NT - 2, 0, P)
            fetch(NT, 0, NS)
            norm(NT - 1, 1, P)
            norm(NT, 0, NS)

        @block.vector
        def _(v):
            st = Steps(v, s_ch)
            v.wait_ge(s_c.sem, s_c.at(3 + B))

            def tile(t, par, rows):
                zt = z[0:rows, par, :]
                w = route["w"]
                v.wait_ge(s_y[par].sem, s_y[par].at(2 * (t // 2) + 2))
                v.wait_ge(s_o.sem, s_o.at(t - 1))
                st.link(nc.vector.tensor_scalar(zt, y1[0:rows, par, :], w[0:rows, 0, ds(t, 1)], None, ALU.mult))
                st.link(nc.vector.scalar_tensor_tensor(out=zt, in0=y2[0:rows, par, :], scalar=w[0:rows, 1, ds(t, 1)], in1=zt,
                                                       op0=ALU.mult, op1=ALU.add))
                st.link(nc.vector.tensor_tensor(zt, zt, (gt if rows == P else gq)[0:rows, :], ALU.mult))
                v.wait_ge(s_x[par].sem, s_x[par].at(t // 2 + 1))
                nc.vector.scalar_tensor_tensor(out=zt, in0=x1[0:rows, par, :], scalar=ALPHA, in1=zt, op0=ALU.mult, op1=ALU.add).then_inc(s_z.sem, s_z.unit)
                v.wait_ge(s_z.sem, s_z.at(t + 1))
                for j in range(2):
                    st.after(nc.vector.bn_stats(stt[0:rows, j, :], z[0:rows, par, j * 512:(j + 1) * 512]))
                st.last()
                v.sem_inc(s_pass, 1)
                st.link(nc.vector.bn_aggr(mv[0:rows, :], stt[0:rows, :, :]))
                nc.vector.tensor_scalar(mv[0:rows, 1:2], mv[0:rows, 1:2], EPS, None, ALU.add).then_inc(s_var.sem, s_var.unit)
                v.wait_ge(s_rs.sem, s_rs.at(t + 1))
                nc.vector.tensor_scalar(zt, zt, mv[0:rows, 0:1], rs[0:rows, :], ALU.subtract, ALU.mult).then_inc(s_xn.sem, s_xn.unit)

            st.enter(12)
            with v.Fori(0, NT // 2) as i:
                st.round(i)
                for par in range(2):
                    tile(2 * i + par, par, P)
            st.leave(NT // 2)
            tile(NT, 0, NS)


def constants():
    f = np.float32
    k = {"k_ident": np.eye(P, dtype=f)}
    pos = np.zeros((NT + 1, P), f)
    pos[:NT] = np.arange(SEQ, dtype=f).reshape(NT, P)
    pos[NT, :NS] = PAST + np.arange(NS) % TS
    half = HD // 2
    inv = (f(10000.0) ** (-np.arange(half, dtype=f) * f(2.0) / f(HD))).astype(f)
    ang = pos[:, :, None] * inv
    c, s = np.cos(ang).astype(f), np.sin(ang).astype(f)
    k["k_cos"] = np.ascontiguousarray(c.transpose(1, 0, 2))
    k["k_sin"] = np.ascontiguousarray(np.concatenate([-s, s], -1).transpose(1, 0, 2))

    def bias(count):
        return np.where(count > 0, 8.0 * np.log(np.maximum(count, 1)), NEG).astype(f)

    def windows(dist):
        live = dist >= 0
        return live * ((dist <= 128).astype(int) + ((dist % 4 == 0) & (dist <= 512)) + ((dist % 16 == 0) & (dist <= 2048)))

    dist = np.arange(P)[:, None] + (NT - 1) * P - np.arange(SEQ)[None, :]
    k["k_bias"] = bias(windows(dist))
    p = np.arange(P)
    near = np.concatenate([PAST - NEAR + 4 * p + i for i in range(4)])
    far = np.concatenate([16 * np.arange(FARM) + i for i in range(TS)])
    cached = np.concatenate([near, far])
    t = np.arange(P) % TS
    c = np.arange(P) // NS
    sb_ = np.full((P, B // 4, SKEYS), NEG, f)
    for g in range(B // 4):
        sb_[:, g, :SKEYS - NS] = bias(windows(PAST + t[:, None] - cached[None, :]))
        n = np.arange(NS)
        own = n[None, :] // TS == 4 * g + c[:, None]
        sb_[:, g, SKEYS - NS:] = bias(windows(t[:, None] - n[None, :] % TS) * own)
    k["k_sbias"] = sb_
    h = (np.arange(P) % NS) // TS
    k["k_own"] = (h[:, None] == np.arange(DB)[None, :] // HD).astype(f)
    k["k_sel"] = np.stack([(4 * g + c) * TS + t for g in range(B // 4)], 1)[:, :, None] == np.arange(NS)
    k["k_sel"] = k["k_sel"].astype(f)
    k["k_ranks"] = np.tile(np.arange(4, 0, -1, dtype=f), (P, 1))
    valid = np.ones((P, NT + 1), f)
    valid[NS:, NT] = 0
    k["k_valid"] = valid
    k["k_before"] = (p[:, None] < p[None, :]).astype(f)
    restart = np.ones((P, NE, NT + 1), f)
    restart[:, :, 0] = 0
    k["k_restart"] = restart
    k["k_steps"] = np.tile(P * np.arange(1, NT + 2, dtype=f), (P, 1))
    k["k_tiles"] = np.tile(np.arange(SLOT_TILES, dtype=f), (P, 1))
    k["k_tokid"] = (p[:, None] + P * np.arange(NT + 1)[None, :]).astype(f)
    return k


_INS = ["x_prompt", "x_sample", "state_conv", "state_rglru", "cache_win_k", "cache_win_v", "c_prompt", "c_sample",
        "w_ada", "b_ada", "w_in", "conv_w", "conv_b", "w_rg_a", "b_rg_a", "w_rg_x", "b_rg_x", "rg_lambda",
        "g_norm_a", "g_norm_b", "w_out", "ln1_g", "ln1_b", "w_router_group", "b_router_group",
        "w_router_expert", "b_router_expert", "w_exp_gate", "w_exp_up", "w_exp_down", "ln2_g", "ln2_b"]
_OUTS = [("y_p", (1, SEQ, D)), ("y_s", (B, TS, D)), ("conv_p", (1, CONVW - 1, DA)), ("h_p", (1, DA)),
         ("k_p", (1, SEQ, H, HD)), ("v_p", (1, SEQ, H, HD)), ("conv_s", (B, CONVW - 1, DA)), ("h_s", (B, DA)),
         ("k_s", (B, PAST, H, HD)), ("v_s", (B, PAST, H, HD))]
_SCRATCH = [("mod", (1 + B, NMOD * D)), ("x1", (TOK, D)), ("u2", (TOK, D)), ("tok", (SLOT_TILES * P, 1)),
            ("y", (SLOT_TILES * P, D)), ("k_new", (NS, DB)), ("v_new", (NS, DB))]


def kernel(**inputs):
    import concourse.bacc as bacc
    from concourse.bass_utils import run_bass_kernel_spmd

    nc = bacc.Bacc("TRN2", target_bir_lowering=False, num_devices=1)
    arrays = {f"in_{n}": np.ascontiguousarray(inputs[n]) for n in _INS}
    arrays.update({f"in_{n}": v for n, v in constants().items()})
    a = {n[3:]: nc.dram_tensor(n, v.shape, mybir.dt.from_np(v.dtype), kind="ExternalInput").ap() for n, v in arrays.items()}
    out = {n: nc.dram_tensor(f"out_{n}", s, F32, kind="ExternalOutput").ap() for n, s in _OUTS}
    dram = {n: nc.dram_tensor(f"scratch_{n}", s, F32, kind="Internal").ap() for n, s in _SCRATCH}
    program(nc, a, out, dram)
    r = run_bass_kernel_spmd(nc, [arrays], core_ids=[0])
    return tuple(r.results[0][f"out_{n}"] for n, _ in _OUTS)
```

```python
import math
from contextlib import ExitStack

import numpy as np
import concourse.bass as bass
from concourse import mybir

F32 = mybir.dt.float32
I32 = mybir.dt.int32
ALU = mybir.AluOpType
ACT = mybir.ActivationFunctionType
X = mybir.AxisListType.X

P = 128
D = 1024
KD = D // P
SEQ = 1024
NT = SEQ // P
B = 8
TS = 4
NS = B * TS
TOK = SEQ + NS
DA = 512
CT = DA // P
DB = 512
H = 8
HD = 64
PAIRS = H // 2
PAST = 2048
NMOD = 6
NSEQ = 1 + B
MW = 512
NE = 16
NG = 4
FE = 512
KF = FE // P
SLOT_TILES = 2 * TOK // P + NE
ALPHA = 2.0 ** 0.25
EPS = 1e-5
NEG = -1e30
CONVW = 4
NEAR = 512
FARM = (PAST - NEAR) // 16
SKEYS = NEAR + TS * FARM + NS
DEBUG = False


def ds(a, n):
    return bass.ds(a, n)


class Sem:

    def __init__(self, sem, unit=1, credit=0):
        self.sem, self.unit, self.credit = sem, unit, credit

    def at(self, events):
        value = (events + self.credit) * self.unit
        assert not isinstance(value, int) or value > 0, "no wait is needed here"
        return value


class Steps:

    def __init__(self, eng, handle):
        self.eng, self.handle, self.base, self.n = eng, handle, 0, 0

    def after(self, ins):
        self.n += 1
        ins.then_inc(self.handle, 1)
        return ins

    def last(self):
        self.eng.wait_ge(self.handle, self.base + self.n)

    def link(self, ins):
        self.after(ins)
        self.last()

    def enter(self, per):
        self.outer, self.per = self.base + self.n, per

    def round(self, i):
        self.base, self.n = self.outer + i * self.per, 0

    def leave(self, rounds):
        assert self.n == self.per, (self.n, self.per)
        self.base, self.n = self.outer + rounds * self.per, 0


def block_semaphores(nc, ctx):
    taken = []

    def new(name):
        taken.append(nc.alloc_semaphore(name))
        return taken[-1]

    def clear():
        nc.clear_and_free_semaphores(taken)
        nc.all_engine_barrier()

    ctx.callback(clear)
    return new


def program(nc, a, out, dram):
    ctx = ExitStack()
    with ctx:
        def alloc(c):
            return lambda name, shape, dt=F32: c.enter_context(nc.sbuf_tensor(name, shape, dt))

        sb = alloc(ctx)
        ident = sb("ident", [P, P])
        cols = sb("cols", [P, 40])
        silu = sb("silu", [P, KD, NSEQ])
        modulation(nc, a, dram, ident, cols, silu)
        with ExitStack() as late:
            sbl = alloc(late)
            gelu_in = sbl("gelu_in", [P, CT, TOK])
            ssq = sbl("ssq", [P, NT + 1, CT])
            logits = sbl("logits", [P, NT + 1, NG + NE])
            with ExitStack() as c2:
                sb2 = alloc(c2)
                qT = sb2("qT", [P, PAIRS, TOK])
                kT = sb2("kT", [P, PAIRS, TOK])
                v = sb2("v", [P, NT + 1, DB])
                with ExitStack() as c3:
                    uT = alloc(c3)("uT", [P, KD, TOK])
                    projection(nc, a, out, dram, ident, qT, kT, v, uT)
                    xa = alloc(c3)("xa", [P, CT, CONVW - 1 + SEQ])
                    xs = alloc(c3)("xs", [P, CT, B, CONVW - 1 + TS])
                    branch_in(nc, a, uT, xa, xs, gelu_in)
                    recurrence(nc, a, out, ident, cols, xa, xs, gelu_in, ssq)
                yb = sb2("yb", [P, NT + 1, DB])
                attention(nc, a, out, dram, ident, silu, qT, kT, v, yb)
                sampling(nc, a, ident, qT, kT, v, yb)
                mixing(nc, a, out, dram, ident, cols, gelu_in, yb, ssq, logits)
            with ExitStack() as c4:
                sb4 = alloc(c4)
                route = {
                    "w": sb4("w12", [P, 2, NT + 1]),
                    "slot": sb4("slot_i", [P, 2, NT + 1], I32),
                    "expert": sb4("expert_i", [1, SLOT_TILES], I32),
                    "end": sb4("end_i", [1, NE], I32),
                    "pairs": sb4("pairs_i", [1, 1], I32),
                    "ids": sb4("ids", [P, SLOT_TILES], I32),
                }
                with ExitStack() as c5:
                    sb5 = alloc(c5)
                    new_sem = block_semaphores(nc, c5)
                    ew = {
                        "gate": sb5("e_wg", [P, 2 * KD, FE]),
                        "up": sb5("e_wu", [P, 2 * KD, FE]),
                        "down": sb5("e_wd", [P, 2 * KF, D]),
                        "s_gu": [Sem(new_sem(f"e_wgu{p}"), 16, p) for p in range(2)],
                        "s_d": [Sem(new_sem(f"e_wd{p}"), 16, p) for p in range(2)],
                    }
                    routing(nc, a, out, dram, ident, logits, route, ew)
                    experts(nc, a, out, dram, ident, route, ew)
                finish(nc, a, out, dram, route)


def modulation(nc, a, dram, ident, cols, silu):
    NCH = 2 * D // MW
    with ExitStack() as ctx:
        new_sem = block_semaphores(nc, ctx)
        sb = lambda n, s, dt=F32: ctx.enter_context(nc.sbuf_tensor(n, s, dt))
        ps = lambda n, s: ctx.enter_context(nc.psum_tensor(n, s, F32))
        crow = sb("crow", [NSEQ, D])
        th = sb("th", [NSEQ, D])
        cs = sb("cs", [NSEQ, D])
        cT = sb("cT", [P, KD, P])
        ones = sb("ones9", [1, P])
        wring = sb("wring", [P, NCH, KD, MW])
        brow = sb("brow", [1, NCH * MW])
        mod = sb("mod", [NSEQ, NCH * MW])
        rows = sb("rows", [40, P])
        psT = ps("m_psT", [P, KD * NSEQ])
        psR = ps("m_psR", [P, 40])
        psM = ps("m_psM", [P, NCH, MW])
        s_c = new_sem("m_c")
        s_rows = new_sem("m_rows")
        s_w = [Sem(new_sem(f"m_w{r}"), 16) for r in range(NCH)]
        s_th = new_sem("m_th")
        s_v = new_sem("m_v")
        s_pe = new_sem("m_pe")
        s_cT = new_sem("m_cT")
        s_mm = Sem(new_sem("m_mm"))
        s_ev = Sem(new_sem("m_ev"))
        s_out = new_sem("m_out")
        s_ones = new_sem("m_ones")
        block = ctx.enter_context(nc.Block())
        w = a["w_ada"].rearrange("(k p) n -> p k n", p=P)

        @block.sync
        def _(sp):
            sp.dma_start(crow[0:1, :], a["c_prompt"]).then_inc(s_c, 16)
            sp.dma_start(crow[1:NSEQ, :], a["c_sample"]).then_inc(s_c, 16)
            sp.dma_start(ident[:, :], a["k_ident"]).then_inc(s_c, 16)
            sp.dma_start(brow[:, :], a["b_ada"].rearrange("(o n) -> o n", o=1)[:, 0:NCH * MW]).then_inc(s_c, 16)
            r = 0
            for name, v in (("conv_w", a["conv_w"].rearrange("j (c p) -> (j c) p", p=P)),
                            ("conv_b", a["conv_b"].rearrange("(c p) -> c p", p=P)),
                            ("b_rg_a", a["b_rg_a"].rearrange("(c h) w -> c (h w)", h=2)),
                            ("b_rg_x", a["b_rg_x"].rearrange("(c h) w -> c (h w)", h=2)),
                            ("rg_lambda", a["rg_lambda"].rearrange("(c p) -> c p", p=P)),
                            ("g_norm_a", a["g_norm_a"].rearrange("(c p) -> c p", p=P)),
                            ("g_norm_b", a["g_norm_b"].rearrange("(c p) -> c p", p=P))):
                n = v.shape[0]
                sp.dma_start(rows[r:r + n, :], v).then_inc(s_rows, 16)
                r += n
            for i in range(NCH):
                sp.dma_start(wring[:, i, :, :], w[:, :, i * MW:(i + 1) * MW]).then_inc(s_w[i].sem, s_w[i].unit)
            sp.wait_ge(s_ev.sem, s_ev.at(NCH))
            sp.dma_start(dram["mod"][:, 0:NCH * MW], mod[:, :]).then_inc(s_out, 16)
            sp.wait_ge(s_out, 16)

        @block.gpsimd
        def _(pool):
            nc.gpsimd.memset(ones[:, :], 1.0).then_inc(s_ones, 1)
            nc.gpsimd.memset(cT[:, :, :], 0.0).then_inc(s_ones, 1)

        @block.scalar
        def _(act):
            act.wait_ge(s_c, 64)
            nc.scalar.activation(th[:, :], crow[:, :], ACT.Tanh, scale=0.5).then_inc(s_th, 1)
            for i in range(NCH):
                act.wait_ge(s_mm.sem, s_mm.at(i + 1))
                nc.scalar.copy(mod[:, i * MW:(i + 1) * MW], psM[0:NSEQ, i, :]).then_inc(s_ev.sem, s_ev.unit)

        @block.vector
        def _(v):
            v.wait_ge(s_th, 1)
            nc.vector.scalar_tensor_tensor(out=cs[:, :], in0=th[:, :], scalar=1.0, in1=crow[:, :],
                                           op0=ALU.add, op1=ALU.mult).then_inc(s_v, 1)
            v.wait_ge(s_pe, 1)
            v.wait_ge(s_ones, 2)
            nc.vector.tensor_scalar(cT[:, :, 0:NSEQ], psT[:, :].rearrange("p (k s) -> p k s", k=KD), 0.5, None,
                                    ALU.mult).then_inc(s_cT, 1)
            v.wait_ge(s_cT, 1)
            nc.vector.tensor_copy(silu[:, :, :], cT[:, :, 0:NSEQ]).then_inc(s_v, 1)
            v.wait_ge(s_pe, 2)
            nc.vector.tensor_copy(cols[:, :], psR[:, :]).then_inc(s_v, 1)

        @block.tensor
        def _(pe):
            pe.wait_ge(s_v, 1)
            for k in range(KD):
                last = nc.tensor.transpose(psT[:, k * NSEQ:(k + 1) * NSEQ], cs[:, k * P:(k + 1) * P],
                                           ident[0:NSEQ, 0:NSEQ])
            last.then_inc(s_pe, 1)
            pe.wait_ge(s_rows, 16 * 7)
            nc.tensor.transpose(psR[:, :], rows[:, :], ident[0:40, 0:40]).then_inc(s_pe, 1)
            pe.wait_ge(s_cT, 1)
            pe.wait_ge(s_ones, 2)
            for i in range(NCH):
                pe.wait_ge(s_w[i].sem, s_w[i].at(1))
                for k in range(KD):
                    nc.tensor.matmul(psM[:, i, :], cT[:, k, :], wring[:, i, k, :], start=(k == 0), stop=False)
                nc.tensor.matmul(psM[:, i, :], ones[:, :], brow[:, i * MW:(i + 1) * MW], start=False, stop=True).then_inc(s_mm.sem, s_mm.unit)


def projection(nc, a, out, dram, ident, qT, kT, v_all, uT):
    with ExitStack() as ctx:
        new_sem = block_semaphores(nc, ctx)
        sb = lambda n, s, dt=F32: ctx.enter_context(nc.sbuf_tensor(n, s, dt))
        ps = lambda n, s: ctx.enter_context(nc.psum_tensor(n, s, F32))
        S = lambda n, unit=1, credit=0: Sem(new_sem(n), unit, credit)
        wq = sb("wqkv", [P, KD, 3 * DB])
        mods = {k: sb(f"mod_{k}", [P, D]) for k in ("sh", "sc")}
        modq = {k: sb(f"mods_{k}", [NS, D]) for k in ("sh", "sc")}
        xt = sb("xt", [P, 2, D])
        ut = xt
        uTs = sb("uTs", [P, 2, KD, P])
        qk = sb("qk", [P, 2, 2, DB])
        rot = sb("rot", [P, 2, 2, DB])
        tmp = sb("tmpr", [P, 2, DB])
        cos = sb("cos", [P, NT + 1, HD // 2])
        sin = sb("sin", [P, NT + 1, HD])
        psT = ps("p_psT", [P, KD, P])
        psQKV = ps("p_qkv", [P, 3, DB])
        psQ = ps("p_qT", [P, 2, PAIRS, P])
        s_in = S("p_in", 16)
        s_wq = S("p_wq", 16)
        s_x = [S(f"p_x{p}", 16) for p in range(2)]
        s_ch = new_sem("p_ch")
        s_u = S("p_u", 1, 2)
        s_uT = S("p_uT", 1, 2)
        s_uTs = S("p_uTs", 1, 1)
        s_big = S("p_big", 1, 2)
        s_qkv = S("p_sqkv", 1)
        s_ev = S("p_ev", 1, 3)
        s_rot = S("p_rot", 1, 4)
        s_qT = S("p_sqT", 1, 4)
        s_qe = S("p_qe", 1, 2)
        s_ko = [S(f"p_ko{p}", 16, 1) for p in range(2)]
        s_out = new_sem("p_out")
        block = ctx.enter_context(nc.Block())
        modrow = dram["mod"]

        @block.gpsimd
        def _(pool):
            for s in (s_u, s_uT, s_uTs, s_big, s_ev, s_rot, s_qT, s_qe):
                pool.sem_inc(s.sem, s.credit)
            for s in s_ko:
                pool.sem_inc(s.sem, 16)

            def tile(t, par, rows):
                pool.wait_ge(s_uTs.sem, s_uTs.at(t + 1))
                nc.gpsimd.tensor_copy(uT[:, :, ds(t * P, rows)], uTs[:, par, :, 0:rows]).then_inc(s_big.sem, s_big.unit)

            with pool.Fori(0, NT // 2) as i:
                for par in range(2):
                    tile(2 * i + par, par, P)
            tile(NT, 0, NS)

        @block.sync
        def _(sp):
            def bcast(j, n, row):
                return modrow[row:row + 1, j * D:(j + 1) * D].to_broadcast([n, D])

            def load(t, par, rows, src):
                sp.wait_ge(s_uT.sem, s_uT.at(t - 1))
                sp.dma_start(xt[0:rows, par, :], src).then_inc(s_x[par].sem, s_x[par].unit)

            for j, k in ((0, "sh"), (1, "sc")):
                sp.dma_start(mods[k][:, :], bcast(j, P, 0)).then_inc(s_in.sem, s_in.unit)
                for b in range(B):
                    sp.dma_start(modq[k][TS * b:TS * (b + 1), :], bcast(j, TS, 1 + b)).then_inc(s_in.sem, s_in.unit)
            sp.dma_start(cos[:, :, :], a["k_cos"]).then_inc(s_in.sem, s_in.unit)
            sp.dma_start(sin[:, :, :], a["k_sin"]).then_inc(s_in.sem, s_in.unit)
            xp = a["x_prompt"].rearrange("o s d -> (o s) d")
            load(0, 0, P, xp[0:P, :])
            load(1, 1, P, xp[P:2 * P, :])
            w = a["w_in"].rearrange("(k p) n -> p k n", p=P)
            for j in range(3):
                sp.dma_start(wq[:, :, j * DB:(j + 1) * DB], w[:, :, 2 * DA + j * DB:2 * DA + (j + 1) * DB]).then_inc(s_wq.sem, s_wq.unit)
            with sp.Fori(1, NT // 2) as i:
                for par in range(2):
                    load(2 * i + par, par, P, xp[ds((2 * i + par) * P, P), :])
            load(NT, 0, NS, a["x_sample"].rearrange("b t d -> (b t) d"))

        @block.scalar
        def _(act):
            def turned(t, par, rows):
                act.wait_ge(s_uT.sem, s_uT.at(t + 1))
                act.wait_ge(s_big.sem, s_big.at(t - 1))
                nc.scalar.copy(uTs[:, par, :, 0:rows], psT[:, :, 0:rows]).then_inc(s_uTs.sem, s_uTs.unit)

            def products(t, par, rows):
                for j in range(2):
                    act.wait_ge(s_qkv.sem, s_qkv.at(3 * t + j + 1))
                    act.wait_ge(s_rot.sem, s_rot.at(2 * (t - 2) + j + 1))
                    nc.scalar.copy(qk[0:rows, par, j, :], psQKV[0:rows, j, :]).then_inc(s_ev.sem, s_ev.unit)
                act.wait_ge(s_qkv.sem, s_qkv.at(3 * t + 3))
                nc.scalar.copy(v_all[0:rows, ds(t, 1), :], psQKV[0:rows, 2:3, :]).then_inc(s_ev.sem, s_ev.unit)

            def finished(t, par, rows, k_dst, v_dst):
                for j, dst in enumerate((qT, kT)):
                    act.wait_ge(s_qT.sem, s_qT.at(2 * t + j + 1))
                    nc.scalar.copy(dst[:, :, ds(t * P, rows)], psQ[:, j, :, 0:rows]).then_inc(s_qe.sem, s_qe.unit)
                act.wait_ge(s_rot.sem, s_rot.at(2 * t + 2))
                act.dma_start(k_dst, rot[0:rows, par, 1, :]).then_inc(s_ko[par].sem, s_ko[par].unit)
                act.wait_ge(s_ev.sem, s_ev.at(3 * t + 3))
                act.dma_start(v_dst, v_all[0:rows, ds(t, 1), :]).then_inc(s_out, 16)

            kp, vp = (out[n].rearrange("o s h d -> (o s) (h d)") for n in ("k_p", "v_p"))

            def finished_prompt(t, par):
                finished(t, par, P, kp[ds(t * P, P), :], vp[ds(t * P, P), :].unsqueeze(1))

            turned(0, 0, P)
            products(0, 0, P)
            turned(1, 1, P)
            with act.Fori(0, NT // 2 - 1) as i:
                for q in range(2):
                    t = 2 * i + 1 + q
                    products(t, 1 - q, P)
                    turned(t + 1, q, P)
                    finished_prompt(t - 1, q)
            products(NT - 1, 1, P)
            turned(NT, 0, NS)
            finished_prompt(NT - 2, 0)
            products(NT, 0, NS)
            finished_prompt(NT - 1, 1)
            finished(NT, 0, NS, dram["k_new"], dram["v_new"].unsqueeze(1))
            act.wait_ge(s_out, 16 * (NT + 1))
            act.wait_ge(s_ko[0].sem, s_ko[0].at(NT // 2 + 1))
            act.wait_ge(s_ko[1].sem, s_ko[1].at(NT // 2))

        @block.vector
        def _(v):
            st = Steps(v, s_ch)
            v.wait_ge(s_in.sem, s_in.at(20))
            st.after(nc.vector.tensor_scalar(mods["sc"][:, :], mods["sc"][:, :], 1.0, None, ALU.add))
            st.after(nc.vector.tensor_scalar(modq["sc"][:, :], modq["sc"][:, :], 1.0, None, ALU.add))
            st.last()

            def modulate(t, par, rows, m):
                v.wait_ge(s_x[par].sem, s_x[par].at(t // 2 + 1))
                v.wait_ge(s_uT.sem, s_uT.at(t - 1))
                st.link(nc.vector.tensor_tensor(ut[0:rows, par, :], xt[0:rows, par, :], m["sc"][0:rows, :], ALU.mult))
                nc.vector.tensor_tensor(ut[0:rows, par, :], ut[0:rows, par, :], m["sh"][0:rows, :], ALU.add).then_inc(s_u.sem, s_u.unit)

            def rotate(t, par, rows):
                for j in range(2):
                    v.wait_ge(s_ev.sem, s_ev.at(3 * t + j + 1))
                    src = qk[0:rows, par, j, :].rearrange("p (h s e) -> p h s e", s=2, e=HD // 2)
                    o = rot[0:rows, par, j, :].rearrange("p (h s e) -> p h s e", s=2, e=HD // 2)
                    straight = tmp[0:rows, 0, :].rearrange("p (h e) -> p h e", e=HD // 2)
                    crossed = tmp[0:rows, 1, :].rearrange("p (h s e) -> p h s e", s=2, e=HD // 2)
                    c = cos[0:rows, ds(t, 1), :].to_broadcast([rows, 2 * H, HD // 2])
                    st.after(nc.vector.tensor_tensor(straight, qk[0:rows, par, j, :].rearrange("p (h e) -> p h e", e=HD // 2), c, ALU.mult))
                    for s in range(2):
                        sn = sin[0:rows, ds(t, 1), s * HD // 2:(s + 1) * HD // 2].to_broadcast([rows, H, HD // 2])
                        st.after(nc.vector.tensor_tensor(crossed[:, :, s, :], src[:, :, 1 - s, :], sn, ALU.mult))
                    st.last()
                    v.wait_ge(s_qT.sem, s_qT.at(2 * (t - 2) + j + 1))
                    if j == 1:
                        v.wait_ge(s_ko[par].sem, s_ko[par].at(t // 2))
                    nc.vector.tensor_tensor(rot[0:rows, par, j, :], tmp[0:rows, 0, :], tmp[0:rows, 1, :], ALU.add).then_inc(s_rot.sem, s_rot.unit)
                    v.wait_ge(s_rot.sem, s_rot.at(2 * t + j + 1))

            modulate(0, 0, P, mods)
            modulate(1, 1, P, mods)
            rotate(0, 0, P)
            modulate(2, 0, P, mods)
            rotate(1, 1, P)
            modulate(3, 1, P, mods)
            st.enter(14)
            with v.Fori(1, NT // 2 - 1) as i:
                st.round(i - 1)
                for par in range(2):
                    t = 2 * i + par
                    rotate(t, par, P)
                    modulate(t + 2, par, P, mods)
            st.leave(NT // 2 - 2)
            rotate(NT - 2, 0, P)
            modulate(NT, 0, NS, modq)
            rotate(NT - 1, 1, P)
            rotate(NT, 0, NS)

        @block.tensor
        def _(pe):
            def turn(t, par, rows):
                pe.wait_ge(s_u.sem, s_u.at(t + 1))
                pe.wait_ge(s_uTs.sem, s_uTs.at(t))
                for k in range(KD):
                    last = nc.tensor.transpose(psT[:, k, 0:rows], ut[0:rows, par, k * P:(k + 1) * P],
                                               ident[0:rows, 0:rows])
                last.then_inc(s_uT.sem, s_uT.unit)

            def multiply(t, par, rows):
                pe.wait_ge(s_uTs.sem, s_uTs.at(t + 1))
                for j in range(3):
                    pe.wait_ge(s_ev.sem, s_ev.at(3 * (t - 1) + j + 1))
                    for k in range(KD):
                        last = nc.tensor.matmul(psQKV[0:rows, j, :], uTs[:, par, k, 0:rows],
                                                wq[:, k, j * DB:(j + 1) * DB], start=(k == 0), stop=(k == KD - 1))
                    last.then_inc(s_qkv.sem, s_qkv.unit)

            def turn_qk(t, par, rows):
                for j in range(2):
                    pe.wait_ge(s_rot.sem, s_rot.at(2 * t + j + 1))
                    pe.wait_ge(s_qe.sem, s_qe.at(2 * (t - 1) + j + 1))
                    for p in range(PAIRS):
                        last = nc.tensor.transpose(psQ[:, j, p, 0:rows], rot[0:rows, par, j, p * P:(p + 1) * P],
                                                   ident[0:rows, 0:rows])
                    last.then_inc(s_qT.sem, s_qT.unit)

            turn(0, 0, P)
            pe.wait_ge(s_wq.sem, s_wq.at(3))
            multiply(0, 0, P)
            turn(1, 1, P)
            with pe.Fori(0, NT // 2 - 1) as i:
                for q in range(2):
                    t = 2 * i + 1 + q
                    multiply(t, 1 - q, P)
                    turn(t + 1, q, P)
                    turn_qk(t - 1, q, P)
            multiply(NT - 1, 1, P)
            turn(NT, 0, NS)
            turn_qk(NT - 2, 0, P)
            multiply(NT, 0, NS)
            turn_qk(NT - 1, 1, P)
            turn_qk(NT, 0, NS)


def branch_in(nc, a, uT, xa, xs, ga):
    with ExitStack() as ctx:
        new_sem = block_semaphores(nc, ctx)
        sb = lambda n, s, dt=F32: ctx.enter_context(nc.sbuf_tensor(n, s, dt))
        ps = lambda n, s: ctx.enter_context(nc.psum_tensor(n, s, F32))
        S = lambda n, unit=1, credit=0: Sem(new_sem(n), unit, credit)
        w = sb("w_xg", [P, KD, 2 * DA])
        psP = ps("b_psP", [P, 2, 2, 512])
        psS = ps("b_psS", [P, 2, 512])
        s_w = [S(f"b_w{j}", 16) for j in range(4)]
        s_mm = S("b_mm")
        s_ev = S("b_ev")
        s_es = S("b_es")
        s_z = S("b_z")
        block = ctx.enter_context(nc.Block())
        wi = a["w_in"].rearrange("(k p) n -> p k n", p=P)

        @block.sync
        def _(sp):
            for j in range(4):
                sp.dma_start(w[:, :, j * 256:(j + 1) * 256], wi[:, :, j * 256:(j + 1) * 256]).then_inc(s_w[j].sem, s_w[j].unit)

        @block.gpsimd
        def _(pool):
            nc.gpsimd.memset(xa[:, :, 0:CONVW - 1], 0.0).then_inc(s_z.sem, s_z.unit)

        @block.tensor
        def _(pe):
            for c in range(2 * CT):
                pe.wait_ge(s_w[c // 2].sem, s_w[c // 2].at(1))
                if c >= 2:
                    pe.wait_ge(s_ev.sem, s_ev.at(c - 1))
                if c >= 2:
                    pe.wait_ge(s_es.sem, s_es.at(c - 1))
                for dst, lo, n in ((psP[:, c % 2, 0, :], 0, 512), (psP[:, c % 2, 1, :], 512, 512),
                                   (psS[:, c % 2, 0:NS], SEQ, NS)):
                    for k in range(KD):
                        last = nc.tensor.matmul(dst, w[:, k, c * P:(c + 1) * P], uT[:, k, lo:lo + n],
                                                start=(k == 0), stop=(k == KD - 1))
                last.then_inc(s_mm.sem, s_mm.unit)

        @block.scalar
        def _(act):
            for c in range(2 * CT):
                act.wait_ge(s_mm.sem, s_mm.at(c + 1))
                dst = xa[:, c, CONVW - 1:].rearrange("p (h n) -> p h n", h=2) if c < CT else \
                    ga[:, c - CT, 0:SEQ].rearrange("p (h n) -> p h n", h=2)
                nc.scalar.copy(dst, psP[:, c % 2, :, :]).then_inc(s_ev.sem, s_ev.unit)

        @block.vector
        def _(v):
            for c in range(2 * CT):
                v.wait_ge(s_mm.sem, s_mm.at(c + 1))
                dst = xs[:, c, :, CONVW - 1:] if c < CT else ga[:, c - CT, SEQ:].rearrange("p (b t) -> p b t", t=TS)
                nc.vector.tensor_copy(dst, psS[:, c % 2, 0:NS].rearrange("p (b t) -> p b t", t=TS)).then_inc(s_es.sem, s_es.unit)


def recurrence(nc, a, out, ident, cols, xa, xs, ga, ssq):
    CV, CB, BA, BX, LM = 0, 16, 20, 24, 28
    with ExitStack() as ctx:
        new_sem = block_semaphores(nc, ctx)
        sb = lambda n, s, dt=F32: ctx.enter_context(nc.sbuf_tensor(n, s, dt))
        ps = lambda n, s: ctx.enter_context(nc.psum_tensor(n, s, F32))
        S = lambda n, unit=1, credit=0: Sem(new_sem(n), unit, credit)
        wa = sb("wa", [P, CT, P])
        wx = sb("wx", [P, CT, P])
        st_rows = sb("st_rows", [B * (CONVW - 1) + B, DA])
        h0 = sb("h0", [P, CT, B])
        sm = sb("sm", [P, 10, CT])
        xc = sb("xc", [P, 2, TOK])
        tr = sb("tr", [P, TOK])
        ti = sb("ti", [P, TOK])
        av = sb("av", [P, TOK])
        tl = sb("tl", [P, TOK])
        gg = sb("gg", [P, TOK])
        t2 = sb("t2", [P, TOK])
        hh = sb("hh", [P, TOK])
        sq = sb("sq", [P, TOK])
        NTAIL = B * TS + (CONVW - 1) + 1 + B
        tail = sb("tail", [P, CT, NTAIL])
        tail_rows = sb("tail_rows", [NTAIL, DA])
        one = sb("one_col", [P, 1])
        NSR = B * (CONVW - 1) + B
        psG = ps("r_psG", [P, 2, 3, 512])
        psX = ps("r_psX", [P, 512])
        psQ = ps("r_psQ", [P, 512])
        s_z = S("r_z")
        s_w = S("r_w", 16)
        s_st = S("r_st", 16)
        s_t = S("r_t")
        s_ch = new_sem("r_ch")
        s_xc = S("r_xc")
        s_g = S("r_g")
        s_a = S("r_a")
        s_ga = S("r_ga")
        s_v = S("r_v")
        s_v2 = S("r_v2")
        s_v3 = S("r_v3")
        s_cc = S("r_cc")
        s_sq = S("r_sq")
        s_ss = S("r_ss")
        s_tl = S("r_tl")
        s_tt = S("r_tt")
        s_tr = S("r_tr")
        s_out = new_sem("r_out")
        s_cp = S("r_cp", 16)
        s_ac = new_sem("r_ac")
        block = ctx.enter_context(nc.Block())
        TAIL_S, TAIL_P, TAIL_HP, TAIL_HS = 0, NS, NS + 3, NS + 4

        @block.gpsimd
        def _(pool):
            nc.gpsimd.memset(wa[:, :, :], 0.0).then_inc(s_z.sem, s_z.unit)
            nc.gpsimd.memset(wx[:, :, :], 0.0).then_inc(s_z.sem, s_z.unit)
            nc.gpsimd.memset(one[:, :], 1.0).then_inc(s_z.sem, s_z.unit)

        @block.sync
        def _(sp):
            sp.dma_start(st_rows[0:B * (CONVW - 1), :], a["state_conv"].rearrange("b j n -> (b j) n")).then_inc(s_st.sem, s_st.unit)
            sp.dma_start(st_rows[B * (CONVW - 1):NSR, :], a["state_rglru"]).then_inc(s_st.sem, s_st.unit)
            sp.wait_ge(s_z.sem, s_z.at(3))
            for w, src in ((wa, a["w_rg_a"]), (wx, a["w_rg_x"])):
                for h in range(2):
                    sp.dma_start(w[h * 64:(h + 1) * 64, :, h * 64:(h + 1) * 64],
                                          src.rearrange("(c h) i j -> h i c j", h=2)[h]).then_inc(s_w.sem, s_w.unit)
            kc, ko = (x.rearrange("b s h d -> b s (h d)") for x in (a["cache_win_k"], out["k_s"]))
            with sp.Fori(0, B) as b:
                sp.dma_start(ko[ds(b, 1), 0:PAST - TS, :], kc[ds(b, 1), TS:PAST, :]).then_inc(s_cp.sem, s_cp.unit)
            sp.wait_ge(s_tr.sem, s_tr.at(1))
            rows = tail_rows
            for b in range(B):
                sp.dma_start(out["conv_s"][b, :, :], rows[TS * b + 1:TS * b + TS, :]).then_inc(s_out, 16)
            sp.dma_start(out["conv_p"][0, :, :], rows[TAIL_P:TAIL_P + 3, :]).then_inc(s_out, 16)
            sp.dma_start(out["h_p"], rows[TAIL_HP:TAIL_HP + 1, :]).then_inc(s_out, 16)
            sp.dma_start(out["h_s"], rows[TAIL_HS:TAIL_HS + B, :]).then_inc(s_out, 16)
            sp.wait_ge(s_out, 16 * (B + 3))
            sp.wait_ge(s_cp.sem, s_cp.at(B))

        @block.tensor
        def _(pe):
            pe.wait_ge(s_st.sem, s_st.at(2))
            for c in range(CT):
                last = nc.tensor.transpose(psX[:, c * NSR:(c + 1) * NSR], st_rows[:, c * P:(c + 1) * P], ident[0:NSR, 0:NSR])
            last.then_inc(s_t.sem, s_t.unit)
            pe.wait_ge(s_w.sem, s_w.at(4))
            for c in range(CT + 1):
                if c < CT:
                    pe.wait_ge(s_xc.sem, s_xc.at(c + 1))
                    if c >= 1:
                        pe.wait_ge(s_a.sem, s_a.at(2 * c))
                    for j, w in enumerate((wa, wx)):
                        for n, lo, m in ((0, 0, 512), (1, 512, 512), (2, 1024, NS)):
                            last = nc.tensor.matmul(psG[:, j, n, 0:m], w[:, c, :], xc[:, c % 2, lo:lo + m], start=True, stop=True)
                        last.then_inc(s_g.sem, s_g.unit)
                if c > 0:
                    pe.wait_ge(s_sq.sem, s_sq.at(c))
                    pe.wait_ge(s_z.sem, s_z.at(3))
                    for t in range(NT + 1):
                        rows = P if t < NT else NS
                        last = nc.tensor.matmul(psQ[0:rows, t * CT + c - 1:t * CT + c], sq[:, t * P:t * P + rows], one[:, :],
                                                start=True, stop=True)
                    last.then_inc(s_ss.sem, s_ss.unit)
            pe.wait_ge(s_tl.sem, s_tl.at(CT))
            for c in range(CT):
                last = nc.tensor.transpose(psX[0:NTAIL, c * P:(c + 1) * P], tail[:, c, :], ident[:, :])
            last.then_inc(s_tt.sem, s_tt.unit)

        @block.scalar
        def _(act):
            nc.scalar.activation(sm[:, 0, :], cols[:, LM:LM + CT], ACT.Abs).then_inc(s_ac, 1)
            act.wait_ge(s_ac, 1)
            nc.scalar.activation(sm[:, 1, :], sm[:, 0, :], ACT.Exp, scale=-1.0).then_inc(s_ac, 1)
            act.wait_ge(s_ac, 2)
            nc.scalar.activation(sm[:, 2, :], sm[:, 1, :], ACT.Ln, bias=1.0).then_inc(s_ac, 1)
            act.wait_ge(s_cc.sem, s_cc.at(1))
            for c in range(CT):
                for j, (dst, b) in enumerate(((tr, 6), (ti, 7))):
                    act.wait_ge(s_g.sem, s_g.at(2 * c + j + 1))
                    if c >= 1:
                        act.wait_ge(s_v.sem, s_v.at(c))
                    nc.scalar.activation(dst[:, 0:SEQ].rearrange("p (h n) -> p h n", h=2), psG[:, j, 0:2, :], ACT.Tanh,
                                         scale=0.5, bias=sm[:, b, c:c + 1]).then_inc(s_ac, 1)
                    nc.scalar.activation(dst[:, SEQ:TOK], psG[:, j, 2, 0:NS], ACT.Tanh,
                                                  scale=0.5, bias=sm[:, b, c:c + 1]).then_inc(s_a.sem, s_a.unit)
                n = 3 + 3 * c
                act.wait_ge(s_ac, n + 2)
                act.wait_ge(s_a.sem, s_a.at(2 * c + 2))
                nc.scalar.activation(av[:, :], tr[:, :], ACT.Exp, scale=sm[:, 4, c:c + 1], bias=sm[:, 4, c:c + 1]).then_inc(s_ga.sem, s_ga.unit)
                nc.scalar.activation(tl[:, :], tr[:, :], ACT.Tanh, scale=sm[:, 5, c:c + 1], bias=sm[:, 5, c:c + 1]).then_inc(s_ga.sem, s_ga.unit)
                act.wait_ge(s_v3.sem, s_v3.at(c + 1))
                nc.scalar.activation(gg[:, :], t2[:, :], ACT.Tanh, scale=math.sqrt(2.0 / math.pi)).then_inc(s_ga.sem, s_ga.unit)
                act.wait_ge(s_v2.sem, s_v2.at(c + 1))
                nc.scalar.activation(tl[:, :], tl[:, :], ACT.Sqrt, scale=0.25).then_inc(s_ga.sem, s_ga.unit)
                act.wait_ge(s_v.sem, s_v.at(c + 1))
                if c >= 1:
                    act.wait_ge(s_ss.sem, s_ss.at(c))
                nc.scalar.activation(sq[:, :], ga[:, c, :], ACT.Square).then_inc(s_sq.sem, s_sq.unit)
                nc.scalar.copy(tail[:, c, TAIL_HP:TAIL_HP + 1], hh[:, SEQ - 1:SEQ]).then_inc(s_ac, 1)
                act.wait_ge(s_ac, n + 3)
                nc.scalar.copy(tail[:, c, TAIL_HS:], hh[:, SEQ:TOK].rearrange("p (b t) -> p b t", t=TS)[:, :, TS - 1]).then_inc(s_tl.sem, s_tl.unit)

        @block.vector
        def _(v):
            st = Steps(v, s_ch)
            v.wait_ge(s_t.sem, s_t.at(1))
            states = psX[:, 0:CT * NSR].rearrange("p (c r) -> p c r", c=CT)
            for c in range(CT):
                st.after(nc.vector.tensor_copy(xs[:, c, :, 0:CONVW - 1], states[:, c, 0:24].rearrange("p (b j) -> p b j", b=B)))
            st.after(nc.vector.tensor_copy(h0[:, :, :], states[:, :, 24:NSR]))
            for c in range(CT):
                st.after(nc.vector.tensor_copy(tail[:, c, 0:NS].rearrange("p (b t) -> p b t", t=TS), xs[:, c, :, CONVW - 1:]))
            st.link(nc.vector.tensor_copy(tail[:, :, TAIL_P:TAIL_P + 3], xa[:, :, SEQ:SEQ + 3]))
            v.wait_ge(s_ac, 3)
            st.link(nc.vector.tensor_scalar(sm[:, 3, :], cols[:, LM:LM + CT], -1.0, 0.0, ALU.mult, ALU.max))
            st.link(nc.vector.tensor_tensor(sm[:, 3, :], sm[:, 3, :], sm[:, 2, :], ALU.add))
            st.after(nc.vector.tensor_scalar(sm[:, 4, :], sm[:, 3, :], -4.0, None, ALU.mult))
            st.after(nc.vector.tensor_scalar(sm[:, 5, :], sm[:, 3, :], 4.0, None, ALU.mult))
            st.after(nc.vector.tensor_scalar(sm[:, 6, :], cols[:, BA:BA + CT], 0.5, None, ALU.mult))
            st.after(nc.vector.tensor_scalar(sm[:, 7, :], cols[:, BX:BX + CT], 0.5, None, ALU.mult))
            st.last()
            nc.vector.tensor_copy(sm[:, 8, :], sm[:, 7, :]).then_inc(s_cc.sem, s_cc.unit)
            for c in range(CT):
                x = xc[:, c % 2, :]
                xq = x[:, SEQ:TOK].rearrange("p (b t) -> p b t", t=TS)
                for j in range(CONVW):
                    wj = cols[:, CV + 4 * j + c:CV + 4 * j + c + 1]
                    src, srq = xa[:, c, j:j + SEQ], xs[:, c, :, j:j + TS]
                    if j == 0:
                        cb = cols[:, CB + c:CB + c + 1]
                        st.after(nc.vector.tensor_scalar(x[:, 0:SEQ], src, wj, cb, ALU.mult, ALU.add))
                        st.link(nc.vector.tensor_scalar(xq, srq, wj, cb, ALU.mult, ALU.add))
                    elif j < CONVW - 1:
                        st.after(nc.vector.scalar_tensor_tensor(out=x[:, 0:SEQ], in0=src, scalar=wj, in1=x[:, 0:SEQ], op0=ALU.mult, op1=ALU.add))
                        st.link(nc.vector.scalar_tensor_tensor(out=xq, in0=srq, scalar=wj, in1=xq, op0=ALU.mult, op1=ALU.add))
                    else:
                        st.link(nc.vector.scalar_tensor_tensor(out=x[:, 0:SEQ], in0=src, scalar=wj, in1=x[:, 0:SEQ], op0=ALU.mult, op1=ALU.add))
                        nc.vector.scalar_tensor_tensor(out=xq, in0=srq, scalar=wj, in1=xq, op0=ALU.mult, op1=ALU.add).then_inc(s_xc.sem, s_xc.unit)
                g = ga[:, c, :]
                if c >= 1:
                    v.wait_ge(s_sq.sem, s_sq.at(c))
                st.link(nc.vector.tensor_tensor(t2[:, :], g, g, ALU.mult))
                st.link(nc.vector.tensor_scalar(t2[:, :], t2[:, :], 0.044715, 1.0, ALU.mult, ALU.add))
                nc.vector.tensor_tensor(t2[:, :], t2[:, :], g, ALU.mult).then_inc(s_v3.sem, s_v3.unit)
                v.wait_ge(s_ga.sem, s_ga.at(4 * c + 2))
                v.wait_ge(s_v3.sem, s_v3.at(c + 1))
                if c >= 1:
                    v.wait_ge(s_tl.sem, s_tl.at(c))
                st.link(nc.vector.tensor_tensor(hh[:, :], av[:, :], av[:, :], ALU.mult))
                nc.vector.scalar_tensor_tensor(out=tl[:, :], in0=hh[:, :], scalar=1.0, in1=tl[:, :], op0=ALU.add, op1=ALU.mult).then_inc(s_v2.sem, s_v2.unit)
                v.wait_ge(s_xc.sem, s_xc.at(c + 1))
                v.wait_ge(s_v2.sem, s_v2.at(c + 1))
                v.wait_ge(s_ga.sem, s_ga.at(4 * c + 3))
                st.after(nc.vector.scalar_tensor_tensor(out=ti[:, :], in0=ti[:, :], scalar=1.0, in1=x, op0=ALU.add, op1=ALU.mult))
                st.after(nc.vector.scalar_tensor_tensor(out=gg[:, :], in0=gg[:, :], scalar=1.0, in1=g, op0=ALU.add, op1=ALU.mult))
                v.wait_ge(s_ga.sem, s_ga.at(4 * c + 4))
                st.last()
                st.link(nc.vector.tensor_tensor(ti[:, :], ti[:, :], tl[:, :], ALU.mult))
                st.after(nc.vector.tensor_tensor_scan(hh[:, 0:SEQ], av[:, 0:SEQ], ti[:, 0:SEQ], 0.0, ALU.mult, ALU.add))
                hq, aq, uq = (z[:, SEQ:TOK].rearrange("p (b t) -> p b t", t=TS) for z in (hh, av, ti))
                for t in range(TS):
                    prev = h0[:, c, :] if t == 0 else hq[:, :, t - 1]
                    st.link(nc.vector.tensor_tensor(hq[:, :, t], aq[:, :, t], prev, ALU.mult))
                    st.link(nc.vector.tensor_tensor(hq[:, :, t], hq[:, :, t], uq[:, :, t], ALU.add))
                nc.vector.scalar_tensor_tensor(out=g, in0=gg[:, :], scalar=0.5, in1=hh[:, :], op0=ALU.mult, op1=ALU.mult).then_inc(s_v.sem, s_v.unit)
                v.wait_ge(s_v.sem, s_v.at(c + 1))
            v.wait_ge(s_ss.sem, s_ss.at(CT))
            st.after(nc.vector.tensor_copy(ssq[:, 0:NT, :], psQ[:, 0:NT * CT].rearrange("p (t c) -> p t c", c=CT)))
            st.after(nc.vector.tensor_copy(ssq[0:NS, NT, :], psQ[0:NS, NT * CT:(NT + 1) * CT]))
            v.wait_ge(s_tt.sem, s_tt.at(1))
            nc.vector.tensor_copy(tail_rows[:, :], psX[0:NTAIL, :]).then_inc(s_tr.sem, s_tr.unit)


def attention(nc, a, out, dram, ident, silu, qT, kT, v_all, yb):
    FIRST = 2 * D // MW
    assert NMOD * D // MW - FIRST == 2 * PAIRS and KD == NT
    with ExitStack() as ctx:
        new_sem = block_semaphores(nc, ctx)
        sb = lambda n, s, dt=F32: ctx.enter_context(nc.sbuf_tensor(n, s, dt))
        ps = lambda n, s: ctx.enter_context(nc.psum_tensor(n, s, F32))
        S = lambda n, unit=1, credit=0: Sem(new_sem(n), unit, credit)
        s_pass = new_sem("a_pass")
        bias = sb("bias", [P, SEQ])
        qp = sb("qp", [P, SEQ])
        kp = sb("kp", [P, SEQ])
        lg = sb("lg", [P, 2, SEQ])
        pr = sb("pr", [P, 2, SEQ])
        pT = sb("pT", [P, 2, NT, P])
        mn = sb("mn", [P, 2])
        den = sb("den", [P, 2])
        rden = sb("rden", [P, 2])
        psS = ps("a_psS", [P, 2, SEQ])
        psT = ps("a_psT", [P, 2, 4, P])
        psO = ps("a_psO", [P, 2, HD])
        psM = ps("a_psM", [P, MW])
        wring = sb("a_wring", [P, 2, KD, MW])
        brow = sb("a_brow", [1, 2, MW])
        mod = sb("a_mod", [NSEQ, 2, MW])
        cT = sb("a_cT", [P, KD, P])
        ones = sb("a_ones", [1, P])
        s_in = S("a_in", 16)
        s_cp = S("a_cp", 16)
        s_cT = S("a_cT")
        s_mw = [S(f"a_mw{p}", 16) for p in range(2)]
        s_mm = S("a_mm", 1, 2)
        s_me = S("a_me", 1, 1)
        s_mo = [S(f"a_mo{p}", 16, 1) for p in range(2)]
        N = 2 * NT
        s_pair = S("a_pair", 1, 0)
        s_s = S("a_s", 1, 2)
        s_lg = S("a_lg", 1, 2)
        s_p = S("a_p", 1, 2)
        s_t = S("a_t", 1, 3)
        s_tc = S("a_tc", 1, 2)
        s_o = S("a_o", 1, 2)
        s_y = S("a_y", 1, 2)
        s_r = S("a_r", 1, 2)
        block = ctx.enter_context(nc.Block())
        halves = [(t + 4) // 4 for _ in range(2) for t in range(NT)]
        before = [sum(halves[:n]) for n in range(N + 1)]
        TB = before[N]
        cv = a["cache_win_v"].rearrange("b s h d -> b s (h d)")
        ok, ov = (out[n].rearrange("b s h d -> b s (h d)") for n in ("k_s", "v_s"))

        @block.sync
        def _(sp):
            sp.dma_start(bias[:, :], a["k_bias"]).then_inc(s_in.sem, s_in.unit)
            w_ada = a["w_ada"].rearrange("(k p) n -> p k n", p=P)
            b_ada = a["b_ada"].rearrange("(o n) -> o n", o=1)
            with sp.Fori(0, PAIRS) as p:
                for slot in range(2):
                    j = 2 * p + slot
                    sp.wait_ge(s_mm.sem, s_mm.at(j - 1))
                    sp.dma_start(wring[:, slot, :, :], w_ada[:, :, ds((FIRST + j) * MW, MW)]).then_inc(s_mw[slot].sem, s_mw[slot].unit)
                    sp.dma_start(brow[:, slot, :], b_ada[:, ds((FIRST + j) * MW, MW)]).then_inc(s_mw[slot].sem, s_mw[slot].unit)
                for h in range(B // PAIRS):
                    b = (B // PAIRS) * p + h
                    sp.dma_start(ov[ds(b, 1), 0:PAST - TS, :], cv[ds(b, 1), TS:PAST, :]).then_inc(s_cp.sem, s_cp.unit)
                    for dst, new in ((ok, "k_new"), (ov, "v_new")):
                        sp.dma_start(dst[ds(b, 1), PAST - TS:PAST, :],
                                     dram[new].rearrange("(b t) n -> b t n", t=TS)[ds(b, 1), :, :]).then_inc(s_cp.sem, s_cp.unit)
            sp.wait_ge(s_cp.sem, s_cp.at(3 * B))

        @block.gpsimd
        def _(pool):
            for s in (s_s, s_lg, s_p, s_t, s_tc, s_o, s_y, s_r, s_mm, s_me):
                pool.sem_inc(s.sem, s.credit)
            for s in s_mo:
                pool.sem_inc(s.sem, 16)
            nc.gpsimd.memset(ones[:, :], 1.0).then_inc(s_cT.sem, s_cT.unit)
            nc.gpsimd.memset(cT[:, :, :], 0.0).then_inc(s_cT.sem, s_cT.unit)
            pool.wait_ge(s_cT.sem, s_cT.at(2))
            nc.gpsimd.tensor_copy(cT[:, :, 0:NSEQ], silu[:, :, :]).then_inc(s_cT.sem, s_cT.unit)
            with pool.Fori(0, PAIRS) as p:
                pool.wait_ge(s_s.sem, s_s.at(N * p))
                nc.gpsimd.tensor_copy(qp[:, :], qT[:, ds(p, 1), 0:SEQ])
                nc.gpsimd.tensor_copy(kp[:, :], kT[:, ds(p, 1), 0:SEQ]).then_inc(s_pair.sem, s_pair.unit)

        @block.tensor
        def _(pe):
            pe.wait_ge(s_cT.sem, s_cT.at(3))
            with pe.Fori(0, PAIRS) as p:
                def scores(n):
                    hh, t = divmod(n, NT)
                    pe.wait_ge(s_lg.sem, s_lg.at(N * p + n - 1))
                    keys = (t + 1) * P
                    for lo in range(0, keys, 512):
                        m = min(512, keys - lo)
                        last = nc.tensor.matmul(psS[:, n % 2, lo:lo + m], qp[64 * hh:64 * hh + 64, t * P:(t + 1) * P],
                                                kp[64 * hh:64 * hh + 64, lo:lo + m], start=True, stop=True)
                    last.then_inc(s_s.sem, s_s.unit)

                def turn(n):
                    t = n % NT
                    pe.wait_ge(s_p.sem, s_p.at(N * p + n + 1))
                    for half in range(halves[n]):
                        pe.wait_ge(s_tc.sem, s_tc.at(TB * p + before[n] + half - 1))
                        for b in range(4 * half, min(4 * half + 4, t + 1)):
                            last = nc.tensor.transpose(psT[:, (before[n] + half) % 2, b % 4, :], pr[:, n % 2, b * P:(b + 1) * P], ident[:, :])
                        last.then_inc(s_t.sem, s_t.unit)

                def values(n):
                    hh, t = divmod(n, NT)
                    pe.wait_ge(s_tc.sem, s_tc.at(TB * p + before[n + 1]))
                    pe.wait_ge(s_y.sem, s_y.at(N * p + n))
                    for b in range(t + 1):
                        last = nc.tensor.matmul(psO[:, n % 2, 0:HD], pT[:, n % 2, b, :],
                                                v_all[:, b, ds(p * P + hh * HD, HD)], start=(b == 0), stop=(b == t))
                    last.then_inc(s_o.sem, s_o.unit)

                def modulate(n):
                    slot, k = divmod(n, KD)
                    if k == 0:
                        pe.wait_ge(s_mw[slot].sem, s_mw[slot].at(2 * p + 2))
                        pe.wait_ge(s_me.sem, s_me.at(2 * p + slot))
                    nc.tensor.matmul(psM[:, :], cT[:, k, :], wring[:, slot, k, :], start=(k == 0), stop=False)
                    if k == KD - 1:
                        nc.tensor.matmul(psM[:, :], ones[:, :], brow[:, slot, :], start=False, stop=True).then_inc(s_mm.sem, s_mm.unit)

                pe.wait_ge(s_pair.sem, s_pair.at(p + 1))
                scores(0)
                for n in range(N):
                    if n + 1 < N:
                        scores(n + 1)
                    modulate(n)
                    turn(n)
                    if n > 0:
                        values(n - 1)
                values(N - 1)

        @block.vector
        def _(v):
            v.wait_ge(s_in.sem, s_in.at(1))
            with v.Fori(0, PAIRS) as p:
                def mask(n):
                    t = n % NT
                    keys = (t + 1) * P
                    v.wait_ge(s_s.sem, s_s.at(N * p + n + 1))
                    v.wait_ge(s_p.sem, s_p.at(N * p + n - 1))
                    v.sem_inc(s_pass, 1)
                    nc.vector.tensor_tensor_reduce(
                        out=lg[:, n % 2, 0:keys], in0=psS[:, n % 2, 0:keys], in1=bias[:, SEQ - keys:SEQ],
                        scale=-0.125, scalar=3e38, op0=ALU.add, op1=ALU.min, accum_out=mn[:, n % 2:n % 2 + 1]).then_inc(s_lg.sem, s_lg.unit)

                def copy_odd(n):
                    for half in range(halves[n]):
                        k = before[n] + half
                        if k % 2 == 1:
                            t = n % NT
                            m = min(4, t + 1 - 4 * half)
                            v.wait_ge(s_t.sem, s_t.at(TB * p + k + 1))
                            v.wait_ge(s_tc.sem, s_tc.at(TB * p + k))
                            v.wait_ge(s_o.sem, s_o.at(N * p + n - 1))
                            nc.vector.tensor_copy(pT[:, n % 2, 4 * half:4 * half + m, :], psT[:, 1, 0:m, :]).then_inc(s_tc.sem, s_tc.unit)

                def write(n):
                    hh, t = divmod(n, NT)
                    v.wait_ge(s_p.sem, s_p.at(N * p + n + 1))
                    nc.vector.reciprocal(rden[:, n % 2:n % 2 + 1], den[:, n % 2:n % 2 + 1]).then_inc(s_r.sem, s_r.unit)
                    v.wait_ge(s_o.sem, s_o.at(N * p + n + 1))
                    v.wait_ge(s_r.sem, s_r.at(N * p + n + 1))
                    nc.vector.tensor_scalar(yb[:, t, ds(p * P + hh * HD, HD)], psO[:, n % 2, 0:HD],
                                                     rden[:, n % 2:n % 2 + 1], None, ALU.mult).then_inc(s_y.sem, s_y.unit)

                mask(0)
                for n in range(N):
                    if n + 1 < N:
                        mask(n + 1)
                    copy_odd(n)
                    if n > 0:
                        write(n - 1)
                write(N - 1)

        @block.scalar
        def _(act):
            with act.Fori(0, PAIRS) as p:
                for n in range(N):
                    t = n % NT
                    keys = (t + 1) * P
                    act.wait_ge(s_lg.sem, s_lg.at(N * p + n + 1))
                    act.wait_ge(s_t.sem, s_t.at(TB * p + (before[n - 1] if n else before[0] - halves[N - 1])))
                    act.wait_ge(s_r.sem, s_r.at(N * p + n - 1))
                    nc.scalar.activation(pr[:, n % 2, 0:keys], lg[:, n % 2, 0:keys], ACT.Exp, scale=-1.0,
                                                  bias=mn[:, n % 2:n % 2 + 1], accum_out=den[:, n % 2:n % 2 + 1]).then_inc(s_p.sem, s_p.unit)
                    for half in range(halves[n]):
                        k = before[n] + half
                        if k % 2 == 0:
                            m = min(4, t + 1 - 4 * half)
                            act.wait_ge(s_t.sem, s_t.at(TB * p + k + 1))
                            act.wait_ge(s_tc.sem, s_tc.at(TB * p + k))
                            act.wait_ge(s_o.sem, s_o.at(N * p + n - 1))
                            nc.scalar.copy(pT[:, n % 2, 4 * half:4 * half + m, :], psT[:, 0, 0:m, :]).then_inc(s_tc.sem, s_tc.unit)
                    slot, k = divmod(n, KD)
                    if k == KD - 1:
                        j = 2 * p + slot
                        act.wait_ge(s_mm.sem, s_mm.at(j + 1))
                        act.wait_ge(s_mo[slot].sem, s_mo[slot].at(p))
                        nc.scalar.copy(mod[:, slot, :], psM[0:NSEQ, :]).then_inc(s_me.sem, s_me.unit)
                        act.wait_ge(s_me.sem, s_me.at(j + 1))
                        act.dma_start(dram["mod"][:, ds((FIRST + j) * MW, MW)], mod[:, slot, :]).then_inc(s_mo[slot].sem, s_mo[slot].unit)
            for slot in range(2):
                act.wait_ge(s_mo[slot].sem, s_mo[slot].at(PAIRS))


def sampling(nc, a, ident, qT, kT, v_all, yb):
    G = B // 4
    with ExitStack() as ctx:
        new_sem = block_semaphores(nc, ctx)
        sb = lambda n, s, dt=F32: ctx.enter_context(nc.sbuf_tensor(n, s, dt))
        ps = lambda n, s: ctx.enter_context(nc.psum_tensor(n, s, F32))
        S = lambda n, unit=1, credit=0: Sem(new_sem(n), unit, credit)
        s_pass = new_sem("s_pass")
        KT_ = 8
        kt = sb("s_kt", [P, KT_, DB])
        vt = sb("s_vt", [P, 4, KT_, DB])
        kTs = sb("s_kTs", [P, PAIRS, SKEYS - NS])
        qz = sb("s_qz", [P, B, PAIRS, NS])
        qst = sb("s_qst", [P, PAIRS, NS])
        bias = sb("s_bias", [P, SKEYS])
        lg = sb("s_lg", [P, SKEYS])
        pr = lg
        pT = sb("s_pT", [P, KT_ + 1, P])
        own = sb("s_own", [P, DB])
        om = sb("s_om", [P, DB])
        sel = sb("s_sel", [P, G, NS])
        selst = sb("s_selst", [P, NS])
        mn = sb("s_mn", [P, 1])
        den = sb("s_den", [P, 1])
        rden = sb("s_rden", [P, 1])
        psK = ps("s_psK", [P, 2, PAIRS, P])
        psS = ps("s_psS", [P, 2, 512])
        psP = ps("s_psP", [P, 2, 4, P])
        psO = ps("s_psO", [P, DB])
        psY = ps("s_psY", [P, DB])
        s_in = S("s_in", 16)
        s_b = S("s_b", 16)
        s_k = [S(f"s_k{j}", 16) for j in range(2)]

        s_v = S("s_v", 16)
        s_z = S("s_z")
        s_q = S("s_q")
        s_qs = S("s_qs", 1, 1)
        s_tp = S("s_tp", 1, KT_ + 1)
        s_tc = S("s_tc", 1, 2)
        s_sc = S("s_sc", 1, 1)
        s_lg = S("s_slg", 1, 1)
        s_pr = S("s_spr", 1, 1)
        s_pt = S("s_pt", 1, 2)
        s_pc = S("s_pc", 1, 2)
        s_o = S("s_o", 1, 1)
        s_sel = S("s_ssel", 1, 1)
        s_r = S("s_r", 1)
        s_om = S("s_om", 1, 1)
        s_y = S("s_sy", 1, 1)
        s_yy = S("s_syy", 1, 1)
        block = ctx.enter_context(nc.Block())
        near = [P] * 4 + [FARM] * 4
        at = [0, P, 2 * P, 3 * P] + [NEAR + FARM * i for i in range(4)]

        @block.gpsimd
        def _(pool):
            for s in (s_qs, s_tp, s_tc, s_sc, s_lg, s_pr, s_pt, s_pc, s_o, s_sel, s_om, s_y, s_yy):
                pool.sem_inc(s.sem, s.credit)
            nc.gpsimd.memset(qz[:, :, :, :], 0.0).then_inc(s_z.sem, s_z.unit)
            nc.gpsimd.memset(yb[:, NT, :], 0.0).then_inc(s_z.sem, s_z.unit)
            pool.wait_ge(s_q.sem, s_q.at(1))
            with pool.Fori(0, G) as g:
                for c in range(4):
                    pool.wait_ge(s_sc.sem, s_sc.at(4 * g + c))
                    nc.gpsimd.tensor_copy(qst[:, :, :], qz[:, ds(4 * g + c, 1), :, :]).then_inc(s_qs.sem, s_qs.unit)
                pool.wait_ge(s_y.sem, s_y.at(g))
                pool.wait_ge(s_in.sem, s_in.at(2))
                nc.gpsimd.tensor_copy(selst[:, :], sel[:, ds(g, 1), :]).then_inc(s_sel.sem, s_sel.unit)

        @block.sync
        def _(sp):
            sp.dma_start(own[:, :], a["k_own"]).then_inc(s_in.sem, s_in.unit)
            sp.dma_start(sel[:, :, :], a["k_sel"]).then_inc(s_in.sem, s_in.unit)

            def load(cache, b, dst, s, far_free=None):
                rows = cache[ds(b, 1), :, :, :].rearrange("o s h d -> (o s) (h d)")
                sp.dma_start(dst[:, 0:4, :], rows[PAST - NEAR:PAST, :].rearrange("(p i) n -> p i n", i=4)).then_inc(s[0].sem, s[0].unit)
                if far_free is not None:
                    sp.wait_ge(s_tp.sem, s_tp.at(far_free))
                    sp.sem_inc(s_pass, 1)
                sp.dma_start(dst[0:FARM, 4:8, :], rows[0:PAST - NEAR, :].rearrange("(m i) n -> m i n", i=16)[:, 0:4, :]).then_inc(s[1].sem, s[1].unit)

            with sp.Fori(0, G) as g:
                sp.wait_ge(s_lg.sem, s_lg.at(g))
                sp.dma_start(bias[:, :], a["k_sbias"][:, ds(g, 1), :].rearrange("p o n -> p (o n)")).then_inc(s_b.sem, s_b.unit)
                for c in range(4):
                    sp.wait_ge(s_tp.sem, s_tp.at(KT_ * (4 * g + c - 1) + 4))
                    sp.sem_inc(s_pass, 1)
                    load(a["cache_win_k"], 4 * g + c, kt, s_k, KT_ * (4 * g + c))
                    if c == 0:
                        sp.wait_ge(s_o.sem, s_o.at(g))
                        sp.sem_inc(s_pass, 1)
                    load(a["cache_win_v"], 4 * g + c, vt[:, c, :, :], (s_v, s_v))

        @block.tensor
        def _(pe):
            with pe.Fori(0, G) as g:
                for c in range(4):
                    for i in range(KT_):
                        if i % 4 == 0:
                            pe.wait_ge(s_k[i // 4].sem, s_k[i // 4].at(4 * g + c + 1))
                        n = KT_ * (4 * g + c) + i
                        pe.wait_ge(s_tc.sem, s_tc.at(n - 1))
                        for p in range(PAIRS):
                            last = nc.tensor.transpose(psK[:, i % 2, p, 0:near[i]], kt[0:near[i], i, p * P:(p + 1) * P],
                                                       ident[0:near[i], 0:near[i]])
                        last.then_inc(s_tp.sem, s_tp.unit)
                    pe.wait_ge(s_tc.sem, s_tc.at(KT_ * (4 * g + c) + KT_))
                    pe.wait_ge(s_qs.sem, s_qs.at(4 * g + c + 1))
                    if c == 0:
                        pe.wait_ge(s_lg.sem, s_lg.at(g))
                    for lo, n, src in ((0, 512, kTs[:, :, 0:512]), (512, 384, kTs[:, :, 512:896]), (896, NS, kT[:, :, SEQ:TOK])):
                        for p in range(PAIRS):
                            last = nc.tensor.matmul(psS[NS * c:NS * (c + 1), lo // 512, lo % 512:lo % 512 + n], qst[:, p, :], src[:, p, :],
                                                    start=(p == 0), stop=(p == PAIRS - 1))
                    last.then_inc(s_sc.sem, s_sc.unit)
                pe.wait_ge(s_pr.sem, s_pr.at(g + 1))
                keys = near + [NS]
                start = at + [SKEYS - NS]
                for r, tiles in enumerate(((0, 1, 2, 3), (4, 5, 6, 7), (8,))):
                    pe.wait_ge(s_pc.sem, s_pc.at(3 * g + max(0, r - 1)))
                    for j, i in enumerate(tiles):
                        last = nc.tensor.transpose(psP[0:keys[i], r % 2, j, :],
                                                   pr[:, start[i]:start[i] + keys[i]], ident[:, :])
                    last.then_inc(s_pt.sem, s_pt.unit)
                pe.wait_ge(s_pc.sem, s_pc.at(3 * g + 3))
                pe.wait_ge(s_v.sem, s_v.at(8 * g + 8))
                pe.wait_ge(s_om.sem, s_om.at(g))
                for c in range(4):
                    for i in range(KT_ + 1):
                        rhs = vt[0:keys[i], c, i, :] if i < KT_ else v_all[0:NS, NT, :]
                        last = nc.tensor.matmul(psO[NS * c:NS * (c + 1), :], pT[0:keys[i], i, NS * c:NS * (c + 1)], rhs,
                                                start=(i == 0), stop=(i == KT_))
                last.then_inc(s_o.sem, s_o.unit)
                pe.wait_ge(s_om.sem, s_om.at(g + 1))
                pe.wait_ge(s_sel.sem, s_sel.at(g + 1))
                pe.wait_ge(s_yy.sem, s_yy.at(g))
                nc.tensor.matmul(psY[0:NS, :], selst[:, :], om[:, :], start=True, stop=True).then_inc(s_y.sem, s_y.unit)

        @block.scalar
        def _(act):
            with act.Fori(0, G) as g:
                for c in range(4):
                    for i in range(1, KT_, 2):
                        n = KT_ * (4 * g + c) + i
                        act.wait_ge(s_tp.sem, s_tp.at(n + 1))
                        act.wait_ge(s_tc.sem, s_tc.at(n))
                        act.wait_ge(s_sc.sem, s_sc.at(4 * g + c))
                        nc.scalar.copy(kTs[:, :, at[i]:at[i] + near[i]], psK[:, i % 2, :, 0:near[i]]).then_inc(s_tc.sem, s_tc.unit)
                act.wait_ge(s_lg.sem, s_lg.at(g + 1))
                act.wait_ge(s_pt.sem, s_pt.at(3 * g))
                nc.scalar.activation(pr[:, :], lg[:, :], ACT.Exp, scale=-1.0, bias=mn[:, :], accum_out=den[:, :]).then_inc(s_pr.sem, s_pr.unit)
                act.wait_ge(s_pt.sem, s_pt.at(3 * g + 2))
                act.wait_ge(s_pc.sem, s_pc.at(3 * g + 1))
                act.wait_ge(s_o.sem, s_o.at(g))
                nc.scalar.copy(pT[0:FARM, 4:8, :], psP[0:FARM, 1, :, :]).then_inc(s_pc.sem, s_pc.unit)

        @block.vector
        def _(v):
            v.wait_ge(s_z.sem, s_z.at(2))
            for p in range(PAIRS):
                for hh in range(2):
                    part = slice(64 * hh, 64 * hh + 64)
                    h = 2 * p + hh
                    last = nc.vector.tensor_copy(qz[part, :, p, TS * h:TS * (h + 1)],
                                                 qT[part, p, SEQ:TOK].rearrange("p (b t) -> p b t", t=TS))
            last.then_inc(s_q.sem, s_q.unit)
            v.wait_ge(s_in.sem, s_in.at(2))
            with v.Fori(0, G) as g:
                for c in range(4):
                    for i in range(0, KT_, 2):
                        n = KT_ * (4 * g + c) + i
                        v.wait_ge(s_tp.sem, s_tp.at(n + 1))
                        v.wait_ge(s_tc.sem, s_tc.at(n))
                        v.wait_ge(s_sc.sem, s_sc.at(4 * g + c))
                        nc.vector.tensor_copy(kTs[:, :, at[i]:at[i] + near[i]], psK[:, i % 2, :, 0:near[i]]).then_inc(s_tc.sem, s_tc.unit)
                v.wait_ge(s_sc.sem, s_sc.at(4 * g + 4))
                v.wait_ge(s_pt.sem, s_pt.at(3 * g))
                v.wait_ge(s_b.sem, s_b.at(g + 1))
                v.sem_inc(s_pass, 1)
                nc.vector.tensor_tensor_reduce(
                    out=lg[:, :], in0=psS[:, :, :].rearrange("p a n -> p (a n)")[:, 0:SKEYS], in1=bias[:, :],
                    scale=-0.125, scalar=3e38, op0=ALU.add, op1=ALU.min, accum_out=mn[:, :]).then_inc(s_lg.sem, s_lg.unit)
                v.wait_ge(s_pt.sem, s_pt.at(3 * g + 1))
                v.wait_ge(s_pc.sem, s_pc.at(3 * g))
                v.wait_ge(s_o.sem, s_o.at(g))
                nc.vector.tensor_copy(pT[:, 0:4, :], psP[:, 0, :, :]).then_inc(s_pc.sem, s_pc.unit)
                v.wait_ge(s_pt.sem, s_pt.at(3 * g + 3))
                v.wait_ge(s_pc.sem, s_pc.at(3 * g + 2))
                nc.vector.tensor_copy(pT[0:NS, 8, :], psP[0:NS, 0, 0, :]).then_inc(s_pc.sem, s_pc.unit)
                nc.vector.reciprocal(rden[:, :], den[:, :]).then_inc(s_r.sem, s_r.unit)
                v.wait_ge(s_r.sem, s_r.at(g + 1))
                v.wait_ge(s_o.sem, s_o.at(g + 1))
                v.wait_ge(s_y.sem, s_y.at(g))
                nc.vector.scalar_tensor_tensor(out=om[:, :], in0=psO[:, :], scalar=rden[:, :], in1=own[:, :],
                                                         op0=ALU.mult, op1=ALU.mult).then_inc(s_om.sem, s_om.unit)
                v.wait_ge(s_y.sem, s_y.at(g + 1))
                v.wait_ge(s_yy.sem, s_yy.at(g))
                nc.vector.tensor_tensor(yb[0:NS, NT, :], yb[0:NS, NT, :], psY[0:NS, :], ALU.add).then_inc(s_yy.sem, s_yy.unit)


def mixing(nc, a, out, dram, ident, cols, ya, yb, ssq, logits):
    GA, GB = 32, 36
    with ExitStack() as ctx:
        new_sem = block_semaphores(nc, ctx)
        sb = lambda n, s, dt=F32: ctx.enter_context(nc.sbuf_tensor(n, s, dt))
        ps = lambda n, s: ctx.enter_context(nc.psum_tensor(n, s, F32))
        S = lambda n, unit=1, credit=0: Sem(new_sem(n), unit, credit)
        s_pass = new_sem("x_pass")
        wo = sb("wo", [P, 2 * CT, D])
        names = {"gt1": 2, "sh2": 3, "sc2": 4}
        mods = {k: sb(f"x_{k}", [P, D]) for k in names}
        modq = {k: sb(f"xs_{k}", [NS, D]) for k in names}
        lng = sb("x_lng", [P, D])
        lnb = sb("x_lnb", [P, D])
        wr = sb("x_wr", [P, KD, NG + NE])
        br = sb("x_br", [P, NG + NE])
        yas = sb("x_yas", [P, 2, CT, P])
        ybs = sb("x_ybs", [P, 2, DB])
        ybT = sb("x_ybT", [P, CT, P])
        xt = sb("x_xt", [P, 2, D])
        tb = sb("x_tb", [P, D])
        z = sb("x_z", [P, 2, D])
        x1 = sb("x_x1", [P, 2, D])
        u2 = sb("x_u2", [P, 2, D])
        u2T = sb("x_u2T", [P, KD, P])
        sqd = sb("x_sqd", [P, DB])
        rab = sb("x_rab", [P, 2, NT + 1])
        half = sb("x_half", [P, 2 * (NT + 1)])
        stt = sb("x_st", [P, 2, 6])
        mv = sb("x_mv", [P, 2])
        rs = sb("x_rs", [P, 1])
        mv9 = sb("x_ssb", [P, NT + 1])
        psA = ps("x_psA", [P, 2, 512])
        psB = ps("x_psB", [P, 2, 512])
        psY = ps("x_psY", [P, CT, P])
        psU = ps("x_psU", [P, KD, P])
        psL = ps("x_psL", [P, 512])
        s_w = [S(f"x_w{j}", 16) for j in range(2)]
        s_c = S("x_c", 16)
        s_x = [S(f"x_xt{p}", 16) for p in range(2)]
        s_z0 = S("x_z0")
        s_ss = S("x_ss")
        s_rab = S("x_rab")
        s_sqd = new_sem("x_sqd")
        s_ws = S("x_ws")
        s_ya = S("x_ya", 1)
        s_yt = S("x_yt", 1, 1)
        s_ye = S("x_ye", 1, 1)
        s_mb = S("x_mb")
        s_mm = S("x_mm", 1, 2)
        s_tb = S("x_tb", 1, 1)
        s_z = S("x_z", 1, 2)
        s_ch = new_sem("x_ch")
        s_gain = S("x_gain")
        s_var = S("x_var", 1)
        s_rs = S("x_rs", 1)
        s_xn = S("x_xn", 1, 2)
        s_x1 = S("x_x1", 1, 2)
        s_u2 = S("x_u2", 1, 2)
        s_ut = S("x_ut", 1, 2)
        s_ue = S("x_ue", 1, 1)
        s_l = S("x_l", 1, 1)
        s_lo = S("x_lo", 1, 1)
        s_o1 = [S(f"x_o1{p}", 16, 1) for p in range(2)]
        s_o2 = [S(f"x_o2{p}", 16, 1) for p in range(2)]
        block = ctx.enter_context(nc.Block())
        modrow = dram["mod"]
        xp = a["x_prompt"].rearrange("o s d -> (o s) d")
        xsm = a["x_sample"].rearrange("b t d -> (b t) d")

        @block.sync
        def _(sp):
            w = a["w_out"].rearrange("(k p) n -> p k n", p=P)
            for j in (1, 0):
                sp.dma_start(wo[:, j * CT:(j + 1) * CT, :], w[:, j * CT:(j + 1) * CT, :]).then_inc(s_w[j].sem, s_w[j].unit)
            sp.dma_start(wr[:, :, 0:NG], a["w_router_group"].rearrange("(k p) g -> p k g", p=P)).then_inc(s_c.sem, s_c.unit)
            for g in range(NG):
                sp.dma_start(wr[:, :, NG + 4 * g:NG + 4 * g + 4], a["w_router_expert"][g].rearrange("(k p) e -> p k e", p=P)).then_inc(s_c.sem, s_c.unit)
            sp.dma_start(br[:, 0:NG], a["b_router_group"].rearrange("(o n) -> o n", o=1).to_broadcast([P, NG])).then_inc(s_c.sem, s_c.unit)
            sp.dma_start(br[:, NG:], a["b_router_expert"].rearrange("(o g) e -> o (g e)", o=1).to_broadcast([P, NE])).then_inc(s_c.sem, s_c.unit)
            sp.dma_start(lng[:, :], a["ln1_g"].rearrange("(o n) -> o n", o=1).to_broadcast([P, D])).then_inc(s_c.sem, s_c.unit)
            sp.dma_start(lnb[:, :], a["ln1_b"].rearrange("(o n) -> o n", o=1).to_broadcast([P, D])).then_inc(s_c.sem, s_c.unit)
            for k, j in names.items():
                sp.dma_start(mods[k][:, :], modrow[0:1, j * D:(j + 1) * D].to_broadcast([P, D])).then_inc(s_c.sem, s_c.unit)
                for b in range(B):
                    sp.dma_start(modq[k][TS * b:TS * (b + 1), :], modrow[1 + b:2 + b, j * D:(j + 1) * D].to_broadcast([TS, D])).then_inc(s_c.sem, s_c.unit)

            def load(t, par, rows):
                sp.wait_ge(s_z.sem, s_z.at(t - 1))
                sp.dma_start(xt[0:rows, par, :], xp[ds(t * P, P), :] if rows == P else xsm).then_inc(s_x[par].sem, s_x[par].unit)

            def store(t, par, rows):
                sp.wait_ge(s_x1.sem, s_x1.at(t + 1))
                sp.dma_start(dram["x1"][ds(t * P, rows), :], x1[0:rows, par, :]).then_inc(s_o1[par].sem, s_o1[par].unit)
                sp.wait_ge(s_u2.sem, s_u2.at(t + 1))
                sp.dma_start(dram["u2"][ds(t * P, rows), :], u2[0:rows, par, :]).then_inc(s_o2[par].sem, s_o2[par].unit)

            load(0, 0, P)
            load(1, 1, P)
            with sp.Fori(0, NT // 2 - 1) as i:
                for par in range(2):
                    load(2 * i + par + 2, par, P)
                    store(2 * i + par, par, P)
            load(NT, 0, NS)
            store(NT - 2, 0, P)
            store(NT - 1, 1, P)
            store(NT, 0, NS)
            for s in (s_o1, s_o2):
                sp.wait_ge(s[0].sem, s[0].at(NT // 2 + 1))
                sp.wait_ge(s[1].sem, s[1].at(NT // 2))

        NC = 9 + 3 * (1 + B)

        @block.gpsimd
        def _(pool):
            for s in (s_yt, s_ye, s_mm, s_tb, s_z, s_xn, s_x1, s_u2, s_ut, s_ue, s_l, s_lo):
                pool.sem_inc(s.sem, s.credit)
            for s in (*s_o1, *s_o2):
                pool.sem_inc(s.sem, 16)
            nc.gpsimd.memset(half[:, :], -0.5).then_inc(s_z0.sem, s_z0.unit)
            nc.gpsimd.memset(logits[:, NT, :], 0.0).then_inc(s_z0.sem, s_z0.unit)
            pool.wait_ge(s_ss.sem, s_ss.at(2))
            pool.wait_ge(s_z0.sem, s_z0.at(1))
            nc.gpsimd.tensor_tensor(rab[:, :, :].rearrange("p a t -> p (a t)"), rab[:, :, :].rearrange("p a t -> p (a t)"),
                                               half[:, :], ALU.pow).then_inc(s_rab.sem, s_rab.unit)
            pool.wait_ge(s_c.sem, s_c.at(NC))

            def tile(t, par, rows):
                pool.wait_ge(s_var.sem, s_var.at(t + 1))
                nc.gpsimd.tensor_tensor(rs[0:rows, :], mv[0:rows, 1:2], half[0:rows, 0:1], ALU.pow).then_inc(s_rs.sem, s_rs.unit)
                pool.wait_ge(s_xn.sem, s_xn.at(t + 1))
                pool.wait_ge(s_o1[par].sem, s_o1[par].at(t // 2))
                pool.wait_ge(s_u2.sem, s_u2.at(t - 1))
                nc.gpsimd.tensor_tensor(x1[0:rows, par, :], z[0:rows, par, :], lng[0:rows, :], ALU.mult).then_inc(s_gain.sem, s_gain.unit)
                pool.wait_ge(s_gain.sem, s_gain.at(t + 1))
                nc.gpsimd.tensor_tensor(x1[0:rows, par, :], x1[0:rows, par, :], lnb[0:rows, :], ALU.add).then_inc(s_x1.sem, s_x1.unit)

            with pool.Fori(0, NT // 2) as i:
                for par in range(2):
                    tile(2 * i + par, par, P)
            tile(NT, 0, NS)

        @block.vector
        def _(v):
            st = Steps(v, s_ch)
            v.wait_ge(s_c.sem, s_c.at(NC))
            st.after(nc.vector.memset(rab[:, :, NT], 1.0))
            v.wait_ge(s_ss.sem, s_ss.at(1))
            st.last()
            st.link(nc.vector.tensor_reduce(rab[:, 0, 0:NT], ssq[:, 0:NT, :], X, ALU.add))
            st.link(nc.vector.tensor_reduce(rab[0:NS, 0, NT:NT + 1], ssq[0:NS, NT, :], X, ALU.add))
            st.after(nc.vector.tensor_copy(rab[:, 1, 0:NT], mv9[:, 0:NT]))
            st.link(nc.vector.tensor_copy(rab[0:NS, 1, NT:NT + 1], mv9[0:NS, NT:NT + 1]))
            nc.vector.tensor_scalar(rab[:, :, :], rab[:, :, :], 1.0 / DA, EPS, ALU.mult, ALU.add).then_inc(s_ss.sem, s_ss.unit)
            for j in (1, 0):
                v.wait_ge(s_w[j].sem, s_w[j].at(1))
                for k in range(j * CT, (j + 1) * CT):
                    last = nc.vector.tensor_scalar(wo[:, k, :], wo[:, k, :], cols[:, GA + k:GA + k + 1], None, ALU.mult)
                last.then_inc(s_ws.sem, s_ws.unit)
            st.after(nc.vector.tensor_scalar(mods["sc2"][:, :], mods["sc2"][:, :], 1.0, None, ALU.add))
            st.link(nc.vector.tensor_scalar(modq["sc2"][:, :], modq["sc2"][:, :], 1.0, None, ALU.add))
            v.wait_ge(s_rab.sem, s_rab.at(1))

            def residual(t, par, rows):
                m = mods if rows == P else modq
                v.wait_ge(s_mm.sem, s_mm.at(t + 1))
                v.wait_ge(s_tb.sem, s_tb.at(t + 1))
                v.wait_ge(s_x1.sem, s_x1.at(t - 1))
                zt = z[0:rows, par, :]
                st.link(nc.vector.scalar_tensor_tensor(out=zt, in0=psA[0:rows, :, :].rearrange("p a n -> p (a n)"),
                                                       scalar=rab[0:rows, 0, ds(t, 1)], in1=tb[0:rows, :], op0=ALU.mult, op1=ALU.add))
                st.link(nc.vector.tensor_tensor(zt, zt, m["gt1"][0:rows, :], ALU.mult))
                v.wait_ge(s_x[par].sem, s_x[par].at(t // 2 + 1))
                nc.vector.scalar_tensor_tensor(out=zt, in0=xt[0:rows, par, :], scalar=ALPHA, in1=zt, op0=ALU.mult, op1=ALU.add).then_inc(s_z.sem, s_z.unit)
                v.wait_ge(s_z.sem, s_z.at(t + 1))
                for j in range(2):
                    st.after(nc.vector.bn_stats(stt[0:rows, j, :], z[0:rows, par, j * 512:(j + 1) * 512]))
                st.last()
                v.sem_inc(s_pass, 1)
                st.link(nc.vector.bn_aggr(mv[0:rows, :], stt[0:rows, :, :]))
                nc.vector.tensor_scalar(mv[0:rows, 1:2], mv[0:rows, 1:2], EPS, None, ALU.add).then_inc(s_var.sem, s_var.unit)

            def normalize(t, par, rows):
                v.wait_ge(s_rs.sem, s_rs.at(t + 1))
                nc.vector.tensor_scalar(z[0:rows, par, :], z[0:rows, par, :], mv[0:rows, 0:1], rs[0:rows, :], ALU.subtract, ALU.mult).then_inc(s_xn.sem, s_xn.unit)

            def modulate(t, par, rows):
                m = mods if rows == P else modq
                v.wait_ge(s_x1.sem, s_x1.at(t + 1))
                v.wait_ge(s_o2[par].sem, s_o2[par].at(t // 2))
                v.wait_ge(s_ut.sem, s_ut.at(t - 1))
                st.link(nc.vector.tensor_tensor(u2[0:rows, par, :], x1[0:rows, par, :], m["sc2"][0:rows, :], ALU.mult))
                nc.vector.tensor_tensor(u2[0:rows, par, :], u2[0:rows, par, :], m["sh2"][0:rows, :], ALU.add).then_inc(s_u2.sem, s_u2.unit)

            def route(t, rows):
                v.wait_ge(s_l.sem, s_l.at(t + 1))
                nc.vector.tensor_tensor(logits[0:rows, ds(t, 1), :], psL[0:rows, 0:NG + NE].unsqueeze(1), br[0:rows, :].unsqueeze(1), ALU.add).then_inc(s_lo.sem, s_lo.unit)

            def step(t, par, rows):
                residual(t, par, rows)
                modulate(t - 1, 1 - par, P)
                normalize(t, par, rows)
                route(t - 2, P)

            residual(0, 0, P)
            normalize(0, 0, P)
            residual(1, 1, P)
            modulate(0, 0, P)
            normalize(1, 1, P)
            st.enter(12)
            with v.Fori(1, NT // 2) as i:
                st.round(i - 1)
                for par in range(2):
                    step(2 * i + par, par, P)
            st.leave(NT // 2 - 1)
            step(NT, 0, NS)
            modulate(NT, 0, NS)
            route(NT - 1, P)
            route(NT, NS)

        @block.scalar
        def _(act):
            for t in range(NT + 1):
                rows = P if t < NT else NS
                nc.scalar.activation(sqd[0:rows, :], yb[0:rows, t, :], ACT.Square,
                                     accum_out=mv9[0:rows, t:t + 1]).then_inc(s_sqd, 1)
                act.wait_ge(s_sqd, t + 1)
            nc.scalar.copy(sqd[0:1, 0:1], mv9[0:1, 0:1]).then_inc(s_ss.sem, s_ss.unit)

            def stage(t, par, rows):
                act.wait_ge(s_mm.sem, s_mm.at(t - 1))
                nc.scalar.copy(ybs[0:rows, par, :], yb[0:rows, ds(t, 1), :])
                nc.scalar.copy(yas[:, par, :, 0:rows], ya[:, :, ds(t * P, rows)]).then_inc(s_ya.sem, s_ya.unit)

            def turned_y(t, rows):
                act.wait_ge(s_yt.sem, s_yt.at(t + 1))
                nc.scalar.copy(ybT[:, :, 0:rows], psY[:, :, 0:rows]).then_inc(s_ye.sem, s_ye.unit)

            def scaled(t, rows):
                act.wait_ge(s_mb.sem, s_mb.at(t + 1))
                act.wait_ge(s_z.sem, s_z.at(t))
                nc.scalar.activation(tb[0:rows, :], psB[0:rows, :, :].rearrange("p a n -> p (a n)"), ACT.Copy,
                                               scale=rab[0:rows, 1, ds(t, 1)]).then_inc(s_tb.sem, s_tb.unit)

            def turned_u(t, rows):
                act.wait_ge(s_ut.sem, s_ut.at(t + 1))
                act.wait_ge(s_l.sem, s_l.at(t))
                nc.scalar.copy(u2T[:, :, 0:rows], psU[:, :, 0:rows]).then_inc(s_ue.sem, s_ue.unit)

            stage(0, 0, P)
            stage(1, 1, P)
            turned_y(0, P)
            act.wait_ge(s_rab.sem, s_rab.at(1))
            for t in range(2):
                scaled(t, P)
                turned_y(t + 1, P)
                stage(t + 2, t, P)
            with act.Fori(1, NT // 2 - 1) as i:
                for par in range(2):
                    t = 2 * i + par
                    scaled(t, P)
                    turned_y(t + 1, P)
                    turned_u(t - 2, P)
                    stage(t + 2, par, P)
            scaled(NT - 2, P)
            turned_y(NT - 1, P)
            turned_u(NT - 4, P)
            stage(NT, 0, NS)
            scaled(NT - 1, P)
            turned_y(NT, NS)
            turned_u(NT - 3, P)
            scaled(NT, NS)
            turned_u(NT - 2, P)
            turned_u(NT - 1, P)
            turned_u(NT, NS)

        @block.tensor
        def _(pe):
            def turn_y(t, par, rows):
                pe.wait_ge(s_ya.sem, s_ya.at(t + 1))
                pe.wait_ge(s_ye.sem, s_ye.at(t))
                for k in range(CT):
                    last = nc.tensor.transpose(psY[:, k, 0:rows], ybs[0:rows, par, k * P:(k + 1) * P], ident[0:rows, 0:rows])
                last.then_inc(s_yt.sem, s_yt.unit)

            def product_b(t, rows):
                pe.wait_ge(s_ye.sem, s_ye.at(t + 1))
                pe.wait_ge(s_tb.sem, s_tb.at(t))
                for n in range(2):
                    for k in range(CT):
                        last = nc.tensor.matmul(psB[0:rows, n, :], ybT[:, k, 0:rows], wo[:, CT + k, n * 512:(n + 1) * 512],
                                                start=(k == 0), stop=(k == CT - 1))
                last.then_inc(s_mb.sem, s_mb.unit)

            def product_a(t, par, rows):
                pe.wait_ge(s_z.sem, s_z.at(t))
                for n in range(2):
                    for k in range(CT):
                        last = nc.tensor.matmul(psA[0:rows, n, :], yas[:, par, k, 0:rows], wo[:, k, n * 512:(n + 1) * 512],
                                                start=(k == 0), stop=(k == CT - 1))
                last.then_inc(s_mm.sem, s_mm.unit)

            def turn_u(t, par, rows):
                pe.wait_ge(s_u2.sem, s_u2.at(t + 1))
                pe.wait_ge(s_ue.sem, s_ue.at(t))
                for k in range(KD):
                    last = nc.tensor.transpose(psU[:, k, 0:rows], u2[0:rows, par, k * P:(k + 1) * P], ident[0:rows, 0:rows])
                last.then_inc(s_ut.sem, s_ut.unit)

            def router(t, rows):
                pe.wait_ge(s_ue.sem, s_ue.at(t + 1))
                pe.wait_ge(s_lo.sem, s_lo.at(t))
                for k in range(KD):
                    last = nc.tensor.matmul(psL[0:rows, 0:NG + NE], u2T[:, k, 0:rows], wr[:, k, :], start=(k == 0), stop=(k == KD - 1))
                last.then_inc(s_l.sem, s_l.unit)

            turn_y(0, 0, P)
            pe.wait_ge(s_ws.sem, s_ws.at(1))
            product_b(0, P)
            turn_y(1, 1, P)
            pe.wait_ge(s_ws.sem, s_ws.at(2))
            product_a(0, 0, P)
            product_b(1, P)
            turn_y(2, 0, P)
            product_a(1, 1, P)
            pe.wait_ge(s_c.sem, s_c.at(NC))
            with pe.Fori(1, NT // 2 - 1) as i:
                for par in range(2):
                    t = 2 * i + par
                    product_b(t, P)
                    turn_y(t + 1, 1 - par, P)
                    turn_u(t - 2, par, P)
                    product_a(t, par, P)
                    router(t - 2, P)
            product_b(NT - 2, P)
            turn_y(NT - 1, 1, P)
            turn_u(NT - 4, 0, P)
            product_a(NT - 2, 0, P)
            router(NT - 4, P)
            product_b(NT - 1, P)
            turn_y(NT, 0, NS)
            turn_u(NT - 3, 1, P)
            product_a(NT - 1, 1, P)
            router(NT - 3, P)
            product_b(NT, NS)
            turn_u(NT - 2, 0, P)
            product_a(NT, 0, NS)
            router(NT - 2, P)
            turn_u(NT - 1, 1, P)
            router(NT - 1, P)
            turn_u(NT, 0, NS)
            router(NT, NS)


def routing(nc, a, out, dram, ident, logits, route, ew):
    NTT = NT + 1
    with ExitStack() as ctx:
        new_sem = block_semaphores(nc, ctx)
        sb = lambda n, s, dt=F32: ctx.enter_context(nc.sbuf_tensor(n, s, dt))
        ps = lambda n, s: ctx.enter_context(nc.psum_tensor(n, s, F32))
        S = lambda n, unit=1, credit=0: Sem(new_sem(n), unit, credit)
        ranks = sb("ranks", [P, 4])
        valid = sb("valid", [P, NTT])
        before = sb("before", [P, P])
        ones = sb("ones_r", [P, P])
        restart = sb("restart", [P, NE, NTT])
        steps_ = sb("steps", [P, NTT])
        tiles_k = sb("tiles_k", [P, SLOT_TILES])
        tokid = sb("tokid", [P, NTT])
        zero = sb("zero_r", [SLOT_TILES, P])
        m1 = sb("m1", [P, NTT])
        m2 = sb("m2", [P, NTT])
        pg = sb("pg", [P, NTT])
        e1 = sb("e1", [P, NTT])
        r1 = sb("r1", [P, NTT])
        d4 = sb("d4", [P, NTT, 4])
        x4 = sb("x4", [P, NTT, 4])
        oh = sb("oh", [P, 3, NTT, 4])
        sel = sb("rsel", [P, NTT, 4])
        t16 = sb("t16", [P, NTT, 4, 4])
        hot = sb("hot", [P, 2, NTT, NE])
        both = sb("both", [P, NTT, NE])
        tot = sb("tot", [P, NE, NTT])
        base = sb("base", [P, NE, NTT])
        shifted = sb("shifted", [P, NE, NTT])
        count = sb("count", [P, NE])
        cmp = sb("cmp", [P, NE, NTT - 1])
        ntl = sb("ntl", [P, NE])
        one16 = sb("one16", [P, NE])
        end = sb("end_f", [P, NE])
        first = sb("first_f", [P, NE])
        slotE = sb("slotE", [P, NE, NTT])
        pick = sb("pick", [P, NTT, NE])
        slot = sb("slot_f", [P, 2, NTT])
        ek = sb("ek", [P, SLOT_TILES, NE])
        ekr = sb("ekr", [P, SLOT_TILES])
        idrow = sb("idrow", [SLOT_TILES, P])
        even = sb("even", [1, SLOT_TILES // 2 - 1, 1])
        npair = sb("npair", [1, 1])
        psW = ps("o_psW", [P, NTT, NE])
        psC = ps("o_psC", [P, NTT, NE])
        psI = ps("o_psI", [P, SLOT_TILES])
        s_in = S("o_in", 16)
        s_zr = S("o_zr")
        s_z = S("o_z", 16)
        s_ch = new_sem("o_ch")
        s_d = S("o_d")
        s_e = S("o_e")
        s_m = S("o_m")
        s_pe = S("o_pe")
        s_slot = S("o_slot")
        s_sc = S("o_sc", 16)
        s_id = S("o_id", 16)
        s_it = S("o_it")
        block = ctx.enter_context(nc.Block())

        @block.sync
        def _(sp):
            for t, n in ((ranks, "k_ranks"), (valid, "k_valid"), (before, "k_before"), (restart, "k_restart"),
                         (steps_, "k_steps"), (tiles_k, "k_tiles"), (tokid, "k_tokid")):
                sp.dma_start(t[tuple(slice(None) for _ in t.shape)], a[n]).then_inc(s_in.sem, s_in.unit)
            sp.wait_ge(s_zr.sem, s_zr.at(1))
            sp.dma_start(dram["tok"].rearrange("(k p) o -> k (p o)", p=P), zero[:, :]).then_inc(s_z.sem, s_z.unit)
            sp.sem_inc(ew["s_gu"][1].sem, 16)
            sp.sem_inc(ew["s_d"][1].sem, 16)
            for e in range(2):
                for name in ("gate", "up"):
                    sp.dma_start(ew[name][:, e * KD:(e + 1) * KD, :],
                                 a[f"w_exp_{name}"][e, :, :].rearrange("(k p) f -> p k f", p=P)).then_inc(ew["s_gu"][e].sem, 16)
            sp.wait_ge(s_sc.sem, s_sc.at(2 * NTT))
            sp.dma_start(idrow[:, :], dram["tok"].rearrange("(k p) o -> k (p o)", p=P)).then_inc(s_id.sem, s_id.unit)

        @block.gpsimd
        def _(pool):
            nc.gpsimd.memset(zero[:, :], 0.0).then_inc(s_zr.sem, s_zr.unit)
            pool.wait_ge(s_slot.sem, s_slot.at(1))
            pool.wait_ge(s_z.sem, s_z.at(1))
            pool.wait_ge(s_in.sem, s_in.at(7))
            for t in range(NTT):
                rows = P if t < NT else NS
                for k in range(2):
                    nc.gpsimd.indirect_dma_start(
                        out=dram["tok"], out_offset=bass.IndirectOffsetOnAxis(ap=route["slot"][0:rows, k, t:t + 1], axis=0),
                        in_=tokid[0:rows, t:t + 1], in_offset=None).then_inc(s_sc.sem, s_sc.unit)

        @block.scalar
        def _(act):
            act.wait_ge(s_d.sem, s_d.at(1))
            nc.scalar.activation(x4[:, :, :], d4[:, :, :], ACT.Exp).then_inc(s_e.sem, s_e.unit)
            act.wait_ge(s_d.sem, s_d.at(2))
            nc.scalar.activation(e1[:, :], m2[:, :], ACT.Exp).then_inc(s_e.sem, s_e.unit)

        @block.tensor
        def _(pe):
            pe.wait_ge(s_m.sem, s_m.at(1))
            pe.wait_ge(s_in.sem, s_in.at(7))
            nc.tensor.matmul(psW[:, :, :], before[:, :], both[:, :, :], start=True, stop=True)
            nc.tensor.matmul(psC[:, :, :], ones[:, :], both[:, :, :], start=True, stop=True).then_inc(s_pe.sem, s_pe.unit)
            pe.wait_ge(s_id.sem, s_id.at(1))
            nc.tensor.transpose(psI[:, :], idrow[:, :], ident[0:SLOT_TILES, 0:SLOT_TILES]).then_inc(s_it.sem, s_it.unit)

        @block.vector
        def _(v):
            st = Steps(v, s_ch)
            v.wait_ge(s_in.sem, s_in.at(7))
            g = logits[:, :, 0:NG]
            wide = lambda t: t.unsqueeze(2).to_broadcast([P, NTT, 4])
            r4 = ranks[:, :].unsqueeze(1).to_broadcast([P, NTT, 4])

            def first_of_max(src, mx, dst):
                st.link(nc.vector.tensor_reduce(mx, src, X, ALU.max))
                st.link(nc.vector.tensor_tensor(d4[:, :, :], src, wide(mx), ALU.is_equal))
                st.link(nc.vector.tensor_tensor(d4[:, :, :], d4[:, :, :], r4, ALU.mult))
                st.link(nc.vector.tensor_reduce(r1[:, :], d4[:, :, :], X, ALU.max))
                st.link(nc.vector.tensor_tensor(dst, d4[:, :, :], wide(r1[:, :]), ALU.is_equal))

            st.after(nc.vector.memset(ones[:, :], 1.0))
            st.after(nc.vector.memset(one16[:, :], 1.0))
            st.after(nc.vector.memset(shifted[:, :, :], 0.0))
            first_of_max(g, m1[:, :], oh[:, 0, :, :])
            nc.vector.tensor_tensor(d4[:, :, :], g, wide(m1[:, :]), ALU.subtract).then_inc(s_d.sem, s_d.unit)
            v.wait_ge(s_e.sem, s_e.at(1))
            st.link(nc.vector.tensor_reduce(r1[:, :], x4[:, :, :], X, ALU.add))
            st.link(nc.vector.reciprocal(pg[:, :], r1[:, :]))
            le = logits[:, :, NG:].rearrange("p t (g e) -> p t e g", g=NG)
            for e in range(4):
                st.after(nc.vector.tensor_tensor(t16[:, :, e, :], le[:, :, e, :], oh[:, 0, :, :], ALU.mult))
            st.last()
            st.link(nc.vector.tensor_reduce(sel[:, :, :], t16[:, :, :, :], X, ALU.add))
            first_of_max(sel[:, :, :], m1[:, :], oh[:, 1, :, :])
            st.link(nc.vector.scalar_tensor_tensor(out=sel[:, :, :], in0=oh[:, 1, :, :], scalar=NEG, in1=sel[:, :, :], op0=ALU.mult, op1=ALU.add))
            first_of_max(sel[:, :, :], m2[:, :], oh[:, 2, :, :])
            nc.vector.tensor_tensor(m2[:, :], m2[:, :], m1[:, :], ALU.subtract).then_inc(s_d.sem, s_d.unit)
            v.wait_ge(s_e.sem, s_e.at(2))
            st.link(nc.vector.tensor_scalar(r1[:, :], e1[:, :], 1.0, None, ALU.add))
            st.link(nc.vector.reciprocal(r1[:, :], r1[:, :]))
            st.link(nc.vector.tensor_tensor(route["w"][:, 0, :], r1[:, :], pg[:, :], ALU.mult))
            st.after(nc.vector.tensor_tensor(route["w"][:, 1, :], route["w"][:, 0, :], e1[:, :], ALU.mult))
            for k in range(2):
                h4 = hot[:, k, :, :].rearrange("p t (g e) -> p t g e", g=NG)
                for q in range(NG):
                    st.after(nc.vector.tensor_tensor(h4[:, :, q, :], oh[:, 1 + k, :, :],
                                                     oh[:, 0, :, q:q + 1].to_broadcast([P, NTT, 4]), ALU.mult))
            st.last()
            st.link(nc.vector.tensor_tensor(both[:, :, :], hot[:, 0, :, :], hot[:, 1, :, :], ALU.add))
            nc.vector.tensor_tensor(both[:, :, :], both[:, :, :], valid[:, :].unsqueeze(2).to_broadcast([P, NTT, NE]), ALU.mult).then_inc(s_m.sem, s_m.unit)
            v.wait_ge(s_pe.sem, s_pe.at(1))
            st.link(nc.vector.tensor_copy(tot[:, :, :], psC[:, :, :].rearrange("p t e -> p e t")))
            st.link(nc.vector.tensor_copy(shifted[:, :, 1:NTT], tot[:, :, 0:NT]))
            flat = lambda t: t[:, :, :].rearrange("p e t -> p (e t)")
            st.link(nc.vector.tensor_tensor_scan(flat(base), flat(restart), flat(shifted), 0.0, ALU.mult, ALU.add))
            st.link(nc.vector.tensor_tensor(count[:, :], base[:, :, NT], tot[:, :, NT], ALU.add))
            st.link(nc.vector.tensor_tensor(cmp[:, :, :], count[:, :].unsqueeze(2).to_broadcast([P, NE, NT]),
                                            steps_[:, 0:NT].unsqueeze(1).to_broadcast([P, NE, NT]), ALU.is_gt))
            st.link(nc.vector.tensor_reduce(ntl[:, :], cmp[:, :, :], X, ALU.add))
            st.link(nc.vector.tensor_scalar(ntl[:, :], ntl[:, :], 1.0, None, ALU.add))
            st.link(nc.vector.tensor_tensor_scan(end[:, :], one16[:, :], ntl[:, :], 0.0, ALU.mult, ALU.add))
            st.link(nc.vector.tensor_tensor(first[:, :], end[:, :], ntl[:, :], ALU.subtract))
            st.link(nc.vector.tensor_scalar(first[:, :], first[:, :], float(P), None, ALU.mult))
            st.link(nc.vector.tensor_tensor(slotE[:, :, :], psW[:, :, :].rearrange("p t e -> p e t"), base[:, :, :], ALU.add))
            st.link(nc.vector.tensor_tensor(slotE[:, :, :], slotE[:, :, :], first[:, :].unsqueeze(2).to_broadcast([P, NE, NTT]), ALU.add))
            for k in range(2):
                st.link(nc.vector.tensor_tensor(pick[:, :, :], hot[:, k, :, :], slotE[:, :, :].rearrange("p e t -> p t e"), ALU.mult))
                st.link(nc.vector.tensor_reduce(slot[:, k, :], pick[:, :, :], X, ALU.add))
            nc.vector.tensor_copy(route["slot"][:, :, :], slot[:, :, :]).then_inc(s_slot.sem, s_slot.unit)
            st.link(nc.vector.tensor_tensor(ek[:, :, :], end[:, :].unsqueeze(1).to_broadcast([P, SLOT_TILES, NE]),
                                            tiles_k[:, :].unsqueeze(2).to_broadcast([P, SLOT_TILES, NE]), ALU.is_le))
            st.link(nc.vector.tensor_reduce(ekr[:, :], ek[:, :, :], X, ALU.add))
            st.link(nc.vector.tensor_scalar(ekr[:, :], ekr[:, :], float(NE - 1), None, ALU.min))
            st.link(nc.vector.tensor_copy(route["expert"][:, :], ekr[0:1, :]))
            st.link(nc.vector.tensor_copy(route["end"][:, :], end[0:1, :]))
            st.link(nc.vector.tensor_scalar(even[:, :, :], tiles_k[0:1, :].rearrange("p (i j) -> p i j", j=2)[:, 1:, 0:1],
                                            end[0:1, NE - 1:NE], None, ALU.is_lt))
            st.link(nc.vector.tensor_reduce(npair[:, :], even[:, :, 0], X, ALU.add))
            st.link(nc.vector.tensor_copy(route["pairs"][:, :], npair[:, :]))
            v.wait_ge(s_it.sem, s_it.at(1))
            st.link(nc.vector.tensor_copy(route["ids"][:, :], psI[:, :]))


def experts(nc, a, out, dram, ident, route, ew):
    with ExitStack() as ctx:
        new_sem = block_semaphores(nc, ctx)
        sb = lambda n, s, dt=F32: ctx.enter_context(nc.sbuf_tensor(n, s, dt))
        ps = lambda n, s: ctx.enter_context(nc.psum_tensor(n, s, F32))
        S = lambda n, unit=1, credit=0: Sem(new_sem(n), unit, credit)
        s_pass = new_sem("e_pass")
        wg, wu, wd, s_gu_w, s_d_w = (ew[n] for n in ("gate", "up", "down", "s_gu", "s_d"))
        ids = sb("e_ids", [P, 2], I32)
        xg = sb("e_x", [P, 2, D])
        xT = sb("e_xT", [P, 2, KD, P])
        th = sb("e_th", [P, FE])
        th2 = sb("e_th2", [P, FE])
        hs = sb("e_h", [P, FE])
        hT = sb("e_hT", [P, 2, KF, P])
        y = sb("e_y", [P, 2, D])
        zero = sb("e_zero", [P, D])
        psT = ps("e_psT", [P, 4, P])
        psG = ps("e_psG", [P, 2, 2, FE])
        psH = ps("e_psH", [P, KF, P])
        psY = ps("e_psY", [P, 2, 512])
        s_id = S("e_id")
        s_x = [S(f"e_x{p}", 16) for p in range(2)]
        s_t = S("e_t", 1, 4)
        s_tc = S("e_tc", 1, 2)
        s_gu = S("e_gu", 1, 2)
        s_th = S("e_th", 1)
        s_h1 = S("e_h1", 1)
        s_h2 = S("e_h2", 1, 1)
        s_h = S("e_h", 1, 2)
        s_ht = S("e_ht", 1, 1)
        s_hc = S("e_hc", 1, 1)
        s_dn = S("e_dn", 1, 4)
        s_y = S("e_y", 1, 2)
        s_zero = S("e_zero")
        s_un = S("e_un", 16)
        s_o = [S(f"e_o{p}", 16, 1) for p in range(2)]
        block = ctx.enter_context(nc.Block())
        PAIRED = (SLOT_TILES - 1) // 2
        FULL = (NE - 1) // 2

        def each_pair(eng, fn):
            with eng.Fori(0, FULL) as i:
                fn(2 * i)
            n = eng.value_load(route["pairs"][0:1, 0:1], min_val=FULL, max_val=PAIRED)
            with eng.Fori(FULL, PAIRED) as i:
                with eng.If(i < n):
                    fn(2 * i)
            return 2 * n

        @block.sync
        def _(sp):
            def load_gate_up(e, slot):
                for name in ("gate", "up"):
                    sp.dma_start(ew[name][:, slot * KD:(slot + 1) * KD, :],
                                 a[f"w_exp_{name}"][ds(e, 1), :, :].rearrange("o (k p) f -> p (o k) f", p=P)).then_inc(s_gu_w[slot].sem, s_gu_w[slot].unit)

            def load_down(e, slot):
                sp.dma_start(wd[:, slot * KF:(slot + 1) * KF, :],
                             a["w_exp_down"][ds(e, 1), :, :].rearrange("o (k p) f -> p (o k) f", p=P)).then_inc(s_d_w[slot].sem, s_d_w[slot].unit)

            sp.wait_ge(s_x[0].sem, s_x[0].at(1))
            load_down(0, 0)
            load_down(1, 1)
            with sp.Fori(1, NE // 2) as i:
                for slot in range(2):
                    last = sp.value_load(route["end"][0:1, ds(2 * i + slot - 2, 1)], min_val=1, max_val=SLOT_TILES)
                    sp.wait_ge(s_gu.sem, s_gu.at(last))
                    load_gate_up(2 * i + slot, slot)
                    sp.wait_ge(s_dn.sem, s_dn.at(2 * last))
                    load_down(2 * i + slot, slot)
            n = sp.value_load(route["pairs"][0:1, 0:1], min_val=FULL, max_val=PAIRED)
            sp.wait_ge(s_zero.sem, s_zero.at(1))
            with sp.Fori(FULL + 1, PAIRED + 1) as i:
                with sp.If(i > n):
                    for par in range(2):
                        sp.dma_start(dram["y"][ds((2 * i + par) * P, P), :], zero[:, :]).then_inc(s_un.sem, s_un.unit)
                with sp.If(i <= n):
                    sp.sem_inc(s_un.sem, 2 * s_un.unit)
            sp.wait_ge(s_un.sem, s_un.at(2 * (PAIRED - FULL)))

        @block.scalar
        def _(act):
            def x_half(t, par, half):
                act.wait_ge(s_t.sem, s_t.at(2 * t + half + 1))
                act.wait_ge(s_gu.sem, s_gu.at(t - 1))
                nc.scalar.copy(xT[:, par, 4 * half:4 * half + 4, :], psT[:, :, :]).then_inc(s_tc.sem, s_tc.unit)

            def hidden(t, par):
                act.wait_ge(s_gu.sem, s_gu.at(t + 1))
                act.wait_ge(s_h1.sem, s_h1.at(t))
                nc.scalar.activation(th[:, :], psG[:, par, 0, :], ACT.Tanh, scale=0.5).then_inc(s_th.sem, s_th.unit)
                act.wait_ge(s_ht.sem, s_ht.at(t + 1))
                act.wait_ge(s_dn.sem, s_dn.at(2 * (t - 1)))
                nc.scalar.copy(hT[:, par, :, :], psH[:, :, :]).then_inc(s_hc.sem, s_hc.unit)
                act.wait_ge(s_o[par].sem, s_o[par].at(t // 2))

            def y_half(t, par, half):
                act.wait_ge(s_dn.sem, s_dn.at(2 * t + half + 1))
                nc.scalar.copy(y[:, par, half * 512:(half + 1) * 512], psY[:, half, :]).then_inc(s_y.sem, s_y.unit)

            def store(t, par):
                act.wait_ge(s_y.sem, s_y.at(2 * t + 2))
                act.dma_start(dram["y"][ds(t * P, P), :], y[:, par, :]).then_inc(s_o[par].sem, s_o[par].unit)

            def pair(t0):
                for par in range(2):
                    t = t0 + par
                    hidden(t, par)
                    for half in range(2):
                        x_half(t + 2, par, half)
                        y_half(t, par, half)
                    store(t, par)

            for par in range(2):
                for half in range(2):
                    x_half(par, par, half)
            t = each_pair(act, pair)
            for par in range(2):
                hidden(t + par, par)
                y_half(t + par, par, 0)
                y_half(t + par, par, 1)
                store(t + par, par)
            for p in range(2):
                act.wait_ge(s_o[p].sem, s_o[p].at(t // 2 + 1))
            act.sem_inc(s_pass, 1)

        @block.gpsimd
        def _(pool):
            for s in (s_t, s_tc, s_gu, s_h2, s_h, s_ht, s_hc, s_dn, s_y):
                pool.sem_inc(s.sem, s.credit)
            for s in s_o:
                pool.sem_inc(s.sem, 16)
            nc.gpsimd.memset(zero[:, :], 0.0).then_inc(s_zero.sem, s_zero.unit)

            def pair(t0):
                for par in range(2):
                    t = t0 + par
                    pool.wait_ge(s_t.sem, s_t.at(2 * (t - 1)))
                    nc.gpsimd.tensor_copy(ids[:, par:par + 1], route["ids"][:, ds(t, 1)]).then_inc(s_id.sem, s_id.unit)
                    pool.wait_ge(s_id.sem, s_id.at(t + 1))
                    pool.sem_inc(s_pass, 1)
                    nc.gpsimd.indirect_dma_start(
                        out=xg[:, par, :], out_offset=None, in_=dram["u2"],
                        in_offset=bass.IndirectOffsetOnAxis(ap=ids[:, par:par + 1], axis=0)).then_inc(s_x[par].sem, s_x[par].unit)

            pair(each_pair(pool, pair))

        @block.vector
        def _(v):
            def pair(t0):
                for par in range(2):
                    t = t0 + par
                    v.wait_ge(s_th.sem, s_th.at(t + 1))
                    nc.vector.scalar_tensor_tensor(out=th2[:, :], in0=th[:, :], scalar=1.0, in1=psG[:, par, 0, :],
                                                             op0=ALU.add, op1=ALU.mult).then_inc(s_h1.sem, s_h1.unit)
                    v.wait_ge(s_h1.sem, s_h1.at(t + 1))
                    v.wait_ge(s_ht.sem, s_ht.at(t))
                    nc.vector.scalar_tensor_tensor(out=hs[:, :], in0=th2[:, :], scalar=0.5, in1=psG[:, par, 1, :],
                                                            op0=ALU.mult, op1=ALU.mult).then_inc(s_h.sem, s_h.unit)

            pair(each_pair(v, pair))

        @block.tensor
        def _(pe):
            def turn(t, par, half):
                pe.wait_ge(s_x[par].sem, s_x[par].at(t // 2 + 1))
                pe.wait_ge(s_tc.sem, s_tc.at(2 * t + half))
                for b in range(4):
                    k = 4 * half + b
                    last = nc.tensor.transpose(psT[:, b, :], xg[:, par, k * P:(k + 1) * P], ident[:, :])
                last.then_inc(s_t.sem, s_t.unit)

            def up(t, par):
                e = pe.value_load(route["expert"][0:1, ds(t, 1)], min_val=0, max_val=NE - 1)
                pe.wait_ge(s_gu_w[0].sem, s_gu_w[0].at(2 * ((e + 2) // 2)))
                pe.wait_ge(s_gu_w[1].sem, s_gu_w[1].at(2 * ((e + 1) // 2)))
                pe.wait_ge(s_tc.sem, s_tc.at(2 * t + 2))
                pe.wait_ge(s_h.sem, s_h.at(t - 1))
                for j, w in enumerate((wg, wu)):
                    for k in range(KD):
                        last = nc.tensor.matmul(psG[:, par, j, :], xT[:, par, k, :], w[:, ds((e % 2) * KD + k, 1), :],
                                                start=(k == 0), stop=(k == KD - 1))
                last.then_inc(s_gu.sem, s_gu.unit)

            def down(t, par, turn_next):
                pe.wait_ge(s_h.sem, s_h.at(t + 1))
                pe.wait_ge(s_hc.sem, s_hc.at(t))
                for k in range(KF):
                    last = nc.tensor.transpose(psH[:, k, :], hs[:, k * P:(k + 1) * P], ident[:, :])
                last.then_inc(s_ht.sem, s_ht.unit)
                e = pe.value_load(route["expert"][0:1, ds(t, 1)], min_val=0, max_val=NE - 1)
                pe.wait_ge(s_d_w[0].sem, s_d_w[0].at((e + 2) // 2))
                pe.wait_ge(s_d_w[1].sem, s_d_w[1].at((e + 1) // 2))
                for n in range(2):
                    if turn_next:
                        turn(t + 2, par, n)
                    pe.wait_ge(s_hc.sem, s_hc.at(t + 1))
                    pe.wait_ge(s_y.sem, s_y.at(2 * t + n - 1))
                    for k in range(KF):
                        last = nc.tensor.matmul(psY[:, n, :], hT[:, par, k, :], wd[:, ds((e % 2) * KF + k, 1), n * 512:(n + 1) * 512],
                                                start=(k == 0), stop=(k == KF - 1))
                    last.then_inc(s_dn.sem, s_dn.unit)

            def pair(t0):
                for par in range(2):
                    up(t0 + par + 1, 1 - par)
                    down(t0 + par, par, True)

            turn(0, 0, 0)
            turn(0, 0, 1)
            up(0, 0)
            turn(1, 1, 0)
            turn(1, 1, 1)
            t = each_pair(pe, pair)
            up(t + 1, 1)
            down(t, 0, False)
            down(t + 1, 1, False)


def finish(nc, a, out, dram, route):
    with ExitStack() as ctx:
        new_sem = block_semaphores(nc, ctx)
        sb = lambda n, s, dt=F32: ctx.enter_context(nc.sbuf_tensor(n, s, dt))
        S = lambda n, unit=1, credit=0: Sem(new_sem(n), unit, credit)
        s_pass = new_sem("f_pass")
        gt = sb("f_gt", [P, D])
        gq = sb("f_gq", [NS, D])
        lng = sb("f_lng", [P, D])
        lnb = sb("f_lnb", [P, D])
        idx = sb("f_idx", [P, 2, 2], I32)
        y1 = sb("f_y1", [P, 2, D])
        y2 = sb("f_y2", [P, 2, D])
        x1 = sb("f_x1", [P, 2, D])
        z = sb("f_z", [P, 2, D])
        o = sb("f_o", [P, 2, D])
        stt = sb("f_st", [P, 2, 6])
        mv = sb("f_mv", [P, 2])
        rs = sb("f_rs", [P, 1])
        half = sb("f_half", [P, 1])
        s_c = S("f_c", 16)
        s_h = S("f_h")
        s_ix = S("f_ix")
        s_y = [S(f"f_y{p}", 16) for p in range(2)]
        s_x = [S(f"f_x{p}", 16) for p in range(2)]
        s_ch = new_sem("f_ch")
        s_z = S("f_sz", 1, 2)
        s_var = S("f_var")
        s_rs = S("f_rs")
        s_xn = S("f_xn")
        s_gain = S("f_gain")
        s_o = S("f_so", 1, 2)
        s_w1 = S("f_w1")
        s_out = [S(f"f_out{p}", 16, 1) for p in range(2)]
        block = ctx.enter_context(nc.Block())
        modrow = dram["mod"]
        J = 5
        yp = out["y_p"].rearrange("o s d -> (o s) d")
        ys = out["y_s"].rearrange("b t d -> (b t) d")

        @block.sync
        def _(sp):
            sp.dma_start(gt[:, :], modrow[0:1, J * D:(J + 1) * D].to_broadcast([P, D])).then_inc(s_c.sem, s_c.unit)
            for b in range(B):
                sp.dma_start(gq[TS * b:TS * (b + 1), :], modrow[1 + b:2 + b, J * D:(J + 1) * D].to_broadcast([TS, D])).then_inc(s_c.sem, s_c.unit)
            sp.dma_start(lng[:, :], a["ln2_g"].rearrange("(o n) -> o n", o=1).to_broadcast([P, D])).then_inc(s_c.sem, s_c.unit)
            sp.dma_start(lnb[:, :], a["ln2_b"].rearrange("(o n) -> o n", o=1).to_broadcast([P, D])).then_inc(s_c.sem, s_c.unit)

            def load(t, par, rows):
                sp.wait_ge(s_z.sem, s_z.at(t - 1))
                sp.dma_start(x1[0:rows, par, :], dram["x1"][ds(t * P, rows), :]).then_inc(s_x[par].sem, s_x[par].unit)

            def store(t, par, rows):
                sp.wait_ge(s_o.sem, s_o.at(t + 1))
                sp.dma_start(yp[ds(t * P, P), :] if rows == P else ys, o[0:rows, par, :]).then_inc(s_out[par].sem, s_out[par].unit)

            load(0, 0, P)
            load(1, 1, P)
            with sp.Fori(0, NT // 2 - 1) as i:
                for par in range(2):
                    load(2 * i + par + 2, par, P)
                    store(2 * i + par, par, P)
            load(NT, 0, NS)
            store(NT - 2, 0, P)
            store(NT - 1, 1, P)
            store(NT, 0, NS)
            sp.wait_ge(s_out[0].sem, s_out[0].at(NT // 2 + 1))
            sp.wait_ge(s_out[1].sem, s_out[1].at(NT // 2))

        @block.scalar
        def _(act):
            def tile(t, par, rows):
                act.wait_ge(s_y[par].sem, s_y[par].at(2 * (t // 2) + 2))
                nc.scalar.activation(y1[0:rows, par, :], y1[0:rows, par, :], ACT.Copy,
                                     scale=route["w"][0:rows, 0, ds(t, 1)]).then_inc(s_w1.sem, s_w1.unit)

            with act.Fori(0, NT // 2) as i:
                for par in range(2):
                    tile(2 * i + par, par, P)
            tile(NT, 0, NS)

        @block.gpsimd
        def _(pool):
            for s in (s_z, s_o):
                pool.sem_inc(s.sem, s.credit)
            for s in s_out:
                pool.sem_inc(s.sem, 16)
            nc.gpsimd.memset(half[:, :], -0.5).then_inc(s_h.sem, s_h.unit)

            def fetch(t, par, rows):
                pool.wait_ge(s_z.sem, s_z.at(t - 1))
                nc.gpsimd.tensor_copy(idx[0:rows, par, :], route["slot"][0:rows, :, ds(t, 1)].rearrange("p k o -> p (k o)")).then_inc(s_ix.sem, s_ix.unit)
                pool.wait_ge(s_ix.sem, s_ix.at(t + 1))
                pool.sem_inc(s_pass, 1)
                for k, y in enumerate((y1, y2)):
                    nc.gpsimd.indirect_dma_start(
                        out=y[0:rows, par, :], out_offset=None, in_=dram["y"],
                        in_offset=bass.IndirectOffsetOnAxis(ap=idx[0:rows, par, k:k + 1], axis=0)).then_inc(s_y[par].sem, s_y[par].unit)

            def deviation(t, rows):
                pool.wait_ge(s_var.sem, s_var.at(t + 1))
                nc.gpsimd.tensor_tensor(rs[0:rows, :], mv[0:rows, 1:2], half[0:rows, :], ALU.pow).then_inc(s_rs.sem, s_rs.unit)

            def gain(t, par, rows):
                pool.wait_ge(s_xn.sem, s_xn.at(t + 1))
                pool.wait_ge(s_out[par].sem, s_out[par].at(t // 2))
                nc.gpsimd.tensor_tensor(o[0:rows, par, :], z[0:rows, par, :], lng[0:rows, :], ALU.mult).then_inc(s_gain.sem, s_gain.unit)

            fetch(0, 0, P)
            fetch(1, 1, P)
            pool.wait_ge(s_h.sem, s_h.at(1))
            pool.wait_ge(s_c.sem, s_c.at(3 + B))
            with pool.Fori(0, NT // 2 - 1) as i:
                for par in range(2):
                    deviation(2 * i + par, P)
                    fetch(2 * i + par + 2, par, P)
                    gain(2 * i + par, par, P)
            deviation(NT - 2, P)
            fetch(NT, 0, NS)
            gain(NT - 2, 0, P)
            deviation(NT - 1, P)
            gain(NT - 1, 1, P)
            deviation(NT, NS)
            gain(NT, 0, NS)

        @block.vector
        def _(v):
            st = Steps(v, s_ch)
            v.wait_ge(s_c.sem, s_c.at(3 + B))

            def combine(t, par, rows):
                zt = z[0:rows, par, :]
                v.wait_ge(s_w1.sem, s_w1.at(t + 1))
                if not isinstance(t, int) or t >= 2:
                    v.wait_ge(s_gain.sem, s_gain.at(t - 1))
                st.link(nc.vector.scalar_tensor_tensor(out=zt, in0=y2[0:rows, par, :], scalar=route["w"][0:rows, 1, ds(t, 1)],
                                                       in1=y1[0:rows, par, :], op0=ALU.mult, op1=ALU.add))
                st.link(nc.vector.tensor_tensor(zt, zt, (gt if rows == P else gq)[0:rows, :], ALU.mult))
                v.wait_ge(s_x[par].sem, s_x[par].at(t // 2 + 1))
                nc.vector.scalar_tensor_tensor(out=zt, in0=x1[0:rows, par, :], scalar=ALPHA, in1=zt, op0=ALU.mult, op1=ALU.add).then_inc(s_z.sem, s_z.unit)
                v.wait_ge(s_z.sem, s_z.at(t + 1))
                for j in range(2):
                    st.after(nc.vector.bn_stats(stt[0:rows, j, :], z[0:rows, par, j * 512:(j + 1) * 512]))
                st.last()
                v.sem_inc(s_pass, 1)
                st.link(nc.vector.bn_aggr(mv[0:rows, :], stt[0:rows, :, :]))
                nc.vector.tensor_scalar(mv[0:rows, 1:2], mv[0:rows, 1:2], EPS, None, ALU.add).then_inc(s_var.sem, s_var.unit)

            def shift(t, par, rows):
                v.wait_ge(s_gain.sem, s_gain.at(t + 1))
                nc.vector.tensor_tensor(o[0:rows, par, :], o[0:rows, par, :], lnb[0:rows, :], ALU.add).then_inc(s_o.sem, s_o.unit)

            def normalize(t, par, rows):
                v.wait_ge(s_rs.sem, s_rs.at(t + 1))
                nc.vector.tensor_scalar(z[0:rows, par, :], z[0:rows, par, :], mv[0:rows, 0:1], rs[0:rows, :], ALU.subtract, ALU.mult).then_inc(s_xn.sem, s_xn.unit)

            def step(t, par, rows):
                combine(t, par, rows)
                shift(t - 1, 1 - par, P)
                normalize(t, par, rows)

            combine(0, 0, P)
            normalize(0, 0, P)
            step(1, 1, P)
            st.enter(10)
            with v.Fori(1, NT // 2) as i:
                st.round(i - 1)
                for par in range(2):
                    step(2 * i + par, par, P)
            st.leave(NT // 2 - 1)
            step(NT, 0, NS)
            shift(NT, 0, NS)


def constants():
    f = np.float32
    k = {"k_ident": np.eye(P, dtype=f)}
    pos = np.zeros((NT + 1, P), f)
    pos[:NT] = np.arange(SEQ, dtype=f).reshape(NT, P)
    pos[NT, :NS] = PAST + np.arange(NS) % TS
    half = HD // 2
    inv = (f(10000.0) ** (-np.arange(half, dtype=f) * f(2.0) / f(HD))).astype(f)
    ang = pos[:, :, None] * inv
    c, s = np.cos(ang).astype(f), np.sin(ang).astype(f)
    k["k_cos"] = np.ascontiguousarray(c.transpose(1, 0, 2))
    k["k_sin"] = np.ascontiguousarray(np.concatenate([-s, s], -1).transpose(1, 0, 2))

    def bias(count):
        return np.where(count > 0, 8.0 * np.log(np.maximum(count, 1)), NEG).astype(f)

    def windows(dist):
        live = dist >= 0
        return live * ((dist <= 128).astype(int) + ((dist % 4 == 0) & (dist <= 512)) + ((dist % 16 == 0) & (dist <= 2048)))

    dist = np.arange(P)[:, None] + (NT - 1) * P - np.arange(SEQ)[None, :]
    k["k_bias"] = bias(windows(dist))
    p = np.arange(P)
    near = np.concatenate([PAST - NEAR + 4 * p + i for i in range(4)])
    far = np.concatenate([16 * np.arange(FARM) + i for i in range(TS)])
    cached = np.concatenate([near, far])
    t = np.arange(P) % TS
    c = np.arange(P) // NS
    sb_ = np.full((P, B // 4, SKEYS), NEG, f)
    for g in range(B // 4):
        sb_[:, g, :SKEYS - NS] = bias(windows(PAST + t[:, None] - cached[None, :]))
        n = np.arange(NS)
        own = n[None, :] // TS == 4 * g + c[:, None]
        sb_[:, g, SKEYS - NS:] = bias(windows(t[:, None] - n[None, :] % TS) * own)
    k["k_sbias"] = sb_
    h = (np.arange(P) % NS) // TS
    k["k_own"] = (h[:, None] == np.arange(DB)[None, :] // HD).astype(f)
    k["k_sel"] = np.stack([(4 * g + c) * TS + t for g in range(B // 4)], 1)[:, :, None] == np.arange(NS)
    k["k_sel"] = k["k_sel"].astype(f)
    k["k_ranks"] = np.tile(np.arange(4, 0, -1, dtype=f), (P, 1))
    valid = np.ones((P, NT + 1), f)
    valid[NS:, NT] = 0
    k["k_valid"] = valid
    k["k_before"] = (p[:, None] < p[None, :]).astype(f)
    restart = np.ones((P, NE, NT + 1), f)
    restart[:, :, 0] = 0
    k["k_restart"] = restart
    k["k_steps"] = np.tile(P * np.arange(1, NT + 2, dtype=f), (P, 1))
    k["k_tiles"] = np.tile(np.arange(SLOT_TILES, dtype=f), (P, 1))
    k["k_tokid"] = (p[:, None] + P * np.arange(NT + 1)[None, :]).astype(f)
    return k


_INS = ["x_prompt", "x_sample", "state_conv", "state_rglru", "cache_win_k", "cache_win_v", "c_prompt", "c_sample",
        "w_ada", "b_ada", "w_in", "conv_w", "conv_b", "w_rg_a", "b_rg_a", "w_rg_x", "b_rg_x", "rg_lambda",
        "g_norm_a", "g_norm_b", "w_out", "ln1_g", "ln1_b", "w_router_group", "b_router_group",
        "w_router_expert", "b_router_expert", "w_exp_gate", "w_exp_up", "w_exp_down", "ln2_g", "ln2_b"]
_OUTS = [("y_p", (1, SEQ, D)), ("y_s", (B, TS, D)), ("conv_p", (1, CONVW - 1, DA)), ("h_p", (1, DA)),
         ("k_p", (1, SEQ, H, HD)), ("v_p", (1, SEQ, H, HD)), ("conv_s", (B, CONVW - 1, DA)), ("h_s", (B, DA)),
         ("k_s", (B, PAST, H, HD)), ("v_s", (B, PAST, H, HD))]
_SCRATCH = [("mod", (1 + B, NMOD * D)), ("x1", (TOK, D)), ("u2", (TOK, D)), ("tok", (SLOT_TILES * P, 1)),
            ("y", (SLOT_TILES * P, D)), ("k_new", (NS, DB)), ("v_new", (NS, DB))]


def kernel(**inputs):
    import concourse.bacc as bacc
    from concourse.bass_utils import run_bass_kernel_spmd

    nc = bacc.Bacc("TRN2", target_bir_lowering=False, num_devices=1)
    arrays = {f"in_{n}": np.ascontiguousarray(inputs[n]) for n in _INS}
    arrays.update({f"in_{n}": v for n, v in constants().items()})
    a = {n[3:]: nc.dram_tensor(n, v.shape, mybir.dt.from_np(v.dtype), kind="ExternalInput").ap() for n, v in arrays.items()}
    out = {n: nc.dram_tensor(f"out_{n}", s, F32, kind="ExternalOutput").ap() for n, s in _OUTS}
    dram = {n: nc.dram_tensor(f"scratch_{n}", s, F32, kind="Internal").ap() for n, s in _SCRATCH}
    program(nc, a, out, dram)
    r = run_bass_kernel_spmd(nc, [arrays], core_ids=[0])
    return tuple(r.results[0][f"out_{n}"] for n, _ in _OUTS)
```

```python
import math
from contextlib import ExitStack

import numpy as np
import concourse.bass as bass
from concourse import mybir

F32 = mybir.dt.float32
F32R = mybir.dt.float32r
I32 = mybir.dt.int32
ALU = mybir.AluOpType
ACT = mybir.ActivationFunctionType
X = mybir.AxisListType.X

P = 128
D = 1024
KD = D // P
SEQ = 1024
NT = SEQ // P
B = 8
TS = 4
NS = B * TS
TOK = SEQ + NS
DA = 512
CT = DA // P
DB = 512
H = 8
HD = 64
PAIRS = H // 2
PAST = 2048
NMOD = 6
NSEQ = 1 + B
MW = 512
NE = 16
NG = 4
FE = 512
KF = FE // P
SLOT_TILES = 2 * TOK // P + NE
ALPHA = 2.0 ** 0.25
EPS = 1e-5
NEG = -1e30
CONVW = 4
NEAR = 512
FARM = (PAST - NEAR) // 16
SKEYS = NEAR + TS * FARM + NS


def ds(a, n):
    return bass.ds(a, n)


class Sem:

    def __init__(self, sem, unit=1, credit=0):
        self.sem, self.unit, self.credit = sem, unit, credit

    def at(self, events):
        value = (events + self.credit) * self.unit
        assert not isinstance(value, int) or value > 0, "no wait is needed here"
        return value


class Steps:

    def __init__(self, eng, handle):
        self.eng, self.handle, self.base, self.n = eng, handle, 0, 0

    def after(self, ins):
        self.n += 1
        ins.then_inc(self.handle, 1)
        return ins

    def last(self):
        self.eng.wait_ge(self.handle, self.base + self.n)

    def link(self, ins):
        self.after(ins)
        self.last()

    def enter(self, per):
        self.outer, self.per = self.base + self.n, per

    def round(self, i):
        self.base, self.n = self.outer + i * self.per, 0

    def leave(self, rounds):
        assert self.n == self.per, (self.n, self.per)
        self.base, self.n = self.outer + rounds * self.per, 0


def block_semaphores(nc, ctx):
    taken = []

    def new(name):
        taken.append(nc.alloc_semaphore(name))
        return taken[-1]

    def clear():
        nc.clear_and_free_semaphores(taken)
        nc.all_engine_barrier()

    ctx.callback(clear)
    return new


def program(nc, a, out, dram):
    ctx = ExitStack()
    with ctx:
        def alloc(c):
            return lambda name, shape, dt=F32: c.enter_context(nc.sbuf_tensor(name, shape, dt))

        sb = alloc(ctx)
        ident = sb("ident", [P, P])
        cols = sb("cols", [P, 40])
        silu = sb("silu", [P, KD, NSEQ])
        with ExitStack() as late:
            sbl = alloc(late)
            gelu_in = sbl("gelu_in", [P, CT, TOK])
            ssq = sbl("ssq", [P, NT + 1, CT])
            logits = sbl("logits", [P, NT + 1, NG + NE])
            with ExitStack() as c2:
                sb2 = alloc(c2)
                qT = sb2("qT", [P, PAIRS, TOK])
                kT = sb2("kT", [P, PAIRS, TOK])
                v = sb2("v", [P, NT + 1, DB])
                with ExitStack() as c3:
                    uT = alloc(c3)("uT", [P, KD, TOK])
                    with ExitStack() as c4:
                        sb4 = alloc(c4)
                        new_sem = block_semaphores(nc, c4)
                        pw = {
                            "wqkv": sb4("wqkv", [P, KD, 3 * DB]),
                            "cos": sb4("cos", [P, NT + 1, HD // 2]),
                            "sin": sb4("sin", [P, NT + 1, HD]),
                            "s_w": Sem(new_sem("p_wq"), 16),
                            "s_tables": Sem(new_sem("p_tab"), 16),
                        }
                        flat = uT[:, :, :].rearrange("p k t -> p (k t)")
                        chunk = KD * MW
                        ring = [flat[:, 0:chunk], flat[:, chunk:2 * chunk]]
                        ring += [t[:, :, :].rearrange("p k t -> p (k t)")[:, 0:chunk] for t in (qT, kT)]
                        modulation(nc, a, dram, ident, cols, silu, pw, [r.rearrange("p (k n) -> p k n", k=KD) for r in ring])
                        projection(nc, a, out, dram, ident, qT, kT, v, uT, pw)
                    xa = alloc(c3)("xa", [P, CT, CONVW - 1 + SEQ])
                    xs = alloc(c3)("xs", [P, CT, B, CONVW - 1 + TS])
                    branch_in(nc, a, uT, xa, xs, gelu_in)
                    recurrence(nc, a, out, ident, cols, xa, xs, gelu_in, ssq)
                yb = sb2("yb", [P, NT + 1, DB])
                attention(nc, a, out, dram, ident, silu, qT, kT, v, yb)
                sampling(nc, a, ident, qT, kT, v, yb)
                mixing(nc, a, out, dram, ident, cols, gelu_in, yb, ssq, logits)
            with ExitStack() as c4:
                sb4 = alloc(c4)
                route = {
                    "w": sb4("w12", [P, 2, NT + 1]),
                    "slot": sb4("slot_i", [P, 2, NT + 1], I32),
                    "expert": sb4("expert_i", [1, SLOT_TILES], I32),
                    "end": sb4("end_i", [1, NE], I32),
                    "pairs": sb4("pairs_i", [1, 1], I32),
                    "ids": sb4("ids", [P, SLOT_TILES], I32),
                }
                with ExitStack() as c5:
                    sb5 = alloc(c5)
                    new_sem = block_semaphores(nc, c5)
                    ew = {
                        "gate": sb5("e_wg", [P, KD, FE]),
                        "up": sb5("e_wu", [P, KD, FE]),
                        "down": sb5("e_wd", [P, KF, D]),
                        "s_gate": Sem(new_sem("e_wgate"), 16),
                        "s_up": Sem(new_sem("e_wup"), 16),
                        "s_d": Sem(new_sem("e_wdn"), 16),
                    }
                    routing(nc, a, out, dram, ident, logits, route, ew)
                    experts(nc, a, out, dram, ident, route, ew)
                finish(nc, a, out, dram, route)


def modulation(nc, a, dram, ident, cols, silu, pw, wring):
    NCH = 2 * D // MW
    with ExitStack() as ctx:
        new_sem = block_semaphores(nc, ctx)
        sb = lambda n, s, dt=F32: ctx.enter_context(nc.sbuf_tensor(n, s, dt))
        ps = lambda n, s: ctx.enter_context(nc.psum_tensor(n, s, F32))
        crow = sb("crow", [NSEQ, D])
        th = sb("th", [NSEQ, D])
        cs = sb("cs", [NSEQ, D])
        cT = sb("cT", [P, KD, P])
        ones = sb("ones9", [1, P])
        brow = sb("brow", [1, NCH * MW])
        mod = sb("mod", [NSEQ, NCH * MW])
        rows = sb("rows", [40, P])
        psT = ps("m_psT", [P, KD * NSEQ])
        psR = ps("m_psR", [P, 40])
        psM = ps("m_psM", [P, NCH, MW])
        s_c = new_sem("m_c")
        s_rows = new_sem("m_rows")
        s_w = [Sem(new_sem(f"m_w{r}"), 16) for r in range(NCH)]
        s_th = new_sem("m_th")
        s_v = new_sem("m_v")
        s_pe = new_sem("m_pe")
        s_cT = new_sem("m_cT")
        s_mm = Sem(new_sem("m_mm"))
        s_ev = Sem(new_sem("m_ev"))
        s_out = new_sem("m_out")
        s_ones = new_sem("m_ones")
        block = ctx.enter_context(nc.Block())
        w = a["w_ada"].rearrange("(k p) n -> p k n", p=P)

        @block.sync
        def _(sp):
            sp.dma_start(crow[0:1, :], a["c_prompt"]).then_inc(s_c, 16)
            sp.dma_start(crow[1:NSEQ, :], a["c_sample"]).then_inc(s_c, 16)
            sp.dma_start(ident[:, :], a["k_ident"]).then_inc(s_c, 16)
            sp.dma_start(brow[:, :], a["b_ada"].rearrange("(o n) -> o n", o=1)[:, 0:NCH * MW]).then_inc(s_c, 16)
            r = 0
            for name, v in (("conv_w", a["conv_w"].rearrange("j (c p) -> (j c) p", p=P)),
                            ("conv_b", a["conv_b"].rearrange("(c p) -> c p", p=P)),
                            ("b_rg_a", a["b_rg_a"].rearrange("(c h) w -> c (h w)", h=2)),
                            ("b_rg_x", a["b_rg_x"].rearrange("(c h) w -> c (h w)", h=2)),
                            ("rg_lambda", a["rg_lambda"].rearrange("(c p) -> c p", p=P)),
                            ("g_norm_a", a["g_norm_a"].rearrange("(c p) -> c p", p=P)),
                            ("g_norm_b", a["g_norm_b"].rearrange("(c p) -> c p", p=P))):
                n = v.shape[0]
                sp.dma_start(rows[r:r + n, :], v).then_inc(s_rows, 16)
                r += n
            for i in range(NCH):
                sp.dma_start(wring[i], w[:, :, i * MW:(i + 1) * MW]).then_inc(s_w[i].sem, s_w[i].unit)
            sp.dma_start(pw["cos"][:, :, :], a["k_cos"]).then_inc(pw["s_tables"].sem, 16)
            sp.dma_start(pw["sin"][:, :, :], a["k_sin"]).then_inc(pw["s_tables"].sem, 16)
            w_in = a["w_in"].rearrange("(k p) n -> p k n", p=P)
            for j in range(3):
                sp.dma_start(pw["wqkv"][:, :, j * DB:(j + 1) * DB], w_in[:, :, 2 * DA + j * DB:2 * DA + (j + 1) * DB]).then_inc(pw["s_w"].sem, 16)
            sp.wait_ge(s_ev.sem, s_ev.at(NCH))
            sp.dma_start(dram["mod"][:, 0:NCH * MW], mod[:, :]).then_inc(s_out, 16)
            sp.wait_ge(s_out, 16)

        @block.gpsimd
        def _(pool):
            nc.gpsimd.memset(ones[:, :], 1.0).then_inc(s_ones, 1)
            nc.gpsimd.memset(cT[:, :, :], 0.0).then_inc(s_ones, 1)

        @block.scalar
        def _(act):
            act.wait_ge(s_c, 64)
            nc.scalar.activation(th[:, :], crow[:, :], ACT.Tanh, scale=0.5).then_inc(s_th, 1)
            for i in range(NCH):
                act.wait_ge(s_mm.sem, s_mm.at(i + 1))
                nc.scalar.copy(mod[:, i * MW:(i + 1) * MW], psM[0:NSEQ, i, :]).then_inc(s_ev.sem, s_ev.unit)

        @block.vector
        def _(v):
            v.wait_ge(s_th, 1)
            nc.vector.scalar_tensor_tensor(out=cs[:, :], in0=th[:, :], scalar=1.0, in1=crow[:, :],
                                           op0=ALU.add, op1=ALU.mult).then_inc(s_v, 1)
            v.wait_ge(s_pe, 1)
            v.wait_ge(s_ones, 2)
            nc.vector.tensor_scalar(cT[:, :, 0:NSEQ], psT[:, :].rearrange("p (k s) -> p k s", k=KD), 0.5, None,
                                    ALU.mult).then_inc(s_cT, 1)
            v.wait_ge(s_cT, 1)
            nc.vector.tensor_copy(silu[:, :, :], cT[:, :, 0:NSEQ]).then_inc(s_v, 1)
            v.wait_ge(s_pe, 2)
            nc.vector.tensor_copy(cols[:, :], psR[:, :]).then_inc(s_v, 1)

        @block.tensor
        def _(pe):
            pe.wait_ge(s_v, 1)
            for k in range(KD):
                last = nc.tensor.transpose(psT[:, k * NSEQ:(k + 1) * NSEQ], cs[:, k * P:(k + 1) * P],
                                           ident[0:NSEQ, 0:NSEQ])
            last.then_inc(s_pe, 1)
            pe.wait_ge(s_rows, 16 * 7)
            nc.tensor.transpose(psR[:, :], rows[:, :], ident[0:40, 0:40]).then_inc(s_pe, 1)
            pe.wait_ge(s_cT, 1)
            pe.wait_ge(s_ones, 2)
            for i in range(NCH):
                pe.wait_ge(s_w[i].sem, s_w[i].at(1))
                for k in range(KD):
                    nc.tensor.matmul(psM[:, i, :], cT[:, k, :], wring[i][:, k, :], start=(k == 0), stop=False)
                nc.tensor.matmul(psM[:, i, :], ones[:, :], brow[:, i * MW:(i + 1) * MW], start=False, stop=True).then_inc(s_mm.sem, s_mm.unit)


def projection(nc, a, out, dram, ident, qT, kT, v_all, uT, pw):
    with ExitStack() as ctx:
        new_sem = block_semaphores(nc, ctx)
        sb = lambda n, s, dt=F32: ctx.enter_context(nc.sbuf_tensor(n, s, dt))
        ps = lambda n, s: ctx.enter_context(nc.psum_tensor(n, s, F32))
        S = lambda n, unit=1, credit=0: Sem(new_sem(n), unit, credit)
        wq, cos, sin, s_wq = (pw[n] for n in ("wqkv", "cos", "sin", "s_w"))
        mods = {k: sb(f"mod_{k}", [P, D]) for k in ("sh", "sc")}
        modq = {k: sb(f"mods_{k}", [NS, D]) for k in ("sh", "sc")}
        xt = sb("xt", [P, 2, D])
        ut = xt
        uTs = sb("uTs", [P, 2, KD, P])
        qk = sb("qk", [P, 2, 2, DB])
        rot = sb("rot", [P, 2, 2, DB])
        tmp = sb("tmpr", [P, 2, DB])
        psT = ps("p_psT", [P, KD, P])
        psQKV = ps("p_qkv", [P, 3, DB])
        psQ = ps("p_qT", [P, 2, PAIRS, P])
        s_in = S("p_in", 16)
        s_inq = S("p_inq", 16)
        s_x = [S(f"p_x{p}", 16) for p in range(2)]
        s_ch = new_sem("p_ch")
        s_u = S("p_u", 1, 2)
        s_uT = S("p_uT", 1, 2)
        s_uTs = S("p_uTs", 1, 1)
        s_big = S("p_big", 1, 2)
        s_qkv = S("p_sqkv", 1)
        s_ev = S("p_ev", 1, 3)
        s_rot = S("p_rot", 1, 4)
        s_qT = S("p_sqT", 1, 4)
        s_qe = S("p_qe", 1, 2)
        s_ko = [S(f"p_ko{p}", 16, 1) for p in range(2)]
        s_out = new_sem("p_out")
        block = ctx.enter_context(nc.Block())
        modrow = dram["mod"]

        @block.gpsimd
        def _(pool):
            for s in (s_u, s_uT, s_uTs, s_big, s_ev, s_rot, s_qT, s_qe):
                pool.sem_inc(s.sem, s.credit)
            for s in s_ko:
                pool.sem_inc(s.sem, 16)

            def tile(t, par, rows):
                pool.wait_ge(s_uTs.sem, s_uTs.at(t + 1))
                nc.gpsimd.tensor_copy(uT[:, :, ds(t * P, rows)], uTs[:, par, :, 0:rows]).then_inc(s_big.sem, s_big.unit)

            with pool.Fori(0, NT // 2) as i:
                for par in range(2):
                    tile(2 * i + par, par, P)
            tile(NT, 0, NS)

        @block.sync
        def _(sp):
            def bcast(j, n, row):
                return modrow[row:row + 1, j * D:(j + 1) * D].to_broadcast([n, D])

            def load(t, par, rows, src):
                sp.wait_ge(s_uT.sem, s_uT.at(t - 1))
                sp.dma_start(xt[0:rows, par, :], src).then_inc(s_x[par].sem, s_x[par].unit)

            xp = a["x_prompt"].rearrange("o s d -> (o s) d")
            for j, k in ((1, "sc"), (0, "sh")):
                sp.dma_start(mods[k][:, :], bcast(j, P, 0)).then_inc(s_in.sem, s_in.unit)
            load(0, 0, P, xp[0:P, :])
            for j, k in ((1, "sc"), (0, "sh")):
                for b in range(B):
                    sp.dma_start(modq[k][TS * b:TS * (b + 1), :], bcast(j, TS, 1 + b)).then_inc(s_inq.sem, s_inq.unit)
            load(1, 1, P, xp[P:2 * P, :])
            with sp.Fori(1, NT // 2) as i:
                for par in range(2):
                    load(2 * i + par, par, P, xp[ds((2 * i + par) * P, P), :])
            load(NT, 0, NS, a["x_sample"].rearrange("b t d -> (b t) d"))

        @block.scalar
        def _(act):
            def turned(t, par, rows):
                act.wait_ge(s_uT.sem, s_uT.at(t + 1))
                act.wait_ge(s_big.sem, s_big.at(t - 1))
                nc.scalar.copy(uTs[:, par, :, 0:rows], psT[:, :, 0:rows]).then_inc(s_uTs.sem, s_uTs.unit)

            def products(t, par, rows):
                for j in range(2):
                    act.wait_ge(s_qkv.sem, s_qkv.at(3 * t + j + 1))
                    act.wait_ge(s_rot.sem, s_rot.at(2 * (t - 2) + j + 1))
                    nc.scalar.copy(qk[0:rows, par, j, :], psQKV[0:rows, j, :]).then_inc(s_ev.sem, s_ev.unit)
                act.wait_ge(s_qkv.sem, s_qkv.at(3 * t + 3))
                nc.scalar.copy(v_all[0:rows, ds(t, 1), :], psQKV[0:rows, 2:3, :]).then_inc(s_ev.sem, s_ev.unit)

            def finished(t, par, rows, k_dst, v_dst):
                for j, dst in enumerate((qT, kT)):
                    act.wait_ge(s_qT.sem, s_qT.at(2 * t + j + 1))
                    nc.scalar.copy(dst[:, :, ds(t * P, rows)], psQ[:, j, :, 0:rows]).then_inc(s_qe.sem, s_qe.unit)
                act.wait_ge(s_rot.sem, s_rot.at(2 * t + 2))
                act.dma_start(k_dst, rot[0:rows, par, 1, :]).then_inc(s_ko[par].sem, s_ko[par].unit)
                act.wait_ge(s_ev.sem, s_ev.at(3 * t + 3))
                act.dma_start(v_dst, v_all[0:rows, ds(t, 1), :]).then_inc(s_out, 16)

            kp, vp = (out[n].rearrange("o s h d -> (o s) (h d)") for n in ("k_p", "v_p"))

            def finished_prompt(t, par):
                finished(t, par, P, kp[ds(t * P, P), :], vp[ds(t * P, P), :].unsqueeze(1))

            turned(0, 0, P)
            products(0, 0, P)
            turned(1, 1, P)
            with act.Fori(0, NT // 2 - 1) as i:
                for q in range(2):
                    t = 2 * i + 1 + q
                    products(t, 1 - q, P)
                    turned(t + 1, q, P)
                    finished_prompt(t - 1, q)
            products(NT - 1, 1, P)
            turned(NT, 0, NS)
            finished_prompt(NT - 2, 0)
            products(NT, 0, NS)
            finished_prompt(NT - 1, 1)
            finished(NT, 0, NS, dram["k_new"], dram["v_new"].unsqueeze(1))
            act.wait_ge(s_out, 16 * (NT + 1))
            act.wait_ge(s_ko[0].sem, s_ko[0].at(NT // 2 + 1))
            act.wait_ge(s_ko[1].sem, s_ko[1].at(NT // 2))

        @block.vector
        def _(v):
            st = Steps(v, s_ch)
            v.wait_ge(s_in.sem, s_in.at(2))
            v.wait_ge(pw["s_tables"].sem, 32)
            st.link(nc.vector.tensor_scalar(mods["sc"][:, :], mods["sc"][:, :], 1.0, None, ALU.add))

            def modulate(t, par, rows, m):
                v.wait_ge(s_x[par].sem, s_x[par].at(t // 2 + 1))
                v.wait_ge(s_uT.sem, s_uT.at(t - 1))
                st.link(nc.vector.tensor_tensor(ut[0:rows, par, :], xt[0:rows, par, :], m["sc"][0:rows, :], ALU.mult))
                nc.vector.tensor_tensor(ut[0:rows, par, :], ut[0:rows, par, :], m["sh"][0:rows, :], ALU.add).then_inc(s_u.sem, s_u.unit)

            def rotate(t, par, rows):
                for j in range(2):
                    v.wait_ge(s_ev.sem, s_ev.at(3 * t + j + 1))
                    src = qk[0:rows, par, j, :].rearrange("p (h s e) -> p h s e", s=2, e=HD // 2)
                    o = rot[0:rows, par, j, :].rearrange("p (h s e) -> p h s e", s=2, e=HD // 2)
                    straight = tmp[0:rows, 0, :].rearrange("p (h e) -> p h e", e=HD // 2)
                    crossed = tmp[0:rows, 1, :].rearrange("p (h s e) -> p h s e", s=2, e=HD // 2)
                    c = cos[0:rows, ds(t, 1), :].to_broadcast([rows, 2 * H, HD // 2])
                    st.after(nc.vector.tensor_tensor(straight, qk[0:rows, par, j, :].rearrange("p (h e) -> p h e", e=HD // 2), c, ALU.mult))
                    for s in range(2):
                        sn = sin[0:rows, ds(t, 1), s * HD // 2:(s + 1) * HD // 2].to_broadcast([rows, H, HD // 2])
                        st.after(nc.vector.tensor_tensor(crossed[:, :, s, :], src[:, :, 1 - s, :], sn, ALU.mult))
                    st.last()
                    v.wait_ge(s_qT.sem, s_qT.at(2 * (t - 2) + j + 1))
                    if j == 1:
                        v.wait_ge(s_ko[par].sem, s_ko[par].at(t // 2))
                    nc.vector.tensor_tensor(rot[0:rows, par, j, :], tmp[0:rows, 0, :], tmp[0:rows, 1, :], ALU.add).then_inc(s_rot.sem, s_rot.unit)
                    v.wait_ge(s_rot.sem, s_rot.at(2 * t + j + 1))

            modulate(0, 0, P, mods)
            modulate(1, 1, P, mods)
            v.wait_ge(s_inq.sem, s_inq.at(2 * B))
            st.link(nc.vector.tensor_scalar(modq["sc"][:, :], modq["sc"][:, :], 1.0, None, ALU.add))
            rotate(0, 0, P)
            modulate(2, 0, P, mods)
            rotate(1, 1, P)
            modulate(3, 1, P, mods)
            st.enter(14)
            with v.Fori(1, NT // 2 - 1) as i:
                st.round(i - 1)
                for par in range(2):
                    t = 2 * i + par
                    rotate(t, par, P)
                    modulate(t + 2, par, P, mods)
            st.leave(NT // 2 - 2)
            rotate(NT - 2, 0, P)
            modulate(NT, 0, NS, modq)
            rotate(NT - 1, 1, P)
            rotate(NT, 0, NS)

        @block.tensor
        def _(pe):
            def turn(t, par, rows):
                pe.wait_ge(s_u.sem, s_u.at(t + 1))
                pe.wait_ge(s_uTs.sem, s_uTs.at(t))
                for k in range(KD):
                    last = nc.tensor.transpose(psT[:, k, 0:rows], ut[0:rows, par, k * P:(k + 1) * P],
                                               ident[0:rows, 0:rows])
                last.then_inc(s_uT.sem, s_uT.unit)

            def multiply(t, par, rows):
                pe.wait_ge(s_uTs.sem, s_uTs.at(t + 1))
                for j in range(3):
                    pe.wait_ge(s_ev.sem, s_ev.at(3 * (t - 1) + j + 1))
                    for k in range(KD):
                        last = nc.tensor.matmul(psQKV[0:rows, j, :], uTs[:, par, k, 0:rows],
                                                wq[:, k, j * DB:(j + 1) * DB], start=(k == 0), stop=(k == KD - 1))
                    last.then_inc(s_qkv.sem, s_qkv.unit)

            def turn_qk(t, par, rows):
                for j in range(2):
                    pe.wait_ge(s_rot.sem, s_rot.at(2 * t + j + 1))
                    pe.wait_ge(s_qe.sem, s_qe.at(2 * (t - 1) + j + 1))
                    for p in range(PAIRS):
                        last = nc.tensor.transpose(psQ[:, j, p, 0:rows], rot[0:rows, par, j, p * P:(p + 1) * P],
                                                   ident[0:rows, 0:rows])
                    last.then_inc(s_qT.sem, s_qT.unit)

            turn(0, 0, P)
            pe.wait_ge(s_wq.sem, s_wq.at(3))
            multiply(0, 0, P)
            turn(1, 1, P)
            with pe.Fori(0, NT // 2 - 1) as i:
                for q in range(2):
                    t = 2 * i + 1 + q
                    multiply(t, 1 - q, P)
                    turn(t + 1, q, P)
                    turn_qk(t - 1, q, P)
            multiply(NT - 1, 1, P)
            turn(NT, 0, NS)
            turn_qk(NT - 2, 0, P)
            multiply(NT, 0, NS)
            turn_qk(NT - 1, 1, P)
            turn_qk(NT, 0, NS)


def branch_in(nc, a, uT, xa, xs, ga):
    with ExitStack() as ctx:
        new_sem = block_semaphores(nc, ctx)
        sb = lambda n, s, dt=F32: ctx.enter_context(nc.sbuf_tensor(n, s, dt))
        ps = lambda n, s: ctx.enter_context(nc.psum_tensor(n, s, F32))
        S = lambda n, unit=1, credit=0: Sem(new_sem(n), unit, credit)
        w = sb("w_xg", [P, KD, P])
        wh = sb("w_xg_h", [P, 2, KD, P], F32R)
        wl = sb("w_xg_l", [P, 2, KD, P], F32R)
        uh = sb("u_h", [P, KD, TOK], F32R)
        ul = sb("u_l", [P, KD, TOK], F32R)
        psP = ps("b_psP", [P, 2, 2, 512])
        psS = ps("b_psS", [P, 2, 512])
        s_w = S("b_w", 16)
        s_wh = S("b_wh")
        s_wl = S("b_wl")
        s_uh = S("b_uh")
        s_ul = S("b_ul")
        s_mm = S("b_mm")
        s_ev = S("b_ev")
        s_es = S("b_es")
        s_z = S("b_z")
        block = ctx.enter_context(nc.Block())
        wi = a["w_in"].rearrange("(k p) n -> p k n", p=P)

        @block.sync
        def _(sp):
            for c in range(2 * CT):
                if c >= 1:
                    sp.wait_ge(s_wl.sem, s_wl.at(c))
                sp.dma_start(w[:, :, :], wi[:, :, c * P:(c + 1) * P]).then_inc(s_w.sem, s_w.unit)

        @block.gpsimd
        def _(pool):
            nc.gpsimd.memset(xa[:, :, 0:CONVW - 1], 0.0).then_inc(s_z.sem, s_z.unit)

        @block.tensor
        def _(pe):
            for c in range(2 * CT):
                pe.wait_ge(s_wl.sem, s_wl.at(c + 1))
                if c >= 2:
                    pe.wait_ge(s_ev.sem, s_ev.at(c - 1))
                    pe.wait_ge(s_es.sem, s_es.at(c - 1))
                for n, (dst, lo, m) in enumerate(((psP[:, c % 2, 0, :], 0, 512), (psP[:, c % 2, 1, :], 512, 512),
                                                  (psS[:, c % 2, 0:NS], SEQ, NS))):
                    for k in range(KD):
                        if c == 0 and n == 0:
                            pe.wait_ge(s_ul.sem, s_ul.at(k + 1))
                        nc.tensor.matmul(dst, wh[:, c % 2, k, :], uh[:, k, lo:lo + m], start=(k == 0), stop=False)
                        nc.tensor.matmul(dst, wl[:, c % 2, k, :], uh[:, k, lo:lo + m], start=False, stop=False)
                        last = nc.tensor.matmul(dst, wh[:, c % 2, k, :], ul[:, k, lo:lo + m], start=False, stop=(k == KD - 1))
                last.then_inc(s_mm.sem, s_mm.unit)

        @block.scalar
        def _(act):
            def lead(c):
                act.wait_ge(s_w.sem, s_w.at(c + 1))
                if c >= 2:
                    act.wait_ge(s_mm.sem, s_mm.at(c - 1))
                nc.scalar.copy(wh[:, c % 2, :, :], w[:, :, :]).then_inc(s_wh.sem, s_wh.unit)

            for k in range(KD):
                nc.scalar.copy(uh[:, k, :], uT[:, k, :]).then_inc(s_uh.sem, s_uh.unit)
                if k == 3:
                    lead(0)
            lead(1)
            for c in range(2 * CT):
                act.wait_ge(s_mm.sem, s_mm.at(c + 1))
                dst = xa[:, c, CONVW - 1:].rearrange("p (h n) -> p h n", h=2) if c < CT else \
                    ga[:, c - CT, 0:SEQ].rearrange("p (h n) -> p h n", h=2)
                nc.scalar.copy(dst, psP[:, c % 2, :, :]).then_inc(s_ev.sem, s_ev.unit)
                if c + 2 < 2 * CT:
                    lead(c + 2)

        @block.vector
        def _(v):
            def rest(c):
                v.wait_ge(s_wh.sem, s_wh.at(c + 1))
                nc.vector.tensor_tensor(wl[:, c % 2, :, :], w[:, :, :], wh[:, c % 2, :, :], ALU.subtract).then_inc(s_wl.sem, s_wl.unit)

            for k in range(KD):
                v.wait_ge(s_uh.sem, s_uh.at(k + 1))
                nc.vector.tensor_tensor(ul[:, k, :], uT[:, k, :], uh[:, k, :], ALU.subtract).then_inc(s_ul.sem, s_ul.unit)
                if k == 3:
                    rest(0)
            rest(1)
            for c in range(2 * CT):
                v.wait_ge(s_mm.sem, s_mm.at(c + 1))
                dst = xs[:, c, :, CONVW - 1:] if c < CT else ga[:, c - CT, SEQ:].rearrange("p (b t) -> p b t", t=TS)
                nc.vector.tensor_copy(dst, psS[:, c % 2, 0:NS].rearrange("p (b t) -> p b t", t=TS)).then_inc(s_es.sem, s_es.unit)
                if c + 2 < 2 * CT:
                    rest(c + 2)


def recurrence(nc, a, out, ident, cols, xa, xs, ga, ssq):
    CV, CB, BA, BX, LM = 0, 16, 20, 24, 28
    with ExitStack() as ctx:
        new_sem = block_semaphores(nc, ctx)
        sb = lambda n, s, dt=F32: ctx.enter_context(nc.sbuf_tensor(n, s, dt))
        ps = lambda n, s: ctx.enter_context(nc.psum_tensor(n, s, F32))
        S = lambda n, unit=1, credit=0: Sem(new_sem(n), unit, credit)
        wa = sb("wa", [P, CT, P])
        wx = sb("wx", [P, CT, P])
        st_rows = sb("st_rows", [B * (CONVW - 1) + B, DA])
        h0 = sb("h0", [P, CT, B])
        sm = sb("sm", [P, 10, CT])
        xc = sb("xc", [P, 2, TOK])
        tr = sb("tr", [P, TOK])
        ti_ = sb("ti", [P, 2, TOK])
        av_ = sb("av", [P, 2, TOK])
        tl_ = sb("tl", [P, 2, TOK])
        gg_ = sb("gg", [P, 2, TOK])
        t2 = sb("t2", [P, TOK])
        hh_ = sb("hh", [P, 2, TOK])
        sq = sb("sq", [P, TOK])
        NTAIL = B * TS + (CONVW - 1) + 1 + B
        tail = sb("tail", [P, CT, NTAIL])
        tail_rows = sb("tail_rows", [NTAIL, DA])
        one = sb("one_col", [P, 1])
        NSR = B * (CONVW - 1) + B
        psG = ps("r_psG", [P, 2, 3, 512])
        psX = ps("r_psX", [P, 512])
        psQ = ps("r_psQ", [P, 512])
        s_z = S("r_z")
        s_w = S("r_w", 16)
        s_st = S("r_st", 16)
        s_t = S("r_t")
        s_ch = new_sem("r_ch")
        s_xc = S("r_xc")
        s_g = S("r_g")
        s_a = S("r_a")
        s_ga = S("r_ga")
        s_gg = S("r_gg")
        s_sr = S("r_sr")
        s_v = S("r_v")
        s_v2 = S("r_v2")
        s_v3 = S("r_v3")
        s_cc = S("r_cc")
        s_sq = S("r_sq")
        s_ss = S("r_ss")
        s_tl = S("r_tl")
        s_tt = S("r_tt")
        s_tr = S("r_tr")
        s_out = new_sem("r_out")
        s_cp = S("r_cp", 16)
        s_ac = new_sem("r_ac")
        s_gt = new_sem("r_gt")
        s_hp = new_sem("r_hp")
        block = ctx.enter_context(nc.Block())
        TAIL_S, TAIL_P, TAIL_HP, TAIL_HS = 0, NS, NS + 3, NS + 4

        @block.gpsimd
        def _(pool):
            nc.gpsimd.memset(wa[:, :, :], 0.0).then_inc(s_z.sem, s_z.unit)
            nc.gpsimd.memset(wx[:, :, :], 0.0).then_inc(s_z.sem, s_z.unit)
            nc.gpsimd.memset(one[:, :], 1.0).then_inc(s_z.sem, s_z.unit)

        @block.sync
        def _(sp):
            sp.dma_start(st_rows[0:B * (CONVW - 1), :], a["state_conv"].rearrange("b j n -> (b j) n")).then_inc(s_st.sem, s_st.unit)
            sp.dma_start(st_rows[B * (CONVW - 1):NSR, :], a["state_rglru"]).then_inc(s_st.sem, s_st.unit)
            sp.wait_ge(s_z.sem, s_z.at(3))
            for w, src in ((wa, a["w_rg_a"]), (wx, a["w_rg_x"])):
                for h in range(2):
                    sp.dma_start(w[h * 64:(h + 1) * 64, :, h * 64:(h + 1) * 64],
                                          src.rearrange("(c h) i j -> h i c j", h=2)[h]).then_inc(s_w.sem, s_w.unit)
            kc, ko = (x.rearrange("b s h d -> b s (h d)") for x in (a["cache_win_k"], out["k_s"]))
            with sp.Fori(0, B) as b:
                sp.dma_start(ko[ds(b, 1), 0:PAST - TS, :], kc[ds(b, 1), TS:PAST, :]).then_inc(s_cp.sem, s_cp.unit)
            sp.wait_ge(s_tr.sem, s_tr.at(1))
            rows = tail_rows
            for b in range(B):
                sp.dma_start(out["conv_s"][b, :, :], rows[TS * b + 1:TS * b + TS, :]).then_inc(s_out, 16)
            sp.dma_start(out["conv_p"][0, :, :], rows[TAIL_P:TAIL_P + 3, :]).then_inc(s_out, 16)
            sp.dma_start(out["h_p"], rows[TAIL_HP:TAIL_HP + 1, :]).then_inc(s_out, 16)
            sp.dma_start(out["h_s"], rows[TAIL_HS:TAIL_HS + B, :]).then_inc(s_out, 16)
            sp.wait_ge(s_out, 16 * (B + 3))
            sp.wait_ge(s_cp.sem, s_cp.at(B))

        @block.tensor
        def _(pe):
            pe.wait_ge(s_st.sem, s_st.at(2))
            for c in range(CT):
                last = nc.tensor.transpose(psX[:, c * NSR:(c + 1) * NSR], st_rows[:, c * P:(c + 1) * P], ident[0:NSR, 0:NSR])
            last.then_inc(s_t.sem, s_t.unit)
            pe.wait_ge(s_w.sem, s_w.at(4))
            for c in range(CT + 1):
                if c < CT:
                    pe.wait_ge(s_xc.sem, s_xc.at(c + 1))
                    if c >= 1:
                        pe.wait_ge(s_a.sem, s_a.at(2 * c))
                    for j, w in enumerate((wa, wx)):
                        for n, lo, m in ((0, 0, 512), (1, 512, 512), (2, 1024, NS)):
                            last = nc.tensor.matmul(psG[:, j, n, 0:m], w[:, c, :], xc[:, c % 2, lo:lo + m], start=True, stop=True)
                        last.then_inc(s_g.sem, s_g.unit)
                if c > 0:
                    pe.wait_ge(s_sq.sem, s_sq.at(c))
                    pe.wait_ge(s_z.sem, s_z.at(3))
                    for t in range(NT + 1):
                        rows = P if t < NT else NS
                        last = nc.tensor.matmul(psQ[0:rows, t * CT + c - 1:t * CT + c], sq[:, t * P:t * P + rows], one[:, :],
                                                start=True, stop=True)
                    last.then_inc(s_ss.sem, s_ss.unit)
            pe.wait_ge(s_tl.sem, s_tl.at(CT))
            for c in range(CT):
                last = nc.tensor.transpose(psX[0:NTAIL, c * P:(c + 1) * P], tail[:, c, :], ident[:, :])
            last.then_inc(s_tt.sem, s_tt.unit)

        @block.scalar
        def _(act):
            nc.scalar.activation(sm[:, 0, :], cols[:, LM:LM + CT], ACT.Abs).then_inc(s_ac, 1)
            act.wait_ge(s_ac, 1)
            nc.scalar.activation(sm[:, 1, :], sm[:, 0, :], ACT.Exp, scale=-1.0).then_inc(s_ac, 1)
            act.wait_ge(s_ac, 2)
            nc.scalar.activation(sm[:, 2, :], sm[:, 1, :], ACT.Ln, bias=1.0).then_inc(s_ac, 1)
            act.wait_ge(s_cc.sem, s_cc.at(1))

            def gates(c):
                ti, av, tl = ti_[:, c % 2, :], av_[:, c % 2, :], tl_[:, c % 2, :]
                if c >= 1:
                    act.wait_ge(s_ga.sem, s_ga.at(2 * c))
                if c >= 2:
                    act.wait_ge(s_v.sem, s_v.at(c - 1))
                for j, (dst, b) in enumerate(((tr, 6), (ti, 7))):
                    act.wait_ge(s_g.sem, s_g.at(2 * c + j + 1))
                    nc.scalar.activation(dst[:, 0:SEQ].rearrange("p (h n) -> p h n", h=2), psG[:, j, 0:2, :], ACT.Tanh,
                                         scale=0.5, bias=sm[:, b, c:c + 1]).then_inc(s_gt, 1)
                    nc.scalar.activation(dst[:, SEQ:TOK], psG[:, j, 2, 0:NS], ACT.Tanh,
                                                  scale=0.5, bias=sm[:, b, c:c + 1]).then_inc(s_a.sem, s_a.unit)
                act.wait_ge(s_gt, 2 * c + 2)
                act.wait_ge(s_a.sem, s_a.at(2 * c + 2))
                nc.scalar.activation(av, tr[:, :], ACT.Exp, scale=sm[:, 4, c:c + 1], bias=sm[:, 4, c:c + 1]).then_inc(s_ga.sem, s_ga.unit)
                nc.scalar.activation(tl, tr[:, :], ACT.Tanh, scale=sm[:, 5, c:c + 1], bias=sm[:, 5, c:c + 1]).then_inc(s_ga.sem, s_ga.unit)

            def gelu(c):
                act.wait_ge(s_v3.sem, s_v3.at(c + 1))
                nc.scalar.activation(gg_[:, c % 2, :], t2[:, :], ACT.Tanh, scale=math.sqrt(2.0 / math.pi)).then_inc(s_gg.sem, s_gg.unit)

            gates(0)
            gelu(0)
            for c in range(CT):
                tl, hh = tl_[:, c % 2, :], hh_[:, c % 2, :]
                act.wait_ge(s_v2.sem, s_v2.at(c + 1))
                nc.scalar.activation(tl, tl, ACT.Sqrt, scale=0.25).then_inc(s_sr.sem, s_sr.unit)
                if c + 1 < CT:
                    gates(c + 1)
                    gelu(c + 1)
                act.wait_ge(s_v.sem, s_v.at(c + 1))
                if c >= 1:
                    act.wait_ge(s_ss.sem, s_ss.at(c))
                nc.scalar.activation(sq[:, :], ga[:, c, :], ACT.Square).then_inc(s_sq.sem, s_sq.unit)
                nc.scalar.copy(tail[:, c, TAIL_HP:TAIL_HP + 1], hh[:, SEQ - 1:SEQ]).then_inc(s_hp, 1)
                act.wait_ge(s_hp, c + 1)
                nc.scalar.copy(tail[:, c, TAIL_HS:], hh[:, SEQ:TOK].rearrange("p (b t) -> p b t", t=TS)[:, :, TS - 1]).then_inc(s_tl.sem, s_tl.unit)

        @block.vector
        def _(v):
            st = Steps(v, s_ch)
            v.wait_ge(s_t.sem, s_t.at(1))
            states = psX[:, 0:CT * NSR].rearrange("p (c r) -> p c r", c=CT)
            for c in range(CT):
                st.after(nc.vector.tensor_copy(xs[:, c, :, 0:CONVW - 1], states[:, c, 0:24].rearrange("p (b j) -> p b j", b=B)))
            st.after(nc.vector.tensor_copy(h0[:, :, :], states[:, :, 24:NSR]))
            for c in range(CT):
                st.after(nc.vector.tensor_copy(tail[:, c, 0:NS].rearrange("p (b t) -> p b t", t=TS), xs[:, c, :, CONVW - 1:]))
            st.link(nc.vector.tensor_copy(tail[:, :, TAIL_P:TAIL_P + 3], xa[:, :, SEQ:SEQ + 3]))
            v.wait_ge(s_ac, 3)
            st.link(nc.vector.tensor_scalar(sm[:, 3, :], cols[:, LM:LM + CT], -1.0, 0.0, ALU.mult, ALU.max))
            st.link(nc.vector.tensor_tensor(sm[:, 3, :], sm[:, 3, :], sm[:, 2, :], ALU.add))
            st.after(nc.vector.tensor_scalar(sm[:, 4, :], sm[:, 3, :], -4.0, None, ALU.mult))
            st.after(nc.vector.tensor_scalar(sm[:, 5, :], sm[:, 3, :], 4.0, None, ALU.mult))
            st.after(nc.vector.tensor_scalar(sm[:, 6, :], cols[:, BA:BA + CT], 0.5, None, ALU.mult))
            st.after(nc.vector.tensor_scalar(sm[:, 7, :], cols[:, BX:BX + CT], 0.5, None, ALU.mult))
            st.last()
            nc.vector.tensor_copy(sm[:, 8, :], sm[:, 7, :]).then_inc(s_cc.sem, s_cc.unit)
            def convolution(c):
                x = xc[:, c % 2, :]
                xq = x[:, SEQ:TOK].rearrange("p (b t) -> p b t", t=TS)
                for j in range(CONVW):
                    wj = cols[:, CV + 4 * j + c:CV + 4 * j + c + 1]
                    src, srq = xa[:, c, j:j + SEQ], xs[:, c, :, j:j + TS]
                    if j == 0:
                        cb = cols[:, CB + c:CB + c + 1]
                        st.after(nc.vector.tensor_scalar(x[:, 0:SEQ], src, wj, cb, ALU.mult, ALU.add))
                        st.link(nc.vector.tensor_scalar(xq, srq, wj, cb, ALU.mult, ALU.add))
                    elif j < CONVW - 1:
                        st.after(nc.vector.scalar_tensor_tensor(out=x[:, 0:SEQ], in0=src, scalar=wj, in1=x[:, 0:SEQ], op0=ALU.mult, op1=ALU.add))
                        st.link(nc.vector.scalar_tensor_tensor(out=xq, in0=srq, scalar=wj, in1=xq, op0=ALU.mult, op1=ALU.add))
                    else:
                        st.link(nc.vector.scalar_tensor_tensor(out=x[:, 0:SEQ], in0=src, scalar=wj, in1=x[:, 0:SEQ], op0=ALU.mult, op1=ALU.add))
                        nc.vector.scalar_tensor_tensor(out=xq, in0=srq, scalar=wj, in1=xq, op0=ALU.mult, op1=ALU.add).then_inc(s_xc.sem, s_xc.unit)

            def gelu_argument(c):
                g = ga[:, c, :]
                if c >= 1:
                    v.wait_ge(s_gg.sem, s_gg.at(c))
                st.link(nc.vector.tensor_tensor(t2[:, :], g, g, ALU.mult))
                st.link(nc.vector.tensor_scalar(t2[:, :], t2[:, :], 0.044715, 1.0, ALU.mult, ALU.add))
                nc.vector.tensor_tensor(t2[:, :], t2[:, :], g, ALU.mult).then_inc(s_v3.sem, s_v3.unit)

            def decay(c):
                hh, av, tl = hh_[:, c % 2, :], av_[:, c % 2, :], tl_[:, c % 2, :]
                v.wait_ge(s_ga.sem, s_ga.at(2 * c + 2))
                if c >= 2:
                    v.wait_ge(s_tl.sem, s_tl.at(c - 1))
                st.link(nc.vector.tensor_tensor(hh, av, av, ALU.mult))
                nc.vector.scalar_tensor_tensor(out=tl, in0=hh, scalar=1.0, in1=tl, op0=ALU.add, op1=ALU.mult).then_inc(s_v2.sem, s_v2.unit)

            def scan(c):
                hh, av, tl = hh_[:, c % 2, :], av_[:, c % 2, :], tl_[:, c % 2, :]
                x, g = xc[:, c % 2, :], ga[:, c, :]
                ti, gg = ti_[:, c % 2, :], gg_[:, c % 2, :]
                v.wait_ge(s_xc.sem, s_xc.at(c + 1))
                v.wait_ge(s_v2.sem, s_v2.at(c + 1))
                v.wait_ge(s_gg.sem, s_gg.at(c + 1))
                st.after(nc.vector.scalar_tensor_tensor(out=ti, in0=ti, scalar=1.0, in1=x, op0=ALU.add, op1=ALU.mult))
                st.after(nc.vector.scalar_tensor_tensor(out=gg, in0=gg, scalar=1.0, in1=g, op0=ALU.add, op1=ALU.mult))
                v.wait_ge(s_sr.sem, s_sr.at(c + 1))
                st.last()
                st.link(nc.vector.tensor_tensor(ti, ti, tl, ALU.mult))
                st.after(nc.vector.tensor_tensor_scan(hh[:, 0:SEQ], av[:, 0:SEQ], ti[:, 0:SEQ], 0.0, ALU.mult, ALU.add))
                hq, aq, uq = (z[:, SEQ:TOK].rearrange("p (b t) -> p b t", t=TS) for z in (hh, av, ti))
                for t in range(TS):
                    prev = h0[:, c, :] if t == 0 else hq[:, :, t - 1]
                    st.link(nc.vector.tensor_tensor(hq[:, :, t], aq[:, :, t], prev, ALU.mult))
                    st.link(nc.vector.tensor_tensor(hq[:, :, t], hq[:, :, t], uq[:, :, t], ALU.add))
                nc.vector.scalar_tensor_tensor(out=g, in0=gg, scalar=0.5, in1=hh, op0=ALU.mult, op1=ALU.mult).then_inc(s_v.sem, s_v.unit)
                v.wait_ge(s_v.sem, s_v.at(c + 1))

            convolution(0)
            gelu_argument(0)
            for c in range(CT):
                if c + 1 < CT:
                    convolution(c + 1)
                decay(c)
                if c + 1 < CT:
                    gelu_argument(c + 1)
                scan(c)
            v.wait_ge(s_ss.sem, s_ss.at(CT))
            st.after(nc.vector.tensor_copy(ssq[:, 0:NT, :], psQ[:, 0:NT * CT].rearrange("p (t c) -> p t c", c=CT)))
            st.after(nc.vector.tensor_copy(ssq[0:NS, NT, :], psQ[0:NS, NT * CT:(NT + 1) * CT]))
            v.wait_ge(s_tt.sem, s_tt.at(1))
            nc.vector.tensor_copy(tail_rows[:, :], psX[0:NTAIL, :]).then_inc(s_tr.sem, s_tr.unit)


def attention(nc, a, out, dram, ident, silu, qT, kT, v_all, yb):
    FIRST = 2 * D // MW
    assert NMOD * D // MW - FIRST == 2 * PAIRS and KD == NT
    with ExitStack() as ctx:
        new_sem = block_semaphores(nc, ctx)
        sb = lambda n, s, dt=F32: ctx.enter_context(nc.sbuf_tensor(n, s, dt))
        ps = lambda n, s: ctx.enter_context(nc.psum_tensor(n, s, F32))
        S = lambda n, unit=1, credit=0: Sem(new_sem(n), unit, credit)
        s_pass = new_sem("a_pass")
        bias = sb("bias", [P, SEQ])
        qp = sb("qp", [P, SEQ])
        kp = sb("kp", [P, SEQ])
        lg = sb("lg", [P, 2, SEQ])
        pr = sb("pr", [P, 2, SEQ])
        pT = sb("pT", [P, 2, NT, P])
        mn = sb("mn", [P, 2])
        den = sb("den", [P, 2])
        rden = sb("rden", [P, 2])
        psS = ps("a_psS", [P, 2, SEQ])
        psT = ps("a_psT", [P, 2, 4, P])
        psO = ps("a_psO", [P, 2, HD])
        psM = ps("a_psM", [P, MW])
        wring = sb("a_wring", [P, 2, KD, MW])
        brow = sb("a_brow", [1, 2, MW])
        mod = sb("a_mod", [NSEQ, 2, MW])
        cT = sb("a_cT", [P, KD, P])
        ones = sb("a_ones", [1, P])
        s_in = S("a_in", 16)
        s_cp = S("a_cp", 16)
        s_cT = S("a_cT")
        s_mw = [S(f"a_mw{p}", 16) for p in range(2)]
        s_mm = S("a_mm", 1, 2)
        s_me = S("a_me", 1, 1)
        s_mo = [S(f"a_mo{p}", 16, 1) for p in range(2)]
        N = 2 * NT
        s_pair = S("a_pair", 1, 0)
        s_s = S("a_s", 1, 2)
        s_lg = S("a_lg", 1, 2)
        s_p = S("a_p", 1, 2)
        s_t = S("a_t", 1, 3)
        s_tc = S("a_tc", 1, 2)
        s_o = S("a_o", 1, 2)
        s_y = S("a_y", 1, 2)
        s_r = S("a_r", 1, 2)
        block = ctx.enter_context(nc.Block())
        halves = [(t + 4) // 4 for _ in range(2) for t in range(NT)]
        before = [sum(halves[:n]) for n in range(N + 1)]
        TB = before[N]
        cv = a["cache_win_v"].rearrange("b s h d -> b s (h d)")
        ok, ov = (out[n].rearrange("b s h d -> b s (h d)") for n in ("k_s", "v_s"))

        @block.sync
        def _(sp):
            sp.dma_start(bias[:, :], a["k_bias"]).then_inc(s_in.sem, s_in.unit)
            w_ada = a["w_ada"].rearrange("(k p) n -> p k n", p=P)
            b_ada = a["b_ada"].rearrange("(o n) -> o n", o=1)
            with sp.Fori(0, PAIRS) as p:
                for slot in range(2):
                    j = 2 * p + slot
                    sp.wait_ge(s_mm.sem, s_mm.at(j - 1))
                    sp.dma_start(wring[:, slot, :, :], w_ada[:, :, ds((FIRST + j) * MW, MW)]).then_inc(s_mw[slot].sem, s_mw[slot].unit)
                    sp.dma_start(brow[:, slot, :], b_ada[:, ds((FIRST + j) * MW, MW)]).then_inc(s_mw[slot].sem, s_mw[slot].unit)
                for h in range(B // PAIRS):
                    b = (B // PAIRS) * p + h
                    sp.dma_start(ov[ds(b, 1), 0:PAST - TS, :], cv[ds(b, 1), TS:PAST, :]).then_inc(s_cp.sem, s_cp.unit)
                    for dst, new in ((ok, "k_new"), (ov, "v_new")):
                        sp.dma_start(dst[ds(b, 1), PAST - TS:PAST, :],
                                     dram[new].rearrange("(b t) n -> b t n", t=TS)[ds(b, 1), :, :]).then_inc(s_cp.sem, s_cp.unit)
            sp.wait_ge(s_cp.sem, s_cp.at(3 * B))

        @block.gpsimd
        def _(pool):
            for s in (s_s, s_lg, s_p, s_t, s_tc, s_o, s_y, s_r, s_mm, s_me):
                pool.sem_inc(s.sem, s.credit)
            for s in s_mo:
                pool.sem_inc(s.sem, 16)
            nc.gpsimd.memset(ones[:, :], 1.0).then_inc(s_cT.sem, s_cT.unit)
            nc.gpsimd.memset(cT[:, :, :], 0.0).then_inc(s_cT.sem, s_cT.unit)
            pool.wait_ge(s_cT.sem, s_cT.at(2))
            nc.gpsimd.tensor_copy(cT[:, :, 0:NSEQ], silu[:, :, :]).then_inc(s_cT.sem, s_cT.unit)
            with pool.Fori(0, PAIRS) as p:
                pool.wait_ge(s_s.sem, s_s.at(N * p))
                nc.gpsimd.tensor_copy(qp[:, :], qT[:, ds(p, 1), 0:SEQ])
                nc.gpsimd.tensor_copy(kp[:, :], kT[:, ds(p, 1), 0:SEQ]).then_inc(s_pair.sem, s_pair.unit)

        @block.tensor
        def _(pe):
            pe.wait_ge(s_cT.sem, s_cT.at(3))
            with pe.Fori(0, PAIRS) as p:
                def scores(n):
                    hh, t = divmod(n, NT)
                    pe.wait_ge(s_lg.sem, s_lg.at(N * p + n - 1))
                    keys = (t + 1) * P
                    for lo in range(0, keys, 512):
                        m = min(512, keys - lo)
                        last = nc.tensor.matmul(psS[:, n % 2, lo:lo + m], qp[64 * hh:64 * hh + 64, t * P:(t + 1) * P],
                                                kp[64 * hh:64 * hh + 64, lo:lo + m], start=True, stop=True)
                    last.then_inc(s_s.sem, s_s.unit)

                def turn(n):
                    t = n % NT
                    pe.wait_ge(s_p.sem, s_p.at(N * p + n + 1))
                    for half in range(halves[n]):
                        pe.wait_ge(s_tc.sem, s_tc.at(TB * p + before[n] + half - 1))
                        for b in range(4 * half, min(4 * half + 4, t + 1)):
                            last = nc.tensor.transpose(psT[:, (before[n] + half) % 2, b % 4, :], pr[:, n % 2, b * P:(b + 1) * P], ident[:, :])
                        last.then_inc(s_t.sem, s_t.unit)

                def values(n):
                    hh, t = divmod(n, NT)
                    pe.wait_ge(s_tc.sem, s_tc.at(TB * p + before[n + 1]))
                    pe.wait_ge(s_y.sem, s_y.at(N * p + n))
                    for b in range(t + 1):
                        last = nc.tensor.matmul(psO[:, n % 2, 0:HD], pT[:, n % 2, b, :],
                                                v_all[:, b, ds(p * P + hh * HD, HD)], start=(b == 0), stop=(b == t))
                    last.then_inc(s_o.sem, s_o.unit)

                def modulate(n):
                    slot, k = divmod(n, KD)
                    if k == 0:
                        pe.wait_ge(s_mw[slot].sem, s_mw[slot].at(2 * p + 2))
                        pe.wait_ge(s_me.sem, s_me.at(2 * p + slot))
                    nc.tensor.matmul(psM[:, :], cT[:, k, :], wring[:, slot, k, :], start=(k == 0), stop=False)
                    if k == KD - 1:
                        nc.tensor.matmul(psM[:, :], ones[:, :], brow[:, slot, :], start=False, stop=True).then_inc(s_mm.sem, s_mm.unit)

                pe.wait_ge(s_pair.sem, s_pair.at(p + 1))
                scores(0)
                for n in range(N):
                    if n + 1 < N:
                        scores(n + 1)
                    modulate(n)
                    turn(n)
                    if n > 0:
                        values(n - 1)
                values(N - 1)

        @block.vector
        def _(v):
            v.wait_ge(s_in.sem, s_in.at(1))
            with v.Fori(0, PAIRS) as p:
                def mask(n):
                    t = n % NT
                    keys = (t + 1) * P
                    v.wait_ge(s_s.sem, s_s.at(N * p + n + 1))
                    v.wait_ge(s_p.sem, s_p.at(N * p + n - 1))
                    v.sem_inc(s_pass, 1)
                    nc.vector.tensor_tensor_reduce(
                        out=lg[:, n % 2, 0:keys], in0=psS[:, n % 2, 0:keys], in1=bias[:, SEQ - keys:SEQ],
                        scale=-0.125, scalar=3e38, op0=ALU.add, op1=ALU.min, accum_out=mn[:, n % 2:n % 2 + 1]).then_inc(s_lg.sem, s_lg.unit)

                def copy_odd(n):
                    for half in range(halves[n]):
                        k = before[n] + half
                        if k % 2 == 1:
                            t = n % NT
                            m = min(4, t + 1 - 4 * half)
                            v.wait_ge(s_t.sem, s_t.at(TB * p + k + 1))
                            v.wait_ge(s_tc.sem, s_tc.at(TB * p + k))
                            v.wait_ge(s_o.sem, s_o.at(N * p + n - 1))
                            nc.vector.tensor_copy(pT[:, n % 2, 4 * half:4 * half + m, :], psT[:, 1, 0:m, :]).then_inc(s_tc.sem, s_tc.unit)

                def write(n):
                    hh, t = divmod(n, NT)
                    v.wait_ge(s_p.sem, s_p.at(N * p + n + 1))
                    nc.vector.reciprocal(rden[:, n % 2:n % 2 + 1], den[:, n % 2:n % 2 + 1]).then_inc(s_r.sem, s_r.unit)
                    v.wait_ge(s_o.sem, s_o.at(N * p + n + 1))
                    v.wait_ge(s_r.sem, s_r.at(N * p + n + 1))
                    nc.vector.tensor_scalar(yb[:, t, ds(p * P + hh * HD, HD)], psO[:, n % 2, 0:HD],
                                                     rden[:, n % 2:n % 2 + 1], None, ALU.mult).then_inc(s_y.sem, s_y.unit)

                mask(0)
                for n in range(N):
                    if n + 1 < N:
                        mask(n + 1)
                    copy_odd(n)
                    if n > 0:
                        write(n - 1)
                write(N - 1)

        @block.scalar
        def _(act):
            with act.Fori(0, PAIRS) as p:
                for n in range(N):
                    t = n % NT
                    keys = (t + 1) * P
                    act.wait_ge(s_lg.sem, s_lg.at(N * p + n + 1))
                    act.wait_ge(s_t.sem, s_t.at(TB * p + (before[n - 1] if n else before[0] - halves[N - 1])))
                    act.wait_ge(s_r.sem, s_r.at(N * p + n - 1))
                    nc.scalar.activation(pr[:, n % 2, 0:keys], lg[:, n % 2, 0:keys], ACT.Exp, scale=-1.0,
                                                  bias=mn[:, n % 2:n % 2 + 1], accum_out=den[:, n % 2:n % 2 + 1]).then_inc(s_p.sem, s_p.unit)
                    for half in range(halves[n]):
                        k = before[n] + half
                        if k % 2 == 0:
                            m = min(4, t + 1 - 4 * half)
                            act.wait_ge(s_t.sem, s_t.at(TB * p + k + 1))
                            act.wait_ge(s_tc.sem, s_tc.at(TB * p + k))
                            act.wait_ge(s_o.sem, s_o.at(N * p + n - 1))
                            nc.scalar.copy(pT[:, n % 2, 4 * half:4 * half + m, :], psT[:, 0, 0:m, :]).then_inc(s_tc.sem, s_tc.unit)
                    slot, k = divmod(n, KD)
                    if k == KD - 1:
                        j = 2 * p + slot
                        act.wait_ge(s_mm.sem, s_mm.at(j + 1))
                        act.wait_ge(s_mo[slot].sem, s_mo[slot].at(p))
                        nc.scalar.copy(mod[:, slot, :], psM[0:NSEQ, :]).then_inc(s_me.sem, s_me.unit)
                        act.wait_ge(s_me.sem, s_me.at(j + 1))
                        act.dma_start(dram["mod"][:, ds((FIRST + j) * MW, MW)], mod[:, slot, :]).then_inc(s_mo[slot].sem, s_mo[slot].unit)
            for slot in range(2):
                act.wait_ge(s_mo[slot].sem, s_mo[slot].at(PAIRS))


def sampling(nc, a, ident, qT, kT, v_all, yb):
    G = B // 4
    with ExitStack() as ctx:
        new_sem = block_semaphores(nc, ctx)
        sb = lambda n, s, dt=F32: ctx.enter_context(nc.sbuf_tensor(n, s, dt))
        ps = lambda n, s: ctx.enter_context(nc.psum_tensor(n, s, F32))
        S = lambda n, unit=1, credit=0: Sem(new_sem(n), unit, credit)
        s_pass = new_sem("s_pass")
        KT_ = 8
        kt = sb("s_kt", [P, KT_, DB])
        vt = sb("s_vt", [P, 4, KT_, DB])
        kTs = sb("s_kTs", [P, PAIRS, SKEYS - NS])
        qz = sb("s_qz", [P, B, PAIRS, NS])
        qst = sb("s_qst", [P, PAIRS, NS])
        bias = sb("s_bias", [P, SKEYS])
        lg = sb("s_lg", [P, SKEYS])
        pr = lg
        pT = sb("s_pT", [P, KT_ + 1, P])
        own = sb("s_own", [P, DB])
        om = sb("s_om", [P, DB])
        sel = sb("s_sel", [P, G, NS])
        selst = sb("s_selst", [P, NS])
        mn = sb("s_mn", [P, 1])
        den = sb("s_den", [P, 1])
        rden = sb("s_rden", [P, 1])
        psK = ps("s_psK", [P, 2, PAIRS, P])
        psS = ps("s_psS", [P, 2, 512])
        psP = ps("s_psP", [P, 2, 4, P])
        psO = ps("s_psO", [P, DB])
        psY = ps("s_psY", [P, DB])
        s_in = S("s_in", 16)
        s_b = S("s_b", 16)
        s_k = [S(f"s_k{j}", 16) for j in range(2)]

        s_v = S("s_v", 16)
        s_z = S("s_z")
        s_q = S("s_q")
        s_qs = S("s_qs", 1, 1)
        s_tp = S("s_tp", 1, KT_ + 1)
        s_tc = S("s_tc", 1, 2)
        s_sc = S("s_sc", 1, 1)
        s_lg = S("s_slg", 1, 1)
        s_pr = S("s_spr", 1, 1)
        s_pt = S("s_pt", 1, 2)
        s_pc = S("s_pc", 1, 2)
        s_o = S("s_o", 1, 1)
        s_sel = S("s_ssel", 1, 1)
        s_r = S("s_r", 1)
        s_om = S("s_om", 1, 1)
        s_y = S("s_sy", 1, 1)
        s_yy = S("s_syy", 1, 1)
        block = ctx.enter_context(nc.Block())
        near = [P] * 4 + [FARM] * 4
        at = [0, P, 2 * P, 3 * P] + [NEAR + FARM * i for i in range(4)]

        @block.gpsimd
        def _(pool):
            for s in (s_qs, s_tp, s_tc, s_sc, s_lg, s_pr, s_pt, s_pc, s_o, s_sel, s_om, s_y, s_yy):
                pool.sem_inc(s.sem, s.credit)
            nc.gpsimd.memset(qz[:, :, :, :], 0.0).then_inc(s_z.sem, s_z.unit)
            nc.gpsimd.memset(yb[:, NT, :], 0.0).then_inc(s_z.sem, s_z.unit)
            pool.wait_ge(s_q.sem, s_q.at(1))
            with pool.Fori(0, G) as g:
                for c in range(4):
                    pool.wait_ge(s_sc.sem, s_sc.at(4 * g + c))
                    nc.gpsimd.tensor_copy(qst[:, :, :], qz[:, ds(4 * g + c, 1), :, :]).then_inc(s_qs.sem, s_qs.unit)
                pool.wait_ge(s_y.sem, s_y.at(g))
                pool.wait_ge(s_in.sem, s_in.at(2))
                nc.gpsimd.tensor_copy(selst[:, :], sel[:, ds(g, 1), :]).then_inc(s_sel.sem, s_sel.unit)

        @block.sync
        def _(sp):
            sp.dma_start(own[:, :], a["k_own"]).then_inc(s_in.sem, s_in.unit)
            sp.dma_start(sel[:, :, :], a["k_sel"]).then_inc(s_in.sem, s_in.unit)

            def load(cache, b, dst, s, far_free=None):
                rows = cache[ds(b, 1), :, :, :].rearrange("o s h d -> (o s) (h d)")
                sp.dma_start(dst[:, 0:4, :], rows[PAST - NEAR:PAST, :].rearrange("(p i) n -> p i n", i=4)).then_inc(s[0].sem, s[0].unit)
                if far_free is not None:
                    sp.wait_ge(s_tp.sem, s_tp.at(far_free))
                    sp.sem_inc(s_pass, 1)
                sp.dma_start(dst[0:FARM, 4:8, :], rows[0:PAST - NEAR, :].rearrange("(m i) n -> m i n", i=16)[:, 0:4, :]).then_inc(s[1].sem, s[1].unit)

            with sp.Fori(0, G) as g:
                sp.wait_ge(s_lg.sem, s_lg.at(g))
                sp.dma_start(bias[:, :], a["k_sbias"][:, ds(g, 1), :].rearrange("p o n -> p (o n)")).then_inc(s_b.sem, s_b.unit)
                for c in range(4):
                    sp.wait_ge(s_tp.sem, s_tp.at(KT_ * (4 * g + c - 1) + 4))
                    sp.sem_inc(s_pass, 1)
                    load(a["cache_win_k"], 4 * g + c, kt, s_k, KT_ * (4 * g + c))
                    if c == 0:
                        sp.wait_ge(s_o.sem, s_o.at(g))
                        sp.sem_inc(s_pass, 1)
                    load(a["cache_win_v"], 4 * g + c, vt[:, c, :, :], (s_v, s_v))

        @block.tensor
        def _(pe):
            with pe.Fori(0, G) as g:
                for c in range(4):
                    for i in range(KT_):
                        if i % 4 == 0:
                            pe.wait_ge(s_k[i // 4].sem, s_k[i // 4].at(4 * g + c + 1))
                        n = KT_ * (4 * g + c) + i
                        pe.wait_ge(s_tc.sem, s_tc.at(n - 1))
                        for p in range(PAIRS):
                            last = nc.tensor.transpose(psK[:, i % 2, p, 0:near[i]], kt[0:near[i], i, p * P:(p + 1) * P],
                                                       ident[0:near[i], 0:near[i]])
                        last.then_inc(s_tp.sem, s_tp.unit)
                    pe.wait_ge(s_tc.sem, s_tc.at(KT_ * (4 * g + c) + KT_))
                    pe.wait_ge(s_qs.sem, s_qs.at(4 * g + c + 1))
                    if c == 0:
                        pe.wait_ge(s_lg.sem, s_lg.at(g))
                    for lo, n, src in ((0, 512, kTs[:, :, 0:512]), (512, 384, kTs[:, :, 512:896]), (896, NS, kT[:, :, SEQ:TOK])):
                        for p in range(PAIRS):
                            last = nc.tensor.matmul(psS[NS * c:NS * (c + 1), lo // 512, lo % 512:lo % 512 + n], qst[:, p, :], src[:, p, :],
                                                    start=(p == 0), stop=(p == PAIRS - 1))
                    last.then_inc(s_sc.sem, s_sc.unit)
                pe.wait_ge(s_pr.sem, s_pr.at(g + 1))
                keys = near + [NS]
                start = at + [SKEYS - NS]
                for r, tiles in enumerate(((0, 1, 2, 3), (4, 5, 6, 7), (8,))):
                    pe.wait_ge(s_pc.sem, s_pc.at(3 * g + max(0, r - 1)))
                    for j, i in enumerate(tiles):
                        last = nc.tensor.transpose(psP[0:keys[i], r % 2, j, :],
                                                   pr[:, start[i]:start[i] + keys[i]], ident[:, :])
                    last.then_inc(s_pt.sem, s_pt.unit)
                pe.wait_ge(s_pc.sem, s_pc.at(3 * g + 3))
                pe.wait_ge(s_v.sem, s_v.at(8 * g + 8))
                pe.wait_ge(s_om.sem, s_om.at(g))
                for c in range(4):
                    for i in range(KT_ + 1):
                        rhs = vt[0:keys[i], c, i, :] if i < KT_ else v_all[0:NS, NT, :]
                        last = nc.tensor.matmul(psO[NS * c:NS * (c + 1), :], pT[0:keys[i], i, NS * c:NS * (c + 1)], rhs,
                                                start=(i == 0), stop=(i == KT_))
                last.then_inc(s_o.sem, s_o.unit)
                pe.wait_ge(s_om.sem, s_om.at(g + 1))
                pe.wait_ge(s_sel.sem, s_sel.at(g + 1))
                pe.wait_ge(s_yy.sem, s_yy.at(g))
                nc.tensor.matmul(psY[0:NS, :], selst[:, :], om[:, :], start=True, stop=True).then_inc(s_y.sem, s_y.unit)

        @block.scalar
        def _(act):
            with act.Fori(0, G) as g:
                for c in range(4):
                    for i in range(1, KT_, 2):
                        n = KT_ * (4 * g + c) + i
                        act.wait_ge(s_tp.sem, s_tp.at(n + 1))
                        act.wait_ge(s_tc.sem, s_tc.at(n))
                        act.wait_ge(s_sc.sem, s_sc.at(4 * g + c))
                        nc.scalar.copy(kTs[:, :, at[i]:at[i] + near[i]], psK[:, i % 2, :, 0:near[i]]).then_inc(s_tc.sem, s_tc.unit)
                act.wait_ge(s_lg.sem, s_lg.at(g + 1))
                act.wait_ge(s_pt.sem, s_pt.at(3 * g))
                nc.scalar.activation(pr[:, :], lg[:, :], ACT.Exp, scale=-1.0, bias=mn[:, :], accum_out=den[:, :]).then_inc(s_pr.sem, s_pr.unit)
                act.wait_ge(s_pt.sem, s_pt.at(3 * g + 2))
                act.wait_ge(s_pc.sem, s_pc.at(3 * g + 1))
                act.wait_ge(s_o.sem, s_o.at(g))
                nc.scalar.copy(pT[0:FARM, 4:8, :], psP[0:FARM, 1, :, :]).then_inc(s_pc.sem, s_pc.unit)

        @block.vector
        def _(v):
            v.wait_ge(s_z.sem, s_z.at(2))
            for p in range(PAIRS):
                for hh in range(2):
                    part = slice(64 * hh, 64 * hh + 64)
                    h = 2 * p + hh
                    last = nc.vector.tensor_copy(qz[part, :, p, TS * h:TS * (h + 1)],
                                                 qT[part, p, SEQ:TOK].rearrange("p (b t) -> p b t", t=TS))
            last.then_inc(s_q.sem, s_q.unit)
            v.wait_ge(s_in.sem, s_in.at(2))
            with v.Fori(0, G) as g:
                for c in range(4):
                    for i in range(0, KT_, 2):
                        n = KT_ * (4 * g + c) + i
                        v.wait_ge(s_tp.sem, s_tp.at(n + 1))
                        v.wait_ge(s_tc.sem, s_tc.at(n))
                        v.wait_ge(s_sc.sem, s_sc.at(4 * g + c))
                        nc.vector.tensor_copy(kTs[:, :, at[i]:at[i] + near[i]], psK[:, i % 2, :, 0:near[i]]).then_inc(s_tc.sem, s_tc.unit)
                v.wait_ge(s_sc.sem, s_sc.at(4 * g + 4))
                v.wait_ge(s_pt.sem, s_pt.at(3 * g))
                v.wait_ge(s_b.sem, s_b.at(g + 1))
                v.sem_inc(s_pass, 1)
                nc.vector.tensor_tensor_reduce(
                    out=lg[:, :], in0=psS[:, :, :].rearrange("p a n -> p (a n)")[:, 0:SKEYS], in1=bias[:, :],
                    scale=-0.125, scalar=3e38, op0=ALU.add, op1=ALU.min, accum_out=mn[:, :]).then_inc(s_lg.sem, s_lg.unit)
                v.wait_ge(s_pt.sem, s_pt.at(3 * g + 1))
                v.wait_ge(s_pc.sem, s_pc.at(3 * g))
                v.wait_ge(s_o.sem, s_o.at(g))
                nc.vector.tensor_copy(pT[:, 0:4, :], psP[:, 0, :, :]).then_inc(s_pc.sem, s_pc.unit)
                v.wait_ge(s_pt.sem, s_pt.at(3 * g + 3))
                v.wait_ge(s_pc.sem, s_pc.at(3 * g + 2))
                nc.vector.tensor_copy(pT[0:NS, 8, :], psP[0:NS, 0, 0, :]).then_inc(s_pc.sem, s_pc.unit)
                nc.vector.reciprocal(rden[:, :], den[:, :]).then_inc(s_r.sem, s_r.unit)
                v.wait_ge(s_r.sem, s_r.at(g + 1))
                v.wait_ge(s_o.sem, s_o.at(g + 1))
                v.wait_ge(s_y.sem, s_y.at(g))
                nc.vector.scalar_tensor_tensor(out=om[:, :], in0=psO[:, :], scalar=rden[:, :], in1=own[:, :],
                                                         op0=ALU.mult, op1=ALU.mult).then_inc(s_om.sem, s_om.unit)
                v.wait_ge(s_y.sem, s_y.at(g + 1))
                v.wait_ge(s_yy.sem, s_yy.at(g))
                nc.vector.tensor_tensor(yb[0:NS, NT, :], yb[0:NS, NT, :], psY[0:NS, :], ALU.add).then_inc(s_yy.sem, s_yy.unit)


def mixing(nc, a, out, dram, ident, cols, ya, yb, ssq, logits):
    GA, GB = 32, 36
    with ExitStack() as ctx:
        new_sem = block_semaphores(nc, ctx)
        sb = lambda n, s, dt=F32: ctx.enter_context(nc.sbuf_tensor(n, s, dt))
        ps = lambda n, s: ctx.enter_context(nc.psum_tensor(n, s, F32))
        S = lambda n, unit=1, credit=0: Sem(new_sem(n), unit, credit)
        s_pass = new_sem("x_pass")
        wo = sb("wo", [P, 2 * CT, D])
        names = {"gt1": 2, "sh2": 3, "sc2": 4}
        mods = {k: sb(f"x_{k}", [P, D]) for k in names}
        modq = {k: sb(f"xs_{k}", [NS, D]) for k in names}
        lng = sb("x_lng", [P, D])
        lnb = sb("x_lnb", [P, D])
        wr = sb("x_wr", [P, KD, NG + NE])
        br = sb("x_br", [P, NG + NE])
        yas = sb("x_yas", [P, 2, CT, P])
        ybs = sb("x_ybs", [P, 2, DB])
        ybT = sb("x_ybT", [P, CT, P])
        xt = sb("x_xt", [P, 2, D])
        tb = sb("x_tb", [P, D])
        z = sb("x_z", [P, 2, D])
        x1 = sb("x_x1", [P, 2, D])
        u2 = sb("x_u2", [P, 2, D])
        u2T = sb("x_u2T", [P, KD, P])
        sqd = sb("x_sqd", [P, DB])
        rab = sb("x_rab", [P, 2, NT + 1])
        half = sb("x_half", [P, 2 * (NT + 1)])
        stt = sb("x_st", [P, 2, 6])
        mv = sb("x_mv", [P, 2])
        rs = sb("x_rs", [P, 1])
        mv9 = sb("x_ssb", [P, NT + 1])
        psA = ps("x_psA", [P, 2, 512])
        psB = ps("x_psB", [P, 2, 512])
        psY = ps("x_psY", [P, CT, P])
        psU = ps("x_psU", [P, KD, P])
        psL = ps("x_psL", [P, 512])
        s_w = [S(f"x_w{j}", 16) for j in range(2)]
        s_c = S("x_c", 16)
        s_x = [S(f"x_xt{p}", 16) for p in range(2)]
        s_z0 = S("x_z0")
        s_ss = S("x_ss")
        s_rab = S("x_rab")
        s_sqd = new_sem("x_sqd")
        s_ws = S("x_ws")
        s_ya = S("x_ya", 1)
        s_yt = S("x_yt", 1, 1)
        s_ye = S("x_ye", 1, 1)
        s_mb = S("x_mb")
        s_mm = S("x_mm", 1, 2)
        s_tb = S("x_tb", 1, 1)
        s_z = S("x_z", 1, 2)
        s_ch = new_sem("x_ch")
        s_gain = S("x_gain")
        s_var = S("x_var", 1)
        s_rs = S("x_rs", 1)
        s_xn = S("x_xn", 1, 2)
        s_x1 = S("x_x1", 1, 2)
        s_u2 = S("x_u2", 1, 2)
        s_ut = S("x_ut", 1, 2)
        s_ue = S("x_ue", 1, 1)
        s_l = S("x_l", 1, 1)
        s_lo = S("x_lo", 1, 1)
        s_o1 = [S(f"x_o1{p}", 16, 1) for p in range(2)]
        s_o2 = [S(f"x_o2{p}", 16, 1) for p in range(2)]
        block = ctx.enter_context(nc.Block())
        modrow = dram["mod"]
        xp = a["x_prompt"].rearrange("o s d -> (o s) d")
        xsm = a["x_sample"].rearrange("b t d -> (b t) d")

        @block.sync
        def _(sp):
            w = a["w_out"].rearrange("(k p) n -> p k n", p=P)
            for j in (1, 0):
                sp.dma_start(wo[:, j * CT:(j + 1) * CT, :], w[:, j * CT:(j + 1) * CT, :]).then_inc(s_w[j].sem, s_w[j].unit)
            sp.dma_start(wr[:, :, 0:NG], a["w_router_group"].rearrange("(k p) g -> p k g", p=P)).then_inc(s_c.sem, s_c.unit)
            for g in range(NG):
                sp.dma_start(wr[:, :, NG + 4 * g:NG + 4 * g + 4], a["w_router_expert"][g].rearrange("(k p) e -> p k e", p=P)).then_inc(s_c.sem, s_c.unit)
            sp.dma_start(br[:, 0:NG], a["b_router_group"].rearrange("(o n) -> o n", o=1).to_broadcast([P, NG])).then_inc(s_c.sem, s_c.unit)
            sp.dma_start(br[:, NG:], a["b_router_expert"].rearrange("(o g) e -> o (g e)", o=1).to_broadcast([P, NE])).then_inc(s_c.sem, s_c.unit)
            sp.dma_start(lng[:, :], a["ln1_g"].rearrange("(o n) -> o n", o=1).to_broadcast([P, D])).then_inc(s_c.sem, s_c.unit)
            sp.dma_start(lnb[:, :], a["ln1_b"].rearrange("(o n) -> o n", o=1).to_broadcast([P, D])).then_inc(s_c.sem, s_c.unit)
            for k, j in names.items():
                sp.dma_start(mods[k][:, :], modrow[0:1, j * D:(j + 1) * D].to_broadcast([P, D])).then_inc(s_c.sem, s_c.unit)
                for b in range(B):
                    sp.dma_start(modq[k][TS * b:TS * (b + 1), :], modrow[1 + b:2 + b, j * D:(j + 1) * D].to_broadcast([TS, D])).then_inc(s_c.sem, s_c.unit)

            def load(t, par, rows):
                sp.wait_ge(s_z.sem, s_z.at(t - 1))
                sp.dma_start(xt[0:rows, par, :], xp[ds(t * P, P), :] if rows == P else xsm).then_inc(s_x[par].sem, s_x[par].unit)

            def store(t, par, rows):
                sp.wait_ge(s_x1.sem, s_x1.at(t + 1))
                sp.dma_start(dram["x1"][ds(t * P, rows), :], x1[0:rows, par, :]).then_inc(s_o1[par].sem, s_o1[par].unit)
                sp.wait_ge(s_u2.sem, s_u2.at(t + 1))
                sp.dma_start(dram["u2"][ds(t * P, rows), :], u2[0:rows, par, :]).then_inc(s_o2[par].sem, s_o2[par].unit)

            load(0, 0, P)
            load(1, 1, P)
            with sp.Fori(0, NT // 2 - 1) as i:
                for par in range(2):
                    load(2 * i + par + 2, par, P)
                    store(2 * i + par, par, P)
            load(NT, 0, NS)
            store(NT - 2, 0, P)
            store(NT - 1, 1, P)
            store(NT, 0, NS)
            for s in (s_o1, s_o2):
                sp.wait_ge(s[0].sem, s[0].at(NT // 2 + 1))
                sp.wait_ge(s[1].sem, s[1].at(NT // 2))

        NC = 9 + 3 * (1 + B)

        @block.gpsimd
        def _(pool):
            for s in (s_yt, s_ye, s_mm, s_tb, s_z, s_xn, s_x1, s_u2, s_ut, s_ue, s_l, s_lo):
                pool.sem_inc(s.sem, s.credit)
            for s in (*s_o1, *s_o2):
                pool.sem_inc(s.sem, 16)
            nc.gpsimd.memset(half[:, :], -0.5).then_inc(s_z0.sem, s_z0.unit)
            nc.gpsimd.memset(logits[:, NT, :], 0.0).then_inc(s_z0.sem, s_z0.unit)
            pool.wait_ge(s_ss.sem, s_ss.at(2))
            pool.wait_ge(s_z0.sem, s_z0.at(1))
            nc.gpsimd.tensor_tensor(rab[:, :, :].rearrange("p a t -> p (a t)"), rab[:, :, :].rearrange("p a t -> p (a t)"),
                                               half[:, :], ALU.pow).then_inc(s_rab.sem, s_rab.unit)
            pool.wait_ge(s_c.sem, s_c.at(NC))

            def tile(t, par, rows):
                pool.wait_ge(s_var.sem, s_var.at(t + 1))
                nc.gpsimd.tensor_tensor(rs[0:rows, :], mv[0:rows, 1:2], half[0:rows, 0:1], ALU.pow).then_inc(s_rs.sem, s_rs.unit)
                pool.wait_ge(s_xn.sem, s_xn.at(t + 1))
                pool.wait_ge(s_o1[par].sem, s_o1[par].at(t // 2))
                pool.wait_ge(s_u2.sem, s_u2.at(t - 1))
                nc.gpsimd.tensor_tensor(x1[0:rows, par, :], z[0:rows, par, :], lng[0:rows, :], ALU.mult).then_inc(s_gain.sem, s_gain.unit)
                pool.wait_ge(s_gain.sem, s_gain.at(t + 1))
                nc.gpsimd.tensor_tensor(x1[0:rows, par, :], x1[0:rows, par, :], lnb[0:rows, :], ALU.add).then_inc(s_x1.sem, s_x1.unit)

            with pool.Fori(0, NT // 2) as i:
                for par in range(2):
                    tile(2 * i + par, par, P)
            tile(NT, 0, NS)

        @block.vector
        def _(v):
            st = Steps(v, s_ch)
            for j in (1, 0):
                v.wait_ge(s_w[j].sem, s_w[j].at(1))
                for k in range(j * CT, (j + 1) * CT):
                    last = nc.vector.tensor_scalar(wo[:, k, :], wo[:, k, :], cols[:, GA + k:GA + k + 1], None, ALU.mult)
                last.then_inc(s_ws.sem, s_ws.unit)
            st.after(nc.vector.memset(rab[:, :, NT], 1.0))
            v.wait_ge(s_ss.sem, s_ss.at(1))
            st.last()
            st.link(nc.vector.tensor_reduce(rab[:, 0, 0:NT], ssq[:, 0:NT, :], X, ALU.add))
            st.link(nc.vector.tensor_reduce(rab[0:NS, 0, NT:NT + 1], ssq[0:NS, NT, :], X, ALU.add))
            st.after(nc.vector.tensor_copy(rab[:, 1, 0:NT], mv9[:, 0:NT]))
            st.link(nc.vector.tensor_copy(rab[0:NS, 1, NT:NT + 1], mv9[0:NS, NT:NT + 1]))
            nc.vector.tensor_scalar(rab[:, :, :], rab[:, :, :], 1.0 / DA, EPS, ALU.mult, ALU.add).then_inc(s_ss.sem, s_ss.unit)
            v.wait_ge(s_c.sem, s_c.at(NC))
            st.after(nc.vector.tensor_scalar(mods["sc2"][:, :], mods["sc2"][:, :], 1.0, None, ALU.add))
            st.link(nc.vector.tensor_scalar(modq["sc2"][:, :], modq["sc2"][:, :], 1.0, None, ALU.add))
            v.wait_ge(s_rab.sem, s_rab.at(1))

            def residual(t, par, rows):
                m = mods if rows == P else modq
                v.wait_ge(s_mm.sem, s_mm.at(t + 1))
                v.wait_ge(s_tb.sem, s_tb.at(t + 1))
                v.wait_ge(s_x1.sem, s_x1.at(t - 1))
                zt = z[0:rows, par, :]
                st.link(nc.vector.scalar_tensor_tensor(out=zt, in0=psA[0:rows, :, :].rearrange("p a n -> p (a n)"),
                                                       scalar=rab[0:rows, 0, ds(t, 1)], in1=tb[0:rows, :], op0=ALU.mult, op1=ALU.add))
                st.link(nc.vector.tensor_tensor(zt, zt, m["gt1"][0:rows, :], ALU.mult))
                v.wait_ge(s_x[par].sem, s_x[par].at(t // 2 + 1))
                nc.vector.scalar_tensor_tensor(out=zt, in0=xt[0:rows, par, :], scalar=ALPHA, in1=zt, op0=ALU.mult, op1=ALU.add).then_inc(s_z.sem, s_z.unit)
                v.wait_ge(s_z.sem, s_z.at(t + 1))
                for j in range(2):
                    st.after(nc.vector.bn_stats(stt[0:rows, j, :], z[0:rows, par, j * 512:(j + 1) * 512]))
                st.last()
                v.sem_inc(s_pass, 1)
                st.link(nc.vector.bn_aggr(mv[0:rows, :], stt[0:rows, :, :]))
                nc.vector.tensor_scalar(mv[0:rows, 1:2], mv[0:rows, 1:2], EPS, None, ALU.add).then_inc(s_var.sem, s_var.unit)

            def normalize(t, par, rows):
                v.wait_ge(s_rs.sem, s_rs.at(t + 1))
                nc.vector.tensor_scalar(z[0:rows, par, :], z[0:rows, par, :], mv[0:rows, 0:1], rs[0:rows, :], ALU.subtract, ALU.mult).then_inc(s_xn.sem, s_xn.unit)

            def modulate(t, par, rows):
                m = mods if rows == P else modq
                v.wait_ge(s_x1.sem, s_x1.at(t + 1))
                v.wait_ge(s_o2[par].sem, s_o2[par].at(t // 2))
                v.wait_ge(s_ut.sem, s_ut.at(t - 1))
                st.link(nc.vector.tensor_tensor(u2[0:rows, par, :], x1[0:rows, par, :], m["sc2"][0:rows, :], ALU.mult))
                nc.vector.tensor_tensor(u2[0:rows, par, :], u2[0:rows, par, :], m["sh2"][0:rows, :], ALU.add).then_inc(s_u2.sem, s_u2.unit)

            def route(t, rows):
                v.wait_ge(s_l.sem, s_l.at(t + 1))
                nc.vector.tensor_tensor(logits[0:rows, ds(t, 1), :], psL[0:rows, 0:NG + NE].unsqueeze(1), br[0:rows, :].unsqueeze(1), ALU.add).then_inc(s_lo.sem, s_lo.unit)

            def step(t, par, rows):
                residual(t, par, rows)
                modulate(t - 1, 1 - par, P)
                normalize(t, par, rows)
                route(t - 2, P)

            residual(0, 0, P)
            normalize(0, 0, P)
            residual(1, 1, P)
            modulate(0, 0, P)
            normalize(1, 1, P)
            st.enter(12)
            with v.Fori(1, NT // 2) as i:
                st.round(i - 1)
                for par in range(2):
                    step(2 * i + par, par, P)
            st.leave(NT // 2 - 1)
            step(NT, 0, NS)
            modulate(NT, 0, NS)
            route(NT - 1, P)
            route(NT, NS)

        @block.scalar
        def _(act):
            def stage(t, par, rows):
                act.wait_ge(s_mm.sem, s_mm.at(t - 1))
                nc.scalar.copy(ybs[0:rows, par, :], yb[0:rows, ds(t, 1), :])
                nc.scalar.copy(yas[:, par, :, 0:rows], ya[:, :, ds(t * P, rows)]).then_inc(s_ya.sem, s_ya.unit)

            def turned_y(t, rows):
                act.wait_ge(s_yt.sem, s_yt.at(t + 1))
                nc.scalar.copy(ybT[:, :, 0:rows], psY[:, :, 0:rows]).then_inc(s_ye.sem, s_ye.unit)

            def scaled(t, rows):
                act.wait_ge(s_mb.sem, s_mb.at(t + 1))
                act.wait_ge(s_z.sem, s_z.at(t))
                nc.scalar.activation(tb[0:rows, :], psB[0:rows, :, :].rearrange("p a n -> p (a n)"), ACT.Copy,
                                               scale=rab[0:rows, 1, ds(t, 1)]).then_inc(s_tb.sem, s_tb.unit)

            def turned_u(t, rows):
                act.wait_ge(s_ut.sem, s_ut.at(t + 1))
                act.wait_ge(s_l.sem, s_l.at(t))
                nc.scalar.copy(u2T[:, :, 0:rows], psU[:, :, 0:rows]).then_inc(s_ue.sem, s_ue.unit)

            stage(0, 0, P)
            stage(1, 1, P)
            turned_y(0, P)
            for t in range(NT + 1):
                rows = P if t < NT else NS
                nc.scalar.activation(sqd[0:rows, :], yb[0:rows, t, :], ACT.Square,
                                     accum_out=mv9[0:rows, t:t + 1]).then_inc(s_sqd, 1)
                act.wait_ge(s_sqd, t + 1)
            nc.scalar.copy(sqd[0:1, 0:1], mv9[0:1, 0:1]).then_inc(s_ss.sem, s_ss.unit)
            act.wait_ge(s_rab.sem, s_rab.at(1))
            for t in range(2):
                scaled(t, P)
                turned_y(t + 1, P)
                stage(t + 2, t, P)
            with act.Fori(1, NT // 2 - 1) as i:
                for par in range(2):
                    t = 2 * i + par
                    scaled(t, P)
                    turned_y(t + 1, P)
                    turned_u(t - 2, P)
                    stage(t + 2, par, P)
            scaled(NT - 2, P)
            turned_y(NT - 1, P)
            turned_u(NT - 4, P)
            stage(NT, 0, NS)
            scaled(NT - 1, P)
            turned_y(NT, NS)
            turned_u(NT - 3, P)
            scaled(NT, NS)
            turned_u(NT - 2, P)
            turned_u(NT - 1, P)
            turned_u(NT, NS)

        @block.tensor
        def _(pe):
            def turn_y(t, par, rows):
                pe.wait_ge(s_ya.sem, s_ya.at(t + 1))
                pe.wait_ge(s_ye.sem, s_ye.at(t))
                for k in range(CT):
                    last = nc.tensor.transpose(psY[:, k, 0:rows], ybs[0:rows, par, k * P:(k + 1) * P], ident[0:rows, 0:rows])
                last.then_inc(s_yt.sem, s_yt.unit)

            def product_b(t, rows):
                pe.wait_ge(s_ye.sem, s_ye.at(t + 1))
                pe.wait_ge(s_tb.sem, s_tb.at(t))
                for n in range(2):
                    for k in range(CT):
                        last = nc.tensor.matmul(psB[0:rows, n, :], ybT[:, k, 0:rows], wo[:, CT + k, n * 512:(n + 1) * 512],
                                                start=(k == 0), stop=(k == CT - 1))
                last.then_inc(s_mb.sem, s_mb.unit)

            def product_a(t, par, rows):
                pe.wait_ge(s_z.sem, s_z.at(t))
                for n in range(2):
                    for k in range(CT):
                        last = nc.tensor.matmul(psA[0:rows, n, :], yas[:, par, k, 0:rows], wo[:, k, n * 512:(n + 1) * 512],
                                                start=(k == 0), stop=(k == CT - 1))
                last.then_inc(s_mm.sem, s_mm.unit)

            def turn_u(t, par, rows):
                pe.wait_ge(s_u2.sem, s_u2.at(t + 1))
                pe.wait_ge(s_ue.sem, s_ue.at(t))
                for k in range(KD):
                    last = nc.tensor.transpose(psU[:, k, 0:rows], u2[0:rows, par, k * P:(k + 1) * P], ident[0:rows, 0:rows])
                last.then_inc(s_ut.sem, s_ut.unit)

            def router(t, rows):
                pe.wait_ge(s_ue.sem, s_ue.at(t + 1))
                pe.wait_ge(s_lo.sem, s_lo.at(t))
                for k in range(KD):
                    last = nc.tensor.matmul(psL[0:rows, 0:NG + NE], u2T[:, k, 0:rows], wr[:, k, :], start=(k == 0), stop=(k == KD - 1))
                last.then_inc(s_l.sem, s_l.unit)

            turn_y(0, 0, P)
            pe.wait_ge(s_ws.sem, s_ws.at(1))
            product_b(0, P)
            turn_y(1, 1, P)
            pe.wait_ge(s_ws.sem, s_ws.at(2))
            product_a(0, 0, P)
            product_b(1, P)
            turn_y(2, 0, P)
            product_a(1, 1, P)
            pe.wait_ge(s_c.sem, s_c.at(NC))
            with pe.Fori(1, NT // 2 - 1) as i:
                for par in range(2):
                    t = 2 * i + par
                    product_b(t, P)
                    turn_y(t + 1, 1 - par, P)
                    turn_u(t - 2, par, P)
                    product_a(t, par, P)
                    router(t - 2, P)
            product_b(NT - 2, P)
            turn_y(NT - 1, 1, P)
            turn_u(NT - 4, 0, P)
            product_a(NT - 2, 0, P)
            router(NT - 4, P)
            product_b(NT - 1, P)
            turn_y(NT, 0, NS)
            turn_u(NT - 3, 1, P)
            product_a(NT - 1, 1, P)
            router(NT - 3, P)
            product_b(NT, NS)
            turn_u(NT - 2, 0, P)
            product_a(NT, 0, NS)
            router(NT - 2, P)
            turn_u(NT - 1, 1, P)
            router(NT - 1, P)
            turn_u(NT, 0, NS)
            router(NT, NS)


def routing(nc, a, out, dram, ident, logits, route, ew):
    NTT = NT + 1
    with ExitStack() as ctx:
        new_sem = block_semaphores(nc, ctx)
        sb = lambda n, s, dt=F32: ctx.enter_context(nc.sbuf_tensor(n, s, dt))
        ps = lambda n, s: ctx.enter_context(nc.psum_tensor(n, s, F32))
        S = lambda n, unit=1, credit=0: Sem(new_sem(n), unit, credit)
        ranks = sb("ranks", [P, 4])
        valid = sb("valid", [P, NTT])
        before = sb("before", [P, P])
        ones = sb("ones_r", [P, P])
        restart = sb("restart", [P, NE, NTT])
        steps_ = sb("steps", [P, NTT])
        tiles_k = sb("tiles_k", [P, SLOT_TILES])
        tokid = sb("tokid", [P, NTT])
        zero = sb("zero_r", [SLOT_TILES, P])
        m1 = sb("m1", [P, NTT])
        m2 = sb("m2", [P, NTT])
        pg = sb("pg", [P, NTT])
        e1 = sb("e1", [P, NTT])
        r1 = sb("r1", [P, NTT])
        d4 = sb("d4", [P, NTT, 4])
        x4 = sb("x4", [P, NTT, 4])
        oh = sb("oh", [P, 3, NTT, 4])
        sel = sb("rsel", [P, NTT, 4])
        t16 = sb("t16", [P, NTT, 4, 4])
        hot = sb("hot", [P, 2, NTT, NE])
        both = sb("both", [P, NTT, NE])
        tot = sb("tot", [P, NE, NTT])
        base = sb("base", [P, NE, NTT])
        shifted = sb("shifted", [P, NE, NTT])
        count = sb("count", [P, NE])
        cmp = sb("cmp", [P, NE, NTT - 1])
        ntl = sb("ntl", [P, NE])
        one16 = sb("one16", [P, NE])
        end = sb("end_f", [P, NE])
        first = sb("first_f", [P, NE])
        slotE = sb("slotE", [P, NE, NTT])
        pick = sb("pick", [P, NTT, NE])
        slot = sb("slot_f", [P, 2, NTT])
        ek = sb("ek", [P, SLOT_TILES, NE])
        ekr = sb("ekr", [P, SLOT_TILES])
        idrow = sb("idrow", [SLOT_TILES, P])
        even = sb("even", [1, SLOT_TILES // 2 - 1, 1])
        npair = sb("npair", [1, 1])
        psW = ps("o_psW", [P, NTT, NE])
        psC = ps("o_psC", [P, NTT, NE])
        psI = ps("o_psI", [P, SLOT_TILES])
        s_in = S("o_in", 16)
        s_zr = S("o_zr")
        s_z = S("o_z", 16)
        s_ch = new_sem("o_ch")
        s_d = S("o_d")
        s_e = S("o_e")
        s_m = S("o_m")
        s_pe = S("o_pe")
        s_slot = S("o_slot")
        s_sc = S("o_sc", 16)
        s_id = S("o_id", 16)
        s_it = S("o_it")
        block = ctx.enter_context(nc.Block())

        @block.sync
        def _(sp):
            for t, n in ((ranks, "k_ranks"), (valid, "k_valid"), (before, "k_before"), (restart, "k_restart"),
                         (steps_, "k_steps"), (tiles_k, "k_tiles"), (tokid, "k_tokid")):
                sp.dma_start(t[tuple(slice(None) for _ in t.shape)], a[n]).then_inc(s_in.sem, s_in.unit)
            sp.wait_ge(s_zr.sem, s_zr.at(1))
            sp.dma_start(dram["tok"].rearrange("(k p) o -> k (p o)", p=P), zero[:, :]).then_inc(s_z.sem, s_z.unit)
            for name in ("gate", "up"):
                sp.dma_start(ew[name][:, :, :], a[f"w_exp_{name}"][0, :, :].rearrange("(k p) f -> p k f", p=P)).then_inc(ew[f"s_{name}"].sem, 16)
            sp.wait_ge(s_sc.sem, s_sc.at(2 * NTT))
            sp.dma_start(idrow[:, :], dram["tok"].rearrange("(k p) o -> k (p o)", p=P)).then_inc(s_id.sem, s_id.unit)

        @block.gpsimd
        def _(pool):
            nc.gpsimd.memset(zero[:, :], 0.0).then_inc(s_zr.sem, s_zr.unit)
            pool.wait_ge(s_slot.sem, s_slot.at(1))
            pool.wait_ge(s_z.sem, s_z.at(1))
            pool.wait_ge(s_in.sem, s_in.at(7))
            for t in range(NTT):
                rows = P if t < NT else NS
                for k in range(2):
                    nc.gpsimd.indirect_dma_start(
                        out=dram["tok"], out_offset=bass.IndirectOffsetOnAxis(ap=route["slot"][0:rows, k, t:t + 1], axis=0),
                        in_=tokid[0:rows, t:t + 1], in_offset=None).then_inc(s_sc.sem, s_sc.unit)

        @block.scalar
        def _(act):
            act.wait_ge(s_d.sem, s_d.at(1))
            nc.scalar.activation(x4[:, :, :], d4[:, :, :], ACT.Exp).then_inc(s_e.sem, s_e.unit)
            act.wait_ge(s_d.sem, s_d.at(2))
            nc.scalar.activation(e1[:, :], m2[:, :], ACT.Exp).then_inc(s_e.sem, s_e.unit)

        @block.tensor
        def _(pe):
            pe.wait_ge(s_m.sem, s_m.at(1))
            pe.wait_ge(s_in.sem, s_in.at(7))
            nc.tensor.matmul(psW[:, :, :], before[:, :], both[:, :, :], start=True, stop=True)
            nc.tensor.matmul(psC[:, :, :], ones[:, :], both[:, :, :], start=True, stop=True).then_inc(s_pe.sem, s_pe.unit)
            pe.wait_ge(s_id.sem, s_id.at(1))
            nc.tensor.transpose(psI[:, :], idrow[:, :], ident[0:SLOT_TILES, 0:SLOT_TILES]).then_inc(s_it.sem, s_it.unit)

        @block.vector
        def _(v):
            st = Steps(v, s_ch)
            v.wait_ge(s_in.sem, s_in.at(7))
            g = logits[:, :, 0:NG]
            wide = lambda t: t.unsqueeze(2).to_broadcast([P, NTT, 4])
            r4 = ranks[:, :].unsqueeze(1).to_broadcast([P, NTT, 4])

            def first_of_max(src, mx, dst):
                st.link(nc.vector.tensor_reduce(mx, src, X, ALU.max))
                st.link(nc.vector.tensor_tensor(d4[:, :, :], src, wide(mx), ALU.is_equal))
                st.link(nc.vector.tensor_tensor(d4[:, :, :], d4[:, :, :], r4, ALU.mult))
                st.link(nc.vector.tensor_reduce(r1[:, :], d4[:, :, :], X, ALU.max))
                st.link(nc.vector.tensor_tensor(dst, d4[:, :, :], wide(r1[:, :]), ALU.is_equal))

            st.after(nc.vector.memset(ones[:, :], 1.0))
            st.after(nc.vector.memset(one16[:, :], 1.0))
            st.after(nc.vector.memset(shifted[:, :, :], 0.0))
            first_of_max(g, m1[:, :], oh[:, 0, :, :])
            nc.vector.tensor_tensor(d4[:, :, :], g, wide(m1[:, :]), ALU.subtract).then_inc(s_d.sem, s_d.unit)
            v.wait_ge(s_e.sem, s_e.at(1))
            st.link(nc.vector.tensor_reduce(r1[:, :], x4[:, :, :], X, ALU.add))
            st.link(nc.vector.reciprocal(pg[:, :], r1[:, :]))
            le = logits[:, :, NG:].rearrange("p t (g e) -> p t e g", g=NG)
            for e in range(4):
                st.after(nc.vector.tensor_tensor(t16[:, :, e, :], le[:, :, e, :], oh[:, 0, :, :], ALU.mult))
            st.last()
            st.link(nc.vector.tensor_reduce(sel[:, :, :], t16[:, :, :, :], X, ALU.add))
            first_of_max(sel[:, :, :], m1[:, :], oh[:, 1, :, :])
            st.link(nc.vector.scalar_tensor_tensor(out=sel[:, :, :], in0=oh[:, 1, :, :], scalar=NEG, in1=sel[:, :, :], op0=ALU.mult, op1=ALU.add))
            first_of_max(sel[:, :, :], m2[:, :], oh[:, 2, :, :])
            nc.vector.tensor_tensor(m2[:, :], m2[:, :], m1[:, :], ALU.subtract).then_inc(s_d.sem, s_d.unit)
            v.wait_ge(s_e.sem, s_e.at(2))
            st.link(nc.vector.tensor_scalar(r1[:, :], e1[:, :], 1.0, None, ALU.add))
            st.link(nc.vector.reciprocal(r1[:, :], r1[:, :]))
            st.link(nc.vector.tensor_tensor(route["w"][:, 0, :], r1[:, :], pg[:, :], ALU.mult))
            st.after(nc.vector.tensor_tensor(route["w"][:, 1, :], route["w"][:, 0, :], e1[:, :], ALU.mult))
            for k in range(2):
                h4 = hot[:, k, :, :].rearrange("p t (g e) -> p t g e", g=NG)
                for q in range(NG):
                    st.after(nc.vector.tensor_tensor(h4[:, :, q, :], oh[:, 1 + k, :, :],
                                                     oh[:, 0, :, q:q + 1].to_broadcast([P, NTT, 4]), ALU.mult))
            st.last()
            st.link(nc.vector.tensor_tensor(both[:, :, :], hot[:, 0, :, :], hot[:, 1, :, :], ALU.add))
            nc.vector.tensor_tensor(both[:, :, :], both[:, :, :], valid[:, :].unsqueeze(2).to_broadcast([P, NTT, NE]), ALU.mult).then_inc(s_m.sem, s_m.unit)
            v.wait_ge(s_pe.sem, s_pe.at(1))
            st.link(nc.vector.tensor_copy(tot[:, :, :], psC[:, :, :].rearrange("p t e -> p e t")))
            st.link(nc.vector.tensor_copy(shifted[:, :, 1:NTT], tot[:, :, 0:NT]))
            flat = lambda t: t[:, :, :].rearrange("p e t -> p (e t)")
            st.link(nc.vector.tensor_tensor_scan(flat(base), flat(restart), flat(shifted), 0.0, ALU.mult, ALU.add))
            st.link(nc.vector.tensor_tensor(count[:, :], base[:, :, NT], tot[:, :, NT], ALU.add))
            st.link(nc.vector.tensor_tensor(cmp[:, :, :], count[:, :].unsqueeze(2).to_broadcast([P, NE, NT]),
                                            steps_[:, 0:NT].unsqueeze(1).to_broadcast([P, NE, NT]), ALU.is_gt))
            st.link(nc.vector.tensor_reduce(ntl[:, :], cmp[:, :, :], X, ALU.add))
            st.link(nc.vector.tensor_scalar(ntl[:, :], ntl[:, :], 1.0, None, ALU.add))
            st.link(nc.vector.tensor_tensor_scan(end[:, :], one16[:, :], ntl[:, :], 0.0, ALU.mult, ALU.add))
            st.link(nc.vector.tensor_tensor(first[:, :], end[:, :], ntl[:, :], ALU.subtract))
            st.link(nc.vector.tensor_scalar(first[:, :], first[:, :], float(P), None, ALU.mult))
            st.link(nc.vector.tensor_tensor(slotE[:, :, :], psW[:, :, :].rearrange("p t e -> p e t"), base[:, :, :], ALU.add))
            st.link(nc.vector.tensor_tensor(slotE[:, :, :], slotE[:, :, :], first[:, :].unsqueeze(2).to_broadcast([P, NE, NTT]), ALU.add))
            for k in range(2):
                st.link(nc.vector.tensor_tensor(pick[:, :, :], hot[:, k, :, :], slotE[:, :, :].rearrange("p e t -> p t e"), ALU.mult))
                st.link(nc.vector.tensor_reduce(slot[:, k, :], pick[:, :, :], X, ALU.add))
            nc.vector.tensor_copy(route["slot"][:, :, :], slot[:, :, :]).then_inc(s_slot.sem, s_slot.unit)
            st.link(nc.vector.tensor_tensor(ek[:, :, :], end[:, :].unsqueeze(1).to_broadcast([P, SLOT_TILES, NE]),
                                            tiles_k[:, :].unsqueeze(2).to_broadcast([P, SLOT_TILES, NE]), ALU.is_le))
            st.link(nc.vector.tensor_reduce(ekr[:, :], ek[:, :, :], X, ALU.add))
            st.link(nc.vector.tensor_scalar(ekr[:, :], ekr[:, :], float(NE - 1), None, ALU.min))
            st.link(nc.vector.tensor_copy(route["expert"][:, :], ekr[0:1, :]))
            st.link(nc.vector.tensor_copy(route["end"][:, :], end[0:1, :]))
            st.link(nc.vector.tensor_scalar(even[:, :, :], tiles_k[0:1, :].rearrange("p (i j) -> p i j", j=2)[:, 1:, 0:1],
                                            end[0:1, NE - 1:NE], None, ALU.is_lt))
            st.link(nc.vector.tensor_reduce(npair[:, :], even[:, :, 0], X, ALU.add))
            st.link(nc.vector.tensor_copy(route["pairs"][:, :], npair[:, :]))
            v.wait_ge(s_it.sem, s_it.at(1))
            st.link(nc.vector.tensor_copy(route["ids"][:, :], psI[:, :]))


def experts(nc, a, out, dram, ident, route, ew):
    with ExitStack() as ctx:
        new_sem = block_semaphores(nc, ctx)
        sb = lambda n, s, dt=F32: ctx.enter_context(nc.sbuf_tensor(n, s, dt))
        ps = lambda n, s: ctx.enter_context(nc.psum_tensor(n, s, F32))
        S = lambda n, unit=1, credit=0: Sem(new_sem(n), unit, credit)
        s_pass = new_sem("e_pass")
        s_gu_w, s_d_w = {n: ew[f"s_{n}"] for n in ("gate", "up")}, ew["s_d"]
        H_, L_ = 0, 1
        w = {n: [sb(f"e_{n}{p}", [P, KD, FE] if n != "down" else [P, KF, D], F32R) for p in "hl"] for n in ("gate", "up", "down")}
        ids = sb("e_ids", [P, 2], I32)
        xg = sb("e_x", [P, 2, D])
        xT = [sb(f"e_xT{p}", [P, 2, KD, P], F32R) for p in "hl"]
        th = sb("e_th", [P, FE])
        th2 = sb("e_th2", [P, FE])
        hs = sb("e_h", [P, FE])
        hT = [sb(f"e_hT{p}", [P, 2, KF, P], F32R) for p in "hl"]
        y = sb("e_y", [P, 2, D // 2])
        zero = sb("e_zero", [P, D // 2])
        psT = ps("e_psT", [P, 4, P])
        psG = ps("e_psG", [P, 2, 2, FE])
        psH = ps("e_psH", [P, KF, P])
        psY = ps("e_psY", [P, 2, 512])
        s_id = S("e_id")
        s_x = [S(f"e_x{p}", 16) for p in range(2)]
        s_t = S("e_t", 1, 4)
        s_tc = S("e_tc", 1, 2)
        s_xh = S("e_xh")
        s_hh = S("e_hh")
        GUC = KD
        s_wh = S("e_wh")
        s_wl = S("e_wl")
        s_dh = S("e_dh")
        s_dl = S("e_dl")
        POOL_KS = range(0, KF, 2)
        VEC_KS = range(1, KF, 2)
        s_dp = S("e_dp")
        s_gu = S("e_gu", 1, 2)
        s_th = S("e_th", 1)
        s_h1 = S("e_h1", 1, 1)
        s_h = S("e_h", 1, 2)
        s_ht = S("e_ht", 1, 1)
        s_hc = S("e_hc", 1, 1)
        s_dn = S("e_dn", 1, 4)
        s_y = S("e_y", 1, 2)
        s_zero = S("e_zero")
        s_un = S("e_un", 16)
        s_o = [S(f"e_o{p}", 16, 1) for p in range(2)]
        block = ctx.enter_context(nc.Block())
        PAIRED = (SLOT_TILES - 1) // 2
        FULL = (NE - 1) // 2

        def each_pair(eng, fn, start=0):
            with eng.Fori(start, FULL) as i:
                fn(2 * i)
            n = eng.value_load(route["pairs"][0:1, 0:1], min_val=FULL, max_val=PAIRED)
            with eng.Fori(FULL, PAIRED) as i:
                with eng.If(i < n):
                    fn(2 * i)
            return 2 * n

        def when_new(eng, t, fn, *more):
            e = eng.value_load(route["expert"][0:1, ds(t, 1)], min_val=0, max_val=NE - 1)
            before = eng.value_load(route["expert"][0:1, ds(t - 1, 1)], min_val=0, max_val=NE - 1)
            with eng.If(before < e):
                fn(e, t, *more)

        @block.sync
        def _(sp):
            def load_gate_up(e):
                for name, split in (("gate", GUC // 2), ("up", GUC)):
                    sp.wait_ge(s_wl.sem, s_wl.at(GUC * (e - 1) + split))
                    sp.dma_start(ew[name][:, :, :], a[f"w_exp_{name}"][ds(e, 1), :, :].rearrange("o (k p) f -> p (o k) f", p=P)).then_inc(s_gu_w[name].sem, s_gu_w[name].unit)

            def load_down(e):
                if not isinstance(e, int) or e >= 1:
                    sp.wait_ge(s_dl.sem, s_dl.at(len(VEC_KS) * e))
                    sp.wait_ge(s_dp.sem, s_dp.at(len(POOL_KS) * e))
                sp.dma_start(ew["down"][:, :, :], a["w_exp_down"][ds(e, 1), :, :].rearrange("o (k p) f -> p (o k) f", p=P)).then_inc(s_d_w.sem, s_d_w.unit)

            sp.wait_ge(s_x[0].sem, s_x[0].at(1))
            load_down(0)
            load_gate_up(1)
            with sp.Fori(2, NE) as e:
                load_gate_up(e)
                load_down(e - 1)
            load_down(NE - 1)
            n = sp.value_load(route["pairs"][0:1, 0:1], min_val=FULL, max_val=PAIRED)
            sp.wait_ge(s_zero.sem, s_zero.at(1))
            with sp.Fori(FULL + 1, PAIRED + 1) as i:
                with sp.If(i > n):
                    for par in range(2):
                        for half in range(2):
                            sp.dma_start(dram["y"][ds((2 * i + par) * P, P), half * 512:(half + 1) * 512], zero[:, :]).then_inc(s_un.sem, s_un.unit)
                with sp.If(i <= n):
                    sp.sem_inc(s_un.sem, 4 * s_un.unit)
            sp.wait_ge(s_un.sem, s_un.at(4 * (PAIRED - FULL)))

        @block.scalar
        def _(act):
            def split(e, t, name):
                act.wait_ge(s_gu_w[name].sem, s_gu_w[name].at(e + 1))
                act.wait_ge(s_gu.sem, s_gu.at(t))
                act.sem_inc(s_pass, 1)
                for k in range(0, KD, 2):
                    nc.scalar.copy(w[name][H_][:, k:k + 2, :], ew[name][:, k:k + 2, :]).then_inc(s_wh.sem, s_wh.unit)

            def split_down(e, t):
                act.wait_ge(s_d_w.sem, s_d_w.at(e + 1))
                act.wait_ge(s_dn.sem, s_dn.at(2 * t))
                act.sem_inc(s_pass, 1)
                for k in range(KF):
                    nc.scalar.copy(w["down"][H_][:, k, :], ew["down"][:, k, :]).then_inc(s_dh.sem, s_dh.unit)

            def x_half(t, par, half):
                act.wait_ge(s_t.sem, s_t.at(2 * t + half + 1))
                act.wait_ge(s_gu.sem, s_gu.at(t - 1))
                nc.scalar.copy(xT[H_][:, par, 4 * half:4 * half + 4, :], psT[:, :, :]).then_inc(s_xh.sem, s_xh.unit)

            def gate_tanh(t, par):
                act.wait_ge(s_gu.sem, s_gu.at(t + 1))
                act.wait_ge(s_h1.sem, s_h1.at(t))
                nc.scalar.activation(th[:, :], psG[:, par, 0, :], ACT.Tanh, scale=0.5).then_inc(s_th.sem, s_th.unit)

            def hidden(t, par):
                act.wait_ge(s_ht.sem, s_ht.at(t + 1))
                act.wait_ge(s_dn.sem, s_dn.at(2 * (t - 1)))
                nc.scalar.copy(hT[H_][:, par, :, :], psH[:, :, :]).then_inc(s_hh.sem, s_hh.unit)

            def y_half(t, half):
                act.wait_ge(s_dn.sem, s_dn.at(2 * t + half + 1))
                act.wait_ge(s_o[half].sem, s_o[half].at(t))
                nc.scalar.copy(y[:, half, :], psY[:, half, :]).then_inc(s_y.sem, s_y.unit)
                act.wait_ge(s_y.sem, s_y.at(2 * t + half + 1))
                act.dma_start(dram["y"][ds(t * P, P), half * 512:(half + 1) * 512], y[:, half, :]).then_inc(s_o[half].sem, s_o[half].unit)

            def pair(t0):
                for par in range(2):
                    t = t0 + par
                    hidden(t, par)
                    x_half(t + 2, par, 0)
                    when_new(act, t + 2, split, "gate")
                    x_half(t + 2, par, 1)
                    y_half(t, 0)
                    when_new(act, t + 2, split, "up")
                    y_half(t, 1)
                    gate_tanh(t + 1, 1 - par)
                    when_new(act, t + 1, split_down)

            split(0, 0, "gate")
            split(0, 0, "up")
            x_half(0, 0, 0)
            x_half(0, 0, 1)
            split_down(0, 0)
            x_half(1, 1, 0)
            x_half(1, 1, 1)
            when_new(act, 1, split, "gate")
            gate_tanh(0, 0)
            when_new(act, 1, split, "up")
            t = each_pair(act, pair)
            for par in range(2):
                hidden(t + par, par)
                y_half(t + par, 0)
                y_half(t + par, 1)
                if par == 0:
                    gate_tanh(t + 1, 1)
                    when_new(act, t + 1, split_down)
            for p in range(2):
                act.wait_ge(s_o[p].sem, s_o[p].at(t + 2))
            act.sem_inc(s_pass, 1)

        @block.gpsimd
        def _(pool):
            for s in (s_t, s_tc, s_gu, s_h1, s_h, s_ht, s_hc, s_dn, s_y):
                pool.sem_inc(s.sem, s.credit)
            for s in s_o:
                pool.sem_inc(s.sem, 16)
            nc.gpsimd.memset(zero[:, :], 0.0).then_inc(s_zero.sem, s_zero.unit)

            def rest_down(e, t):
                for k in POOL_KS:
                    pool.wait_ge(s_dh.sem, s_dh.at(KF * e + k + 1))
                    nc.gpsimd.tensor_tensor(w["down"][L_][:, k, :], ew["down"][:, k, :], w["down"][H_][:, k, :], ALU.subtract).then_inc(s_dp.sem, s_dp.unit)

            def fetch(t, par):
                pool.wait_ge(s_t.sem, s_t.at(2 * (t - 1)))
                nc.gpsimd.tensor_copy(ids[:, par:par + 1], route["ids"][:, ds(t, 1)]).then_inc(s_id.sem, s_id.unit)
                pool.wait_ge(s_id.sem, s_id.at(t + 1))
                pool.sem_inc(s_pass, 1)
                nc.gpsimd.indirect_dma_start(
                    out=xg[:, par, :], out_offset=None, in_=dram["u2"],
                    in_offset=bass.IndirectOffsetOnAxis(ap=ids[:, par:par + 1], axis=0)).then_inc(s_x[par].sem, s_x[par].unit)

            def pair(t0):
                for par in range(2):
                    fetch(t0 + par, par)
                    when_new(pool, t0 + par - 2, rest_down)

            fetch(0, 0)
            fetch(1, 1)
            fetch(2, 0)
            rest_down(0, 0)
            fetch(3, 1)
            when_new(pool, 1, rest_down)
            t = each_pair(pool, pair, 2)
            pair(t)
            for par in range(2):
                when_new(pool, t + par, rest_down)

        @block.vector
        def _(v):
            def rest(e, t, name):
                first = GUC // 2 if name == "up" else 0
                for i in range(GUC // 2):
                    v.wait_ge(s_wh.sem, s_wh.at(GUC * e + first + i + 1))
                    nc.vector.tensor_tensor(w[name][L_][:, 2 * i:2 * i + 2, :], ew[name][:, 2 * i:2 * i + 2, :], w[name][H_][:, 2 * i:2 * i + 2, :],
                                            ALU.subtract).then_inc(s_wl.sem, s_wl.unit)

            def rest_down(e, t):
                for k in VEC_KS:
                    v.wait_ge(s_dh.sem, s_dh.at(KF * e + k + 1))
                    nc.vector.tensor_tensor(w["down"][L_][:, k, :], ew["down"][:, k, :], w["down"][H_][:, k, :], ALU.subtract).then_inc(s_dl.sem, s_dl.unit)

            def x_half(t, par, half):
                v.wait_ge(s_xh.sem, s_xh.at(2 * t + half + 1))
                blocks = slice(4 * half, 4 * half + 4)
                nc.vector.tensor_tensor(xT[L_][:, par, blocks, :], psT[:, :, :], xT[H_][:, par, blocks, :], ALU.subtract).then_inc(s_tc.sem, s_tc.unit)

            def hidden(t, par):
                v.wait_ge(s_th.sem, s_th.at(t + 1))
                nc.vector.scalar_tensor_tensor(out=th2[:, :], in0=th[:, :], scalar=1.0, in1=psG[:, par, 0, :],
                                                         op0=ALU.add, op1=ALU.mult).then_inc(s_h1.sem, s_h1.unit)
                v.wait_ge(s_h1.sem, s_h1.at(t + 1))
                v.wait_ge(s_ht.sem, s_ht.at(t))
                nc.vector.scalar_tensor_tensor(out=hs[:, :], in0=th2[:, :], scalar=0.5, in1=psG[:, par, 1, :],
                                                        op0=ALU.mult, op1=ALU.mult).then_inc(s_h.sem, s_h.unit)

            def hidden_rest(t, par):
                v.wait_ge(s_hh.sem, s_hh.at(t + 1))
                nc.vector.tensor_tensor(hT[L_][:, par, :, :], psH[:, :, :], hT[H_][:, par, :, :], ALU.subtract).then_inc(s_hc.sem, s_hc.unit)

            def pair(t0):
                for par in range(2):
                    t = t0 + par
                    hidden_rest(t, par)
                    x_half(t + 2, par, 0)
                    when_new(v, t + 2, rest, "gate")
                    x_half(t + 2, par, 1)
                    when_new(v, t + 2, rest, "up")
                    hidden(t + 1, 1 - par)
                    when_new(v, t + 1, rest_down)

            rest(0, 0, "gate")
            rest(0, 0, "up")
            x_half(0, 0, 0)
            x_half(0, 0, 1)
            rest_down(0, 0)
            x_half(1, 1, 0)
            x_half(1, 1, 1)
            when_new(v, 1, rest, "gate")
            hidden(0, 0)
            when_new(v, 1, rest, "up")
            t = each_pair(v, pair)
            hidden_rest(t, 0)
            hidden(t + 1, 1)
            when_new(v, t + 1, rest_down)
            hidden_rest(t + 1, 1)

        @block.tensor
        def _(pe):
            def turn(t, par, half):
                pe.wait_ge(s_x[par].sem, s_x[par].at(t // 2 + 1))
                pe.wait_ge(s_tc.sem, s_tc.at(2 * t + half))
                for b in range(4):
                    k = 4 * half + b
                    last = nc.tensor.transpose(psT[:, b, :], xg[:, par, k * P:(k + 1) * P], ident[:, :])
                last.then_inc(s_t.sem, s_t.unit)

            def product(dst, left, right, first, last):
                nc.tensor.matmul(dst, left[H_], right[H_], start=first, stop=False)
                nc.tensor.matmul(dst, left[L_], right[H_], start=False, stop=False)
                return nc.tensor.matmul(dst, left[H_], right[L_], start=False, stop=last)

            def up(t, par):
                e = pe.value_load(route["expert"][0:1, ds(t, 1)], min_val=0, max_val=NE - 1)
                pe.wait_ge(s_tc.sem, s_tc.at(2 * t + 2))
                pe.wait_ge(s_h.sem, s_h.at(t - 1))
                for j, name in enumerate(("gate", "up")):
                    for k in range(KD):
                        if k % 2 == 0:
                            pe.wait_ge(s_wl.sem, s_wl.at(GUC * e + (j * KD + k) // 2 + 1))
                        last = product(psG[:, par, j, :], [x[:, par, k, :] for x in xT], [x[:, k, :] for x in w[name]],
                                       k == 0, k == KD - 1)
                last.then_inc(s_gu.sem, s_gu.unit)

            def down(t, par, turn_next):
                pe.wait_ge(s_h.sem, s_h.at(t + 1))
                pe.wait_ge(s_hc.sem, s_hc.at(t))
                for k in range(KF):
                    last = nc.tensor.transpose(psH[:, k, :], hs[:, k * P:(k + 1) * P], ident[:, :])
                last.then_inc(s_ht.sem, s_ht.unit)
                e = pe.value_load(route["expert"][0:1, ds(t, 1)], min_val=0, max_val=NE - 1)
                for n in range(2):
                    if turn_next:
                        turn(t + 2, par, n)
                    pe.wait_ge(s_hc.sem, s_hc.at(t + 1))
                    pe.wait_ge(s_y.sem, s_y.at(2 * t + n - 1))
                    if n == 0:
                        pe.wait_ge(s_dl.sem, s_dl.at(len(VEC_KS) * (e + 1)))
                        pe.wait_ge(s_dp.sem, s_dp.at(len(POOL_KS) * (e + 1)))
                    for k in range(KF):
                        last = product(psY[:, n, :], [x[:, par, k, :] for x in hT], [x[:, k, n * 512:(n + 1) * 512] for x in w["down"]],
                                       k == 0, k == KF - 1)
                    last.then_inc(s_dn.sem, s_dn.unit)

            def pair(t0):
                for par in range(2):
                    up(t0 + par + 1, 1 - par)
                    down(t0 + par, par, True)

            turn(0, 0, 0)
            turn(0, 0, 1)
            up(0, 0)
            turn(1, 1, 0)
            turn(1, 1, 1)
            t = each_pair(pe, pair)
            up(t + 1, 1)
            down(t, 0, False)
            down(t + 1, 1, False)


def finish(nc, a, out, dram, route):
    with ExitStack() as ctx:
        new_sem = block_semaphores(nc, ctx)
        sb = lambda n, s, dt=F32: ctx.enter_context(nc.sbuf_tensor(n, s, dt))
        S = lambda n, unit=1, credit=0: Sem(new_sem(n), unit, credit)
        s_pass = new_sem("f_pass")
        gt = sb("f_gt", [P, D])
        gq = sb("f_gq", [NS, D])
        lng = sb("f_lng", [P, D])
        lnb = sb("f_lnb", [P, D])
        idx = sb("f_idx", [P, 2, 2], I32)
        y1 = sb("f_y1", [P, 2, D])
        y2 = sb("f_y2", [P, 2, D])
        x1 = sb("f_x1", [P, 2, D])
        z = sb("f_z", [P, 2, D])
        o = sb("f_o", [P, 2, D])
        stt = sb("f_st", [P, 2, 6])
        mv = sb("f_mv", [P, 2])
        rs = sb("f_rs", [P, 1])
        half = sb("f_half", [P, 1])
        s_c = S("f_c", 16)
        s_h = S("f_h")
        s_ix = S("f_ix")
        s_y = [S(f"f_y{p}", 16) for p in range(2)]
        s_x = [S(f"f_x{p}", 16) for p in range(2)]
        s_ch = new_sem("f_ch")
        s_z = S("f_sz", 1, 2)
        s_var = S("f_var")
        s_rs = S("f_rs")
        s_xn = S("f_xn")
        s_gain = S("f_gain")
        s_o = S("f_so", 1, 2)
        s_w1 = S("f_w1")
        s_out = [S(f"f_out{p}", 16, 1) for p in range(2)]
        block = ctx.enter_context(nc.Block())
        modrow = dram["mod"]
        J = 5
        yp = out["y_p"].rearrange("o s d -> (o s) d")
        ys = out["y_s"].rearrange("b t d -> (b t) d")

        @block.sync
        def _(sp):
            sp.dma_start(gt[:, :], modrow[0:1, J * D:(J + 1) * D].to_broadcast([P, D])).then_inc(s_c.sem, s_c.unit)
            for b in range(B):
                sp.dma_start(gq[TS * b:TS * (b + 1), :], modrow[1 + b:2 + b, J * D:(J + 1) * D].to_broadcast([TS, D])).then_inc(s_c.sem, s_c.unit)
            sp.dma_start(lng[:, :], a["ln2_g"].rearrange("(o n) -> o n", o=1).to_broadcast([P, D])).then_inc(s_c.sem, s_c.unit)
            sp.dma_start(lnb[:, :], a["ln2_b"].rearrange("(o n) -> o n", o=1).to_broadcast([P, D])).then_inc(s_c.sem, s_c.unit)

            def load(t, par, rows):
                sp.wait_ge(s_z.sem, s_z.at(t - 1))
                sp.dma_start(x1[0:rows, par, :], dram["x1"][ds(t * P, rows), :]).then_inc(s_x[par].sem, s_x[par].unit)

            def store(t, par, rows):
                sp.wait_ge(s_o.sem, s_o.at(t + 1))
                sp.dma_start(yp[ds(t * P, P), :] if rows == P else ys, o[0:rows, par, :]).then_inc(s_out[par].sem, s_out[par].unit)

            load(0, 0, P)
            load(1, 1, P)
            with sp.Fori(0, NT // 2 - 1) as i:
                for par in range(2):
                    load(2 * i + par + 2, par, P)
                    store(2 * i + par, par, P)
            load(NT, 0, NS)
            store(NT - 2, 0, P)
            store(NT - 1, 1, P)
            store(NT, 0, NS)
            sp.wait_ge(s_out[0].sem, s_out[0].at(NT // 2 + 1))
            sp.wait_ge(s_out[1].sem, s_out[1].at(NT // 2))

        @block.scalar
        def _(act):
            def tile(t, par, rows):
                act.wait_ge(s_y[par].sem, s_y[par].at(2 * (t // 2) + 2))
                nc.scalar.activation(y1[0:rows, par, :], y1[0:rows, par, :], ACT.Copy,
                                     scale=route["w"][0:rows, 0, ds(t, 1)]).then_inc(s_w1.sem, s_w1.unit)

            with act.Fori(0, NT // 2) as i:
                for par in range(2):
                    tile(2 * i + par, par, P)
            tile(NT, 0, NS)

        @block.gpsimd
        def _(pool):
            for s in (s_z, s_o):
                pool.sem_inc(s.sem, s.credit)
            for s in s_out:
                pool.sem_inc(s.sem, 16)
            nc.gpsimd.memset(half[:, :], -0.5).then_inc(s_h.sem, s_h.unit)

            def fetch(t, par, rows):
                pool.wait_ge(s_z.sem, s_z.at(t - 1))
                nc.gpsimd.tensor_copy(idx[0:rows, par, :], route["slot"][0:rows, :, ds(t, 1)].rearrange("p k o -> p (k o)")).then_inc(s_ix.sem, s_ix.unit)
                pool.wait_ge(s_ix.sem, s_ix.at(t + 1))
                pool.sem_inc(s_pass, 1)
                for k, y in enumerate((y1, y2)):
                    nc.gpsimd.indirect_dma_start(
                        out=y[0:rows, par, :], out_offset=None, in_=dram["y"],
                        in_offset=bass.IndirectOffsetOnAxis(ap=idx[0:rows, par, k:k + 1], axis=0)).then_inc(s_y[par].sem, s_y[par].unit)

            def deviation(t, rows):
                pool.wait_ge(s_var.sem, s_var.at(t + 1))
                nc.gpsimd.tensor_tensor(rs[0:rows, :], mv[0:rows, 1:2], half[0:rows, :], ALU.pow).then_inc(s_rs.sem, s_rs.unit)

            def gain(t, par, rows):
                pool.wait_ge(s_xn.sem, s_xn.at(t + 1))
                pool.wait_ge(s_out[par].sem, s_out[par].at(t // 2))
                nc.gpsimd.tensor_tensor(o[0:rows, par, :], z[0:rows, par, :], lng[0:rows, :], ALU.mult).then_inc(s_gain.sem, s_gain.unit)

            fetch(0, 0, P)
            fetch(1, 1, P)
            pool.wait_ge(s_h.sem, s_h.at(1))
            pool.wait_ge(s_c.sem, s_c.at(3 + B))
            with pool.Fori(0, NT // 2 - 1) as i:
                for par in range(2):
                    deviation(2 * i + par, P)
                    fetch(2 * i + par + 2, par, P)
                    gain(2 * i + par, par, P)
            deviation(NT - 2, P)
            fetch(NT, 0, NS)
            gain(NT - 2, 0, P)
            deviation(NT - 1, P)
            gain(NT - 1, 1, P)
            deviation(NT, NS)
            gain(NT, 0, NS)

        @block.vector
        def _(v):
            st = Steps(v, s_ch)
            v.wait_ge(s_c.sem, s_c.at(3 + B))

            def combine(t, par, rows):
                zt = z[0:rows, par, :]
                v.wait_ge(s_w1.sem, s_w1.at(t + 1))
                if not isinstance(t, int) or t >= 2:
                    v.wait_ge(s_gain.sem, s_gain.at(t - 1))
                st.link(nc.vector.scalar_tensor_tensor(out=zt, in0=y2[0:rows, par, :], scalar=route["w"][0:rows, 1, ds(t, 1)],
                                                       in1=y1[0:rows, par, :], op0=ALU.mult, op1=ALU.add))
                st.link(nc.vector.tensor_tensor(zt, zt, (gt if rows == P else gq)[0:rows, :], ALU.mult))
                v.wait_ge(s_x[par].sem, s_x[par].at(t // 2 + 1))
                nc.vector.scalar_tensor_tensor(out=zt, in0=x1[0:rows, par, :], scalar=ALPHA, in1=zt, op0=ALU.mult, op1=ALU.add).then_inc(s_z.sem, s_z.unit)
                v.wait_ge(s_z.sem, s_z.at(t + 1))
                for j in range(2):
                    st.after(nc.vector.bn_stats(stt[0:rows, j, :], z[0:rows, par, j * 512:(j + 1) * 512]))
                st.last()
                v.sem_inc(s_pass, 1)
                st.link(nc.vector.bn_aggr(mv[0:rows, :], stt[0:rows, :, :]))
                nc.vector.tensor_scalar(mv[0:rows, 1:2], mv[0:rows, 1:2], EPS, None, ALU.add).then_inc(s_var.sem, s_var.unit)

            def shift(t, par, rows):
                v.wait_ge(s_gain.sem, s_gain.at(t + 1))
                nc.vector.tensor_tensor(o[0:rows, par, :], o[0:rows, par, :], lnb[0:rows, :], ALU.add).then_inc(s_o.sem, s_o.unit)

            def normalize(t, par, rows):
                v.wait_ge(s_rs.sem, s_rs.at(t + 1))
                nc.vector.tensor_scalar(z[0:rows, par, :], z[0:rows, par, :], mv[0:rows, 0:1], rs[0:rows, :], ALU.subtract, ALU.mult).then_inc(s_xn.sem, s_xn.unit)

            def step(t, par, rows):
                combine(t, par, rows)
                shift(t - 1, 1 - par, P)
                normalize(t, par, rows)

            combine(0, 0, P)
            normalize(0, 0, P)
            step(1, 1, P)
            st.enter(10)
            with v.Fori(1, NT // 2) as i:
                st.round(i - 1)
                for par in range(2):
                    step(2 * i + par, par, P)
            st.leave(NT // 2 - 1)
            step(NT, 0, NS)
            shift(NT, 0, NS)


def constants():
    f = np.float32
    k = {"k_ident": np.eye(P, dtype=f)}
    pos = np.zeros((NT + 1, P), f)
    pos[:NT] = np.arange(SEQ, dtype=f).reshape(NT, P)
    pos[NT, :NS] = PAST + np.arange(NS) % TS
    half = HD // 2
    inv = (f(10000.0) ** (-np.arange(half, dtype=f) * f(2.0) / f(HD))).astype(f)
    ang = pos[:, :, None] * inv
    c, s = np.cos(ang).astype(f), np.sin(ang).astype(f)
    k["k_cos"] = np.ascontiguousarray(c.transpose(1, 0, 2))
    k["k_sin"] = np.ascontiguousarray(np.concatenate([-s, s], -1).transpose(1, 0, 2))

    def bias(count):
        return np.where(count > 0, 8.0 * np.log(np.maximum(count, 1)), NEG).astype(f)

    def windows(dist):
        live = dist >= 0
        return live * ((dist <= 128).astype(int) + ((dist % 4 == 0) & (dist <= 512)) + ((dist % 16 == 0) & (dist <= 2048)))

    dist = np.arange(P)[:, None] + (NT - 1) * P - np.arange(SEQ)[None, :]
    k["k_bias"] = bias(windows(dist))
    p = np.arange(P)
    near = np.concatenate([PAST - NEAR + 4 * p + i for i in range(4)])
    far = np.concatenate([16 * np.arange(FARM) + i for i in range(TS)])
    cached = np.concatenate([near, far])
    t = np.arange(P) % TS
    c = np.arange(P) // NS
    sb_ = np.full((P, B // 4, SKEYS), NEG, f)
    for g in range(B // 4):
        sb_[:, g, :SKEYS - NS] = bias(windows(PAST + t[:, None] - cached[None, :]))
        n = np.arange(NS)
        own = n[None, :] // TS == 4 * g + c[:, None]
        sb_[:, g, SKEYS - NS:] = bias(windows(t[:, None] - n[None, :] % TS) * own)
    k["k_sbias"] = sb_
    h = (np.arange(P) % NS) // TS
    k["k_own"] = (h[:, None] == np.arange(DB)[None, :] // HD).astype(f)
    k["k_sel"] = np.stack([(4 * g + c) * TS + t for g in range(B // 4)], 1)[:, :, None] == np.arange(NS)
    k["k_sel"] = k["k_sel"].astype(f)
    k["k_ranks"] = np.tile(np.arange(4, 0, -1, dtype=f), (P, 1))
    valid = np.ones((P, NT + 1), f)
    valid[NS:, NT] = 0
    k["k_valid"] = valid
    k["k_before"] = (p[:, None] < p[None, :]).astype(f)
    restart = np.ones((P, NE, NT + 1), f)
    restart[:, :, 0] = 0
    k["k_restart"] = restart
    k["k_steps"] = np.tile(P * np.arange(1, NT + 2, dtype=f), (P, 1))
    k["k_tiles"] = np.tile(np.arange(SLOT_TILES, dtype=f), (P, 1))
    k["k_tokid"] = (p[:, None] + P * np.arange(NT + 1)[None, :]).astype(f)
    return k


_INS = ["x_prompt", "x_sample", "state_conv", "state_rglru", "cache_win_k", "cache_win_v", "c_prompt", "c_sample",
        "w_ada", "b_ada", "w_in", "conv_w", "conv_b", "w_rg_a", "b_rg_a", "w_rg_x", "b_rg_x", "rg_lambda",
        "g_norm_a", "g_norm_b", "w_out", "ln1_g", "ln1_b", "w_router_group", "b_router_group",
        "w_router_expert", "b_router_expert", "w_exp_gate", "w_exp_up", "w_exp_down", "ln2_g", "ln2_b"]
_OUTS = [("y_p", (1, SEQ, D)), ("y_s", (B, TS, D)), ("conv_p", (1, CONVW - 1, DA)), ("h_p", (1, DA)),
         ("k_p", (1, SEQ, H, HD)), ("v_p", (1, SEQ, H, HD)), ("conv_s", (B, CONVW - 1, DA)), ("h_s", (B, DA)),
         ("k_s", (B, PAST, H, HD)), ("v_s", (B, PAST, H, HD))]
_SCRATCH = [("mod", (1 + B, NMOD * D)), ("x1", (TOK, D)), ("u2", (TOK, D)), ("tok", (SLOT_TILES * P, 1)),
            ("y", (SLOT_TILES * P, D)), ("k_new", (NS, DB)), ("v_new", (NS, DB))]


def kernel(**inputs):
    import concourse.bacc as bacc
    from concourse.bass_utils import run_bass_kernel_spmd

    nc = bacc.Bacc("TRN2", target_bir_lowering=False, num_devices=1)
    arrays = {f"in_{n}": np.ascontiguousarray(inputs[n]) for n in _INS}
    arrays.update({f"in_{n}": v for n, v in constants().items()})
    a = {n[3:]: nc.dram_tensor(n, v.shape, mybir.dt.from_np(v.dtype), kind="ExternalInput").ap() for n, v in arrays.items()}
    out = {n: nc.dram_tensor(f"out_{n}", s, F32, kind="ExternalOutput").ap() for n, s in _OUTS}
    dram = {n: nc.dram_tensor(f"scratch_{n}", s, F32, kind="Internal").ap() for n, s in _SCRATCH}
    program(nc, a, out, dram)
    r = run_bass_kernel_spmd(nc, [arrays], core_ids=[0])
    return tuple(r.results[0][f"out_{n}"] for n, _ in _OUTS)
```
